# Optimizing a Trainium2 kernel written in Bass

```python
import math
import jax, jax.numpy as jnp
from jax import lax
import numpy as np

D_MODEL = 1024
BATCH = 1
SEQ = 512
DEPTH = 1

CHUNK = 64
QBLK = 128
ATT_HEADS = 16
ATT_HEAD_DIM = 64
ATT_WIDTH = ATT_HEADS * ATT_HEAD_DIM
POOL_WINDOWS = (2, 4, 8, 16)
POOL_GROUPS = len(POOL_WINDOWS)
POOL_WIDTH = D_MODEL
POOL_GROUP_DIM = POOL_WIDTH // POOL_GROUPS
SSM_EXPAND = 2
SSM_INNER = SSM_EXPAND * D_MODEL
SSM_HEAD_DIM = 64
SSM_HEADS = SSM_INNER // SSM_HEAD_DIM
SSM_GROUPS = 4
SSM_HEADS_PER_GROUP = SSM_HEADS // SSM_GROUPS
SSM_STATE = 128
SSM_CONV = 4
SSM_CONV_DIM = SSM_INNER + 2 * SSM_GROUPS * SSM_STATE
N_BRANCHES = 3
N_EXPERTS = 16
N_EXPERT_GROUPS = 4
EXPERTS_PER_GROUP = N_EXPERTS // N_EXPERT_GROUPS
TOP_K = 2
EXPERT_DFF = 512
MOE_BLOCK = 256
DEEPNORM_ALPHA = (2 * DEPTH) ** 0.25
DEEPNORM_BETA = (8 * DEPTH) ** -0.25
LN_EPS = 1e-5
RMS_EPS = 1e-6
IN_SPLITS = (ATT_WIDTH, ATT_WIDTH, ATT_WIDTH, ATT_HEADS, POOL_WIDTH,
             SSM_INNER, SSM_CONV_DIM, SSM_HEADS, N_BRANCHES * D_MODEL)
IN_WIDTH = sum(IN_SPLITS)


def layer_norm(x, g=None, b=None):
    x32 = x.astype(jnp.float32)
    mu = jnp.mean(x32, axis=-1, keepdims=True)
    xc = x32 - mu
    y = xc * lax.rsqrt(jnp.mean(xc * xc, axis=-1, keepdims=True) + LN_EPS)
    if g is not None:
        y = y * g + b
    return y.astype(x.dtype)

def split_columns(proj):
    points, acc = [], 0
    for w in IN_SPLITS[:-1]:
        acc += w
        points.append(acc)
    return jnp.split(proj, points, axis=-1)

def forgetting_attention(q, k, v, log_f):
    S = q.shape[1]
    scale = ATT_HEAD_DIM ** -0.5
    F = jnp.transpose(jnp.cumsum(log_f, axis=1), (0, 2, 1))
    q, k, v = (jnp.transpose(t, (0, 2, 1, 3)) for t in (q, k, v))
    outs = []
    for blk in range(S // QBLK):
        s0, s1 = blk * QBLK, (blk + 1) * QBLK
        logits = jnp.einsum('bhqd,bhkd->bhqk', q[:, :, s0:s1], k[:, :, :s1]).astype(jnp.float32) * scale
        logits = logits + F[:, :, s0:s1, None] - F[:, :, None, :s1]
        mask = jnp.arange(s0, s1)[:, None] >= jnp.arange(s1)[None, :]
        p = jax.nn.softmax(jnp.where(mask, logits, -jnp.inf), axis=-1)
        outs.append(jnp.einsum('bhqk,bhkd->bhqd', p.astype(v.dtype), v[:, :, :s1]))
    o = jnp.concatenate(outs, axis=2)
    B_ = o.shape[0]
    return jnp.transpose(o, (0, 2, 1, 3)).reshape(B_, S, ATT_WIDTH)

def multiscale_pool(u, w_pool, pool_scale):
    Bsz, S, _ = u.shape
    u32 = u.astype(jnp.float32).reshape(Bsz, S, POOL_GROUPS, POOL_GROUP_DIM)
    cs = jnp.cumsum(u32, axis=1)
    pos = jnp.arange(1, S + 1, dtype=jnp.float32)[:, None]
    pooled = []
    for g, w in enumerate(POOL_WINDOWS):
        csg = cs[:, :, g]
        lagged = jnp.pad(csg, ((0, 0), (w, 0), (0, 0)))[:, :S]
        pooled.append((csg - lagged) / jnp.minimum(pos, float(w)) - u32[:, :, g])
    pooled = jnp.stack(pooled, axis=2)
    y = jnp.einsum('bsgc,gcd->bsgd', pooled, w_pool.astype(jnp.float32)).reshape(Bsz, S, POOL_WIDTH)
    return (y * pool_scale).astype(u.dtype)

def causal_depthwise_conv(u, w, b):
    out = lax.conv_general_dilated(
        u, w[:, None, :].astype(u.dtype), window_strides=(1,),
        padding=[(SSM_CONV - 1, 0)], dimension_numbers=('NWC', 'WIO', 'NWC'),
        feature_group_count=u.shape[-1])
    return out + b

def ssd_mixer(z, xbc, dt_raw, conv_w, conv_b, dt_bias, a_log, d_skip, norm_w, w_o):
    Bsz, S, _ = z.shape
    nc = S // CHUNK
    G, R, P, N, L = SSM_GROUPS, SSM_HEADS_PER_GROUP, SSM_HEAD_DIM, SSM_STATE, CHUNK
    f32 = jnp.float32
    xbc = jax.nn.silu(causal_depthwise_conv(xbc, conv_w, conv_b))
    xs, bm, cm = jnp.split(xbc, [SSM_INNER, SSM_INNER + G * N], axis=-1)
    xs = xs.astype(f32).reshape(Bsz, nc, L, G, R, P)
    bm = bm.astype(f32).reshape(Bsz, nc, L, G, N)
    cm = cm.astype(f32).reshape(Bsz, nc, L, G, N)
    dt = jax.nn.softplus(dt_raw.astype(f32) + dt_bias).reshape(Bsz, nc, L, G, R)
    a = -jnp.exp(a_log.astype(f32)).reshape(G, R)
    a_cs = jnp.cumsum(dt * a, axis=2)
    causal = jnp.tril(jnp.ones((L, L), bool))[:, :, None, None]
    seg = a_cs[:, :, :, None] - a_cs[:, :, None, :]
    decay = jnp.where(causal, jnp.exp(jnp.where(causal, seg, 0.0)), 0.0)
    cb = jnp.einsum('bclgn,bcsgn->bclsg', cm, bm)
    scores = cb[..., None] * decay * dt[:, :, None]
    y_diag = jnp.einsum('bclsgr,bcsgrp->bclgrp', scores, xs)
    decay_end = jnp.exp(a_cs[:, :, -1:] - a_cs)
    states = jnp.einsum('bcsgn,bcsgr,bcsgrp->bcgrpn', bm, decay_end * dt, xs)
    chunk_decay = jnp.exp(a_cs[:, :, -1])

    def step(h, inp):
        st, dec = inp
        return dec[..., None, None] * h + st, h

    h0 = jnp.zeros((Bsz, G, R, P, N), states.dtype)
    _, h_prev = lax.scan(step, h0, (jnp.moveaxis(states, 1, 0), jnp.moveaxis(chunk_decay, 1, 0)))
    h_prev = jnp.moveaxis(h_prev, 0, 1)
    y_off = jnp.einsum('bclgn,bcgrpn->bclgrp', cm, h_prev) * jnp.exp(a_cs)[..., None]
    y = y_diag + y_off + d_skip.astype(f32).reshape(G, R)[:, :, None] * xs
    y = y.reshape(Bsz, S, SSM_INNER) * jax.nn.silu(z.astype(f32))
    yg = y.reshape(Bsz, S, G, SSM_INNER // G)
    yg = yg * lax.rsqrt(jnp.mean(yg * yg, axis=-1, keepdims=True) + RMS_EPS)
    y = yg.reshape(Bsz, S, SSM_INNER) * norm_w
    return y.astype(z.dtype) @ w_o

def hybrid_mixer(h, w_in, b_forget, w_attn_o, w_pool, pool_scale, conv_w, conv_b,
                 dt_bias, a_log, d_skip, ssm_norm_w, w_ssm_o, w_out):
    Bsz, S, _ = h.shape
    proj = h @ w_in
    q, k, v, f_raw, u_pool, z, xbc, dt_raw, gate_raw = split_columns(proj)
    log_f = jax.nn.log_sigmoid(f_raw.astype(jnp.float32) + b_forget)
    hs = (Bsz, S, ATT_HEADS, ATT_HEAD_DIM)
    y_att = forgetting_attention(q.reshape(hs), k.reshape(hs), v.reshape(hs), log_f) @ w_attn_o
    y_pool = multiscale_pool(u_pool, w_pool, pool_scale)
    y_ssm = ssd_mixer(z, xbc, dt_raw, conv_w, conv_b, dt_bias, a_log, d_skip, ssm_norm_w, w_ssm_o)
    gates = jax.nn.sigmoid(gate_raw.astype(jnp.float32)).reshape(Bsz, S, N_BRANCHES, D_MODEL)
    merged = gates[:, :, 0] * y_att + gates[:, :, 1] * y_pool + gates[:, :, 2] * y_ssm
    return merged.astype(h.dtype) @ w_out

def grouped_moe(h, w_router, b_router, w1, w3, w2):
    Bsz, S, D = h.shape
    N = Bsz * S
    NK = N * TOP_K
    ht = h.reshape(N, D)
    probs = jax.nn.softmax((ht @ w_router).astype(jnp.float32), axis=-1)
    sel = probs + b_router
    group_score = lax.top_k(sel.reshape(N, N_EXPERT_GROUPS, EXPERTS_PER_GROUP), TOP_K)[0].sum(-1)
    g_idx = jnp.argmax(group_score, axis=-1)
    in_group = (jnp.arange(N_EXPERTS) // EXPERTS_PER_GROUP)[None, :] == g_idx[:, None]
    _, e_idx = lax.top_k(jnp.where(in_group, sel, -jnp.inf), TOP_K)
    gate_w = jnp.take_along_axis(probs, e_idx, axis=1)
    gate_w = gate_w / jnp.sum(gate_w, axis=-1, keepdims=True)
    e_flat = e_idx.reshape(NK)
    tok_flat = jnp.repeat(jnp.arange(N, dtype=jnp.int32), TOP_K)
    w_flat = gate_w.reshape(NK)
    order = jnp.argsort(e_flat)
    e_sorted, tok_sorted, w_sorted = e_flat[order], tok_flat[order], w_flat[order]
    counts = jnp.bincount(e_flat, length=N_EXPERTS)
    starts = jnp.cumsum(counts) - counts
    padded = ((counts + MOE_BLOCK - 1) // MOE_BLOCK) * MOE_BLOCK
    pends = jnp.cumsum(padded)
    pstarts = pends - padded
    dest = pstarts[e_sorted] + (jnp.arange(NK) - starts[e_sorted])
    P = NK + N_EXPERTS * MOE_BLOCK
    nblk = P // MOE_BLOCK
    slot_tok = jnp.full((P,), N, jnp.int32).at[dest].set(tok_sorted)
    slot_w = jnp.zeros((P,), jnp.float32).at[dest].set(w_sorted)
    blk_expert = jnp.minimum(
        jnp.searchsorted(pends, jnp.arange(nblk) * MOE_BLOCK, side='right'), N_EXPERTS - 1)
    x_pad = jnp.concatenate([ht, jnp.zeros((1, D), ht.dtype)], axis=0)
    xs = x_pad[slot_tok].reshape(nblk, MOE_BLOCK, D)

    def expert_block(args):
        xb, e = args
        return (jax.nn.silu(xb @ w1[e]) * (xb @ w3[e])) @ w2[e]

    ys = lax.map(expert_block, (xs, blk_expert)).reshape(P, D) * slot_w[:, None]
    out = jax.ops.segment_sum(ys, slot_tok, num_segments=N + 1)[:N]
    return out.reshape(Bsz, S, D).astype(h.dtype)

def first_inputs(seed: int = 0) -> dict:
    key = jax.random.key(seed)
    ks = jax.random.split(key, 26)

    def nrm(k, shape, scale):
        return jax.random.normal(k, shape, jnp.float32) * scale

    col_scale = jnp.concatenate([
        jnp.ones((2 * ATT_WIDTH,), jnp.float32),
        jnp.full((ATT_WIDTH,), DEEPNORM_BETA, jnp.float32),
        jnp.ones((IN_WIDTH - 3 * ATT_WIDTH,), jnp.float32)])
    dt0 = jnp.exp(jax.random.uniform(ks[9], (DEPTH, SSM_HEADS), jnp.float32,
                                     minval=math.log(1e-3), maxval=math.log(1e-1)))
    return {
        'x': nrm(ks[0], (BATCH, SEQ, D_MODEL), 1.0),
        'c': nrm(ks[1], (BATCH, D_MODEL), 1.0),
        'w_in': nrm(ks[2], (DEPTH, D_MODEL, IN_WIDTH), D_MODEL ** -0.5) * col_scale,
        'b_forget': 4.0 + nrm(ks[3], (DEPTH, ATT_HEADS), 0.5),
        'w_attn_o': nrm(ks[4], (DEPTH, ATT_WIDTH, D_MODEL), DEEPNORM_BETA * ATT_WIDTH ** -0.5),
        'w_pool': nrm(ks[5], (DEPTH, POOL_GROUPS, POOL_GROUP_DIM, POOL_GROUP_DIM), DEEPNORM_BETA * POOL_GROUP_DIM ** -0.5),
        'pool_scale': 1.0 + nrm(ks[6], (DEPTH, POOL_WIDTH), 0.1),
        'conv_w': nrm(ks[7], (DEPTH, SSM_CONV, SSM_CONV_DIM), SSM_CONV ** -0.5),
        'conv_b': nrm(ks[8], (DEPTH, SSM_CONV_DIM), 0.02),
        'dt_bias': dt0 + jnp.log(-jnp.expm1(-dt0)),
        'a_log': jnp.log(jax.random.uniform(ks[10], (DEPTH, SSM_HEADS), jnp.float32, minval=1.0, maxval=16.0)),
        'd_skip': 1.0 + nrm(ks[11], (DEPTH, SSM_HEADS), 0.1),
        'ssm_norm_w': 1.0 + nrm(ks[12], (DEPTH, SSM_INNER), 0.1),
        'w_ssm_o': nrm(ks[13], (DEPTH, SSM_INNER, D_MODEL), DEEPNORM_BETA * SSM_INNER ** -0.5),
        'w_out': nrm(ks[14], (DEPTH, D_MODEL, D_MODEL), DEEPNORM_BETA * D_MODEL ** -0.5),
        'w_ada': nrm(ks[15], (DEPTH, D_MODEL, 6 * D_MODEL), D_MODEL ** -0.5),
        'b_ada': nrm(ks[16], (DEPTH, 6 * D_MODEL), 0.02),
        'ln_mix_g': 1.0 + nrm(ks[17], (DEPTH, D_MODEL), 0.1),
        'ln_mix_b': nrm(ks[18], (DEPTH, D_MODEL), 0.02),
        'ln_ffn_g': 1.0 + nrm(ks[19], (DEPTH, D_MODEL), 0.1),
        'ln_ffn_b': nrm(ks[20], (DEPTH, D_MODEL), 0.02),
        'w_router': nrm(ks[21], (D_MODEL, N_EXPERTS), D_MODEL ** -0.5),
        'b_router': nrm(ks[22], (N_EXPERTS,), 0.01),
        'w_exp_gate': nrm(ks[23], (DEPTH, N_EXPERTS, D_MODEL, EXPERT_DFF), DEEPNORM_BETA * D_MODEL ** -0.5),
        'w_exp_up': nrm(ks[24], (DEPTH, N_EXPERTS, D_MODEL, EXPERT_DFF), DEEPNORM_BETA * D_MODEL ** -0.5),
        'w_exp_down': nrm(ks[25], (DEPTH, N_EXPERTS, EXPERT_DFF, D_MODEL), DEEPNORM_BETA * EXPERT_DFF ** -0.5),
    }

def first_block(x, c, w_in, b_forget, w_attn_o, w_pool, pool_scale, conv_w, conv_b,
              dt_bias, a_log, d_skip, ssm_norm_w, w_ssm_o, w_out, w_ada, b_ada,
              ln_mix_g, ln_mix_b, ln_ffn_g, ln_ffn_b, w_router, b_router,
              w_exp_gate, w_exp_up, w_exp_down):
    cond = jax.nn.silu(c)
    for l in range(DEPTH):
        mod = cond @ w_ada[l] + b_ada[l]
        sh_m, sc_m, g_m, sh_f, sc_f, g_f = jnp.split(mod[:, None, :], 6, axis=-1)
        h = layer_norm(x) * (1.0 + sc_m) + sh_m
        mix = hybrid_mixer(h, w_in[l], b_forget[l], w_attn_o[l], w_pool[l], pool_scale[l],
                           conv_w[l], conv_b[l], dt_bias[l], a_log[l], d_skip[l],
                           ssm_norm_w[l], w_ssm_o[l], w_out[l])
        x = layer_norm(DEEPNORM_ALPHA * x + g_m * mix, ln_mix_g[l], ln_mix_b[l])
        h = layer_norm(x) * (1.0 + sc_f) + sh_f
        ffn = grouped_moe(h, w_router, b_router, w_exp_gate[l], w_exp_up[l], w_exp_down[l])
        x = layer_norm(DEEPNORM_ALPHA * x + g_f * ffn, ln_ffn_g[l], ln_ffn_b[l])
    return x


DEPTH_2 = 2

N_MIXERS = 2
N_MLA = (DEPTH_2 + 1) // 2
N_SSM = DEPTH_2 // 2
MLA_HEADS = 8
QK_NOPE = 128
QK_ROPE = 64
V_DIM = 128
Q_LORA = 256
KV_LORA = 128
ROPE_THETA = 10000.0
Q_BLOCK = 128
SSM_WIDTH = D_MODEL
GROUP_CH = 16
N_GROUPS = SSM_WIDTH // GROUP_CH
STATE = 64
DT_MIN = 0.001
DT_MAX = 0.1
D_FF = 4 * D_MODEL
ALPHA = (2 * DEPTH_2) ** 0.25
BETA = (8 * DEPTH_2) ** -0.25


def layer_norm_2(x, g, b):
    xf = x.astype(jnp.float32)
    mu = jnp.mean(xf, axis=-1, keepdims=True)
    var = jnp.mean(jnp.square(xf - mu), axis=-1, keepdims=True)
    y = (xf - mu) * lax.rsqrt(var + LN_EPS) * g.astype(jnp.float32) + b.astype(jnp.float32)
    return y.astype(x.dtype)

def rms_norm(x, g):
    xf = x.astype(jnp.float32)
    y = xf * lax.rsqrt(jnp.mean(jnp.square(xf), axis=-1, keepdims=True) + RMS_EPS) * g.astype(jnp.float32)
    return y.astype(x.dtype)

def rope_tables(positions):
    inv_freq = ROPE_THETA ** (-jnp.arange(0, QK_ROPE, 2, dtype=jnp.float32) / QK_ROPE)
    ang = positions.astype(jnp.float32)[..., None] * inv_freq
    return jnp.cos(ang), jnp.sin(ang)

def apply_rope(x, cos, sin):
    xf = x.astype(jnp.float32)
    x1, x2 = jnp.split(xf, 2, axis=-1)
    return jnp.concatenate([x1 * cos - x2 * sin, x1 * sin + x2 * cos], axis=-1).astype(x.dtype)

def mla_mixer(h, cos, sin, w_in, q_norm, w_qb, kv_norm, w_kvb, w_o):
    B, L, _ = h.shape
    z = h @ w_in
    cq = rms_norm(z[..., :Q_LORA], q_norm)
    ckv = rms_norm(z[..., Q_LORA:Q_LORA + KV_LORA], kv_norm)
    k_pe = apply_rope(z[..., Q_LORA + KV_LORA:], cos, sin)
    q = (cq @ w_qb).reshape(B, L, MLA_HEADS, QK_NOPE + QK_ROPE)
    q_nope = q[..., :QK_NOPE]
    q_pe = apply_rope(q[..., QK_NOPE:], cos[:, :, None, :], sin[:, :, None, :])
    kv = (ckv @ w_kvb).reshape(B, L, MLA_HEADS, QK_NOPE + V_DIM)
    k_nope = kv[..., :QK_NOPE]
    v = kv[..., QK_NOPE:]
    scale = 1.0 / math.sqrt(QK_NOPE + QK_ROPE)
    nb = L // Q_BLOCK
    qn_b = q_nope.reshape(B, nb, Q_BLOCK, MLA_HEADS, QK_NOPE).transpose(1, 0, 2, 3, 4)
    qp_b = q_pe.reshape(B, nb, Q_BLOCK, MLA_HEADS, QK_ROPE).transpose(1, 0, 2, 3, 4)
    k_idx = jnp.arange(L)

    def attend(args):
        qn, qp, start = args
        s = (jnp.einsum('bqhd,bkhd->bhqk', qn, k_nope)
             + jnp.einsum('bqhr,bkr->bhqk', qp, k_pe)).astype(jnp.float32) * scale
        q_idx = start + jnp.arange(Q_BLOCK)
        causal = k_idx[None, :] <= q_idx[:, None]
        s = jnp.where(causal, s, jnp.float32(-1e30))
        p = jax.nn.softmax(s, axis=-1).astype(v.dtype)
        return jnp.einsum('bhqk,bkhd->bqhd', p, v)

    o = lax.map(attend, (qn_b, qp_b, jnp.arange(nb) * Q_BLOCK))
    o = o.transpose(1, 0, 2, 3, 4).reshape(B, L, MLA_HEADS * V_DIM)
    return o @ w_o

def s5_mixer(h, w_in, log_dt, a_re, a_im, b_re, b_im, c_re, c_im, d_skip, w_glu, b_glu, w_out):
    B, L, _ = h.shape
    u = h @ w_in
    u32 = u.astype(jnp.float32).reshape(B, L, N_GROUPS, GROUP_CH)
    lr = a_re.astype(jnp.float32)
    li = a_im.astype(jnp.float32)
    dt = jnp.exp(log_dt.astype(jnp.float32))[:, None]
    mag = jnp.exp(lr * dt)
    ab_re = mag * jnp.cos(li * dt)
    ab_im = mag * jnp.sin(li * dt)
    den = lr * lr + li * li
    nr = ab_re - 1.0
    coef_re = ((nr * lr + ab_im * li) / den)[..., None]
    coef_im = ((ab_im * lr - nr * li) / den)[..., None]
    br = b_re.astype(jnp.float32)
    bi = b_im.astype(jnp.float32)
    bb_re = coef_re * br - coef_im * bi
    bb_im = coef_re * bi + coef_im * br
    bu_re = jnp.einsum('blgc,gpc->blgp', u32, bb_re)
    bu_im = jnp.einsum('blgc,gpc->blgp', u32, bb_im)
    a_re_t = jnp.broadcast_to(ab_re, (1, L, N_GROUPS, STATE))
    a_im_t = jnp.broadcast_to(ab_im, (1, L, N_GROUPS, STATE))

    def combine(e1, e2):
        a1r, a1i, b1r, b1i = e1
        a2r, a2i, b2r, b2i = e2
        return (a2r * a1r - a2i * a1i,
                a2r * a1i + a2i * a1r,
                a2r * b1r - a2i * b1i + b2r,
                a2r * b1i + a2i * b1r + b2i)

    _, _, xr, xi = lax.associative_scan(combine, (a_re_t, a_im_t, bu_re, bu_im), axis=1)
    y = (jnp.einsum('blgp,gcp->blgc', xr, c_re.astype(jnp.float32))
         - jnp.einsum('blgp,gcp->blgc', xi, c_im.astype(jnp.float32)))
    y = y + d_skip.astype(jnp.float32).reshape(N_GROUPS, GROUP_CH) * u32
    y = y.reshape(B, L, SSM_WIDTH).astype(h.dtype)
    g = jax.nn.gelu(y)
    z = g * jax.nn.sigmoid(g @ w_glu + b_glu)
    return z @ w_out

def sq_relu_mlp(h, w1, b1, w2, b2):
    a = jax.nn.relu(h @ w1 + b1)
    return (a * a) @ w2 + b2

def modulation(cs, w, b):
    m = cs @ w + b
    shift, scale, gate = jnp.split(m, 3, axis=-1)
    return shift[:, None, :], scale[:, None, :], gate[:, None, :]

def second_inputs(seed: int = 0) -> dict:
    key = jax.random.key(seed)
    ks = iter(jax.random.split(key, 40))
    f32 = jnp.float32
    nrm = lambda shape, s: jax.random.normal(next(ks), shape, f32) * s
    D = D_MODEL
    x = jax.random.normal(next(ks), (BATCH, SEQ, D), f32)
    c = jax.random.normal(next(ks), (BATCH, D), f32)
    offs = jax.random.randint(next(ks), (BATCH, 1), 0, 1024, dtype=jnp.int32)
    positions = offs + jnp.arange(SEQ, dtype=jnp.int32)[None, :]
    mla_w_in = nrm((N_MLA, D, Q_LORA + KV_LORA + QK_ROPE), D ** -0.5)
    mla_q_norm = 1.0 + nrm((N_MLA, Q_LORA), 0.02)
    mla_w_qb = nrm((N_MLA, Q_LORA, MLA_HEADS * (QK_NOPE + QK_ROPE)), Q_LORA ** -0.5)
    mla_kv_norm = 1.0 + nrm((N_MLA, KV_LORA), 0.02)
    mla_w_kvb = nrm((N_MLA, KV_LORA, MLA_HEADS * (QK_NOPE + V_DIM)), KV_LORA ** -0.5)
    mla_w_o = nrm((N_MLA, MLA_HEADS * V_DIM, D), BETA * (MLA_HEADS * V_DIM) ** -0.5)
    ssm_w_in = nrm((N_SSM, D, SSM_WIDTH), D ** -0.5)
    ssm_log_dt = jax.random.uniform(next(ks), (N_SSM, N_GROUPS), f32,
                                    math.log(DT_MIN), math.log(DT_MAX))
    n_idx = jnp.arange(STATE, dtype=f32)
    ssm_a_re = -0.5 + nrm((N_SSM, N_GROUPS, STATE), 0.01)
    ssm_a_im = math.pi * n_idx + nrm((N_SSM, N_GROUPS, STATE), 0.01)
    ssm_b_re = nrm((N_SSM, N_GROUPS, STATE, GROUP_CH), (2 * GROUP_CH) ** -0.5)
    ssm_b_im = nrm((N_SSM, N_GROUPS, STATE, GROUP_CH), (2 * GROUP_CH) ** -0.5)
    ssm_c_re = nrm((N_SSM, N_GROUPS, GROUP_CH, STATE), (2 * STATE) ** -0.5)
    ssm_c_im = nrm((N_SSM, N_GROUPS, GROUP_CH, STATE), (2 * STATE) ** -0.5)
    ssm_d = nrm((N_SSM, SSM_WIDTH), 1.0)
    ssm_w_glu = nrm((N_SSM, SSM_WIDTH, SSM_WIDTH), SSM_WIDTH ** -0.5)
    ssm_b_glu = nrm((N_SSM, SSM_WIDTH), 0.01)
    ssm_w_out = nrm((N_SSM, SSM_WIDTH, D), BETA * SSM_WIDTH ** -0.5)
    mlp_w1 = nrm((DEPTH_2, D, D_FF), D ** -0.5)
    mlp_b1 = nrm((DEPTH_2, D_FF), 0.01)
    mlp_w2 = nrm((DEPTH_2, D_FF, D), BETA * D_FF ** -0.5)
    mlp_b2 = nrm((DEPTH_2, D), 0.01)
    mod_mix_w = nrm((DEPTH_2, D, 3 * D), 0.2 * D ** -0.5)
    mod_mix_b = nrm((DEPTH_2, 3 * D), 0.01)
    mod_ffn_w = nrm((DEPTH_2, D, 3 * D), 0.2 * D ** -0.5)
    mod_ffn_b = nrm((DEPTH_2, 3 * D), 0.01)
    ln_mix_g = 1.0 + nrm((DEPTH_2, D), 0.02)
    ln_mix_b = nrm((DEPTH_2, D), 0.01)
    ln_ffn_g = 1.0 + nrm((DEPTH_2, D), 0.02)
    ln_ffn_b = nrm((DEPTH_2, D), 0.01)
    return {"x": x, "c": c, "positions": positions,
            "mla_w_in": mla_w_in, "mla_q_norm": mla_q_norm, "mla_w_qb": mla_w_qb,
            "mla_kv_norm": mla_kv_norm, "mla_w_kvb": mla_w_kvb, "mla_w_o": mla_w_o,
            "ssm_w_in": ssm_w_in, "ssm_log_dt": ssm_log_dt, "ssm_a_re": ssm_a_re,
            "ssm_a_im": ssm_a_im, "ssm_b_re": ssm_b_re, "ssm_b_im": ssm_b_im,
            "ssm_c_re": ssm_c_re, "ssm_c_im": ssm_c_im, "ssm_d": ssm_d,
            "ssm_w_glu": ssm_w_glu, "ssm_b_glu": ssm_b_glu, "ssm_w_out": ssm_w_out,
            "mlp_w1": mlp_w1, "mlp_b1": mlp_b1, "mlp_w2": mlp_w2, "mlp_b2": mlp_b2,
            "mod_mix_w": mod_mix_w, "mod_mix_b": mod_mix_b,
            "mod_ffn_w": mod_ffn_w, "mod_ffn_b": mod_ffn_b,
            "ln_mix_g": ln_mix_g, "ln_mix_b": ln_mix_b,
            "ln_ffn_g": ln_ffn_g, "ln_ffn_b": ln_ffn_b}

def second_block(x, c, positions,
              mla_w_in, mla_q_norm, mla_w_qb, mla_kv_norm, mla_w_kvb, mla_w_o,
              ssm_w_in, ssm_log_dt, ssm_a_re, ssm_a_im, ssm_b_re, ssm_b_im,
              ssm_c_re, ssm_c_im, ssm_d, ssm_w_glu, ssm_b_glu, ssm_w_out,
              mlp_w1, mlp_b1, mlp_w2, mlp_b2,
              mod_mix_w, mod_mix_b, mod_ffn_w, mod_ffn_b,
              ln_mix_g, ln_mix_b, ln_ffn_g, ln_ffn_b):
    cs = jax.nn.silu(c)
    cos, sin = rope_tables(positions)
    for i in range(DEPTH_2):
        shift, scale, gate = modulation(cs, mod_mix_w[i], mod_mix_b[i])
        h = x * (1.0 + scale) + shift
        j = i // N_MIXERS
        if i % N_MIXERS == 0:
            y = mla_mixer(h, cos, sin, mla_w_in[j], mla_q_norm[j], mla_w_qb[j],
                          mla_kv_norm[j], mla_w_kvb[j], mla_w_o[j])
        else:
            y = s5_mixer(h, ssm_w_in[j], ssm_log_dt[j], ssm_a_re[j], ssm_a_im[j],
                         ssm_b_re[j], ssm_b_im[j], ssm_c_re[j], ssm_c_im[j], ssm_d[j],
                         ssm_w_glu[j], ssm_b_glu[j], ssm_w_out[j])
        x = layer_norm_2(ALPHA * x + (1.0 + gate) * y, ln_mix_g[i], ln_mix_b[i])
        shift, scale, gate = modulation(cs, mod_ffn_w[i], mod_ffn_b[i])
        h = x * (1.0 + scale) + shift
        y = sq_relu_mlp(h, mlp_w1[i], mlp_b1[i], mlp_w2[i], mlp_b2[i])
        x = layer_norm_2(ALPHA * x + (1.0 + gate) * y, ln_ffn_g[i], ln_ffn_b[i])
    return x


def setup_inputs(seed=0):
    out = dict(first_inputs(seed))
    for name, value in second_inputs(seed + 1).items():
        if name != "x":
            out[name + "_2"] = value
    return out


def reference(
    x, c, w_in, b_forget, w_attn_o, w_pool, pool_scale, conv_w, conv_b, dt_bias, a_log, d_skip,
    ssm_norm_w, w_ssm_o, w_out, w_ada, b_ada, ln_mix_g, ln_mix_b, ln_ffn_g, ln_ffn_b, w_router,
    b_router, w_exp_gate, w_exp_up, w_exp_down, c_2, positions_2, mla_w_in_2, mla_q_norm_2,
    mla_w_qb_2, mla_kv_norm_2, mla_w_kvb_2, mla_w_o_2, ssm_w_in_2, ssm_log_dt_2, ssm_a_re_2,
    ssm_a_im_2, ssm_b_re_2, ssm_b_im_2, ssm_c_re_2, ssm_c_im_2, ssm_d_2, ssm_w_glu_2,
    ssm_b_glu_2, ssm_w_out_2, mlp_w1_2, mlp_b1_2, mlp_w2_2, mlp_b2_2, mod_mix_w_2, mod_mix_b_2,
    mod_ffn_w_2, mod_ffn_b_2, ln_mix_g_2, ln_mix_b_2, ln_ffn_g_2, ln_ffn_b_2,
):
    x = first_block(
        x, c, w_in, b_forget, w_attn_o, w_pool, pool_scale, conv_w, conv_b, dt_bias, a_log,
        d_skip, ssm_norm_w, w_ssm_o, w_out, w_ada, b_ada, ln_mix_g, ln_mix_b, ln_ffn_g,
        ln_ffn_b, w_router, b_router, w_exp_gate, w_exp_up, w_exp_down,
    )
    return second_block(
        x, c_2, positions_2, mla_w_in_2, mla_q_norm_2, mla_w_qb_2, mla_kv_norm_2, mla_w_kvb_2,
        mla_w_o_2, ssm_w_in_2, ssm_log_dt_2, ssm_a_re_2, ssm_a_im_2, ssm_b_re_2, ssm_b_im_2,
        ssm_c_re_2, ssm_c_im_2, ssm_d_2, ssm_w_glu_2, ssm_b_glu_2, ssm_w_out_2, mlp_w1_2,
        mlp_b1_2, mlp_w2_2, mlp_b2_2, mod_mix_w_2, mod_mix_b_2, mod_ffn_w_2, mod_ffn_b_2,
        ln_mix_g_2, ln_mix_b_2, ln_ffn_g_2, ln_ffn_b_2,
    )


_drawn_inputs = setup_inputs


def setup_inputs(seed=0):
    import zlib

    import numpy as np

    out = dict(_drawn_inputs(seed))
    spreads = {}
    factors = {'b_forget': 44.68,
     'pool_scale': 3.384,
     'conv_b': 8.0,
     'd_skip': 6.687,
     'ssm_norm_w': 3.836,
     'b_ada': 2.943,
     'ln_ffn_b': 2.697,
     'mla_q_norm_2': 8.0,
     'mla_kv_norm_2': 8.0,
     'ssm_log_dt_2': 61.976,
     'ssm_a_re_2': 64.0,
     'ssm_a_im_2': 55.736,
     'ssm_b_re_2': 64.0,
     'ssm_b_im_2': 64.0,
     'ssm_c_re_2': 64.0,
     'ssm_c_im_2': 64.0,
     'ssm_b_glu_2': 64.0,
     'mlp_b1_2': 8.0,
     'mlp_b2_2': 6.092,
     'mod_mix_b_2': 8.0,
     'mod_ffn_b_2': 5.072,
     'ln_mix_b_2': 3.735,
     'ln_ffn_b_2': 3.889}
    for name, (base, spread) in spreads.items():
        noise = np.random.default_rng([zlib.crc32(name.encode()), seed]).standard_normal(out[name].shape)
        drawn = base * np.exp(spread * noise) if base else spread * noise
        out[name] = __import__('jax').numpy.asarray(drawn.astype(out[name].dtype))
    for name, factor in factors.items():
        out[name] = (out[name] * factor).astype(out[name].dtype)
    return out
```

```python
from contextlib import ExitStack, contextmanager
import math

import concourse.bass as bass
from concourse import mybir

F32 = mybir.dt.float32
I32 = mybir.dt.int32
ALU = mybir.AluOpType
ACT = mybir.ActivationFunctionType
AX = mybir.AxisListType

P = 128
D = 1024
KD = D // P
T = 512
TB = T // P
STRIP = 512
FT = STRIP // P

HEADS, HD = 16, 64
G_SSM, R_SSM, P_SSM, N_SSM = 4, 8, 64, 128
SSM_INNER = G_SSM * R_SSM * P_SSM
KG = SSM_INNER // G_SSM // P
KI = SSM_INNER // P
CONV = 4
XBC_TILES = (SSM_INNER + 2 * G_SSM * N_SSM) // P
Q0, K0, V0 = 0, D, 2 * D
F0 = 3 * D
U0 = F0 + HEADS
Z0 = U0 + D
XBC0 = Z0 + SSM_INNER
B0 = XBC0 + SSM_INNER
C0 = B0 + G_SSM * N_SSM
DT0 = XBC0 + XBC_TILES * P
GATE0 = DT0 + G_SSM * R_SSM
IN_WIDTH = GATE0 + 3 * D
POOL_WINDOWS = (2, 4, 8, 16)
PAD = max(POOL_WINDOWS)
NE, EG, DFF = 16, 4, 512
KE = DFF // P
ALPHA_1 = 2 ** 0.25
LN_EPS, RMS_EPS = 1e-5, 1e-6

MLA_HEADS, NOPE, ROPE, VD = 8, 128, 64, 128
QL, KVL = 256, 128
GC, STATE = 16, 64
S5_GROUPS = D // GC
S5_TILES = S5_GROUPS * STATE // P
DF2 = 4 * D
K2 = DF2 // P
ALPHA_2 = 4 ** 0.25

NEG = -1e30
TWO_PI = 2 * math.pi
PI_SAFE = 3.1415925
PI_A = 6.28125
PI_B = 0.0019350051879882812
PI_C = TWO_PI - PI_A - PI_B
ROUND = 12582912.0

VECTORS = [
    ("c", 8), ("b_ada", 48), ("pool_scale", 8), ("conv_b", 24), ("ssm_norm_w", 16), ("ln_mix_g", 8), ("ln_mix_b", 8),
    ("conv_w", 96), ("ln_ffn_g", 8), ("ln_ffn_b", 8), ("c_2", 8), ("mla_kv_norm_2", 1), ("mla_q_norm_2", 2),
    ("mod_mix_b_2", 48), ("mod_ffn_b_2", 48), ("ssm_a_re_2", 32),
    ("mlp_b1_2", 64), ("mlp_b2_2", 16), ("ssm_a_im_2", 32), ("ssm_d_2", 8), ("ssm_b_glu_2", 8),
    ("ln_mix_g_2", 16), ("ln_mix_b_2", 16), ("ln_ffn_g_2", 16), ("ln_ffn_b_2", 16),
]


def vector_places():
    at, places = 0, {}
    for name, rows in VECTORS:
        if at % P + rows > P:
            at += P - at % P
        places[name] = (at, rows)
        at += rows
    return places, (at + P - 1) // P


class Steps:

    def __init__(self, eng, sem, base=0):
        self.eng, self.sem, self.base, self.n = eng, sem, base, 0

    def __call__(self, ins):
        ins.then_inc(self.sem, 1)
        self.n += 1
        self.eng.wait_ge(self.sem, self.base + self.n)


class Kernel:

    def __init__(self, nc, stack, ins):
        self.nc, self.stack, self.ins = nc, stack, ins
        self.finished = []
        self.ps = stack.enter_context(nc.psum_tensor("banks", [P, 8, 512], F32))

    def sb(self, name, shape, dt=F32, stack=None):
        return (stack or self.stack).enter_context(self.nc.sbuf_tensor(name, shape, dt))

    @contextmanager
    def stage(self, name, *sems, primed=()):
        with ExitStack() as stack:
            s = {x: stack.enter_context(self.nc.semaphore(f"{name}_{x}")) for x in sems}
            self.primed = [s[x] for x in primed]
            with self.nc.Block() as block:
                yield block, s, lambda n, shape, dt=F32: self.sb(f"{name}_{n}", shape, dt, stack)
            self.finished = list(s.values())

    def clear(self, sp):
        for x in self.finished:
            sp.sem_clear(x)
        for x in self.primed:
            sp.sem_inc(x, 1)


def constants_stage(k):
    nc, ps = k.nc, k.ps
    places, groups = vector_places()
    k.places = places
    k.ident = k.sb("ident", [P, P])
    k.ones = k.sb("ones", [P, P])
    k.future_mask = k.sb("future_mask", [P, P])
    k.past_cap = k.sb("past_cap", [P, P])
    k.cols = k.sb("cols", [P, groups * P])
    k.eps_ln = k.sb("eps_ln", [P, 1])
    k.eps_rms = k.sb("eps_rms", [P, 1])
    k.silu_c = k.sb("silu_c", [P, 2, KD])
    k.mod = k.sb("mod", [P, 48 + 4 * 24])
    k.x = k.sb("x", [P, KD, T])
    k.h = k.sb("h", [P, KD, T])
    k.neg_f = k.sb("neg_f", [HEADS, T])
    k.gate_t = k.neg_f
    k.w = k.sb("w", [P, 3, KD * STRIP])

    rows_of = {"conv_w": "k (j p) -> (k j) p", "ssm_a_re_2": "(j two) s -> j (two s)", "ssm_a_im_2": "(j two) s -> j (two s)"}

    with k.stage("constants", "rows_zeroed", "rows_loaded", "x_loaded", "pool_step", "consts_ready", "params_turned",
                 "params_copied", "x_turned", "x_copied", "sig_done", "vec_step") as (block, s, sb):
        rows = sb("rows", [P, groups, P])
        xt = sb("xt", [P, TB, D])
        sig = sb("sig", [P, 2, KD])

        @block.sync
        def _(sp):
            k.clear(sp)
            sp.dma_start(xt[:], k.ins["x"][0].rearrange("(b p) d -> p b d", p=P)).then_inc(s["x_loaded"], 16)
            sp.wait_ge(s["rows_zeroed"], 1)
            for name, (at, n) in places.items():
                a = k.ins[name]
                if name in ("conv_w", "ssm_a_re_2", "ssm_a_im_2"):
                    a = a[0].rearrange(rows_of[name], p=P) if name == "conv_w" else a[0].rearrange(rows_of[name], two=2)
                else:
                    a = a.rearrange("l (j p) -> (l j) p", p=P)
                sp.dma_start(rows[at % P:at % P + n, at // P, :], a).then_inc(s["rows_loaded"], 16)

        @block.gpsimd
        def _(pool):
            pool.memset(rows[:], 0.0).then_inc(s["rows_zeroed"], 1)
            pool.memset(k.ident[:], 0.0).then_inc(s["pool_step"], 1)
            pool.memset(k.ones[:], 1.0).then_inc(s["pool_step"], 1)
            pool.memset(k.future_mask[:], 0.0).then_inc(s["pool_step"], 1)
            pool.memset(k.past_cap[:], 0.0).then_inc(s["pool_step"], 1)
            pool.memset(k.eps_ln[:], LN_EPS).then_inc(s["pool_step"], 1)
            pool.memset(k.eps_rms[:], RMS_EPS).then_inc(s["pool_step"], 1)
            pool.wait_ge(s["pool_step"], 6)
            pool.affine_select(out=k.ident[:], in_=k.ident[:], compare_op=ALU.not_equal, fill=1.0, base=0,
                               pattern=[[-1, P]], channel_multiplier=1).then_inc(s["consts_ready"], 1)
            pool.affine_select(out=k.future_mask[:], in_=k.future_mask[:], compare_op=ALU.is_ge, fill=NEG, base=0,
                               pattern=[[-1, P]], channel_multiplier=1).then_inc(s["consts_ready"], 1)
            pool.affine_select(out=k.past_cap[:], in_=k.past_cap[:], compare_op=ALU.is_ge, fill=NEG, base=0,
                               pattern=[[1, P]], channel_multiplier=-1).then_inc(s["consts_ready"], 1)

        @block.tensor
        def _(pe):
            pe.wait_ge(s["consts_ready"], 3)
            pe.wait_ge(s["x_loaded"], 16)
            for c in range(KD):
                if c >= 4:
                    pe.wait_ge(s["x_copied"], c - 3)
                for b in range(TB):
                    mm = pe.transpose(ps[:, c % 4, b * P:(b + 1) * P], xt[:, b, c * P:(c + 1) * P], k.ident[:])
                mm.then_inc(s["x_turned"], 1)
            pe.wait_ge(s["rows_loaded"], 16 * len(places))
            for g in range(groups):
                mm = pe.transpose(ps[:, 4 + g // 4, (g % 4) * P:(g % 4 + 1) * P], rows[:, g, :], k.ident[:])
            mm.then_inc(s["params_turned"], 1)

        @block.scalar
        def _(act):
            for c in range(KD):
                act.wait_ge(s["x_turned"], c + 1)
                act.activation(k.x[:, c, :], ps[:, c % 4, :], ACT.Copy).then_inc(s["x_copied"], 1)
            act.wait_ge(s["params_turned"], 1)
            for g in range(0, groups, 4):
                n = min(4, groups - g) * P
                act.activation(k.cols[:, g * P:g * P + n], ps[:, 4 + g // 4, 0:n], ACT.Copy).then_inc(s["params_copied"], 1)
            act.wait_ge(s["params_copied"], (groups + 3) // 4)
            for j, name in enumerate(("c", "c_2")):
                at = places[name][0]
                act.activation(sig[:, j, :], k.cols[:, at:at + KD], ACT.Sigmoid).then_inc(s["sig_done"], 1)

        @block.vector
        def _(dve):
            dve.wait_ge(s["sig_done"], 2)
            for j, name in enumerate(("c", "c_2")):
                at = places[name][0]
                dve.tensor_tensor(k.silu_c[:, j, :], sig[:, j, :], k.cols[:, at:at + KD], ALU.mult).then_inc(s["vec_step"], 1)

    k.col = lambda name, j=0: k.cols[:, places[name][0] + j:places[name][0] + j + 1]


def strip(k, slot, kt=KD):
    return k.w[:, slot, :].rearrange("p (k n) -> p k n", k=kt)


def modulation_stage(k):
    ps = k.ps
    jobs = [(k.ins["w_ada"][0], 0, 6, 0, "b_ada", 0)]
    for i in range(2):
        jobs.append((k.ins["mod_mix_w_2"][i], 1, 3, 48 + 48 * i, "mod_mix_b_2", 24 * i))
        jobs.append((k.ins["mod_ffn_w_2"][i], 1, 3, 72 + 48 * i, "mod_ffn_b_2", 24 * i))
    with k.stage("modulation", "w_loaded0", "w_loaded1", "w_used0", "w_used1", "vec_step", primed=("w_used0", "w_used1")) as (block, s, sb):
        loaded, used = (s["w_loaded0"], s["w_loaded1"]), (s["w_used0"], s["w_used1"])

        @block.sync
        def _(sp):
            k.clear(sp)
            done = 0
            for w, _, pairs, *_ in jobs:
                with sp.Fori(0, pairs) as i:
                    for slot in range(2):
                        sp.wait_ge(used[slot], 1 + done + i)
                        sp.dma_start(strip(k, slot), w[:, bass.ds((2 * i + slot) * STRIP, STRIP)].rearrange(
                            "(k p) n -> p k n", p=P)).then_inc(loaded[slot], 16)
                done += pairs

        @block.tensor
        def _(pe):
            done = 0
            for _, c, pairs, col, *_ in jobs:
                with pe.Fori(0, pairs) as i:
                    for slot in range(2):
                        pe.wait_ge(loaded[slot], 16 * (done + i + 1))
                        for f in range(FT):
                            for kk in range(KD):
                                mm = pe.matmul(ps[:, 0, bass.ds(col + (2 * i + slot) * FT + f, 1)],
                                               strip(k, slot)[:, kk, f * P:(f + 1) * P], k.silu_c[:, c, kk:kk + 1],
                                               start=(kk == 0), stop=(kk == KD - 1))
                        mm.then_inc(used[slot], 1)
                done += pairs

        @block.vector
        def _(dve):
            total = sum(j[2] for j in jobs)
            for slot in range(2):
                dve.wait_ge(used[slot], 1 + total)
            for _, _, pairs, col, bias, at in jobs:
                n = pairs * 2 * FT
                b = k.places[bias][0] + at
                dve.tensor_tensor(k.mod[:, col:col + n], ps[:, 0, col:col + n], k.cols[:, b:b + n],
                                  ALU.add).then_inc(s["vec_step"], 1)
            dve.wait_ge(s["vec_step"], len(jobs))
            for first, n in ((8, 8), (32, 8)) + tuple((48 + 24 * j + 8, 16) for j in range(4)):
                dve.tensor_scalar(k.mod[:, first:first + n], k.mod[:, first:first + n], 1.0, None,
                                  ALU.add).then_inc(s["vec_step"], 1)


def norm_stage(k, name, src, dst, scale, shift):
    ps = k.ps
    with k.stage(name, "sum_done", "sq_done", "var_done", "std_done", "vec_step", "centred", "scaled", "out_done") as (block, s, sb):
        xc = sb("xc", [P, KD, T])
        sq = sb("sq", [P, KD, T])
        std = sb("std", [P, T])
        rstd = sb("rstd", [P, T])

        @block.sync
        def _(sp):
            k.clear(sp)

        @block.tensor
        def _(pe):
            for c in range(KD):
                mm = pe.matmul(ps[:, 0, :], k.ones[:], src[:, c, :], start=(c == 0), stop=(c == KD - 1))
            mm.then_inc(s["sum_done"], 1)
            for c in range(KD):
                pe.wait_ge(s["sq_done"], c + 1)
                mm = pe.matmul(ps[:, 1, :], k.ones[:], sq[:, c, :], start=(c == 0), stop=(c == KD - 1))
            mm.then_inc(s["var_done"], 1)

        @block.vector
        def _(dve):
            dve.wait_ge(s["sum_done"], 1)
            for c in range(KD):
                dve.scalar_tensor_tensor(out=xc[:, c, :], in0=ps[:, 0, :], scalar=-1.0 / D, in1=src[:, c, :],
                                         op0=ALU.mult, op1=ALU.add).then_inc(s["centred"], 1)
            dve.wait_ge(s["std_done"], 1)
            dve.reciprocal(rstd[:], std[:]).then_inc(s["vec_step"], 1)
            dve.wait_ge(s["vec_step"], 1)
            for c in range(KD):
                dve.tensor_tensor(xc[:, c, :], xc[:, c, :], rstd[:], ALU.mult).then_inc(s["scaled"], 1)

        @block.scalar
        def _(act):
            for c in range(KD):
                act.wait_ge(s["centred"], c + 1)
                act.activation(sq[:, c, :], xc[:, c, :], ACT.Square).then_inc(s["sq_done"], 1)
            act.wait_ge(s["var_done"], 1)
            act.activation(std[:], ps[:, 1, :], ACT.Sqrt, scale=1.0 / D, bias=k.eps_ln[:]).then_inc(s["std_done"], 1)
            for c in range(KD):
                act.wait_ge(s["scaled"], c + 1)
                act.activation(dst[:, c, :], xc[:, c, :], ACT.Identity, scale=scale(c), bias=shift(c)).then_inc(s["out_done"], 1)


def linear(k, block, s, src, pairs, x, finish, kt=KD, banks_of=None):
    ps = k.ps
    loaded, done, free = (s["w_loaded0"], s["w_loaded1"]), (s["tile_done0"], s["tile_done1"]), (s["tile_free0"], s["tile_free1"])
    ft = KD * STRIP // kt // P

    @block.sync
    def _(sp):
        k.clear(sp)
        with sp.Fori(0, pairs) as i:
            for slot in range(2):
                sp.wait_ge(done[slot], 1 + ft * i)
                sp.dma_start(strip(k, slot, kt), src(i, slot)).then_inc(loaded[slot], 16)

    @block.tensor
    def _(pe):
        with pe.Fori(0, pairs) as i:
            for slot in range(2):
                pe.wait_ge(loaded[slot], 16 * (i + 1))
                pe.wait_ge(free[slot], 1 + ft * i)
                for f in range(ft):
                    for kk in range(kt):
                        mm = pe.matmul(ps[:, slot * FT + f, :], strip(k, slot, kt)[:, kk, f * P:(f + 1) * P], x(kk),
                                       start=(kk == 0), stop=(kk == kt - 1))
                    mm.then_inc(done[slot], 1)


LINEAR_PRIMED = ("tile_done0", "tile_done1", "tile_free0", "tile_free1")
LINEAR = ("w_loaded0", "w_loaded1", "tile_done0", "tile_done1", "tile_free0", "tile_free1")


def columns(w, first, n=STRIP):
    return w[:, bass.ds(first, n)].rearrange("(k p) n -> p k n", p=P)


def forget_stage(k):
    ps, w_in = k.ps, k.ins["w_in"][0]
    with k.stage("forget", "loaded", "f_done", "act_step", "vec_step") as (block, s, sb):
        wf = sb("wf", [P, KD, HEADS])
        bias = sb("bias", [HEADS, 1])
        v, e, ln = sb("v", [HEADS, T]), sb("e", [HEADS, T]), sb("ln", [HEADS, T])
        ones = sb("ones", [HEADS, T])

        @block.sync
        def _(sp):
            k.clear(sp)
            sp.dma_start(wf[:], columns(w_in, F0, HEADS)).then_inc(s["loaded"], 16)
            sp.dma_start(bias[:], k.ins["b_forget"].rearrange("l h -> h l")).then_inc(s["loaded"], 16)

        @block.tensor
        def _(pe):
            pe.wait_ge(s["loaded"], 32)
            for kk in range(KD):
                mm = pe.matmul(ps[0:HEADS, 0, :], wf[:, kk, :], k.h[:, kk, :], start=(kk == 0), stop=(kk == KD - 1))
            mm.then_inc(s["f_done"], 1)

        @block.scalar
        def _(act):
            act.wait_ge(s["vec_step"], 3)
            act.activation(e[:], e[:], ACT.Exp).then_inc(s["act_step"], 1)
            act.wait_ge(s["act_step"], 1)
            act.activation(ln[:], e[:], ACT.Ln, bias=1.0).then_inc(s["act_step"], 1)

        @block.vector
        def _(dve):
            step = Steps(dve, s["vec_step"])
            step(dve.memset(ones[:], 1.0))
            dve.wait_ge(s["loaded"], 32)
            dve.wait_ge(s["f_done"], 1)
            step(dve.tensor_scalar(v[:], ps[0:HEADS, 0, :], bias[:], None, ALU.add))
            step(dve.scalar_tensor_tensor(out=e[:], in0=v[:], scalar=-1.0, in1=v[:], op0=ALU.mult, op1=ALU.min))
            dve.wait_ge(s["act_step"], 2)
            step(dve.tensor_scalar(v[:], v[:], 0.0, None, ALU.min))
            step(dve.tensor_tensor(ln[:], ln[:], v[:], ALU.subtract))
            step(dve.tensor_tensor_scan(k.neg_f[:], ones[:], ln[:], 0.0, ALU.mult, ALU.add))


def scan_softmax(k, s, units, scores, p_tiles, pt_tiles, values, nmax, rsum, rinv):
    ps, n_units = k.ps, len(units)

    def tensor(pe, i):
        base = n_units * i

        def logits(n):
            if n >= 3:
                pe.wait_ge(s["exp_done"], 1 + base + n - 2)
            scores(pe, units[n], n % 3).then_inc(s["scores_done"], 1)

        def turn(n):
            pe.wait_ge(s["probs_done"], base + n + 1)
            if n >= 2:
                pe.wait_ge(s["turned_copied"], base + n - 1)
            for kb in range(units[n][1] + 1):
                mm = pe.transpose(ps[:, 3 + n % 2, kb * P:(kb + 1) * P], p_tiles[:, n % 3, kb * P:(kb + 1) * P], k.ident[:])
            mm.then_inc(s["turned"], 1)

        def weigh(n):
            rows, b = units[n]
            pe.wait_ge(s["turned_copied"], base + n + 1)
            if n == 0:
                pe.wait_ge(s["o_copied"], 1 + i)
            for kb in range(b + 1):
                mm = pe.matmul(ps[rows, 5, b * P:(b + 1) * P], values(units[n], kb), pt_tiles[:, n % 2, kb * P:(kb + 1) * P],
                               start=(kb == 0), stop=(kb == b))
            mm.then_inc(s["weighed"], 1)

        logits(0)
        logits(1)
        for n in range(n_units):
            if n + 2 < n_units:
                logits(n + 2)
            turn(n)
            if n >= 1:
                weigh(n - 1)
        weigh(n_units - 1)

    def vector(dve, i):
        base = n_units * i
        step = Steps(dve, s["soft_step"], 2 * base)

        def row_max(n):
            b = units[n][1]
            dve.wait_ge(s["scores_done"], 1 + base + n + 1)
            diagonal = ps[:, n % 3, b * P:(b + 1) * P]
            step(dve.tensor_tensor(diagonal, diagonal, k.future_mask[:], ALU.add))
            if n == 0:
                dve.wait_ge(s["exp_done"], 1 + base)
            dve.tensor_reduce(nmax[:, n:n + 1], ps[:, n % 3, 0:(b + 1) * P], AX.X, ALU.max, negate=True).then_inc(s["max_done"], 1)

        def normalise(n):
            b = units[n][1]
            dve.wait_ge(s["exp_done"], 1 + base + n + 1)
            step(dve.reciprocal(rinv[:, n:n + 1], rsum[:, n:n + 1]))
            row = p_tiles[:, n % 3, 0:(b + 1) * P]
            dve.tensor_scalar(row, row, rinv[:, n:n + 1], None, ALU.mult).then_inc(s["probs_done"], 1)

        row_max(0)
        for n in range(n_units):
            if n + 1 < n_units:
                row_max(n + 1)
            normalise(n)
        return step.n

    def scalar(act, i):
        base = n_units * i

        def exponent(n):
            b = units[n][1]
            act.wait_ge(s["max_done"], base + n + 1)
            if n >= 3:
                act.wait_ge(s["turned"], base + n - 2)
            act.activation(p_tiles[:, n % 3, 0:(b + 1) * P], ps[:, n % 3, 0:(b + 1) * P], ACT.Exp, bias=nmax[:, n:n + 1],
                           accum_out=rsum[:, n:n + 1]).then_inc(s["exp_done"], 1)

        def copy_turned(n):
            b = units[n][1]
            act.wait_ge(s["turned"], base + n + 1)
            if n >= 2:
                act.wait_ge(s["weighed"], 1 + base + n - 1)
            act.activation(pt_tiles[:, n % 2, 0:(b + 1) * P], ps[:, 3 + n % 2, 0:(b + 1) * P], ACT.Copy).then_inc(s["turned_copied"], 1)

        exponent(0)
        for n in range(n_units):
            if n + 1 < n_units:
                exponent(n + 1)
            copy_turned(n)

    return tensor, vector, scalar


SOFTMAX = ("scores_done", "exp_done", "probs_done", "turned", "turned_copied", "weighed", "max_done", "soft_step", "o_copied")


def attention_stage(k, o):
    ps, w_in = k.ps, k.ins["w_in"][0]
    pairs = HEADS // 2
    with k.stage("attention", "w_loaded", "q_done", "k_done", "v_done", "qkv_copied", "f_picked", "picked_used", *SOFTMAX, primed=("exp_done", "o_copied", "qkv_copied", "scores_done", "v_done", "weighed")) as (block, s, sb):
        qt, kt = sb("qt", [P, T]), sb("kt", [P, T])
        v = sb("v", [P, TB, P])
        picked = sb("picked", [HEADS, 2, T])
        p_tiles, pt_tiles = sb("p_tiles", [P, 3, T]), sb("pt_tiles", [P, 2, T])
        nmax, rsum, rinv = sb("nmax", [P, 8]), sb("rsum", [P, 8]), sb("rinv", [P, 8])
        wv = k.w[:, 0:3, 0:KD * P].rearrange("p s (k n) -> p s k n", k=KD)
        units = [(slice(hh * HD, (hh + 1) * HD), b) for hh in range(2) for b in range(TB)]

        def scores(pe, unit, bank):
            rows, b = unit
            hh, n = rows.start // HD, (b + 1) * P
            pe.matmul(ps[:, bank, 0:n], qt[rows, b * P:(b + 1) * P], kt[rows, 0:n], start=True, stop=False)
            return pe.matmul(ps[:, bank, 0:n], k.ones[0:HEADS, :], picked[:, hh, 0:n], start=False, stop=True)

        tensor, vector, scalar = scan_softmax(k, s, units, scores, p_tiles, pt_tiles,
                                              lambda unit, kb: v[:, kb, unit[0]], nmax, rsum, rinv)

        @block.sync
        def _(sp):
            k.clear(sp)
            with sp.Fori(0, pairs) as i:
                sp.wait_ge(s["v_done"], 1 + i)
                for j, first in enumerate((Q0, K0, V0)):
                    sp.dma_start(wv[:, j], columns(w_in, first + i * P, P)).then_inc(s["w_loaded"], 16)

        @block.tensor
        def _(pe):
            with pe.Fori(0, pairs) as i:
                pe.wait_ge(s["w_loaded"], 48 * (i + 1))
                pe.wait_ge(s["qkv_copied"], 1 + 3 * i)
                for j, done in enumerate((s["q_done"], s["k_done"])):
                    for kk in range(KD):
                        mm = pe.matmul(ps[:, 6 + j, :], wv[:, j, kk, :], k.h[:, kk, :], start=(kk == 0), stop=(kk == KD - 1))
                    mm.then_inc(done, 1)
                pe.wait_ge(s["qkv_copied"], 1 + 3 * i + 1)
                for b in range(TB):
                    for kk in range(KD):
                        mm = pe.matmul(ps[:, 6, b * P:(b + 1) * P], k.h[:, kk, b * P:(b + 1) * P], wv[:, 2, kk, :],
                                       start=(kk == 0), stop=(kk == KD - 1))
                mm.then_inc(s["v_done"], 1)
                pe.wait_ge(s["qkv_copied"], 1 + 3 * i + 3)
                pe.wait_ge(s["f_picked"], 2 * i + 2)
                tensor(pe, i)

        @block.scalar
        def _(act):
            with act.Fori(0, pairs) as i:
                act.wait_ge(s["q_done"], i + 1)
                act.wait_ge(s["weighed"], 1 + len(units) * i)
                act.activation(qt[:], ps[:, 6, :], ACT.Copy, scale=HD ** -0.5).then_inc(s["qkv_copied"], 1)
                act.wait_ge(s["k_done"], i + 1)
                act.activation(kt[:], ps[:, 7, :], ACT.Copy).then_inc(s["qkv_copied"], 1)
                act.wait_ge(s["v_done"], 1 + i + 1)
                act.activation(v[:], ps[:, 6, :].rearrange("p (b n) -> p b n", b=TB), ACT.Copy).then_inc(s["qkv_copied"], 1)
                scalar(act, i)

        @block.vector
        def _(dve):
            with dve.Fori(0, pairs) as i:
                dve.wait_ge(s["scores_done"], 1 + len(units) * i)
                for hh in range(2):
                    dve.tensor_scalar(picked[:, hh, :], k.neg_f[:], k.ident[0:HEADS, bass.ds(2 * i + hh, 1)], None,
                                      ALU.mult).then_inc(s["f_picked"], 1)
                n = vector(dve, i)
                assert n == 2 * len(units)
                dve.wait_ge(s["weighed"], 1 + len(units) * (i + 1))
                dve.tensor_copy(o[:, bass.ds(i, 1), :], ps[:, 5:6, :]).then_inc(s["o_copied"], 1)


def ssm_stage(k, ys):
    ps, w_in = k.ps, k.ins["w_in"][0]
    H = R_SSM
    conv0, convb0 = k.places["conv_w"][0], k.places["conv_b"][0]
    NC = 2 + KG
    VEC_STEPS = 79
    with k.stage("ssm", "w_loaded", "z_loaded", "small_loaded", "dt_done", "tile_done", "tile_copied", "conv_done", "sig_done",
                 "act_done", "z_done", "z_sig", "z_gated", "zeroed", "d_loaded", "wend_in", "a_ready", "vec_step", "act_step", "acs_ready", "small_turned", "small_copied",
                 "turned", "turned_copied", "ends_done", "ends_copied", "decay_done", "xw_ready", "cb_done", "cb_copied", "state_done", "state_ready",
                 "row_done", "row_seen", "seg_ready", "seg_exp", "row_exp", "scores_ready", "y_done", "y_read", "sq_done",
                 "ms_done", "std_done", "group_done", primed=("group_done", "ms_done", "tile_done", "z_done")) as (block, s, sb):
        wxs = strip(k, 0)
        wz = strip(k, 1)
        wbc = k.w[:, 2, 0:KD * 2 * P].rearrange("p (k n) -> p k n", k=KD)
        wdt = sb("wdt", [P, KD, H])
        dt_bias, a_log = sb("dt_bias", [H, G_SSM]), sb("a_log", [H, G_SSM])
        d_col = sb("d_col", [P, KI])
        u = sb("u", [P, 2, T + CONV - 1])
        acc = sb("acc", [P, 2, T])
        sig = sb("sig", [P, 2, T])
        xbc = sb("xbc", [P, NC, T])
        z = sb("z", [P, KG, T])
        xt = k.w[:, 2, KD * 2 * P:].rearrange("p (b n) -> p b n", b=TB)
        bt = sb("bt", [P, TB, P])
        xw = sb("xw", [P, TB - 1, KG * P])
        hp = sb("hp", [P, TB - 1, KG * P])
        cb = sb("cb", [P, TB, P])
        dt, acs = sb("dt", [H, T]), sb("acs", [H, T])
        e, t1, t2 = xw[0:H, 0, :], xw[0:H, 1, :], xw[0:H, 2, :]
        ones = sb("ones", [H, T])
        small = sb("small", [P, 2, TB, H])
        ends_in = sb("ends_in", [H, TB, H])
        ends = sb("ends", [P, TB, H])
        decay, wend = sb("decay", [P, TB, H]), sb("wend", [P, TB, H])
        seg, rowx = sb("seg", [P, 2, T]), sb("rowx", [P, 2, T])
        sc, ce = sb("sc", [P, 2, TB, P]), sb("ce", [P, 2, T])
        sq = acc
        std, rstd = seg[:, 0, :], seg[:, 1, :]

        def wcols(i, tile, j):
            at = (16 + i) if tile == 0 else (20 + i) if tile == 1 else KG * i + tile - 2
            first = convb0 if j is None else conv0 + j * XBC_TILES
            return k.cols[:, bass.ds(first + at, 1)]

        @block.sync
        def _(sp):
            k.clear(sp)
            for half in range(2):
                sp.dma_start(d_col[half * P_SSM:(half + 1) * P_SSM, :],
                               k.ins["d_skip"].rearrange("l (j two) -> two l j", two=2)[half].to_broadcast([P_SSM, KI]),
                               allow_slow_non_contiguous=True).then_inc(s["d_loaded"], 16)
            for dst, name in ((dt_bias, "dt_bias"), (a_log, "a_log")):
                sp.dma_start(dst[:], k.ins[name].rearrange("l (g h) -> h (l g)", h=H), allow_slow_non_contiguous=True).then_inc(s["small_loaded"], 16)
            with sp.Fori(0, G_SSM) as i:
                sp.wait_ge(s["tile_done"], 1 + NC * i)
                sp.dma_start(wdt[:], columns(w_in, DT0 + i * H, H)).then_inc(s["w_loaded"], 16)
                sp.dma_start(wbc[:, :, 0:P], columns(w_in, B0 + i * P, P)).then_inc(s["w_loaded"], 16)
                sp.dma_start(wbc[:, :, P:2 * P], columns(w_in, C0 + i * P, P)).then_inc(s["w_loaded"], 16)
                sp.dma_start(wxs, columns(w_in, XBC0 + i * STRIP)).then_inc(s["w_loaded"], 16)
                sp.wait_ge(s["z_done"], 1 + KG * i)
                sp.dma_start(wz, columns(w_in, Z0 + i * STRIP)).then_inc(s["z_loaded"], 16)

        @block.gpsimd
        def _(pool):
            for b in range(2):
                pool.memset(u[:, b, 0:CONV - 1], 0.0).then_inc(s["zeroed"], 1)

        @block.tensor
        def _(pe):
            with pe.Fori(0, G_SSM) as i:
                pe.wait_ge(s["w_loaded"], 64 * (i + 1))
                pe.wait_ge(s["group_done"], 1 + KG * i)
                for kk in range(KD):
                    mm = pe.matmul(ps[0:H, 7, :], wdt[:, kk, :], k.h[:, kk, :], start=(kk == 0), stop=(kk == KD - 1))
                mm.then_inc(s["dt_done"], 1)
                for c in range(NC):
                    for kk in range(KD):
                        w = wbc[:, kk, c * P:(c + 1) * P] if c < 2 else wxs[:, kk, (c - 2) * P:(c - 1) * P]
                        mm = pe.matmul(ps[:, c, :], w, k.h[:, kk, :], start=(kk == 0), stop=(kk == KD - 1))
                    mm.then_inc(s["tile_done"], 1)
                pe.wait_ge(s["acs_ready"], i + 1)
                pe.matmul(ps[:, 7, 0:TB * H], k.ones[0:H, :], ends_in[:].rearrange("p c h -> p (c h)"), start=True,
                          stop=True).then_inc(s["ends_done"], 1)
                for j, m in enumerate((dt, acs)):
                    for c in range(TB):
                        mm = pe.transpose(ps[:, 6, (j * TB + c) * H:(j * TB + c + 1) * H], m[:, c * P:(c + 1) * P], k.ident[0:H, 0:H])
                mm.then_inc(s["small_turned"], 1)
                pe.wait_ge(s["z_loaded"], 16 * (i + 1))
                for f in range(KG):
                    pe.wait_ge(s["tile_copied"], NC * i + f + 1)
                    for kk in range(KD):
                        mm = pe.matmul(ps[:, f, :], wz[:, kk, f * P:(f + 1) * P], k.h[:, kk, :], start=(kk == 0), stop=(kk == KD - 1))
                    mm.then_inc(s["z_done"], 1)
                pe.wait_ge(s["tile_copied"], NC * (i + 1))
                pe.wait_ge(s["act_done"], NC * (i + 1))
                for n in range(1 + TB):
                    if n >= 2:
                        pe.wait_ge(s["turned_copied"], (1 + TB) * i + n - 1)
                    for m in range(TB if n == 0 else KG):
                        src = xbc[:, 0, m * P:(m + 1) * P] if n == 0 else xbc[:, 2 + m, (n - 1) * P:n * P]
                        mm = pe.transpose(ps[:, 4 + n % 2, m * P:(m + 1) * P], src, k.ident[:])
                    mm.then_inc(s["turned"], 1)
                pe.wait_ge(s["small_copied"], i + 1)
                for c in range(TB):
                    mm = pe.matmul(ps[:, 6, c * P:(c + 1) * P], xbc[:, 0, c * P:(c + 1) * P], xbc[:, 1, c * P:(c + 1) * P],
                                   start=True, stop=True)
                mm.then_inc(s["cb_done"], 1)
                pe.wait_ge(s["turned_copied"], (1 + TB) * (i + 1))
                pe.wait_ge(s["z_gated"], KG * (i + 1))
                for c in range(TB - 1):
                    pe.wait_ge(s["xw_ready"], (TB - 1) * i + c + 1)
                    pe.matmul(ps[:, c, :], bt[:, c, :], xw[:, c, :], start=True, stop=True).then_inc(s["state_done"], 1)

                def row(h):
                    if h >= 2:
                        pe.wait_ge(s["row_exp"], H * i + h - 1)
                        pe.wait_ge(s["row_seen"], H * i + h - 1)
                    pe.matmul(ps[:, 4 + h % 2, :], k.ident[0:H, h:h + 1].to_broadcast([H, P]), acs[:], start=True,
                              stop=True).then_inc(s["row_done"], 1)

                pe.wait_ge(s["ends_copied"], i + 1)
                row(0)
                row(1)
                for h in range(H):
                    rows = slice(h % 2 * P_SSM, (h % 2 + 1) * P_SSM)
                    bank = (3, 7)[h // 2 % 2]
                    if h >= 4:
                        pe.wait_ge(s["y_read"], KG * i + h // 2 - 1)
                    pe.wait_ge(s["scores_ready"], H * i + h + 1)
                    if h == 0:
                        pe.wait_ge(s["state_ready"], i + 1)
                    for c in range(TB):
                        mine = slice(c * P, (c + 1) * P)
                        mm = pe.matmul(ps[rows, bank, mine], xt[:, c, h * P_SSM:(h + 1) * P_SSM], sc[:, h % 2, c, :],
                                       start=True, stop=(c == 0))
                        if c:
                            mm = pe.matmul(ps[rows, bank, mine], hp[:, c - 1, h * P_SSM:(h + 1) * P_SSM], ce[:, h % 2, mine],
                                           start=False, stop=True)
                    mm.then_inc(s["y_done"], 1)
                    if h + 2 < H:
                        row(h + 2)
                for f in range(KG):
                    pe.wait_ge(s["sq_done"], KG * i + f + 1)
                    mm = pe.matmul(ps[:, 6, :], k.ones[:], sq[:, f % 2, :], start=(f == 0), stop=(f == KG - 1))
                    mm.then_inc(s["ms_done"], 1)

        @block.scalar
        def _(act):
            act.wait_ge(s["small_loaded"], 32)
            act.activation(a_log[:], a_log[:], ACT.Exp).then_inc(s["a_ready"], 1)
            with act.Fori(0, G_SSM) as i:
                act.wait_ge(s["vec_step"], VEC_STEPS * i + 2)
                act.activation(e[:], e[:], ACT.Exp).then_inc(s["act_step"], 1)
                act.wait_ge(s["vec_step"], VEC_STEPS * i + 3)
                act.activation(t2[:], t1[:], ACT.Ln).then_inc(s["act_step"], 1)
                for c in range(NC):
                    act.wait_ge(s["tile_done"], 1 + NC * i + c + 1)
                    if c >= 2:
                        act.wait_ge(s["conv_done"], NC * i + c - 1)
                    act.activation(u[:, c % 2, CONV - 1:], ps[:, c, :], ACT.Copy).then_inc(s["tile_copied"], 1)
                    if c >= 1:
                        act.wait_ge(s["conv_done"], NC * i + c)
                        act.activation(sig[:, (c - 1) % 2, :], acc[:, (c - 1) % 2, :], ACT.Sigmoid).then_inc(s["sig_done"], 1)
                act.wait_ge(s["conv_done"], NC * (i + 1))
                act.activation(sig[:, (NC - 1) % 2, :], acc[:, (NC - 1) % 2, :], ACT.Sigmoid).then_inc(s["sig_done"], 1)
                act.wait_ge(s["small_turned"], i + 1)
                act.activation(small[:], ps[:, 6, 0:2 * TB * H].rearrange("p (j c h) -> p j c h", j=2, c=TB), ACT.Copy).then_inc(s["small_copied"], 1)
                act.wait_ge(s["ends_done"], i + 1)
                act.activation(ends[:], ps[:, 7, 0:TB * H].rearrange("p (c h) -> p c h", c=TB), ACT.Copy).then_inc(s["ends_copied"], 1)
                for f in range(KG):
                    act.wait_ge(s["z_done"], 1 + KG * i + f + 1)
                    act.wait_ge(s["act_done"], NC * (i + 1))
                    if f >= 2:
                        act.wait_ge(s["z_gated"], KG * i + f - 1)
                    act.activation(sig[:, f % 2, :], ps[:, f, :], ACT.Sigmoid).then_inc(s["z_sig"], 1)
                for n in range(1 + TB):
                    act.wait_ge(s["turned"], (1 + TB) * i + n + 1)
                    dst = bt[:] if n == 0 else xt[:, n - 1, :].rearrange("p (b n) -> p b n", b=KG)
                    act.activation(dst, ps[:, 4 + n % 2, :].rearrange("p (b n) -> p b n", b=TB), ACT.Copy).then_inc(s["turned_copied"], 1)
                act.wait_ge(s["cb_done"], i + 1)
                act.activation(cb[:], ps[:, 6, :].rearrange("p (b n) -> p b n", b=TB), ACT.Copy).then_inc(s["cb_copied"], 1)
                act.wait_ge(s["ends_copied"], i + 1)
                act.activation(decay[:], ends[:], ACT.Exp).then_inc(s["decay_done"], 1)
                act.wait_ge(s["wend_in"], i + 1)
                act.activation(wend[:], wend[:], ACT.Exp).then_inc(s["decay_done"], 1)
                for h in range(H):
                    act.wait_ge(s["row_done"], H * i + h + 1)
                    if h >= 2:
                        act.wait_ge(s["scores_ready"], H * i + h - 1)
                    act.activation(rowx[:, h % 2, :], ps[:, 4 + h % 2, :], ACT.Exp).then_inc(s["row_exp"], 1)
                    act.wait_ge(s["row_seen"], H * i + h + 1)
                    act.activation(seg[:, h % 2, :], seg[:, h % 2, :], ACT.Exp).then_inc(s["seg_exp"], 1)
                for f in range(KG):
                    act.wait_ge(s["y_read"], KG * i + f + 1)
                    if f >= 2:
                        act.wait_ge(s["ms_done"], 1 + KG * i + f - 1)
                    act.activation(sq[:, f % 2, :], z[:, f, :], ACT.Square).then_inc(s["sq_done"], 1)
                act.wait_ge(s["ms_done"], 1 + KG * (i + 1))
                act.activation(std[:], ps[:, 6, :], ACT.Sqrt, scale=1.0 / (KG * P), bias=k.eps_rms[:]).then_inc(s["std_done"], 1)

        @block.vector
        def _(dve):
            dve.memset(ones[:], 1.0).then_inc(s["zeroed"], 1)
            dve.wait_ge(s["zeroed"], 3)
            dve.wait_ge(s["d_loaded"], 32)
            dve.wait_ge(s["small_loaded"], 32)
            dve.wait_ge(s["a_ready"], 1)
            with dve.Fori(0, G_SSM) as i:
                step = Steps(dve, s["vec_step"], VEC_STEPS * i)
                dve.wait_ge(s["dt_done"], i + 1)
                step(dve.tensor_scalar(dt[:], ps[0:H, 7, :], dt_bias[:, bass.ds(i, 1)], None, ALU.add))
                step(dve.scalar_tensor_tensor(out=e[:], in0=dt[:], scalar=-1.0, in1=dt[:], op0=ALU.mult, op1=ALU.min))
                dve.wait_ge(s["act_step"], 2 * i + 1)
                step(dve.tensor_scalar(t1[:], e[:], 1.0, None, ALU.add))
                dve.wait_ge(s["act_step"], 2 * i + 2)
                step(dve.tensor_scalar(t1[:], t1[:], -1.0, None, ALU.add))
                step(dve.tensor_scalar(acs[:], t1[:], 0.0, None, ALU.is_equal))
                step(dve.tensor_tensor(t1[:], t1[:], acs[:], ALU.add))
                step(dve.tensor_tensor(t2[:], t2[:], acs[:], ALU.add))
                step(dve.reciprocal(t1[:], t1[:]))
                step(dve.tensor_tensor(t2[:], t2[:], e[:], ALU.mult))
                step(dve.tensor_tensor(t2[:], t2[:], t1[:], ALU.mult))
                step(dve.scalar_tensor_tensor(out=dt[:], in0=dt[:], scalar=0.0, in1=t2[:], op0=ALU.max, op1=ALU.add))
                step(dve.tensor_scalar(t1[:], dt[:], a_log[:, bass.ds(i, 1)], -1.0, ALU.mult, ALU.mult))
                for c in range(TB):
                    mine = slice(c * P, (c + 1) * P)
                    step(dve.tensor_tensor_scan(acs[:, mine], ones[:, mine], t1[:, mine], 0.0, ALU.mult, ALU.add))
                for c in range(TB):
                    ins = dve.tensor_scalar(ends_in[:, c, :], k.ident[0:H, 0:H], acs[:, (c + 1) * P - 1:(c + 1) * P], None, ALU.mult)
                    if c < TB - 1:
                        step(ins)
                ins.then_inc(s["acs_ready"], 1)
                def silu(c):
                    dve.wait_ge(s["sig_done"], NC * i + c + 1)
                    dve.tensor_tensor(xbc[:, c, :], acc[:, c % 2, :], sig[:, c % 2, :], ALU.mult).then_inc(s["act_done"], 1)

                dve.wait_ge(s["ms_done"], 1 + KG * i)
                for c in range(NC):
                    if c >= 2:
                        silu(c - 2)
                        dve.wait_ge(s["act_done"], NC * i + c - 1)
                    dve.wait_ge(s["tile_copied"], NC * i + c + 1)
                    a = acc[:, c % 2, :]
                    step(dve.tensor_scalar(a, u[:, c % 2, 0:T], wcols(i, c, 0), wcols(i, c, None), ALU.mult, ALU.add))
                    for j in range(1, CONV):
                        ins = dve.scalar_tensor_tensor(out=a, in0=u[:, c % 2, j:j + T], scalar=wcols(i, c, j), in1=a,
                                                       op0=ALU.mult, op1=ALU.add)
                        if j < CONV - 1:
                            step(ins)
                    ins.then_inc(s["conv_done"], 1)
                silu(NC - 2)
                silu(NC - 1)
                dve.wait_ge(s["small_copied"], i + 1)
                dve.wait_ge(s["ends_copied"], i + 1)
                dve.tensor_tensor(wend[:], ends[:], small[:, 1], ALU.subtract).then_inc(s["wend_in"], 1)
                for f in range(KG):
                    dve.wait_ge(s["z_sig"], KG * i + f + 1)
                    dve.tensor_tensor(z[:, f, :], ps[:, f, :], sig[:, f % 2, :], ALU.mult).then_inc(s["z_gated"], 1)
                dve.wait_ge(s["decay_done"], 2 * i + 2)
                step(dve.tensor_tensor(wend[:], wend[:], small[:, 0], ALU.mult))
                dve.wait_ge(s["turned_copied"], (1 + TB) * (i + 1))
                for c in range(TB - 1):
                    dve.tensor_tensor(xw[:, c, :].rearrange("p (h n) -> p h n", h=H), xt[:, c, :].rearrange("p (h n) -> p h n", h=H),
                                      wend[:, c, :].rearrange("p (h o) -> p h o", o=1).to_broadcast([P, H, P_SSM]), ALU.mult).then_inc(s["xw_ready"], 1)
                for c in range(TB - 1):
                    dve.wait_ge(s["state_done"], (TB - 1) * i + c + 1)
                    if c == 0:
                        step(dve.tensor_copy(hp[:, 0, :], ps[:, 0, :]))
                    else:
                        step(dve.tensor_tensor(hp[:, c, :].rearrange("p (h n) -> p h n", h=H), hp[:, c - 1, :].rearrange("p (h n) -> p h n", h=H),
                                               decay[:, c, :].rearrange("p (h o) -> p h o", o=1).to_broadcast([P, H, P_SSM]), ALU.mult))
                        ins = dve.tensor_tensor(hp[:, c, :], hp[:, c, :], ps[:, c, :], ALU.add)
                        if c < TB - 2:
                            step(ins)
                ins.then_inc(s["state_ready"], 1)

                def segment(h):
                    dve.wait_ge(s["row_exp"], H * i + h + 1)
                    for c in range(TB):
                        mine = slice(c * P, (c + 1) * P)
                        ins = dve.scalar_tensor_tensor(out=seg[:, h % 2, mine], in0=ps[:, 4 + h % 2, mine], scalar=small[:, 1, c, h:h + 1],
                                                       in1=k.past_cap[:], op0=ALU.subtract, op1=ALU.min)
                    ins.then_inc(s["row_seen"], 1)

                dve.wait_ge(s["cb_copied"], i + 1)
                segment(0)
                for h in range(H):
                    if h + 1 < H:
                        if h >= 1:
                            dve.wait_ge(s["seg_exp"], H * i + h)
                        segment(h + 1)
                    dve.wait_ge(s["seg_exp"], H * i + h + 1)
                    if h >= 2:
                        dve.wait_ge(s["y_done"], H * i + h - 1)
                    for c in range(TB):
                        mine = slice(c * P, (c + 1) * P)
                        step(dve.scalar_tensor_tensor(out=sc[:, h % 2, c, :], in0=seg[:, h % 2, mine], scalar=small[:, 0, c, h:h + 1],
                                                      in1=cb[:, c, :], op0=ALU.mult, op1=ALU.mult))
                    dve.tensor_tensor(ce[:, h % 2, P:], rowx[:, h % 2, P:], xbc[:, 1, P:], ALU.mult).then_inc(s["scores_ready"], 1)
                    if h % 2:
                        f = h // 2
                        bank = (3, 7)[f % 2]
                        dve.wait_ge(s["y_done"], H * i + h + 1)
                        step(dve.scalar_tensor_tensor(out=xbc[:, 2 + f, :], in0=xbc[:, 2 + f, :], scalar=d_col[:, bass.ds(KG * i + f, 1)],
                                                      in1=ps[:, bank, :], op0=ALU.mult, op1=ALU.add))
                        dve.tensor_tensor(z[:, f, :], z[:, f, :], xbc[:, 2 + f, :], ALU.mult).then_inc(s["y_read"], 1)
                dve.wait_ge(s["std_done"], i + 1)
                step(dve.reciprocal(rstd[:], std[:]))
                for f in range(KG):
                    at = k.places["ssm_norm_w"][0] + KG * i + f
                    dve.scalar_tensor_tensor(out=ys[:, bass.ds(KG * i + f, 1), :], in0=z[:, f:f + 1, :], scalar=k.cols[:, bass.ds(at, 1)],
                                             in1=rstd[:].rearrange("p (o t) -> p o t", o=1), op0=ALU.mult, op1=ALU.mult).then_inc(s["group_done"], 1)
                assert step.n == VEC_STEPS, step.n


def merge_stage(k, name, branch, w_out_of, x, kt, merged):
    ps, w_in = k.ps, k.ins["w_in"][0]
    strips = kt // KD
    ft = FT // strips
    with k.stage(name, "g_loaded", "w_loaded0", "w_loaded1", "gate_done", "gate_ready", "tile_done", "tile_free", "vec_step") as (block, s, sb):
        gate = sb("gate", [P, FT, T])
        tmp = sb("tmp", [P, 2, T])
        loaded = (s["w_loaded0"], s["w_loaded1"])

        @block.sync
        def _(sp):
            k.clear(sp)
            for half in range(2):
                sp.wait_ge(s["gate_done"], FT * half)
                sp.dma_start(strip(k, 2), columns(w_in, GATE0 + branch * D + half * STRIP)).then_inc(s["g_loaded"], 16)
                for j in range(strips):
                    n = half * strips + j
                    if n >= 2:
                        sp.wait_ge(s["tile_done"], ft * (n - 1))
                    sp.dma_start(strip(k, n % 2, kt), w_out_of(half * STRIP + j * ft * P, ft * P)).then_inc(loaded[n % 2], 16)

        @block.tensor
        def _(pe):
            for half in range(2):
                pe.wait_ge(s["g_loaded"], 16 * (half + 1))
                pe.wait_ge(s["gate_ready"], FT * half)
                for f in range(FT):
                    for kk in range(KD):
                        mm = pe.matmul(ps[:, f, :], strip(k, 2)[:, kk, f * P:(f + 1) * P], k.h[:, kk, :], start=(kk == 0), stop=(kk == KD - 1))
                    mm.then_inc(s["gate_done"], 1)
                pe.wait_ge(s["tile_free"], FT * half)
                for j in range(strips):
                    n = half * strips + j
                    pe.wait_ge(loaded[n % 2], 16 * (n // 2 + 1))
                    for f in range(ft):
                        for kk in range(kt):
                            mm = pe.matmul(ps[:, 4 + j * ft + f, :], strip(k, n % 2, kt)[:, kk, f * P:(f + 1) * P], x[:, kk, :],
                                           start=(kk == 0), stop=(kk == kt - 1))
                        mm.then_inc(s["tile_done"], 1)

        @block.scalar
        def _(act):
            for n in range(2 * FT):
                act.wait_ge(s["gate_done"], n + 1)
                if n >= FT:
                    act.wait_ge(s["tile_free"], n - FT + 1)
                act.activation(gate[:, n % FT, :], ps[:, n % FT, :], ACT.Sigmoid).then_inc(s["gate_ready"], 1)

        @block.vector
        def _(dve):
            step = Steps(dve, s["vec_step"])
            for n in range(2 * FT):
                dve.wait_ge(s["gate_ready"], n + 1)
                dve.wait_ge(s["tile_done"], n + 1)
                if branch == 0:
                    dve.tensor_tensor(merged[:, n, :], gate[:, n % FT, :], ps[:, 4 + n % FT, :], ALU.mult).then_inc(s["tile_free"], 1)
                else:
                    step(dve.tensor_tensor(tmp[:, n % 2, :], gate[:, n % FT, :], ps[:, 4 + n % FT, :], ALU.mult))
                    dve.tensor_tensor(merged[:, n, :], merged[:, n, :], tmp[:, n % 2, :], ALU.add).then_inc(s["tile_free"], 1)


def pool_stage(k, pooled):
    ps, w_in = k.ps, k.ins["w_in"][0]
    with k.stage("pool", "zeroed", "counted", "recip", "copied", "pooled_done", "vec_step", *LINEAR, primed=LINEAR_PRIMED) as (block, s, sb):
        u = sb("u", [P, KD, PAD + T])
        a, b = sb("a", [P, PAD + T]), sb("b", [P, PAD + T])
        count = sb("count", [P, len(POOL_WINDOWS), PAD])
        pos = sb("pos", [P, PAD])
        free = (s["tile_free0"], s["tile_free1"])
        done = (s["tile_done0"], s["tile_done1"])
        linear(k, block, s, lambda i, slot: columns(w_in, U0 + (2 * i + slot) * STRIP), 1, lambda kk: k.h[:, kk, :], None)

        @block.gpsimd
        def _(pool):
            pool.memset(u[:, :, 0:PAD], 0.0).then_inc(s["zeroed"], 1)
            pool.memset(a[:], 0.0).then_inc(s["zeroed"], 1)
            pool.memset(b[:], 0.0).then_inc(s["zeroed"], 1)
            pool.iota(pos[:], pattern=[[1, PAD]], base=1, channel_multiplier=0,
                      allow_small_or_imprecise_dtypes=True).then_inc(s["zeroed"], 1)
            pool.wait_ge(s["zeroed"], 4)
            for g, w in enumerate(POOL_WINDOWS):
                pool.tensor_scalar(count[:, g, :], pos[:], float(w), None, ALU.min).then_inc(s["counted"], 1)

        @block.scalar
        def _(act):
            for c in range(KD):
                act.wait_ge(done[c // FT], 1 + c % FT + 1)
                act.activation(u[:, c, PAD:], ps[:, c, :], ACT.Copy).then_inc(free[c // FT], 1)

        @block.vector
        def _(dve):
            step = Steps(dve, s["vec_step"])
            dve.wait_ge(s["counted"], len(POOL_WINDOWS))
            step(dve.reciprocal(count[:], count[:]))
            for c in range(KD):
                g = c // (KD // len(POOL_WINDOWS))
                dve.wait_ge(free[c // FT], 1 + c % FT + 1)
                src, bufs = u[:, c, :], (a, b)
                for j in range(g + 1):
                    dst = bufs[j % 2]
                    step(dve.tensor_tensor(dst[:, PAD:], src[:, PAD:], src[:, PAD - 2 ** j:PAD + T - 2 ** j], ALU.add))
                    src = dst[:, :]
                w = POOL_WINDOWS[g]
                step(dve.scalar_tensor_tensor(out=pooled[:, c, PAD:], in0=src[:, 2 * PAD:], scalar=1.0 / w, in1=u[:, c, 2 * PAD:],
                                              op0=ALU.mult, op1=ALU.subtract))
                step(dve.tensor_tensor(src[:, PAD:2 * PAD], src[:, PAD:2 * PAD], count[:, g, :], ALU.mult))
                step(dve.tensor_tensor(pooled[:, c, 0:PAD], src[:, PAD:2 * PAD], u[:, c, PAD:2 * PAD], ALU.subtract))
    return


def pool_out_stage(k, pooled, merged):
    ps, w_in = k.ps, k.ins["w_in"][0]
    groups = len(POOL_WINDOWS)
    gk = KD // groups
    with k.stage("pool_out", "w_loaded", "g_loaded", "gate_done", "gate_ready", "tile_done", "tile_free", "vec_step") as (block, s, sb):
        gate = sb("gate", [P, 2, T])
        wp = k.w[:, 2, 0:groups * gk * gk * P].rearrange("p (g k n) -> p g k n", g=groups, k=gk)

        @block.sync
        def _(sp):
            k.clear(sp)
            sp.dma_start(wp.rearrange("p g k n -> p (g k) n"), k.ins["w_pool"][0].rearrange("g (k p) n -> p (g k) n", p=P)).then_inc(s["w_loaded"], 16)
            for half in range(2):
                sp.dma_start(strip(k, half), columns(w_in, GATE0 + D + half * STRIP)).then_inc(s["g_loaded"], 16)

        @block.tensor
        def _(pe):
            pe.wait_ge(s["w_loaded"], 16)
            pe.wait_ge(s["g_loaded"], 32)
            for c in range(KD):
                if c >= 4:
                    pe.wait_ge(s["tile_free"], c - 3)
                for kk in range(KD):
                    mm = pe.matmul(ps[:, c % 4, :], strip(k, c // FT)[:, kk, c % FT * P:(c % FT + 1) * P], k.h[:, kk, :],
                                   start=(kk == 0), stop=(kk == KD - 1))
                mm.then_inc(s["gate_done"], 1)
                g = c // gk
                for kk in range(gk):
                    mm = pe.matmul(ps[:, 4 + c % 4, :], wp[:, g, kk, c % gk * P:(c % gk + 1) * P], pooled[:, g * gk + kk, :],
                                   start=(kk == 0), stop=(kk == gk - 1))
                mm.then_inc(s["tile_done"], 1)

        @block.scalar
        def _(act):
            for c in range(KD):
                act.wait_ge(s["gate_done"], c + 1)
                if c >= 2:
                    act.wait_ge(s["tile_free"], c - 1)
                act.activation(gate[:, c % 2, :], ps[:, c % 4, :], ACT.Sigmoid).then_inc(s["gate_ready"], 1)

        @block.vector
        def _(dve):
            step = Steps(dve, s["vec_step"])
            for c in range(KD):
                dve.wait_ge(s["gate_ready"], c + 1)
                dve.wait_ge(s["tile_done"], c + 1)
                step(dve.scalar_tensor_tensor(out=gate[:, c % 2, :], in0=ps[:, 4 + c % 4, :], scalar=k.col("pool_scale", c),
                                              in1=gate[:, c % 2, :], op0=ALU.mult, op1=ALU.mult))
                dve.tensor_tensor(merged[:, c, :], merged[:, c, :], gate[:, c % 2, :], ALU.add).then_inc(s["tile_free"], 1)


def residual_stage(k, name, w, x, alpha, gate, dst=None):
    ps = k.ps
    with k.stage(name, "vec_step", *LINEAR, primed=LINEAR_PRIMED) as (block, s, sb):
        t = sb("t", [P, 2, T])
        done, free = (s["tile_done0"], s["tile_done1"]), (s["tile_free0"], s["tile_free1"])
        linear(k, block, s, lambda i, slot: columns(w, (2 * i + slot) * STRIP), 1, lambda kk: x[:, kk, :], None)

        @block.vector
        def _(dve):
            step = Steps(dve, s["vec_step"])
            for c in range(KD):
                dve.wait_ge(done[c // FT], 1 + c % FT + 1)
                step(dve.tensor_scalar(t[:, c % 2, :], ps[:, c, :], k.mod[:, gate + c:gate + c + 1], None, ALU.mult))
                dve.scalar_tensor_tensor(out=k.x[:, c, :], in0=k.x[:, c, :], scalar=alpha, in1=t[:, c % 2, :], op0=ALU.mult,
                                         op1=ALU.add).then_inc(free[c // FT], 1)


def router_stage(k):
    ps = k.ps
    GR = NE // EG
    with k.stage("router", "loaded", "logits_done", "vec_step", "exp_done", "turned") as (block, s, sb):
        wr = sb("wr", [P, KD, NE])
        br = sb("br", [P, NE])
        probs, sel, share = sb("probs", [P, TB, NE]), sb("sel", [P, TB, NE]), sb("share", [P, TB, NE])
        rank, cmp = sb("rank", [P, TB, NE]), sb("cmp", [P, TB, NE])
        top = sb("top", [P, TB, NE])
        score, grank, gcmp = sb("score", [P, TB, GR]), sb("grank", [P, TB, GR]), sb("gcmp", [P, TB, GR])
        red = sb("red", [P, TB])

        @block.sync
        def _(sp):
            k.clear(sp)
            sp.dma_start(wr[:], k.ins["w_router"].rearrange("(k p) n -> p k n", p=P)).then_inc(s["loaded"], 16)
            sp.dma_start(br[:], k.ins["b_router"].rearrange("(o n) -> o n", o=1).to_broadcast([P, NE])).then_inc(s["loaded"], 16)

        @block.tensor
        def _(pe):
            pe.wait_ge(s["loaded"], 32)
            for b in range(TB):
                for kk in range(KD):
                    mm = pe.matmul(ps[:, 0, b * NE:(b + 1) * NE], k.h[:, kk, b * P:(b + 1) * P], wr[:, kk, :],
                                   start=(kk == 0), stop=(kk == KD - 1))
            mm.then_inc(s["logits_done"], 1)
            pe.wait_ge(s["vec_step"], ROUTER_STEPS)
            for b in range(TB):
                mm = pe.transpose(ps[0:NE, 1, b * P:(b + 1) * P], share[:, b, :], k.ident[:])
            mm.then_inc(s["turned"], 1)

        @block.scalar
        def _(act):
            act.wait_ge(s["vec_step"], 2)
            act.activation(probs[:], sel[:], ACT.Exp).then_inc(s["exp_done"], 1)
            act.wait_ge(s["turned"], 1)
            act.activation(k.gate_t[:], ps[0:NE, 1, :], ACT.Copy).then_inc(s["exp_done"], 1)

        @block.vector
        def _(dve):
            step = Steps(dve, s["vec_step"])

            def over(m, n):
                return m[:].rearrange("p (b o) -> p b o", o=1).to_broadcast([P, TB, n])

            dve.wait_ge(s["loaded"], 32)
            dve.wait_ge(s["logits_done"], 1)
            logits = ps[:, 0, 0:TB * NE].rearrange("p (b n) -> p b n", b=TB)
            step(dve.tensor_reduce(red[:], logits, AX.X, ALU.max))
            step(dve.tensor_tensor(sel[:], logits, over(red, NE), ALU.subtract))
            dve.wait_ge(s["exp_done"], 1)
            step(dve.tensor_reduce(red[:], probs[:], AX.X, ALU.add))
            step(dve.reciprocal(red[:], red[:]))
            step(dve.tensor_tensor(probs[:], probs[:], over(red, NE), ALU.mult))
            step(dve.tensor_tensor(sel[:], probs[:], br[:].rearrange("p (o n) -> p o n", o=1).to_broadcast([P, TB, NE]), ALU.add))

            def rank_in(rank, tmp, val, n, width):
                step(dve.memset(rank, 0.0))
                for a in range(n):
                    for b in range(n):
                        if a != b:
                            step(dve.tensor_tensor(tmp(a), val(b), val(a), ALU.is_ge if b < a else ALU.is_gt))
                            step(dve.tensor_tensor(rank_of(rank, a, n), rank_of(rank, a, n), tmp(a), ALU.add))

            def rank_of(m, a, n):
                return m.rearrange("p b (g n) -> p b g n", n=n)[:, :, :, a]

            rank_in(rank[:], lambda a: rank_of(cmp[:], a, EG), lambda a: rank_of(sel[:], a, EG), EG, GR)
            step(dve.tensor_scalar(rank[:], rank[:], float(2), None, ALU.is_lt))
            step(dve.tensor_tensor(top[:], sel[:], rank[:], ALU.mult))
            step(dve.tensor_reduce(score[:], top[:].rearrange("p b (g n) -> p b g n", n=EG), AX.X, ALU.add))
            rank_in(grank[:], lambda a: rank_of(gcmp[:], a, GR), lambda a: rank_of(score[:], a, GR), GR, 1)
            step(dve.tensor_scalar(grank[:], grank[:], 0.0, None, ALU.is_equal))
            for n in range(EG):
                step(dve.tensor_tensor(rank_of(rank[:], n, EG), rank_of(rank[:], n, EG), grank[:], ALU.mult))
            step(dve.tensor_tensor(share[:], probs[:], rank[:], ALU.mult))
            step(dve.tensor_reduce(red[:], share[:], AX.X, ALU.add))
            step(dve.reciprocal(red[:], red[:]))
            step(dve.tensor_tensor(share[:], share[:], over(red, NE), ALU.mult))
            assert step.n == ROUTER_STEPS, step.n


ROUTER_STEPS = 68


def experts_stage(k, total):
    ps = k.ps
    w1, w3, w2 = k.ins["w_exp_gate"][0], k.ins["w_exp_up"][0], k.ins["w_exp_down"][0]
    with k.stage("experts", "loaded0", "loaded1", "loaded2", "gate_done", "up_done", "down_done", "picked", "row_done", "row_copied",
                 "sig_done", "hidden_done", "vec_step", "summed", "zeroed", primed=("down_done", "gate_done", "hidden_done", "row_copied", "row_done", "summed", "up_done")) as (block, s, sb):
        hidden = sb("hidden", [P, KE, T])
        sig = sb("sig", [P, 2, T])
        t = sb("t", [P, 2, T])
        row = sb("row", [P, T])
        pick = sb("pick", [NE, T])

        @block.sync
        def _(sp):
            k.clear(sp)
            with sp.Fori(0, NE) as e:
                sp.wait_ge(s["gate_done"], 1 + KE * e)
                sp.dma_start(strip(k, 0), w1[bass.ds(e, 1)].rearrange("e (k p) n -> p (e k) n", p=P)).then_inc(s["loaded0"], 16)
                sp.wait_ge(s["up_done"], 1 + KE * e)
                sp.dma_start(strip(k, 1), w3[bass.ds(e, 1)].rearrange("e (k p) n -> p (e k) n", p=P)).then_inc(s["loaded1"], 16)
                sp.wait_ge(s["down_done"], 1 + KD * e)
                sp.dma_start(strip(k, 2, KE), w2[bass.ds(e, 1)].rearrange("e (k p) n -> p (e k) n", p=P)).then_inc(s["loaded2"], 16)

        @block.gpsimd
        def _(pool):
            pool.memset(total[:], 0.0).then_inc(s["zeroed"], 1)

        @block.tensor
        def _(pe):
            with pe.Fori(0, NE) as e:
                pe.wait_ge(s["picked"], e + 1)
                pe.wait_ge(s["row_copied"], 1 + e)
                pe.matmul(ps[:, 0, :], k.ones[0:NE, :], pick[:], start=True, stop=True).then_inc(s["row_done"], 1)
                for f in range(KE):
                    if f == 0:
                        pe.wait_ge(s["loaded0"], 16 * (e + 1))
                    if f >= 2:
                        pe.wait_ge(s["hidden_done"], 1 + KE * e + f - 1)
                    for kk in range(KD):
                        mm = pe.matmul(ps[:, 1 + f % 2, :], strip(k, 0)[:, kk, f * P:(f + 1) * P], k.h[:, kk, :], start=(kk == 0), stop=(kk == KD - 1))
                    mm.then_inc(s["gate_done"], 1)
                    if f == 0:
                        pe.wait_ge(s["loaded1"], 16 * (e + 1))
                    for kk in range(KD):
                        mm = pe.matmul(ps[:, 3 + f % 2, :], strip(k, 1)[:, kk, f * P:(f + 1) * P], k.h[:, kk, :], start=(kk == 0), stop=(kk == KD - 1))
                    mm.then_inc(s["up_done"], 1)
                pe.wait_ge(s["loaded2"], 16 * (e + 1))
                for c in range(KD):
                    if c >= 3:
                        pe.wait_ge(s["summed"], 1 + KD * e + c - 2)
                    else:
                        pe.wait_ge(s["summed"], 1 + KD * e)
                    for f in range(KE):
                        if c == 0:
                            pe.wait_ge(s["hidden_done"], 1 + KE * e + f + 1)
                        mm = pe.matmul(ps[:, 5 + c % 3, :], strip(k, 2, KE)[:, f, c * P:(c + 1) * P], hidden[:, f, :], start=(f == 0), stop=(f == KE - 1))
                    mm.then_inc(s["down_done"], 1)

        @block.scalar
        def _(act):
            with act.Fori(0, NE) as e:
                act.wait_ge(s["row_done"], 1 + e + 1)
                act.wait_ge(s["hidden_done"], 1 + KE * e)
                act.activation(row[:], ps[:, 0, :], ACT.Copy).then_inc(s["row_copied"], 1)
                for f in range(KE):
                    act.wait_ge(s["gate_done"], 1 + KE * e + f + 1)
                    if f >= 2:
                        act.wait_ge(s["hidden_done"], 1 + KE * e + f - 1)
                    act.activation(sig[:, f % 2, :], ps[:, 1 + f % 2, :], ACT.Sigmoid).then_inc(s["sig_done"], 1)

        @block.vector
        def _(dve):
            dve.wait_ge(s["zeroed"], 1)
            with dve.Fori(0, NE) as e:
                step = Steps(dve, s["vec_step"], 2 * KE * e)
                dve.wait_ge(s["row_done"], 1 + e)
                dve.tensor_scalar(pick[:], k.gate_t[:], k.ident[0:NE, bass.ds(e, 1)], None, ALU.mult).then_inc(s["picked"], 1)
                for f in range(KE):
                    dve.wait_ge(s["sig_done"], KE * e + f + 1)
                    dve.wait_ge(s["row_copied"], 1 + e + 1)
                    step(dve.tensor_tensor(t[:, f % 2, :], ps[:, 1 + f % 2, :], sig[:, f % 2, :], ALU.mult))
                    step(dve.tensor_tensor(t[:, f % 2, :], t[:, f % 2, :], row[:], ALU.mult))
                    dve.wait_ge(s["up_done"], 1 + KE * e + f + 1)
                    dve.wait_ge(s["down_done"], 1 + KD * e)
                    dve.tensor_tensor(hidden[:, f, :], t[:, f % 2, :], ps[:, 3 + f % 2, :], ALU.mult).then_inc(s["hidden_done"], 1)
                for c in range(KD):
                    dve.wait_ge(s["down_done"], 1 + KD * e + c + 1)
                    dve.wait_ge(s["summed"], 1 + KD * e)
                    dve.tensor_tensor(total[:, c, :], total[:, c, :], ps[:, 5 + c % 3, :], ALU.add).then_inc(s["summed"], 1)


def add_residual_stage(k, name, alpha, gate, y):
    with k.stage(name, "vec_step") as (block, s, sb):
        @block.sync
        def _(sp):
            k.clear(sp)

        @block.vector
        def _(dve):
            step = Steps(dve, s["vec_step"])
            for c in range(KD):
                step(dve.tensor_scalar(y[:, c, :], y[:, c, :], k.mod[:, gate + c:gate + c + 1], None, ALU.mult))
                step(dve.scalar_tensor_tensor(out=k.x[:, c, :], in0=k.x[:, c, :], scalar=alpha, in1=y[:, c, :], op0=ALU.mult, op1=ALU.add))


def output_stage(k, out):
    ps = k.ps
    with k.stage("output", "turned", "copied", "stored") as (block, s, sb):
        xt = sb("xt", [P, TB, D])

        @block.tensor
        def _(pe):
            for n in range(2 * TB):
                if n >= 4:
                    pe.wait_ge(s["copied"], n - 3)
                for j in range(4):
                    mm = pe.transpose(ps[:, n % 4, j * P:(j + 1) * P], k.x[:, n % 2 * 4 + j, n // 2 * P:(n // 2 + 1) * P], k.ident[:])
                mm.then_inc(s["turned"], 1)

        @block.scalar
        def _(act):
            for n in range(2 * TB):
                act.wait_ge(s["turned"], n + 1)
                act.activation(xt[:, n // 2, n % 2 * 512:(n % 2 + 1) * 512], ps[:, n % 4, :], ACT.Copy).then_inc(s["copied"], 1)

        @block.sync
        def _(sp):
            k.clear(sp)
            for b in range(TB):
                sp.wait_ge(s["copied"], 2 * b + 2)
                sp.dma_start(out[0, b * P:(b + 1) * P, :], xt[:, b, :]).then_inc(s["stored"], 16)
            sp.wait_ge(s["stored"], 16 * TB)


def modulate_stage(k, name, first):
    with k.stage(name, "done") as (block, s, sb):
        @block.sync
        def _(sp):
            k.clear(sp)

        @block.scalar
        def _(act):
            for c in range(0, KD, 2):
                act.activation(k.h[:, c, :], k.x[:, c, :], ACT.Identity, scale=k.mod[:, first + 8 + c:first + 9 + c],
                               bias=k.mod[:, first + c:first + c + 1]).then_inc(s["done"], 1)

        @block.vector
        def _(dve):
            for c in range(1, KD, 2):
                dve.tensor_scalar(k.h[:, c, :], k.x[:, c, :], k.mod[:, first + 8 + c:first + 9 + c],
                                  k.mod[:, first + c:first + c + 1], ALU.mult, ALU.add).then_inc(s["done"], 1)


def reduced_angle(step, dve, out, turns, angle, offset):
    step(dve.tensor_scalar(turns, angle, 1.0 / TWO_PI, offset / TWO_PI, ALU.mult, ALU.add))
    step(dve.tensor_scalar(turns, turns, ROUND, -ROUND, ALU.add, ALU.add))
    step(dve.scalar_tensor_tensor(out=out, in0=turns, scalar=-PI_A, in1=angle, op0=ALU.mult, op1=ALU.add))
    step(dve.scalar_tensor_tensor(out=out, in0=turns, scalar=-PI_B, in1=out, op0=ALU.mult, op1=ALU.add))
    step(dve.scalar_tensor_tensor(out=out, in0=turns, scalar=-PI_C, in1=out, op0=ALU.mult, op1=ALU.add))
    step(dve.tensor_scalar(out, out, offset, None, ALU.add))
    step(dve.tensor_scalar(out, out, PI_SAFE, -PI_SAFE, ALU.min, ALU.max))


def latent_stage(k, cq, ckv, k_pe, cos, sin):
    ps, w = k.ps, k.ins["mla_w_in_2"][0]
    width = QL + KVL + ROPE
    half = ROPE // 2
    with k.stage("latent", "loaded", "freq_ready", "pos_ready", "angle_done", "vec_step", "sin_done", "proj_done", "sq_done", "ms_done",
                 "std_done") as (block, s, sb):
        wl = k.w[:, 0, 0:KD * width].rearrange("p (k n) -> p k n", k=KD)
        pos_i, pos = sb("pos_i", [1, T], I32), sb("pos", [1, T])
        freq = sb("freq", [1, ROPE])
        angle, turns = sb("angle", [ROPE, T]), sb("turns", [ROPE, T])
        sq = sb("sq", [P, 3, T])
        std = sb("std", [P, 2, T])
        raw, swapped = sb("raw", [ROPE, T]), sb("swapped", [ROPE, T])
        NORMS = ((QL, 0, 2, "mla_q_norm_2"), (KVL, 2, 1, "mla_kv_norm_2"))

        @block.sync
        def _(sp):
            k.clear(sp)
            sp.dma_start(pos_i[:], k.ins["positions_2"]).then_inc(s["loaded"], 16)
            sp.dma_start(wl, w.rearrange("(k p) n -> p k n", p=P)).then_inc(s["loaded"], 16)

        @block.gpsimd
        def _(pool):
            for j in range(ROPE):
                pool.memset(freq[:, j:j + 1], ROPE_THETA ** (-2.0 * (j % half) / ROPE)).then_inc(s["freq_ready"], 1)

        @block.tensor
        def _(pe):
            pe.wait_ge(s["freq_ready"], ROPE)
            pe.wait_ge(s["pos_ready"], 1)
            pe.matmul(ps[0:ROPE, 0, :], freq[:], pos[:], start=True, stop=True).then_inc(s["angle_done"], 1)
            pe.wait_ge(s["loaded"], 32)
            for c in range(4):
                n = P if c < 3 else ROPE
                for kk in range(KD):
                    mm = pe.matmul(ps[0:n, 1 + c, :], wl[:, kk, c * P:c * P + n], k.h[:, kk, :], start=(kk == 0), stop=(kk == KD - 1))
                mm.then_inc(s["proj_done"], 1)
            for j, (_, first, n, _) in enumerate(NORMS):
                pe.wait_ge(s["sq_done"], first + n)
                for c in range(n):
                    mm = pe.matmul(ps[:, 5 + j, :], k.ones[:], sq[:, first + c, :], start=(c == 0), stop=(c == n - 1))
                mm.then_inc(s["ms_done"], 1)

        @block.scalar
        def _(act):
            act.wait_ge(s["vec_step"], 15)
            act.activation(sin[:], angle[:], ACT.Sin).then_inc(s["sin_done"], 1)
            act.activation(cos[:], cos[:], ACT.Sin).then_inc(s["sin_done"], 1)
            for c in range(3):
                act.wait_ge(s["proj_done"], c + 1)
                act.activation(sq[:, c, :], ps[:, 1 + c, :], ACT.Square).then_inc(s["sq_done"], 1)
            for j, (width_j, *_) in enumerate(NORMS):
                act.wait_ge(s["ms_done"], j + 1)
                act.activation(std[:, j, :], ps[:, 5 + j, :], ACT.Sqrt, scale=1.0 / width_j, bias=k.eps_rms[:]).then_inc(s["std_done"], 1)

        @block.vector
        def _(dve):
            step = Steps(dve, s["vec_step"])
            dve.wait_ge(s["loaded"], 32)
            dve.tensor_copy(pos[:], pos_i[:]).then_inc(s["pos_ready"], 1)
            dve.wait_ge(s["angle_done"], 1)
            step(dve.tensor_copy(raw[:], ps[0:ROPE, 0, :]))
            reduced_angle(step, dve, angle[:], turns[:], raw[:], 0.0)
            reduced_angle(step, dve, cos[:], turns[:], raw[:], math.pi / 2)
            dve.wait_ge(s["sin_done"], 2)
            step(dve.tensor_scalar(sin[0:half, :], sin[0:half, :], -1.0, None, ALU.mult))
            dve.wait_ge(s["proj_done"], 4)
            rotate(step, dve, k_pe, ps[0:ROPE, 4, :], raw, swapped, cos, sin, 1.0)
            for j, (_, first, n, norm) in enumerate(NORMS):
                dve.wait_ge(s["std_done"], j + 1)
                step(dve.reciprocal(std[:, j, :], std[:, j, :]))
                for c in range(n):
                    dst = cq[:, c, :] if j == 0 else ckv[:]
                    step(dve.scalar_tensor_tensor(out=dst, in0=ps[:, 1 + first + c, :], scalar=k.col(norm, c), in1=std[:, j, :],
                                                  op0=ALU.mult, op1=ALU.mult))


ROPE_THETA = 10000.0


def rotate(step, dve, out, src, raw, swapped, cos, sin, scale, last=None):
    half = ROPE // 2
    step(dve.tensor_scalar(swapped[0:half, :], src[half:ROPE], scale, None, ALU.mult))
    step(dve.tensor_scalar(swapped[half:ROPE, :], src[0:half], scale, None, ALU.mult))
    step(dve.tensor_tensor(swapped[:], swapped[:], sin[:], ALU.mult))
    step(dve.scalar_tensor_tensor(out=raw[:], in0=src, scalar=scale, in1=cos[:], op0=ALU.mult, op1=ALU.mult))
    ins = dve.tensor_tensor(out[:], raw[:], swapped[:], ALU.add)
    if last is None:
        step(ins)
    else:
        ins.then_inc(last, 1)


def latent_attention_stage(k, cq, ckv, k_pe, cos, sin, o):
    ps = k.ps
    scale = 1.0 / math.sqrt(NOPE + ROPE)
    nq = QL // P
    with k.stage("latent_attention", "w_loaded", "qn_done", "qp_done", "kn_done", "v_done", "copied", "q_turned", "rope_step", *SOFTMAX, primed=("copied", "exp_done", "o_copied", "scores_done", "v_done", "weighed")) as (block, s, sb):
        wq, wkv = sb("wq", [P, nq, NOPE + ROPE]), sb("wkv", [P, NOPE + VD])
        qn, kn, qp = sb("qn", [P, T]), sb("kn", [P, T]), sb("qp", [ROPE, T])
        raw, swapped = sb("raw", [ROPE, T]), sb("swapped", [ROPE, T])
        v = sb("v", [P, TB, VD])
        p_tiles, pt_tiles = sb("p_tiles", [P, 3, T]), sb("pt_tiles", [P, 2, T])
        nmax, rsum, rinv = sb("nmax", [P, TB]), sb("rsum", [P, TB]), sb("rinv", [P, TB])
        units = [(slice(0, VD), b) for b in range(TB)]

        def scores(pe, unit, bank):
            b = unit[1]
            n = (b + 1) * P
            pe.matmul(ps[:, bank, 0:n], qn[:, b * P:n], kn[:, 0:n], start=True, stop=False)
            return pe.matmul(ps[:, bank, 0:n], qp[:, b * P:n], k_pe[:, 0:n], start=False, stop=True)

        tensor, vector, scalar = scan_softmax(k, s, units, scores, p_tiles, pt_tiles, lambda unit, kb: v[:, kb, :], nmax, rsum, rinv)

        @block.sync
        def _(sp):
            k.clear(sp)
            with sp.Fori(0, MLA_HEADS) as i:
                sp.wait_ge(s["v_done"], 1 + i)
                sp.dma_start(wq[:], columns(k.ins["mla_w_qb_2"][0], i * (NOPE + ROPE), NOPE + ROPE)).then_inc(s["w_loaded"], 16)
                sp.dma_start(wkv[:], k.ins["mla_w_kvb_2"][0][:, bass.ds(i * (NOPE + VD), NOPE + VD)]).then_inc(s["w_loaded"], 16)

        @block.tensor
        def _(pe):
            with pe.Fori(0, MLA_HEADS) as i:
                pe.wait_ge(s["w_loaded"], 32 * (i + 1))
                pe.wait_ge(s["copied"], 1 + 3 * i)
                for c in range(nq):
                    mm = pe.matmul(ps[:, 6, :], wq[:, c, 0:NOPE], cq[:, c, :], start=(c == 0), stop=(c == nq - 1))
                mm.then_inc(s["qn_done"], 1)
                for c in range(nq):
                    mm = pe.matmul(ps[0:ROPE, 7, :], wq[:, c, NOPE:], cq[:, c, :], start=(c == 0), stop=(c == nq - 1))
                mm.then_inc(s["qp_done"], 1)
                pe.wait_ge(s["copied"], 1 + 3 * i + 1)
                pe.matmul(ps[:, 6, :], wkv[:, 0:NOPE], ckv[:], start=True, stop=True).then_inc(s["kn_done"], 1)
                pe.wait_ge(s["q_turned"], i + 1)
                for b in range(TB):
                    mm = pe.matmul(ps[:, 7, b * P:(b + 1) * P], ckv[:, b * P:(b + 1) * P], wkv[:, NOPE:], start=True, stop=True)
                mm.then_inc(s["v_done"], 1)
                pe.wait_ge(s["copied"], 1 + 3 * i + 3)
                tensor(pe, i)

        @block.scalar
        def _(act):
            with act.Fori(0, MLA_HEADS) as i:
                act.wait_ge(s["qn_done"], i + 1)
                act.wait_ge(s["weighed"], 1 + TB * i)
                act.activation(qn[:], ps[:, 6, :], ACT.Copy, scale=scale).then_inc(s["copied"], 1)
                act.wait_ge(s["kn_done"], i + 1)
                act.activation(kn[:], ps[:, 6, :], ACT.Copy).then_inc(s["copied"], 1)
                act.wait_ge(s["v_done"], 1 + i + 1)
                act.activation(v[:], ps[:, 7, :].rearrange("p (b n) -> p b n", b=TB), ACT.Copy).then_inc(s["copied"], 1)
                scalar(act, i)

        @block.vector
        def _(dve):
            with dve.Fori(0, MLA_HEADS) as i:
                step = Steps(dve, s["rope_step"], 4 * i)
                dve.wait_ge(s["qp_done"], i + 1)
                dve.wait_ge(s["scores_done"], 1 + TB * i)
                rotate(step, dve, qp, ps[0:ROPE, 7, :], raw, swapped, cos, sin, scale, s["q_turned"])
                assert step.n == 4
                n = vector(dve, i)
                assert n == 2 * TB
                dve.wait_ge(s["weighed"], 1 + TB * (i + 1))
                dve.tensor_copy(o[:, bass.ds(i, 1), :], ps[:, 5:6, :]).then_inc(s["o_copied"], 1)


def mlp_up_stage(k, name, layer, hidden):
    ps, w = k.ps, k.ins["mlp_w1_2"][layer]
    first = k.places["mlp_b1_2"][0] + layer * K2
    with k.stage(name, "relu_done", "squared", *LINEAR, primed=LINEAR_PRIMED + ("squared",)) as (block, s, sb):
        r = sb("r", [P, 2, T])
        done, free = (s["tile_done0"], s["tile_done1"]), (s["tile_free0"], s["tile_free1"])
        pairs = DF2 // STRIP // 2
        linear(k, block, s, lambda i, slot: columns(w, (2 * i + slot) * STRIP), pairs, lambda kk: k.h[:, kk, :], None)

        @block.scalar
        def _(act):
            with act.Fori(0, pairs) as i:
                for slot in range(2):
                    for f in range(FT):
                        at = (2 * i + slot) * FT + f
                        act.wait_ge(done[slot], 1 + FT * i + f + 1)
                        if slot * FT + f >= 2:
                            act.wait_ge(s["squared"], 1 + at - 1)
                        else:
                            act.wait_ge(s["squared"], 1 + 2 * FT * i)
                        act.activation(r[:, f % 2, :], ps[:, slot * FT + f, :], ACT.Relu,
                                       bias=k.cols[:, bass.ds(first + at, 1)]).then_inc(free[slot], 1)

        @block.vector
        def _(dve):
            with dve.Fori(0, pairs) as i:
                for slot in range(2):
                    for f in range(FT):
                        dve.wait_ge(free[slot], 1 + FT * i + f + 1)
                        dve.tensor_tensor(hidden[:, bass.ds((2 * i + slot) * FT + f, 1), :], r[:, f % 2:f % 2 + 1, :],
                                          r[:, f % 2:f % 2 + 1, :], ALU.mult).then_inc(s["squared"], 1)


def mlp_down_stage(k, name, layer, hidden, gate):
    ps, w = k.ps, k.ins["mlp_w2_2"][layer]
    chunks = K2 // KD
    with k.stage(name, "loaded0", "loaded1", "used0", "used1", "half_done", "vec_step") as (block, s, sb):
        t = sb("t", [P, 2, T])
        loaded, used = (s["loaded0"], s["loaded1"]), (s["used0"], s["used1"])

        @block.sync
        def _(sp):
            k.clear(sp)
            for n in range(2 * chunks):
                if n >= 2:
                    sp.wait_ge(used[n % 2], n // 2)
                sp.dma_start(strip(k, n % 2), columns(w[n % chunks * D:(n % chunks + 1) * D, :], n // chunks * STRIP)).then_inc(loaded[n % 2], 16)

        @block.tensor
        def _(pe):
            for n in range(2 * chunks):
                half, chunk = n // chunks, n % chunks
                pe.wait_ge(loaded[n % 2], 16 * (n // 2 + 1))
                for f in range(FT):
                    for kk in range(KD):
                        mm = pe.matmul(ps[:, half * FT + f, :], strip(k, n % 2)[:, kk, f * P:(f + 1) * P], hidden[:, chunk * KD + kk, :],
                                       start=(chunk == 0 and kk == 0), stop=(chunk == chunks - 1 and kk == KD - 1))
                mm.then_inc(used[n % 2], 1)

        @block.vector
        def _(dve):
            step = Steps(dve, s["vec_step"])
            for c in range(KD):
                if c % FT == 0:
                    dve.wait_ge(used[1], chunks // 2 * (c // FT + 1))
                step(dve.tensor_scalar(t[:, c % 2, :], ps[:, c, :], k.col("mlp_b2_2", layer * KD + c), k.mod[:, gate + c:gate + c + 1],
                                       ALU.add, ALU.mult))
                step(dve.scalar_tensor_tensor(out=k.x[:, c, :], in0=k.x[:, c, :], scalar=ALPHA_2, in1=t[:, c % 2, :], op0=ALU.mult, op1=ALU.add))


SB = 32


class S5Tables:

    def __init__(self, sb):
        self.mag = sb("mag", [P, S5_TILES])
        self.turn_b = sb("turn_b", [P, 2, S5_TILES, SB])
        self.turn_a = sb("turn_a", [P, 2, S5_TILES, T // SB + 1])
        self.b_t = sb("b_t", [P, 2, KD, P])
        self.c_t = sb("c_t", [P, 3, KD, P])


def s5_tables_stage(k, tab):
    ps = k.ps
    J = S5_TILES
    with k.stage("s5_tables", "loaded", "exp_done", "vec_step", "b_ready", "c_ready", "zeroed", "b_turned", "b_copied", "c_turned", "c_copied") as (block, s, sb):
        dt, angle, turns = sb("dt", [P, J]), sb("angle", [P, J]), sb("turns", [P, J])
        rs, rc = sb("rs", [P, J]), sb("rc", [P, J])
        t1, t2 = sb("t1", [P, J]), sb("t2", [P, J])
        c_re, c_im = sb("coef_re", [P, J]), sb("coef_im", [P, J])
        b_raw = sb("b_raw", [P, 2, J, GC])
        b_tmp = sb("b_tmp", [P, J, GC])
        b_out = sb("b_out", [P, J, GC])
        b_bd = sb("b_bd", [P, 2, J, 2 * GC])
        c_raw = sb("c_raw", [P, 2, KD, STATE])
        c_bd = sb("c_bd", [P, 2, KD, 2 * STATE])
        odd = sb("odd", [P, 2])
        tmp = sb("tmp", [P, J, SB])
        lr = k.cols[:, k.places["ssm_a_re_2"][0]:k.places["ssm_a_re_2"][0] + J]
        li = k.cols[:, k.places["ssm_a_im_2"][0]:k.places["ssm_a_im_2"][0] + J]

        @block.sync
        def _(sp):
            k.clear(sp)
            for half in range(2):
                sp.dma_start(dt[half * STATE:(half + 1) * STATE, :],
                             k.ins["ssm_log_dt_2"].rearrange("l (j two) -> two l j", two=2)[half].to_broadcast([STATE, J]),
                             allow_slow_non_contiguous=True).then_inc(s["loaded"], 16)
            for j, name in enumerate(("ssm_b_re_2", "ssm_b_im_2")):
                sp.dma_start(b_raw[:, j], k.ins[name][0].rearrange("(j two) s c -> (two s) j c", two=2)).then_inc(s["loaded"], 16)
            for j, name in enumerate(("ssm_c_re_2", "ssm_c_im_2")):
                sp.dma_start(c_raw[:, j], k.ins[name][0].rearrange("(k g) c s -> (g c) k s", k=KD)).then_inc(s["loaded"], 16)

        @block.gpsimd
        def _(pool):
            pool.memset(b_bd[:], 0.0).then_inc(s["zeroed"], 1)
            pool.memset(tab.turn_a[:, 0, :, 0:1], 1.0).then_inc(s["zeroed"], 1)
            pool.memset(tab.turn_a[:, 1, :, 0:1], 0.0).then_inc(s["zeroed"], 1)

        @block.scalar
        def _(act):
            act.wait_ge(s["loaded"], 96)
            act.activation(dt[:], dt[:], ACT.Exp).then_inc(s["exp_done"], 1)
            act.wait_ge(s["vec_step"], 2)
            act.activation(tab.mag[:], t1[:], ACT.Exp).then_inc(s["exp_done"], 1)
            act.wait_ge(s["vec_step"], 16)
            act.activation(rs[:], rs[:], ACT.Sin).then_inc(s["exp_done"], 1)
            act.activation(rc[:], rc[:], ACT.Sin).then_inc(s["exp_done"], 1)
            for n in range(2 * KD):
                if n % 4 == 0:
                    act.wait_ge(s["b_turned"], n // 4 + 1)
                    act.activation(tab.b_t[:, n // 8, n % 8:n % 8 + 4, :], ps[:, n // 4, :].rearrange("p (b n) -> p b n", b=4),
                                   ACT.Copy).then_inc(s["b_copied"], 1)
            for n in range(4):
                act.wait_ge(s["c_turned"], n + 1)
                src = ps[:, 4 + n, :].rearrange("p (b n) -> p b n", b=4)
                at = n % 2 * 4
                if n < 2:
                    act.activation(tab.c_t[:, 0, at:at + 4, :], src, ACT.Copy).then_inc(s["c_copied"], 1)
                act.activation(tab.c_t[:, 1 if n < 2 else 2, at:at + 4, :], src, ACT.Copy, scale=-1.0).then_inc(s["c_copied"], 1)

        @block.tensor
        def _(pe):
            pe.wait_ge(s["b_ready"], 4)
            for n in range(2 * KD):
                mm = pe.transpose(ps[:, n // 4, n % 4 * P:(n % 4 + 1) * P],
                                  b_bd[:, n // 8, n % 8 * 4:n % 8 * 4 + 4, :].rearrange("p j c -> p (j c)"), k.ident[:])
                if n % 4 == 3:
                    mm.then_inc(s["b_turned"], 1)
            pe.wait_ge(s["c_ready"], 4)
            for n in range(2 * KD):
                mm = pe.transpose(ps[:, 4 + n // 4, n % 4 * P:(n % 4 + 1) * P], c_bd[:, n // 8, n % 8, :], k.ident[:])
                if n % 4 == 3:
                    mm.then_inc(s["c_turned"], 1)

        @block.vector
        def _(dve):
            step = Steps(dve, s["vec_step"])
            dve.wait_ge(s["exp_done"], 1)
            step(dve.tensor_tensor(angle[:], li, dt[:], ALU.mult))
            step(dve.tensor_tensor(t1[:], lr, dt[:], ALU.mult))
            reduced_angle(step, dve, rs[:], turns[:], angle[:], 0.0)
            reduced_angle(step, dve, rc[:], turns[:], angle[:], math.pi / 2)
            dve.wait_ge(s["exp_done"], 4)
            step(dve.tensor_tensor(t1[:], tab.mag[:], rc[:], ALU.mult))
            step(dve.tensor_scalar(t1[:], t1[:], -1.0, None, ALU.add))
            step(dve.tensor_tensor(t2[:], tab.mag[:], rs[:], ALU.mult))
            step(dve.tensor_tensor(c_re[:], t1[:], lr, ALU.mult))
            step(dve.tensor_tensor(turns[:], t2[:], li, ALU.mult))
            step(dve.tensor_tensor(c_re[:], c_re[:], turns[:], ALU.add))
            step(dve.tensor_tensor(c_im[:], t2[:], lr, ALU.mult))
            step(dve.tensor_tensor(turns[:], t1[:], li, ALU.mult))
            step(dve.tensor_tensor(c_im[:], c_im[:], turns[:], ALU.subtract))
            step(dve.tensor_tensor(t1[:], lr, lr, ALU.mult))
            step(dve.tensor_tensor(t2[:], li, li, ALU.mult))
            step(dve.tensor_tensor(t1[:], t1[:], t2[:], ALU.add))
            step(dve.reciprocal(t1[:], t1[:]))
            step(dve.tensor_tensor(c_re[:], c_re[:], t1[:], ALU.mult))
            step(dve.tensor_tensor(c_im[:], c_im[:], t1[:], ALU.mult))

            def over(m, n):
                return m.rearrange("p (j o) -> p j o", o=1).to_broadcast([P, J, n])

            dve.wait_ge(s["zeroed"], 3)
            for out, (a, b), op in ((0, (c_re, c_im), ALU.subtract), (1, (c_im, c_re), ALU.add)):
                step(dve.tensor_tensor(b_out[:], b_raw[:, 0], over(a[:], GC), ALU.mult))
                step(dve.tensor_tensor(b_tmp[:], b_raw[:, 1], over(b[:], GC), ALU.mult))
                for half in range(2):
                    rows = slice(half * STATE, (half + 1) * STATE)
                    dve.tensor_tensor(b_bd[rows, out, :, half * GC:(half + 1) * GC], b_out[rows], b_tmp[rows], op).then_inc(s["b_ready"], 1)
                dve.wait_ge(s["b_ready"], 2 * out + 2)
            step(dve.tensor_reduce(odd[:, 1:2], k.ident[:].rearrange("p (j two c) -> p j two c", two=2, c=GC)[:, :, 1, :], AX.XY, ALU.add))
            step(dve.tensor_scalar(odd[:, 0:1], odd[:, 1:2], -1.0, 1.0, ALU.mult, ALU.add))
            for j in range(2):
                for half in range(2):
                    dve.tensor_scalar(c_bd[:, j, :, half * STATE:(half + 1) * STATE], c_raw[:, j], odd[:, half:half + 1], None,
                                      ALU.mult).then_inc(s["c_ready"], 1)

            def times(out, n, at, a, first):
                re, im = a[:, 0, :, first:first + n], a[:, 1, :, first:first + n]
                wr, wi = (a[:, j, :, at - 1:at].to_broadcast([P, J, n]) for j in range(2))
                ore, oim = out[:, 0, :, at:at + n], out[:, 1, :, at:at + n]
                step(dve.tensor_tensor(ore, re, wr, ALU.mult))
                step(dve.tensor_tensor(tmp[:, :, 0:n], im, wi, ALU.mult))
                step(dve.tensor_tensor(ore, ore, tmp[:, :, 0:n], ALU.subtract))
                step(dve.tensor_tensor(oim, re, wi, ALU.mult))
                step(dve.tensor_tensor(tmp[:, :, 0:n], im, wr, ALU.mult))
                step(dve.tensor_tensor(oim, oim, tmp[:, :, 0:n], ALU.add))

            for j, m in enumerate((rc, rs)):
                step(dve.tensor_copy(tab.turn_b[:, j, :, 0:1], m[:].rearrange("p (j o) -> p j o", o=1)))
            n = 1
            while n < SB:
                times(tab.turn_b, n, n, tab.turn_b, 0)
                n *= 2
            for j in range(2):
                step(dve.tensor_copy(tab.turn_a[:, j, :, 1:2], tab.turn_b[:, j, :, SB - 1:SB]))
            n = 1
            while n < T // SB:
                times(tab.turn_a, n, n + 1, tab.turn_a, 1)
                n *= 2


def s5_scan_stage(k, tab, u, g):
    ps = k.ps
    NT = S5_TILES // KD
    GELU = 2 * math.sqrt(2 / math.pi)
    VEC = 29
    A = T // 32
    with k.stage("s5_scan", "staged", "bu_done", "table_step", "table_done", "vec_step", "products_done", "table_used", "y_done", "y_out",
                 "sq_done", "inner_done", "sig_done", "g_done", primed=("g_done", "table_used", "y_out")) as (block, s, sb):
        uk, bk, ck = sb("uk", [P, T]), sb("bk", [P, 2, P]), sb("ck", [P, 3, P])
        ta, tb = sb("ta", [P, 2, A]), sb("tb", [P, 2, 32])
        turn, tt = sb("turn", [P, 2, 2, T]), sb("tt", [P, T])
        w, m = sb("w", [P, 2, T]), sb("m", [P, 2, T])
        z = sb("z", [P, 2, T])
        pr = sb("pr", [P, 2, 4, T])
        y, q = sb("y", [P, T]), sb("q", [P, T])

        @block.sync
        def _(sp):
            k.clear(sp)

        @block.gpsimd
        def _(pool):
            with pool.Fori(0, KD) as i:
                pool.wait_ge(s["y_out"], 1 + i)
                pool.tensor_copy(uk[:], u[:, bass.ds(i, 1), :].rearrange("p o t -> p (o t)")).then_inc(s["staged"], 1)
                pool.tensor_copy(bk[:], tab.b_t[:, :, bass.ds(i, 1), :].rearrange("p r o n -> p r (o n)")).then_inc(s["staged"], 1)
                pool.tensor_copy(ck[:], tab.c_t[:, :, bass.ds(i, 1), :].rearrange("p r o n -> p r (o n)")).then_inc(s["staged"], 1)
                step = Steps(pool, s["table_step"], 7 * NT * i)
                for j in range(NT):
                    tile = bass.ds(NT * i + j, 1)
                    step(pool.tensor_copy(ta[:], tab.turn_a[:, :, tile, 0:A].rearrange("p r o a -> p r (o a)")))
                    step(pool.tensor_copy(tb[:], tab.turn_b[:, :, tile, :].rearrange("p r o b -> p r (o b)")))
                    if j >= 2:
                        pool.wait_ge(s["products_done"], NT * i + j - 1)
                    ar, ai = (ta[:, r, :].rearrange("p (a b) -> p a b", b=1).to_broadcast([P, A, 32]) for r in range(2))
                    br, bi = (tb[:, r:r + 1, :].to_broadcast([P, A, 32]) for r in range(2))
                    c, sn = (turn[:, j % 2, r, :].rearrange("p (a b) -> p a b", a=A) for r in range(2))
                    t = tt[:].rearrange("p (a b) -> p a b", a=A)
                    step(pool.tensor_tensor(c, ar, br, ALU.mult))
                    step(pool.tensor_tensor(t, ai, bi, ALU.mult))
                    step(pool.tensor_tensor(c, c, t, ALU.subtract))
                    step(pool.tensor_tensor(sn, ar, bi, ALU.mult))
                    step(pool.tensor_tensor(t, ai, br, ALU.mult))
                    pool.tensor_tensor(sn, sn, t, ALU.add).then_inc(s["table_done"], 1)
                    pool.wait_ge(s["table_done"], NT * i + j + 1)
                assert step.n == 7 * NT

        @block.tensor
        def _(pe):
            with pe.Fori(0, KD) as i:
                pe.wait_ge(s["staged"], 3 * (i + 1))

                def inputs(j):
                    if j >= 2:
                        pe.wait_ge(s["table_used"], 1 + NT * i + j - 1)
                    else:
                        pe.wait_ge(s["table_used"], 1 + NT * i)
                    rows = slice(32 * j, 32 * j + 32)
                    for r in range(2):
                        mm = pe.matmul(ps[:, 2 * (j % 2) + r, :], bk[rows, r, :], uk[rows, :], start=True, stop=True)
                    mm.then_inc(s["bu_done"], 1)

                inputs(0)
                pe.wait_ge(s["y_out"], 1 + i)
                for j in range(NT):
                    if j + 1 < NT:
                        inputs(j + 1)
                    pe.wait_ge(s["products_done"], NT * i + j + 1)
                    rows = slice(32 * j, 32 * j + 32)
                    for n, r in enumerate((0, 1, 2, 2)):
                        mm = pe.matmul(ps[rows, 4, :], ck[:, r, 32 * j:32 * j + 32], pr[:, j % 2, n, :], start=(n == 0), stop=(n == 3))
                    mm.then_inc(s["y_done"], 1)

        @block.scalar
        def _(act):
            with act.Fori(0, KD) as i:
                act.wait_ge(s["y_out"], 1 + i + 1)
                act.activation(q[:], y[:], ACT.Square).then_inc(s["sq_done"], 1)
                act.wait_ge(s["inner_done"], i + 1)
                act.activation(q[:], q[:], ACT.Sigmoid, scale=GELU).then_inc(s["sig_done"], 1)

        @block.vector
        def _(dve):
            with dve.Fori(0, KD) as i:
                step = Steps(dve, s["vec_step"], VEC * i)
                for j in range(NT):
                    c, sn = turn[:, j % 2, 0, :], turn[:, j % 2, 1, :]
                    br, bi = ps[:, 2 * (j % 2), :], ps[:, 2 * (j % 2) + 1, :]
                    dve.wait_ge(s["table_done"], NT * i + j + 1)
                    dve.wait_ge(s["bu_done"], NT * i + j + 1)
                    step(dve.tensor_tensor(w[:, 0, :], c, br, ALU.mult))
                    step(dve.tensor_tensor(m[:, 0, :], sn, bi, ALU.mult))
                    step(dve.tensor_tensor(w[:, 0, :], w[:, 0, :], m[:, 0, :], ALU.add))
                    step(dve.tensor_tensor(w[:, 1, :], c, bi, ALU.mult))
                    dve.tensor_tensor(m[:, 1, :], sn, br, ALU.mult).then_inc(s["table_used"], 1)
                    dve.wait_ge(s["table_used"], 1 + NT * i + j + 1)
                    step(dve.tensor_tensor(w[:, 1, :], w[:, 1, :], m[:, 1, :], ALU.subtract))
                    mag = tab.mag[:, bass.ds(NT * i + j, 1)].to_broadcast([P, T])
                    for r in range(2):
                        step(dve.tensor_tensor_scan(z[:, r, :], mag, w[:, r, :], 0.0, ALU.mult, ALU.add))
                    if j >= 2:
                        dve.wait_ge(s["y_done"], NT * i + j - 1)
                    for n, (a, r) in enumerate(((c, 0), (sn, 1), (c, 1), (sn, 0))):
                        ins = dve.tensor_tensor(pr[:, j % 2, n, :], a, z[:, r, :], ALU.mult)
                    ins.then_inc(s["products_done"], 1)
                dve.wait_ge(s["y_done"], NT * (i + 1))
                dve.wait_ge(s["g_done"], 1 + i)
                dve.scalar_tensor_tensor(out=y[:], in0=uk[:], scalar=k.cols[:, bass.ds(k.places["ssm_d_2"][0] + i, 1)], in1=ps[:, 4, :],
                                         op0=ALU.mult, op1=ALU.add).then_inc(s["y_out"], 1)
                dve.wait_ge(s["y_out"], 1 + i + 1)
                dve.wait_ge(s["sq_done"], i + 1)
                step(dve.tensor_scalar(q[:], q[:], 0.044715, 1.0, ALU.mult, ALU.add))
                dve.tensor_tensor(q[:], q[:], y[:], ALU.mult).then_inc(s["inner_done"], 1)
                dve.wait_ge(s["sig_done"], i + 1)
                dve.tensor_tensor(g[:, bass.ds(i, 1), :], y[:].rearrange("p (o t) -> p o t", o=1), q[:].rearrange("p (o t) -> p o t", o=1),
                                  ALU.mult).then_inc(s["g_done"], 1)
                assert step.n == VEC, step.n


def project_stage(k, name, w, dst):
    ps = k.ps
    with k.stage(name, *LINEAR, primed=LINEAR_PRIMED) as (block, s, sb):
        done, free = (s["tile_done0"], s["tile_done1"]), (s["tile_free0"], s["tile_free1"])
        linear(k, block, s, lambda i, slot: columns(w, (2 * i + slot) * STRIP), 1, lambda kk: k.h[:, kk, :], None)

        @block.scalar
        def _(act):
            for c in range(KD):
                act.wait_ge(done[c // FT], 1 + c % FT + 1)
                act.activation(dst[:, c, :], ps[:, c, :], ACT.Copy).then_inc(free[c // FT], 1)


def glu_stage(k, g, z):
    ps, w = k.ps, k.ins["ssm_w_glu_2"][0]
    with k.stage("glu", "gated", *LINEAR, primed=LINEAR_PRIMED) as (block, s, sb):
        done, free = (s["tile_done0"], s["tile_done1"]), (s["tile_free0"], s["tile_free1"])
        sig = sb("sig", [P, 2, T])
        linear(k, block, s, lambda i, slot: columns(w, (2 * i + slot) * STRIP), 1, lambda kk: g[:, kk, :], None)

        @block.scalar
        def _(act):
            for c in range(KD):
                act.wait_ge(done[c // FT], 1 + c % FT + 1)
                if c >= 2:
                    act.wait_ge(s["gated"], c - 1)
                act.activation(sig[:, c % 2, :], ps[:, c, :], ACT.Sigmoid, bias=k.col("ssm_b_glu_2", c)).then_inc(free[c // FT], 1)

        @block.vector
        def _(dve):
            for c in range(KD):
                dve.wait_ge(free[c // FT], 1 + c % FT + 1)
                dve.tensor_tensor(z[:, c, :], g[:, c, :], sig[:, c % 2, :], ALU.mult).then_inc(s["gated"], 1)


def second_block(k):
    col = lambda name, layer: (lambda c: k.col(name, layer * KD + c))
    for layer in range(2):
        mix, ffn = 48 + 48 * layer, 72 + 48 * layer
        modulate_stage(k, f"mod_mix{layer}", mix)
        with ExitStack() as branch:
            if layer == 0:
                sb = lambda n, shape: k.sb(n, shape, stack=branch)
                cq, ckv, k_pe = sb("cq", [P, QL // P, T]), sb("ckv", [P, T]), sb("k_pe", [ROPE, T])
                cos, sin = sb("cos", [ROPE, T]), sb("sin", [ROPE, T])
                o = sb("latent_out", [P, KD, T])
                latent_stage(k, cq, ckv, k_pe, cos, sin)
                latent_attention_stage(k, cq, ckv, k_pe, cos, sin, o)
                residual_stage(k, "latent_proj", k.ins["mla_w_o_2"][0], o, ALPHA_2, mix + 16)
            else:
                g = k.sb("g", [P, KD, T], stack=branch)
                with ExitStack() as scan:
                    sb = lambda n, shape: k.sb(n, shape, stack=scan)
                    u = sb("u", [P, KD, T])
                    tab = S5Tables(sb)
                    project_stage(k, "s5_in", k.ins["ssm_w_in_2"][0], u)
                    s5_tables_stage(k, tab)
                    s5_scan_stage(k, tab, u, g)
                z = k.sb("z", [P, KD, T], stack=branch)
                glu_stage(k, g, z)
                residual_stage(k, "s5_proj", k.ins["ssm_w_out_2"][0], z, ALPHA_2, mix + 16)
        norm_stage(k, f"norm_mix{layer}", k.x, k.x, col("ln_mix_g_2", layer), col("ln_mix_b_2", layer))
        modulate_stage(k, f"mod_ffn{layer}", ffn)
        with ExitStack() as mlp:
            hidden = k.sb(f"hidden{layer}", [P, K2, T], stack=mlp)
            mlp_up_stage(k, f"mlp_up{layer}", layer, hidden)
            mlp_down_stage(k, f"mlp_down{layer}", layer, hidden, ffn + 16)
        norm_stage(k, f"norm_ffn{layer}", k.x, k.x, col("ln_ffn_g_2", layer), col("ln_ffn_b_2", layer))


def build(nc, ins, out):
    with ExitStack() as stack:
        k = Kernel(nc, stack, ins)
        constants_stage(k)
        modulation_stage(k)
        ones = lambda c: 1.0
        mod = lambda first: (lambda c: k.mod[:, first + c:first + c + 1])
        norm_stage(k, "norm_in", k.x, k.h, mod(8), mod(0))
        with ExitStack() as mix:
            merged = k.sb("merged", [P, KD, T], stack=mix)
            forget_stage(k)
            with ExitStack() as branch:
                o = k.sb("attended", [P, KD, T], stack=branch)
                attention_stage(k, o)
                merge_stage(k, "merge_att", 0, lambda at, n: columns(k.ins["w_attn_o"][0], at, n), o, KD, merged)
            with ExitStack() as branch:
                pooled = k.sb("pooled", [P, KD, T], stack=branch)
                pool_stage(k, pooled)
                pool_out_stage(k, pooled, merged)
            with ExitStack() as branch:
                ys = k.sb("ys", [P, KI, T], stack=branch)
                ssm_stage(k, ys)
                merge_stage(k, "merge_ssm", 2, lambda at, n: columns(k.ins["w_ssm_o"][0], at, n), ys, KI, merged)
            residual_stage(k, "mix_out", k.ins["w_out"][0], merged, ALPHA_1, 16)
        norm_stage(k, "norm_mix", k.x, k.x, lambda c: k.col("ln_mix_g", c), lambda c: k.col("ln_mix_b", c))
        norm_stage(k, "norm_ffn_in", k.x, k.h, mod(32), mod(24))
        router_stage(k)
        with ExitStack() as ffn:
            total = k.sb("total", [P, KD, T], stack=ffn)
            experts_stage(k, total)
            add_residual_stage(k, "ffn_out", ALPHA_1, 40, total)
        norm_stage(k, "norm_ffn", k.x, k.x, lambda c: k.col("ln_ffn_g", c), lambda c: k.col("ln_ffn_b", c))
        second_block(k)
        output_stage(k, out)


_INS = ["x", "c", "w_in", "b_forget", "w_attn_o", "w_pool", "pool_scale", "conv_w", "conv_b", "dt_bias", "a_log", "d_skip",
        "ssm_norm_w", "w_ssm_o", "w_out", "w_ada", "b_ada", "ln_mix_g", "ln_mix_b", "ln_ffn_g", "ln_ffn_b", "w_router",
        "b_router", "w_exp_gate", "w_exp_up", "w_exp_down", "c_2", "positions_2", "mla_w_in_2", "mla_q_norm_2", "mla_w_qb_2",
        "mla_kv_norm_2", "mla_w_kvb_2", "mla_w_o_2", "ssm_w_in_2", "ssm_log_dt_2", "ssm_a_re_2", "ssm_a_im_2", "ssm_b_re_2",
        "ssm_b_im_2", "ssm_c_re_2", "ssm_c_im_2", "ssm_d_2", "ssm_w_glu_2", "ssm_b_glu_2", "ssm_w_out_2", "mlp_w1_2", "mlp_b1_2",
        "mlp_w2_2", "mlp_b2_2", "mod_mix_w_2", "mod_mix_b_2", "mod_ffn_w_2", "mod_ffn_b_2", "ln_mix_g_2", "ln_mix_b_2",
        "ln_ffn_g_2", "ln_ffn_b_2"]


def kernel(**inputs):
    import numpy as _np
    import concourse.bacc as _bacc
    from concourse import mybir as _mybir
    from concourse.bass_utils import run_bass_kernel_spmd as _run

    nc = _bacc.Bacc("TRN2", target_bir_lowering=False, num_devices=1)
    arrays, ins = {}, {}
    for name in _INS:
        a = _np.ascontiguousarray(inputs[name])
        arrays[f"in_{name}_dram"] = a
        ins[name] = nc.dram_tensor(f"in_{name}_dram", a.shape, _mybir.dt.from_np(a.dtype), kind="ExternalInput").ap()
    out = nc.dram_tensor("out_0_dram", (1, T, D), F32, kind="ExternalOutput").ap()
    build(nc, ins, out)
    r = _run(nc, [arrays], core_ids=[0])
    return r.results[0]["out_0_dram"]
```

```python
from contextlib import ExitStack, contextmanager
import math

import concourse.bass as bass
from concourse import mybir

F32 = mybir.dt.float32
I32 = mybir.dt.int32
F32R = mybir.dt.float32r
ALU = mybir.AluOpType
ACT = mybir.ActivationFunctionType
AX = mybir.AxisListType

P = 128
D = 1024
KD = D // P
T = 512
TB = T // P
STRIP = 512
FT = STRIP // P
HALF = STRIP // 2
HT = HALF // P

HEADS, HD = 16, 64
G_SSM, R_SSM, P_SSM, N_SSM = 4, 8, 64, 128
SSM_INNER = G_SSM * R_SSM * P_SSM
KG = SSM_INNER // G_SSM // P
KI = SSM_INNER // P
CONV = 4
XBC_TILES = (SSM_INNER + 2 * G_SSM * N_SSM) // P
Q0, K0, V0 = 0, D, 2 * D
F0 = 3 * D
U0 = F0 + HEADS
Z0 = U0 + D
XBC0 = Z0 + SSM_INNER
B0 = XBC0 + SSM_INNER
C0 = B0 + G_SSM * N_SSM
DT0 = XBC0 + XBC_TILES * P
GATE0 = DT0 + G_SSM * R_SSM
IN_WIDTH = GATE0 + 3 * D
POOL_WINDOWS = (2, 4, 8, 16)
PAD = max(POOL_WINDOWS)
NE, EG, DFF = 16, 4, 512
KE = DFF // P
TOP = 2
NBLK = NE + (TOP * T - NE) // P
ALPHA_1 = 2 ** 0.25
LN_EPS, RMS_EPS = 1e-5, 1e-6

MLA_HEADS, NOPE, ROPE, VD = 8, 128, 64, 128
QL, KVL = 256, 128
GC, STATE = 16, 64
S5_GROUPS = D // GC
S5_TILES = S5_GROUPS * STATE // P
DF2 = 4 * D
K2 = DF2 // P
ALPHA_2 = 4 ** 0.25

NEG = -1e30
TWO_PI = 2 * math.pi
PI_SAFE = 3.1415925
PI_A = 6.28125
PI_B = 0.0019350051879882812
PI_C = TWO_PI - PI_A - PI_B
ROUND = 12582912.0

VECTORS = [
    ("c", 8), ("b_ada", 48), ("pool_scale", 8), ("conv_b", 24), ("ssm_norm_w", 16), ("ln_mix_g", 8), ("ln_mix_b", 8),
    ("conv_w", 96), ("ln_ffn_g", 8), ("ln_ffn_b", 8), ("c_2", 8), ("mla_kv_norm_2", 1), ("mla_q_norm_2", 2),
    ("mod_mix_b_2", 48), ("mod_ffn_b_2", 48), ("ssm_a_re_2", 32),
    ("mlp_b1_2", 64), ("mlp_b2_2", 16), ("ssm_a_im_2", 32), ("ssm_d_2", 8), ("ssm_b_glu_2", 8),
    ("ln_mix_g_2", 16), ("ln_mix_b_2", 16), ("ln_ffn_g_2", 16), ("ln_ffn_b_2", 16),
]


def vector_places():
    at, places = 0, {}
    for name, rows in VECTORS:
        if at % P + rows > P:
            at += P - at % P
        places[name] = (at, rows)
        at += rows
    return places, (at + P - 1) // P


class Steps:

    def __init__(self, eng, sem, base=0):
        self.eng, self.sem, self.base, self.n = eng, sem, base, 0

    def __call__(self, ins):
        ins.then_inc(self.sem, 1)
        self.n += 1
        self.eng.wait_ge(self.sem, self.base + self.n)


class Kernel:

    def __init__(self, nc, stack, ins):
        self.nc, self.stack, self.ins = nc, stack, ins
        self.finished = []
        self.ps = stack.enter_context(nc.psum_tensor("banks", [P, 8, 512], F32))

    def sb(self, name, shape, dt=F32, stack=None):
        return (stack or self.stack).enter_context(self.nc.sbuf_tensor(name, shape, dt))

    @contextmanager
    def stage(self, name, *sems, primed=()):
        with ExitStack() as stack:
            s = {x: stack.enter_context(self.nc.semaphore(f"{name}_{x}")) for x in sems}
            self.primed = [s[x] for x in primed]
            with self.nc.Block() as block:
                yield block, s, lambda n, shape, dt=F32: self.sb(f"{name}_{n}", shape, dt, stack)
            self.finished = list(s.values())

    def clear(self, sp):
        for x in self.finished:
            sp.sem_clear(x)
        for x in self.primed:
            sp.sem_inc(x, 1)


def constants_stage(k):
    nc, ps = k.nc, k.ps
    places, groups = vector_places()
    k.places = places
    k.ident = k.sb("ident", [P, P])
    k.ones = k.sb("ones", [P, P])
    k.future_mask = k.sb("future_mask", [P, P])
    k.past_cap = k.sb("past_cap", [P, P])
    k.cols = k.sb("cols", [P, groups * P])
    k.eps_ln = k.sb("eps_ln", [P, 1])
    k.eps_rms = k.sb("eps_rms", [P, 1])
    k.silu_c = k.sb("silu_c", [P, 2, KD])
    k.mod = k.sb("mod", [P, 48 + 4 * 24])
    k.x = k.sb("x", [P, KD, T])
    k.neg_f = k.sb("neg_f", [HEADS, T])

    rows_of = {"conv_w": "k (j p) -> (k j) p", "ssm_a_re_2": "(j two) s -> j (two s)", "ssm_a_im_2": "(j two) s -> j (two s)"}

    with k.stage("constants", "rows_zeroed", "rows_loaded", "x_loaded", "pool_step", "consts_ready", "params_turned",
                 "params_copied", "x_turned", "x_copied", "sig_done", "vec_step") as (block, s, sb):
        rows = sb("rows", [P, groups, P])
        xt = sb("xt", [P, TB, D])
        sig = sb("sig", [P, 2, KD])

        @block.sync
        def _(sp):
            k.clear(sp)
            sp.dma_start(xt[:], k.ins["x"][0].rearrange("(b p) d -> p b d", p=P)).then_inc(s["x_loaded"], 16)
            sp.wait_ge(s["rows_zeroed"], 1)
            for name, (at, n) in places.items():
                a = k.ins[name]
                if name in ("conv_w", "ssm_a_re_2", "ssm_a_im_2"):
                    a = a[0].rearrange(rows_of[name], p=P) if name == "conv_w" else a[0].rearrange(rows_of[name], two=2)
                else:
                    a = a.rearrange("l (j p) -> (l j) p", p=P)
                sp.dma_start(rows[at % P:at % P + n, at // P, :], a).then_inc(s["rows_loaded"], 16)

        @block.gpsimd
        def _(pool):
            pool.memset(rows[:], 0.0).then_inc(s["rows_zeroed"], 1)
            pool.memset(k.ident[:], 0.0).then_inc(s["pool_step"], 1)
            pool.memset(k.ones[:], 1.0).then_inc(s["pool_step"], 1)
            pool.memset(k.future_mask[:], 0.0).then_inc(s["pool_step"], 1)
            pool.memset(k.past_cap[:], 0.0).then_inc(s["pool_step"], 1)
            pool.memset(k.eps_ln[:], LN_EPS).then_inc(s["pool_step"], 1)
            pool.memset(k.eps_rms[:], RMS_EPS).then_inc(s["pool_step"], 1)
            pool.wait_ge(s["pool_step"], 6)
            pool.affine_select(out=k.ident[:], in_=k.ident[:], compare_op=ALU.not_equal, fill=1.0, base=0,
                               pattern=[[-1, P]], channel_multiplier=1).then_inc(s["consts_ready"], 1)
            pool.affine_select(out=k.future_mask[:], in_=k.future_mask[:], compare_op=ALU.is_ge, fill=NEG, base=0,
                               pattern=[[-1, P]], channel_multiplier=1).then_inc(s["consts_ready"], 1)
            pool.affine_select(out=k.past_cap[:], in_=k.past_cap[:], compare_op=ALU.is_ge, fill=NEG, base=0,
                               pattern=[[1, P]], channel_multiplier=-1).then_inc(s["consts_ready"], 1)

        @block.tensor
        def _(pe):
            pe.wait_ge(s["consts_ready"], 3)
            pe.wait_ge(s["x_loaded"], 16)
            for c in range(KD):
                if c >= 4:
                    pe.wait_ge(s["x_copied"], c - 3)
                for b in range(TB):
                    mm = pe.transpose(ps[:, c % 4, b * P:(b + 1) * P], xt[:, b, c * P:(c + 1) * P], k.ident[:])
                mm.then_inc(s["x_turned"], 1)
            pe.wait_ge(s["rows_loaded"], 16 * len(places))
            for g in range(groups):
                mm = pe.transpose(ps[:, 4 + g // 4, (g % 4) * P:(g % 4 + 1) * P], rows[:, g, :], k.ident[:])
            mm.then_inc(s["params_turned"], 1)

        @block.scalar
        def _(act):
            for c in range(KD):
                act.wait_ge(s["x_turned"], c + 1)
                act.activation(k.x[:, c, :], ps[:, c % 4, :], ACT.Copy).then_inc(s["x_copied"], 1)
            act.wait_ge(s["params_turned"], 1)
            for g in range(0, groups, 4):
                n = min(4, groups - g) * P
                act.activation(k.cols[:, g * P:g * P + n], ps[:, 4 + g // 4, 0:n], ACT.Copy).then_inc(s["params_copied"], 1)
            act.wait_ge(s["params_copied"], (groups + 3) // 4)
            for j, name in enumerate(("c", "c_2")):
                at = places[name][0]
                act.activation(sig[:, j, :], k.cols[:, at:at + KD], ACT.Sigmoid).then_inc(s["sig_done"], 1)

        @block.vector
        def _(dve):
            dve.wait_ge(s["sig_done"], 2)
            for j, name in enumerate(("c", "c_2")):
                at = places[name][0]
                dve.tensor_tensor(k.silu_c[:, j, :], sig[:, j, :], k.cols[:, at:at + KD], ALU.mult).then_inc(s["vec_step"], 1)

    k.col = lambda name, j=0: k.cols[:, places[name][0] + j:places[name][0] + j + 1]


def strip(k, slot, kt=KD):
    return k.w[:, slot, :].rearrange("p (k n) -> p k n", k=kt)


def modulation_stage(k):
    ps, SLOTS = k.ps, 3
    jobs = [(k.ins["w_ada"][0], 0, 12 // SLOTS, 0, "b_ada", 0)]
    for i in range(2):
        jobs.append((k.ins["mod_mix_w_2"][i], 1, 6 // SLOTS, 48 + 48 * i, "mod_mix_b_2", 24 * i))
        jobs.append((k.ins["mod_ffn_w_2"][i], 1, 6 // SLOTS, 72 + 48 * i, "mod_ffn_b_2", 24 * i))
    names = [f"{x}{slot}" for x in ("loaded", "used", "summed", "copied") for slot in range(SLOTS)]
    with k.stage("modulation", *names, "vec_step", "pool_step", primed=names[SLOTS:]) as (block, s, sb):
        loaded, used, summed, copied = (names[j * SLOTS:(j + 1) * SLOTS] for j in range(4))
        acc = sb("acc", [P, SLOTS, STRIP])

        @block.sync
        def _(sp):
            k.clear(sp)
            done = 0
            for w, _, rounds, *_ in jobs:
                with sp.Fori(0, rounds) as i:
                    for slot in range(SLOTS):
                        sp.wait_ge(s[used[slot]], 1 + done + i)
                        sp.dma_start(strip(k, slot), columns(w, (SLOTS * i + slot) * STRIP)).then_inc(s[loaded[slot]], 16)
                done += rounds

        @block.vector
        def _(dve):
            done = 0
            for _, c, rounds, *_ in jobs:
                with dve.Fori(0, rounds) as i:
                    step = Steps(dve, s["vec_step"], SLOTS * (KD - 1) * (done + i))
                    for slot in range(SLOTS):
                        dve.wait_ge(s[loaded[slot]], 16 * (done + i + 1))
                        dve.wait_ge(s[summed[slot]], 1 + done + i)
                        for kk in range(KD):
                            w, by = strip(k, slot)[:, kk, :], k.silu_c[:, c, kk:kk + 1]
                            if kk == 0:
                                ins = dve.tensor_scalar(acc[:, slot, :], w, by, None, ALU.mult)
                            else:
                                ins = dve.scalar_tensor_tensor(out=acc[:, slot, :], in0=w, scalar=by, in1=acc[:, slot, :],
                                                               op0=ALU.mult, op1=ALU.add)
                            if kk < KD - 1:
                                step(ins)
                        ins.then_inc(s[used[slot]], 1)
                done += rounds

        @block.tensor
        def _(pe):
            done = 0
            for _, _, rounds, *_ in jobs:
                with pe.Fori(0, rounds) as i:
                    for slot in range(SLOTS):
                        pe.wait_ge(s[used[slot]], 1 + done + i + 1)
                        pe.wait_ge(s[copied[slot]], 1 + done + i)
                        for f in range(FT):
                            mm = pe.matmul(ps[:, slot, f:f + 1], acc[:, slot, f * P:(f + 1) * P], k.ones[:, 0:1], start=True, stop=True)
                        mm.then_inc(s[summed[slot]], 1)
                done += rounds

        @block.scalar
        def _(act):
            done = 0
            for _, _, rounds, col, *_ in jobs:
                with act.Fori(0, rounds) as i:
                    for slot in range(SLOTS):
                        act.wait_ge(s[summed[slot]], 1 + done + i + 1)
                        act.activation(k.mod[:, bass.ds(col + (SLOTS * i + slot) * FT, FT)], ps[:, slot, 0:FT],
                                       ACT.Copy).then_inc(s[copied[slot]], 1)
                done += rounds

        @block.gpsimd
        def _(pool):
            total = sum(job[2] for job in jobs)
            for slot in range(SLOTS):
                pool.wait_ge(s[copied[slot]], 1 + total)
            for _, _, rounds, col, bias, at in jobs:
                n, b = rounds * SLOTS * FT, k.places[bias][0] + at
                pool.tensor_tensor(k.mod[:, col:col + n], k.mod[:, col:col + n], k.cols[:, b:b + n], ALU.add).then_inc(s["pool_step"], 1)
            pool.wait_ge(s["pool_step"], len(jobs))
            for first, n in ((8, 8), (32, 8)) + tuple((48 + 24 * j + 8, 16) for j in range(4)):
                pool.tensor_scalar(k.mod[:, first:first + n], k.mod[:, first:first + n], 1.0, None,
                                  ALU.add).then_inc(s["pool_step"], 1)


def norm_stage(k, name, src, dst, scale, shift):
    ps = k.ps
    with k.stage(name, "sum_done", "sq_done", "var_done", "std_done", "vec_step", "centred", "scaled", "out_done") as (block, s, sb):
        xc = sb("xc", [P, KD, T])
        sq = sb("sq", [P, KD, T])
        std = sb("std", [P, T])
        rstd = sb("rstd", [P, T])

        @block.sync
        def _(sp):
            k.clear(sp)

        @block.tensor
        def _(pe):
            for c in range(KD):
                mm = pe.matmul(ps[:, 0, :], k.ones[:], src[:, c, :], start=(c == 0), stop=(c == KD - 1))
            mm.then_inc(s["sum_done"], 1)
            for c in range(KD):
                pe.wait_ge(s["sq_done"], c + 1)
                mm = pe.matmul(ps[:, 1, :], k.ones[:], sq[:, c, :], start=(c == 0), stop=(c == KD - 1))
            mm.then_inc(s["var_done"], 1)

        @block.vector
        def _(dve):
            dve.wait_ge(s["sum_done"], 1)
            for c in range(KD):
                dve.scalar_tensor_tensor(out=xc[:, c, :], in0=ps[:, 0, :], scalar=-1.0 / D, in1=src[:, c, :],
                                         op0=ALU.mult, op1=ALU.add).then_inc(s["centred"], 1)
            dve.wait_ge(s["std_done"], 1)
            dve.reciprocal(rstd[:], std[:]).then_inc(s["vec_step"], 1)
            dve.wait_ge(s["vec_step"], 1)
            for c in range(KD):
                dve.tensor_tensor(xc[:, c, :], xc[:, c, :], rstd[:], ALU.mult).then_inc(s["scaled"], 1)

        @block.scalar
        def _(act):
            for c in range(KD):
                act.wait_ge(s["centred"], c + 1)
                act.activation(sq[:, c, :], xc[:, c, :], ACT.Square).then_inc(s["sq_done"], 1)
            act.wait_ge(s["var_done"], 1)
            act.activation(std[:], ps[:, 1, :], ACT.Sqrt, scale=1.0 / D, bias=k.eps_ln[:]).then_inc(s["std_done"], 1)
            for c in range(KD):
                act.wait_ge(s["scaled"], c + 1)
                act.activation(dst[:, c, :], xc[:, c, :], ACT.Identity, scale=scale(c), bias=shift(c)).then_inc(s["out_done"], 1)


def linear(k, block, s, src, pairs, x, finish, kt=KD, banks_of=None):
    ps = k.ps
    loaded, done, free = (s["w_loaded0"], s["w_loaded1"]), (s["tile_done0"], s["tile_done1"]), (s["tile_free0"], s["tile_free1"])
    ft = KD * STRIP // kt // P

    @block.sync
    def _(sp):
        k.clear(sp)
        with sp.Fori(0, pairs) as i:
            for slot in range(2):
                sp.wait_ge(done[slot], 1 + ft * i)
                sp.dma_start(strip(k, slot, kt), src(i, slot)).then_inc(loaded[slot], 16)

    @block.tensor
    def _(pe):
        with pe.Fori(0, pairs) as i:
            for slot in range(2):
                pe.wait_ge(loaded[slot], 16 * (i + 1))
                pe.wait_ge(free[slot], 1 + ft * i)
                for f in range(ft):
                    for kk in range(kt):
                        mm = pe.matmul(ps[:, slot * FT + f, :], strip(k, slot, kt)[:, kk, f * P:(f + 1) * P], x(kk),
                                       start=(kk == 0), stop=(kk == kt - 1))
                    mm.then_inc(done[slot], 1)


LINEAR_PRIMED = ("tile_done0", "tile_done1", "tile_free0", "tile_free1")
LINEAR = ("w_loaded0", "w_loaded1", "tile_done0", "tile_done1", "tile_free0", "tile_free1")


def columns(w, first, n=STRIP):
    return w[:, bass.ds(first, n)].rearrange("(k p) n -> p k n", p=P)


class SplitProducts:

    SEMS = ("raw_loaded0", "raw_loaded1", "raw_loaded2", "raw_loaded3", "high_done", "low_done", "half_used", "x_high", "x_low")
    PRIMED = ("low_done", "half_used")

    def __init__(self, k, s, sb):
        self.k, self.s = k, s
        self.parts = sb("w_parts", [P, 2, 2, KD, HALF], F32R)

    def raw(self, n):
        slot = self.k.w[:, n % 4 // 2, :]
        return slot[:, n % 2 * KD * HALF:(n % 2 + 1) * KD * HALF].rearrange("p (k n) -> p k n", k=KD)

    def load(self, sp, n, src, base=0):
        if n >= 4:
            sp.wait_ge(self.s["low_done"], 1 + base + n - 3)
        elif not isinstance(base, int):
            sp.wait_ge(self.s["low_done"], 1 + base)
        sp.dma_start(self.raw(n), src).then_inc(self.s[f"raw_loaded{n % 4}"], 16)

    def high(self, act, n, base=0, rounds=0):
        s = self.s
        act.wait_ge(s[f"raw_loaded{n % 4}"], 16 * (rounds + n // 4 + 1))
        if n >= 2:
            act.wait_ge(s["half_used"], 1 + base + n - 1)
        elif not isinstance(base, int):
            act.wait_ge(s["half_used"], 1 + base)
        act.activation(self.parts[:, n % 2, 0], self.raw(n), ACT.Copy).then_inc(s["high_done"], 1)

    def low(self, dve, n, base=0):
        s = self.s
        dve.wait_ge(s["high_done"], base + n + 1)
        dve.tensor_tensor(self.parts[:, n % 2, 1], self.raw(n), self.parts[:, n % 2, 0].bitcast(F32),
                          ALU.subtract).then_inc(s["low_done"], 1)

    def products(self, pe, n, x, outs, base=0, start=True, stop=True):
        s = self.s
        pe.wait_ge(s["low_done"], 1 + base + n + 1)
        for f, out in enumerate(outs):
            for kk in range(KD):
                for j, (w, v) in enumerate(((0, 0), (0, 1), (1, 0))):
                    mm = pe.matmul(out, self.parts[:, n % 2, w, kk, f * P:(f + 1) * P], x[:, v, kk, :],
                                   start=(start and kk == 0 and j == 0), stop=(stop and kk == KD - 1 and j == 2))
        mm.then_inc(s["half_used"], 1)


class SplitLinear(SplitProducts):

    HALVES = D // HALF

    def __init__(self, k, block, s, sb, w, x):
        super().__init__(k, s, sb)
        self.x = x
        self.x_parts = sb("x_parts", [P, 2, KD, T], F32R)

        @block.sync
        def _(sp):
            k.clear(sp)
            for n in range(self.HALVES):
                self.load(sp, n, columns(w, n * HALF, HALF))

        @block.tensor
        def _(pe):
            pe.wait_ge(s["x_low"], KD)
            for n in range(self.HALVES):
                self.products(pe, n, self.x_parts, [k.ps[:, n * HT + f, :] for f in range(HT)])

    def scalar(self, act, epilogue=None):
        for kk in range(KD):
            act.activation(self.x_parts[:, 0, kk], self.x[:, kk, :], ACT.Copy).then_inc(self.s["x_high"], 1)
            if kk in (KD // 2, KD - 1):
                self.high(act, kk // (KD // 2 + 1))
        for n in range(self.HALVES):
            if n + 2 < self.HALVES:
                self.high(act, n + 2)
            if epilogue:
                epilogue(n)

    def vector(self, dve, epilogue=None):
        for kk in range(KD):
            dve.wait_ge(self.s["x_high"], kk + 1)
            dve.tensor_tensor(self.x_parts[:, 1, kk], self.x[:, kk, :], self.x_parts[:, 0, kk].bitcast(F32),
                              ALU.subtract).then_inc(self.s["x_low"], 1)
            if kk in (KD // 2, KD - 1):
                self.low(dve, kk // (KD // 2 + 1))
        for n in range(self.HALVES):
            if n + 2 < self.HALVES:
                self.low(dve, n + 2)
            if epilogue:
                epilogue(n)


def forget_stage(k):
    ps, w_in = k.ps, k.ins["w_in"][0]
    with k.stage("forget", "loaded", "f_done", "act_step", "vec_step") as (block, s, sb):
        wf = sb("wf", [P, KD, HEADS])
        bias = sb("bias", [HEADS, 1])
        v, e, ln = sb("v", [HEADS, T]), sb("e", [HEADS, T]), sb("ln", [HEADS, T])
        ones = sb("ones", [HEADS, T])

        @block.sync
        def _(sp):
            k.clear(sp)
            sp.dma_start(wf[:], columns(w_in, F0, HEADS)).then_inc(s["loaded"], 16)
            sp.dma_start(bias[:], k.ins["b_forget"].rearrange("l h -> h l")).then_inc(s["loaded"], 16)

        @block.tensor
        def _(pe):
            pe.wait_ge(s["loaded"], 32)
            for kk in range(KD):
                mm = pe.matmul(ps[0:HEADS, 0, :], wf[:, kk, :], k.h[:, kk, :], start=(kk == 0), stop=(kk == KD - 1))
            mm.then_inc(s["f_done"], 1)

        @block.scalar
        def _(act):
            act.wait_ge(s["vec_step"], 3)
            act.activation(e[:], e[:], ACT.Exp).then_inc(s["act_step"], 1)
            act.wait_ge(s["act_step"], 1)
            act.activation(ln[:], e[:], ACT.Ln, bias=1.0).then_inc(s["act_step"], 1)

        @block.vector
        def _(dve):
            step = Steps(dve, s["vec_step"])
            step(dve.memset(ones[:], 1.0))
            dve.wait_ge(s["loaded"], 32)
            dve.wait_ge(s["f_done"], 1)
            step(dve.tensor_scalar(v[:], ps[0:HEADS, 0, :], bias[:], None, ALU.add))
            step(dve.scalar_tensor_tensor(out=e[:], in0=v[:], scalar=-1.0, in1=v[:], op0=ALU.mult, op1=ALU.min))
            dve.wait_ge(s["act_step"], 2)
            step(dve.tensor_scalar(v[:], v[:], 0.0, None, ALU.min))
            step(dve.tensor_tensor(ln[:], ln[:], v[:], ALU.subtract))
            step(dve.tensor_tensor_scan(k.neg_f[:], ones[:], ln[:], 0.0, ALU.mult, ALU.add))


def scan_softmax(k, s, units, scores, p_tiles, pt_tiles, values, nmax, rsum, rinv):
    ps, n_units = k.ps, len(units)

    def tensor(pe, i):
        base = n_units * i

        def logits(n):
            if n >= 3:
                pe.wait_ge(s["exp_done"], 1 + base + n - 2)
            scores(pe, units[n], n % 3).then_inc(s["scores_done"], 1)

        def turn(n):
            pe.wait_ge(s["probs_done"], base + n + 1)
            if n >= 2:
                pe.wait_ge(s["turned_copied"], base + n - 1)
            for kb in range(units[n][1] + 1):
                mm = pe.transpose(ps[:, 3 + n % 2, kb * P:(kb + 1) * P], p_tiles[:, n % 3, kb * P:(kb + 1) * P], k.ident[:])
            mm.then_inc(s["turned"], 1)

        def weigh(n):
            rows, b = units[n]
            pe.wait_ge(s["turned_copied"], base + n + 1)
            if n == 0:
                pe.wait_ge(s["o_copied"], 1 + i)
            for kb in range(b + 1):
                mm = pe.matmul(ps[rows, 5, b * P:(b + 1) * P], values(units[n], kb), pt_tiles[:, n % 2, kb * P:(kb + 1) * P],
                               start=(kb == 0), stop=(kb == b))
            mm.then_inc(s["weighed"], 1)

        logits(0)
        logits(1)
        for n in range(n_units):
            if n + 2 < n_units:
                logits(n + 2)
            turn(n)
            if n >= 1:
                weigh(n - 1)
        weigh(n_units - 1)

    def vector(dve, i):
        base = n_units * i
        step = Steps(dve, s["soft_step"], 2 * base)

        def row_max(n):
            b = units[n][1]
            dve.wait_ge(s["scores_done"], 1 + base + n + 1)
            diagonal = ps[:, n % 3, b * P:(b + 1) * P]
            step(dve.tensor_tensor(diagonal, diagonal, k.future_mask[:], ALU.add))
            if n == 0:
                dve.wait_ge(s["exp_done"], 1 + base)
            dve.tensor_reduce(nmax[:, n:n + 1], ps[:, n % 3, 0:(b + 1) * P], AX.X, ALU.max, negate=True).then_inc(s["max_done"], 1)

        def normalise(n):
            b = units[n][1]
            dve.wait_ge(s["exp_done"], 1 + base + n + 1)
            step(dve.reciprocal(rinv[:, n:n + 1], rsum[:, n:n + 1]))
            row = p_tiles[:, n % 3, 0:(b + 1) * P]
            dve.tensor_scalar(row, row, rinv[:, n:n + 1], None, ALU.mult).then_inc(s["probs_done"], 1)

        row_max(0)
        for n in range(n_units):
            if n + 1 < n_units:
                row_max(n + 1)
            normalise(n)
        return step.n

    def scalar(act, i):
        base = n_units * i

        def exponent(n):
            b = units[n][1]
            act.wait_ge(s["max_done"], base + n + 1)
            if n >= 3:
                act.wait_ge(s["turned"], base + n - 2)
            act.activation(p_tiles[:, n % 3, 0:(b + 1) * P], ps[:, n % 3, 0:(b + 1) * P], ACT.Exp, bias=nmax[:, n:n + 1],
                           accum_out=rsum[:, n:n + 1]).then_inc(s["exp_done"], 1)

        def copy_turned(n):
            b = units[n][1]
            act.wait_ge(s["turned"], base + n + 1)
            if n >= 2:
                act.wait_ge(s["weighed"], 1 + base + n - 1)
            act.activation(pt_tiles[:, n % 2, 0:(b + 1) * P], ps[:, 3 + n % 2, 0:(b + 1) * P], ACT.Copy).then_inc(s["turned_copied"], 1)

        exponent(0)
        for n in range(n_units):
            if n + 1 < n_units:
                exponent(n + 1)
            copy_turned(n)

    return tensor, vector, scalar


SOFTMAX = ("scores_done", "exp_done", "probs_done", "turned", "turned_copied", "weighed", "max_done", "soft_step", "o_copied")


def attention_stage(k, o):
    ps, w_in = k.ps, k.ins["w_in"][0]
    pairs = HEADS // 2
    with k.stage("attention", "w_loaded", "q_done", "k_done", "v_done", "qkv_copied", "f_picked", "picked_used", *SOFTMAX, primed=("exp_done", "o_copied", "qkv_copied", "scores_done", "v_done", "weighed")) as (block, s, sb):
        qt, kt = sb("qt", [P, T]), sb("kt", [P, T])
        v = sb("v", [P, TB, P])
        picked = sb("picked", [HEADS, 2, T])
        p_tiles, pt_tiles = sb("p_tiles", [P, 3, T]), sb("pt_tiles", [P, 2, T])
        nmax, rsum, rinv = sb("nmax", [P, 8]), sb("rsum", [P, 8]), sb("rinv", [P, 8])
        wv = k.w[:, 0:3, 0:KD * P].rearrange("p s (k n) -> p s k n", k=KD)
        units = [(slice(hh * HD, (hh + 1) * HD), b) for hh in range(2) for b in range(TB)]

        def scores(pe, unit, bank):
            rows, b = unit
            hh, n = rows.start // HD, (b + 1) * P
            pe.matmul(ps[:, bank, 0:n], qt[rows, b * P:(b + 1) * P], kt[rows, 0:n], start=True, stop=False)
            return pe.matmul(ps[:, bank, 0:n], k.ones[0:HEADS, :], picked[:, hh, 0:n], start=False, stop=True)

        tensor, vector, scalar = scan_softmax(k, s, units, scores, p_tiles, pt_tiles,
                                              lambda unit, kb: v[:, kb, unit[0]], nmax, rsum, rinv)

        @block.sync
        def _(sp):
            k.clear(sp)
            with sp.Fori(0, pairs) as i:
                sp.wait_ge(s["v_done"], 1 + i)
                for j, first in enumerate((Q0, K0, V0)):
                    sp.dma_start(wv[:, j], columns(w_in, first + i * P, P)).then_inc(s["w_loaded"], 16)

        @block.tensor
        def _(pe):
            with pe.Fori(0, pairs) as i:
                pe.wait_ge(s["w_loaded"], 48 * (i + 1))
                pe.wait_ge(s["qkv_copied"], 1 + 3 * i)
                for j, done in enumerate((s["q_done"], s["k_done"])):
                    for kk in range(KD):
                        mm = pe.matmul(ps[:, 6 + j, :], wv[:, j, kk, :], k.h[:, kk, :], start=(kk == 0), stop=(kk == KD - 1))
                    mm.then_inc(done, 1)
                pe.wait_ge(s["qkv_copied"], 1 + 3 * i + 1)
                for b in range(TB):
                    for kk in range(KD):
                        mm = pe.matmul(ps[:, 6, b * P:(b + 1) * P], k.h[:, kk, b * P:(b + 1) * P], wv[:, 2, kk, :],
                                       start=(kk == 0), stop=(kk == KD - 1))
                mm.then_inc(s["v_done"], 1)
                pe.wait_ge(s["qkv_copied"], 1 + 3 * i + 3)
                pe.wait_ge(s["f_picked"], 2 * i + 2)
                tensor(pe, i)

        @block.scalar
        def _(act):
            with act.Fori(0, pairs) as i:
                act.wait_ge(s["q_done"], i + 1)
                act.wait_ge(s["weighed"], 1 + len(units) * i)
                act.activation(qt[:], ps[:, 6, :], ACT.Copy, scale=HD ** -0.5).then_inc(s["qkv_copied"], 1)
                act.wait_ge(s["k_done"], i + 1)
                act.activation(kt[:], ps[:, 7, :], ACT.Copy).then_inc(s["qkv_copied"], 1)
                act.wait_ge(s["v_done"], 1 + i + 1)
                act.activation(v[:], ps[:, 6, :].rearrange("p (b n) -> p b n", b=TB), ACT.Copy).then_inc(s["qkv_copied"], 1)
                scalar(act, i)

        @block.vector
        def _(dve):
            with dve.Fori(0, pairs) as i:
                dve.wait_ge(s["scores_done"], 1 + len(units) * i)
                for hh in range(2):
                    dve.tensor_scalar(picked[:, hh, :], k.neg_f[:], k.ident[0:HEADS, bass.ds(2 * i + hh, 1)], None,
                                      ALU.mult).then_inc(s["f_picked"], 1)
                n = vector(dve, i)
                assert n == 2 * len(units)
                dve.wait_ge(s["weighed"], 1 + len(units) * (i + 1))
                dve.tensor_copy(o[:, bass.ds(i, 1), :], ps[:, 5:6, :]).then_inc(s["o_copied"], 1)


def ssm_stage(k, ys):
    ps, w_in = k.ps, k.ins["w_in"][0]
    H = R_SSM
    conv0, convb0 = k.places["conv_w"][0], k.places["conv_b"][0]
    NC = 2 + KG
    VEC_STEPS = 79
    with k.stage("ssm", "w_loaded", "z_loaded", "small_loaded", "dt_done", "tile_done", "tile_copied", "conv_done", "sig_done",
                 "act_done", "z_done", "z_sig", "z_gated", "zeroed", "d_loaded", "wend_in", "a_ready", "vec_step", "act_step", "acs_ready", "small_turned", "small_copied",
                 "turned", "turned_copied", "ends_done", "ends_copied", "decay_done", "xw_ready", "cb_done", "cb_copied", "state_done", "state_ready",
                 "row_done", "row_seen", "seg_ready", "seg_exp", "row_exp", "scores_ready", "y_done", "y_read", "sq_done",
                 "ms_done", "std_done", "group_done", primed=("group_done", "ms_done", "tile_done", "z_done")) as (block, s, sb):
        wxs = strip(k, 0)
        wz = strip(k, 1)
        wbc = k.w[:, 2, 0:KD * 2 * P].rearrange("p (k n) -> p k n", k=KD)
        wdt = sb("wdt", [P, KD, H])
        dt_bias, a_log = sb("dt_bias", [H, G_SSM]), sb("a_log", [H, G_SSM])
        d_col = sb("d_col", [P, KI])
        u = sb("u", [P, 2, T + CONV - 1])
        acc = sb("acc", [P, 2, T])
        sig = sb("sig", [P, 2, T])
        xbc = sb("xbc", [P, NC, T])
        z = sb("z", [P, KG, T])
        xt = k.w[:, 2, KD * 2 * P:].rearrange("p (b n) -> p b n", b=TB)
        bt = sb("bt", [P, TB, P])
        xw = sb("xw", [P, TB - 1, KG * P])
        hp = sb("hp", [P, TB - 1, KG * P])
        cb = sb("cb", [P, TB, P])
        dt, acs = sb("dt", [H, T]), sb("acs", [H, T])
        e, t1, t2 = xw[0:H, 0, :], xw[0:H, 1, :], xw[0:H, 2, :]
        ones = sb("ones", [H, T])
        small = sb("small", [P, 2, TB, H])
        ends_in = sb("ends_in", [H, TB, H])
        ends = sb("ends", [P, TB, H])
        decay, wend = sb("decay", [P, TB, H]), sb("wend", [P, TB, H])
        seg, rowx = sb("seg", [P, 2, T]), sb("rowx", [P, 2, T])
        sc, ce = sb("sc", [P, 2, TB, P]), sb("ce", [P, 2, T])
        sq = acc
        std, rstd = seg[:, 0, :], seg[:, 1, :]

        def wcols(i, tile, j):
            at = (16 + i) if tile == 0 else (20 + i) if tile == 1 else KG * i + tile - 2
            first = convb0 if j is None else conv0 + j * XBC_TILES
            return k.cols[:, bass.ds(first + at, 1)]

        @block.sync
        def _(sp):
            k.clear(sp)
            for half in range(2):
                sp.dma_start(d_col[half * P_SSM:(half + 1) * P_SSM, :],
                               k.ins["d_skip"].rearrange("l (j two) -> two l j", two=2)[half].to_broadcast([P_SSM, KI]),
                               allow_slow_non_contiguous=True).then_inc(s["d_loaded"], 16)
            for dst, name in ((dt_bias, "dt_bias"), (a_log, "a_log")):
                sp.dma_start(dst[:], k.ins[name].rearrange("l (g h) -> h (l g)", h=H), allow_slow_non_contiguous=True).then_inc(s["small_loaded"], 16)
            with sp.Fori(0, G_SSM) as i:
                sp.wait_ge(s["tile_done"], 1 + NC * i)
                sp.dma_start(wdt[:], columns(w_in, DT0 + i * H, H)).then_inc(s["w_loaded"], 16)
                sp.dma_start(wbc[:, :, 0:P], columns(w_in, B0 + i * P, P)).then_inc(s["w_loaded"], 16)
                sp.dma_start(wbc[:, :, P:2 * P], columns(w_in, C0 + i * P, P)).then_inc(s["w_loaded"], 16)
                sp.dma_start(wxs, columns(w_in, XBC0 + i * STRIP)).then_inc(s["w_loaded"], 16)
                sp.wait_ge(s["z_done"], 1 + KG * i)
                sp.dma_start(wz, columns(w_in, Z0 + i * STRIP)).then_inc(s["z_loaded"], 16)

        @block.gpsimd
        def _(pool):
            for b in range(2):
                pool.memset(u[:, b, 0:CONV - 1], 0.0).then_inc(s["zeroed"], 1)

        @block.tensor
        def _(pe):
            with pe.Fori(0, G_SSM) as i:
                pe.wait_ge(s["w_loaded"], 64 * (i + 1))
                pe.wait_ge(s["group_done"], 1 + KG * i)
                for kk in range(KD):
                    mm = pe.matmul(ps[0:H, 7, :], wdt[:, kk, :], k.h[:, kk, :], start=(kk == 0), stop=(kk == KD - 1))
                mm.then_inc(s["dt_done"], 1)
                for c in range(NC):
                    for kk in range(KD):
                        w = wbc[:, kk, c * P:(c + 1) * P] if c < 2 else wxs[:, kk, (c - 2) * P:(c - 1) * P]
                        mm = pe.matmul(ps[:, c, :], w, k.h[:, kk, :], start=(kk == 0), stop=(kk == KD - 1))
                    mm.then_inc(s["tile_done"], 1)
                pe.wait_ge(s["acs_ready"], i + 1)
                pe.matmul(ps[:, 7, 0:TB * H], k.ones[0:H, :], ends_in[:].rearrange("p c h -> p (c h)"), start=True,
                          stop=True).then_inc(s["ends_done"], 1)
                for j, m in enumerate((dt, acs)):
                    for c in range(TB):
                        mm = pe.transpose(ps[:, 6, (j * TB + c) * H:(j * TB + c + 1) * H], m[:, c * P:(c + 1) * P], k.ident[0:H, 0:H])
                mm.then_inc(s["small_turned"], 1)
                pe.wait_ge(s["z_loaded"], 16 * (i + 1))
                for f in range(KG):
                    pe.wait_ge(s["tile_copied"], NC * i + f + 1)
                    for kk in range(KD):
                        mm = pe.matmul(ps[:, f, :], wz[:, kk, f * P:(f + 1) * P], k.h[:, kk, :], start=(kk == 0), stop=(kk == KD - 1))
                    mm.then_inc(s["z_done"], 1)
                pe.wait_ge(s["tile_copied"], NC * (i + 1))
                pe.wait_ge(s["act_done"], NC * (i + 1))
                for n in range(1 + TB):
                    if n >= 2:
                        pe.wait_ge(s["turned_copied"], (1 + TB) * i + n - 1)
                    for m in range(TB if n == 0 else KG):
                        src = xbc[:, 0, m * P:(m + 1) * P] if n == 0 else xbc[:, 2 + m, (n - 1) * P:n * P]
                        mm = pe.transpose(ps[:, 4 + n % 2, m * P:(m + 1) * P], src, k.ident[:])
                    mm.then_inc(s["turned"], 1)
                pe.wait_ge(s["small_copied"], i + 1)
                for c in range(TB):
                    mm = pe.matmul(ps[:, 6, c * P:(c + 1) * P], xbc[:, 0, c * P:(c + 1) * P], xbc[:, 1, c * P:(c + 1) * P],
                                   start=True, stop=True)
                mm.then_inc(s["cb_done"], 1)
                pe.wait_ge(s["turned_copied"], (1 + TB) * (i + 1))
                pe.wait_ge(s["z_gated"], KG * (i + 1))
                for c in range(TB - 1):
                    pe.wait_ge(s["xw_ready"], (TB - 1) * i + c + 1)
                    pe.matmul(ps[:, c, :], bt[:, c, :], xw[:, c, :], start=True, stop=True).then_inc(s["state_done"], 1)

                def row(h):
                    if h >= 2:
                        pe.wait_ge(s["row_exp"], H * i + h - 1)
                        pe.wait_ge(s["row_seen"], H * i + h - 1)
                    pe.matmul(ps[:, 4 + h % 2, :], k.ident[0:H, h:h + 1].to_broadcast([H, P]), acs[:], start=True,
                              stop=True).then_inc(s["row_done"], 1)

                pe.wait_ge(s["ends_copied"], i + 1)
                row(0)
                row(1)
                for h in range(H):
                    rows = slice(h % 2 * P_SSM, (h % 2 + 1) * P_SSM)
                    bank = (3, 7)[h // 2 % 2]
                    if h >= 4:
                        pe.wait_ge(s["y_read"], KG * i + h // 2 - 1)
                    pe.wait_ge(s["scores_ready"], H * i + h + 1)
                    if h == 0:
                        pe.wait_ge(s["state_ready"], i + 1)
                    for c in range(TB):
                        mine = slice(c * P, (c + 1) * P)
                        mm = pe.matmul(ps[rows, bank, mine], xt[:, c, h * P_SSM:(h + 1) * P_SSM], sc[:, h % 2, c, :],
                                       start=True, stop=(c == 0))
                        if c:
                            mm = pe.matmul(ps[rows, bank, mine], hp[:, c - 1, h * P_SSM:(h + 1) * P_SSM], ce[:, h % 2, mine],
                                           start=False, stop=True)
                    mm.then_inc(s["y_done"], 1)
                    if h + 2 < H:
                        row(h + 2)
                for f in range(KG):
                    pe.wait_ge(s["sq_done"], KG * i + f + 1)
                    mm = pe.matmul(ps[:, 6, :], k.ones[:], sq[:, f % 2, :], start=(f == 0), stop=(f == KG - 1))
                    mm.then_inc(s["ms_done"], 1)

        @block.scalar
        def _(act):
            act.wait_ge(s["small_loaded"], 32)
            act.activation(a_log[:], a_log[:], ACT.Exp).then_inc(s["a_ready"], 1)
            with act.Fori(0, G_SSM) as i:
                act.wait_ge(s["vec_step"], VEC_STEPS * i + 2)
                act.activation(e[:], e[:], ACT.Exp).then_inc(s["act_step"], 1)
                act.wait_ge(s["vec_step"], VEC_STEPS * i + 3)
                act.activation(t2[:], t1[:], ACT.Ln).then_inc(s["act_step"], 1)
                for c in range(NC):
                    act.wait_ge(s["tile_done"], 1 + NC * i + c + 1)
                    if c >= 2:
                        act.wait_ge(s["conv_done"], NC * i + c - 1)
                    act.activation(u[:, c % 2, CONV - 1:], ps[:, c, :], ACT.Copy).then_inc(s["tile_copied"], 1)
                    if c >= 1:
                        act.wait_ge(s["conv_done"], NC * i + c)
                        act.activation(sig[:, (c - 1) % 2, :], acc[:, (c - 1) % 2, :], ACT.Sigmoid).then_inc(s["sig_done"], 1)
                act.wait_ge(s["conv_done"], NC * (i + 1))
                act.activation(sig[:, (NC - 1) % 2, :], acc[:, (NC - 1) % 2, :], ACT.Sigmoid).then_inc(s["sig_done"], 1)
                act.wait_ge(s["small_turned"], i + 1)
                act.activation(small[:], ps[:, 6, 0:2 * TB * H].rearrange("p (j c h) -> p j c h", j=2, c=TB), ACT.Copy).then_inc(s["small_copied"], 1)
                act.wait_ge(s["ends_done"], i + 1)
                act.activation(ends[:], ps[:, 7, 0:TB * H].rearrange("p (c h) -> p c h", c=TB), ACT.Copy).then_inc(s["ends_copied"], 1)
                for f in range(KG):
                    act.wait_ge(s["z_done"], 1 + KG * i + f + 1)
                    act.wait_ge(s["act_done"], NC * (i + 1))
                    if f >= 2:
                        act.wait_ge(s["z_gated"], KG * i + f - 1)
                    act.activation(sig[:, f % 2, :], ps[:, f, :], ACT.Sigmoid).then_inc(s["z_sig"], 1)
                for n in range(1 + TB):
                    act.wait_ge(s["turned"], (1 + TB) * i + n + 1)
                    dst = bt[:] if n == 0 else xt[:, n - 1, :].rearrange("p (b n) -> p b n", b=KG)
                    act.activation(dst, ps[:, 4 + n % 2, :].rearrange("p (b n) -> p b n", b=TB), ACT.Copy).then_inc(s["turned_copied"], 1)
                act.wait_ge(s["cb_done"], i + 1)
                act.activation(cb[:], ps[:, 6, :].rearrange("p (b n) -> p b n", b=TB), ACT.Copy).then_inc(s["cb_copied"], 1)
                act.wait_ge(s["ends_copied"], i + 1)
                act.activation(decay[:], ends[:], ACT.Exp).then_inc(s["decay_done"], 1)
                act.wait_ge(s["wend_in"], i + 1)
                act.activation(wend[:], wend[:], ACT.Exp).then_inc(s["decay_done"], 1)
                for h in range(H):
                    act.wait_ge(s["row_done"], H * i + h + 1)
                    if h >= 2:
                        act.wait_ge(s["scores_ready"], H * i + h - 1)
                    act.activation(rowx[:, h % 2, :], ps[:, 4 + h % 2, :], ACT.Exp).then_inc(s["row_exp"], 1)
                    act.wait_ge(s["row_seen"], H * i + h + 1)
                    act.activation(seg[:, h % 2, :], seg[:, h % 2, :], ACT.Exp).then_inc(s["seg_exp"], 1)
                for f in range(KG):
                    act.wait_ge(s["y_read"], KG * i + f + 1)
                    if f >= 2:
                        act.wait_ge(s["ms_done"], 1 + KG * i + f - 1)
                    act.activation(sq[:, f % 2, :], z[:, f, :], ACT.Square).then_inc(s["sq_done"], 1)
                act.wait_ge(s["ms_done"], 1 + KG * (i + 1))
                act.activation(std[:], ps[:, 6, :], ACT.Sqrt, scale=1.0 / (KG * P), bias=k.eps_rms[:]).then_inc(s["std_done"], 1)

        @block.vector
        def _(dve):
            dve.memset(ones[:], 1.0).then_inc(s["zeroed"], 1)
            dve.wait_ge(s["zeroed"], 3)
            dve.wait_ge(s["d_loaded"], 32)
            dve.wait_ge(s["small_loaded"], 32)
            dve.wait_ge(s["a_ready"], 1)
            with dve.Fori(0, G_SSM) as i:
                step = Steps(dve, s["vec_step"], VEC_STEPS * i)
                dve.wait_ge(s["dt_done"], i + 1)
                step(dve.tensor_scalar(dt[:], ps[0:H, 7, :], dt_bias[:, bass.ds(i, 1)], None, ALU.add))
                step(dve.scalar_tensor_tensor(out=e[:], in0=dt[:], scalar=-1.0, in1=dt[:], op0=ALU.mult, op1=ALU.min))
                dve.wait_ge(s["act_step"], 2 * i + 1)
                step(dve.tensor_scalar(t1[:], e[:], 1.0, None, ALU.add))
                dve.wait_ge(s["act_step"], 2 * i + 2)
                step(dve.tensor_scalar(t1[:], t1[:], -1.0, None, ALU.add))
                step(dve.tensor_scalar(acs[:], t1[:], 0.0, None, ALU.is_equal))
                step(dve.tensor_tensor(t1[:], t1[:], acs[:], ALU.add))
                step(dve.tensor_tensor(t2[:], t2[:], acs[:], ALU.add))
                step(dve.reciprocal(t1[:], t1[:]))
                step(dve.tensor_tensor(t2[:], t2[:], e[:], ALU.mult))
                step(dve.tensor_tensor(t2[:], t2[:], t1[:], ALU.mult))
                step(dve.scalar_tensor_tensor(out=dt[:], in0=dt[:], scalar=0.0, in1=t2[:], op0=ALU.max, op1=ALU.add))
                step(dve.tensor_scalar(t1[:], dt[:], a_log[:, bass.ds(i, 1)], -1.0, ALU.mult, ALU.mult))
                for c in range(TB):
                    mine = slice(c * P, (c + 1) * P)
                    step(dve.tensor_tensor_scan(acs[:, mine], ones[:, mine], t1[:, mine], 0.0, ALU.mult, ALU.add))
                for c in range(TB):
                    ins = dve.tensor_scalar(ends_in[:, c, :], k.ident[0:H, 0:H], acs[:, (c + 1) * P - 1:(c + 1) * P], None, ALU.mult)
                    if c < TB - 1:
                        step(ins)
                ins.then_inc(s["acs_ready"], 1)
                def silu(c):
                    dve.wait_ge(s["sig_done"], NC * i + c + 1)
                    dve.tensor_tensor(xbc[:, c, :], acc[:, c % 2, :], sig[:, c % 2, :], ALU.mult).then_inc(s["act_done"], 1)

                dve.wait_ge(s["ms_done"], 1 + KG * i)
                for c in range(NC):
                    if c >= 2:
                        silu(c - 2)
                        dve.wait_ge(s["act_done"], NC * i + c - 1)
                    dve.wait_ge(s["tile_copied"], NC * i + c + 1)
                    a = acc[:, c % 2, :]
                    step(dve.tensor_scalar(a, u[:, c % 2, 0:T], wcols(i, c, 0), wcols(i, c, None), ALU.mult, ALU.add))
                    for j in range(1, CONV):
                        ins = dve.scalar_tensor_tensor(out=a, in0=u[:, c % 2, j:j + T], scalar=wcols(i, c, j), in1=a,
                                                       op0=ALU.mult, op1=ALU.add)
                        if j < CONV - 1:
                            step(ins)
                    ins.then_inc(s["conv_done"], 1)
                silu(NC - 2)
                silu(NC - 1)
                dve.wait_ge(s["small_copied"], i + 1)
                dve.wait_ge(s["ends_copied"], i + 1)
                dve.tensor_tensor(wend[:], ends[:], small[:, 1], ALU.subtract).then_inc(s["wend_in"], 1)
                for f in range(KG):
                    dve.wait_ge(s["z_sig"], KG * i + f + 1)
                    dve.tensor_tensor(z[:, f, :], ps[:, f, :], sig[:, f % 2, :], ALU.mult).then_inc(s["z_gated"], 1)
                dve.wait_ge(s["decay_done"], 2 * i + 2)
                step(dve.tensor_tensor(wend[:], wend[:], small[:, 0], ALU.mult))
                dve.wait_ge(s["turned_copied"], (1 + TB) * (i + 1))
                for c in range(TB - 1):
                    dve.tensor_tensor(xw[:, c, :].rearrange("p (h n) -> p h n", h=H), xt[:, c, :].rearrange("p (h n) -> p h n", h=H),
                                      wend[:, c, :].rearrange("p (h o) -> p h o", o=1).to_broadcast([P, H, P_SSM]), ALU.mult).then_inc(s["xw_ready"], 1)
                for c in range(TB - 1):
                    dve.wait_ge(s["state_done"], (TB - 1) * i + c + 1)
                    if c == 0:
                        step(dve.tensor_copy(hp[:, 0, :], ps[:, 0, :]))
                    else:
                        step(dve.tensor_tensor(hp[:, c, :].rearrange("p (h n) -> p h n", h=H), hp[:, c - 1, :].rearrange("p (h n) -> p h n", h=H),
                                               decay[:, c, :].rearrange("p (h o) -> p h o", o=1).to_broadcast([P, H, P_SSM]), ALU.mult))
                        ins = dve.tensor_tensor(hp[:, c, :], hp[:, c, :], ps[:, c, :], ALU.add)
                        if c < TB - 2:
                            step(ins)
                ins.then_inc(s["state_ready"], 1)

                def segment(h):
                    dve.wait_ge(s["row_exp"], H * i + h + 1)
                    for c in range(TB):
                        mine = slice(c * P, (c + 1) * P)
                        ins = dve.scalar_tensor_tensor(out=seg[:, h % 2, mine], in0=ps[:, 4 + h % 2, mine], scalar=small[:, 1, c, h:h + 1],
                                                       in1=k.past_cap[:], op0=ALU.subtract, op1=ALU.min)
                    ins.then_inc(s["row_seen"], 1)

                dve.wait_ge(s["cb_copied"], i + 1)
                segment(0)
                for h in range(H):
                    if h + 1 < H:
                        if h >= 1:
                            dve.wait_ge(s["seg_exp"], H * i + h)
                        segment(h + 1)
                    dve.wait_ge(s["seg_exp"], H * i + h + 1)
                    if h >= 2:
                        dve.wait_ge(s["y_done"], H * i + h - 1)
                    for c in range(TB):
                        mine = slice(c * P, (c + 1) * P)
                        step(dve.scalar_tensor_tensor(out=sc[:, h % 2, c, :], in0=seg[:, h % 2, mine], scalar=small[:, 0, c, h:h + 1],
                                                      in1=cb[:, c, :], op0=ALU.mult, op1=ALU.mult))
                    dve.tensor_tensor(ce[:, h % 2, P:], rowx[:, h % 2, P:], xbc[:, 1, P:], ALU.mult).then_inc(s["scores_ready"], 1)
                    if h % 2:
                        f = h // 2
                        bank = (3, 7)[f % 2]
                        dve.wait_ge(s["y_done"], H * i + h + 1)
                        step(dve.scalar_tensor_tensor(out=xbc[:, 2 + f, :], in0=xbc[:, 2 + f, :], scalar=d_col[:, bass.ds(KG * i + f, 1)],
                                                      in1=ps[:, bank, :], op0=ALU.mult, op1=ALU.add))
                        dve.tensor_tensor(z[:, f, :], z[:, f, :], xbc[:, 2 + f, :], ALU.mult).then_inc(s["y_read"], 1)
                dve.wait_ge(s["std_done"], i + 1)
                step(dve.reciprocal(rstd[:], std[:]))
                for f in range(KG):
                    at = k.places["ssm_norm_w"][0] + KG * i + f
                    dve.scalar_tensor_tensor(out=ys[:, bass.ds(KG * i + f, 1), :], in0=z[:, f:f + 1, :], scalar=k.cols[:, bass.ds(at, 1)],
                                             in1=rstd[:].rearrange("p (o t) -> p o t", o=1), op0=ALU.mult, op1=ALU.mult).then_inc(s["group_done"], 1)
                assert step.n == VEC_STEPS, step.n


def merge_stage(k, name, branch, w_out_of, x, kt, merged):
    ps, w_in = k.ps, k.ins["w_in"][0]
    strips = kt // KD
    ft = FT // strips
    with k.stage(name, "g_loaded", "w_loaded0", "w_loaded1", "gate_done", "gate_ready", "tile_done", "tile_free", "vec_step") as (block, s, sb):
        gate = sb("gate", [P, FT, T])
        tmp = sb("tmp", [P, 2, T])
        loaded = (s["w_loaded0"], s["w_loaded1"])

        @block.sync
        def _(sp):
            k.clear(sp)
            for half in range(2):
                sp.wait_ge(s["gate_done"], FT * half)
                sp.dma_start(strip(k, 2), columns(w_in, GATE0 + branch * D + half * STRIP)).then_inc(s["g_loaded"], 16)
                for j in range(strips):
                    n = half * strips + j
                    if n >= 2:
                        sp.wait_ge(s["tile_done"], ft * (n - 1))
                    sp.dma_start(strip(k, n % 2, kt), w_out_of(half * STRIP + j * ft * P, ft * P)).then_inc(loaded[n % 2], 16)

        @block.tensor
        def _(pe):
            for half in range(2):
                pe.wait_ge(s["g_loaded"], 16 * (half + 1))
                pe.wait_ge(s["gate_ready"], FT * half)
                for f in range(FT):
                    for kk in range(KD):
                        mm = pe.matmul(ps[:, f, :], strip(k, 2)[:, kk, f * P:(f + 1) * P], k.h[:, kk, :], start=(kk == 0), stop=(kk == KD - 1))
                    mm.then_inc(s["gate_done"], 1)
                pe.wait_ge(s["tile_free"], FT * half)
                for j in range(strips):
                    n = half * strips + j
                    pe.wait_ge(loaded[n % 2], 16 * (n // 2 + 1))
                    for f in range(ft):
                        for kk in range(kt):
                            mm = pe.matmul(ps[:, 4 + j * ft + f, :], strip(k, n % 2, kt)[:, kk, f * P:(f + 1) * P], x[:, kk, :],
                                           start=(kk == 0), stop=(kk == kt - 1))
                        mm.then_inc(s["tile_done"], 1)

        @block.scalar
        def _(act):
            for n in range(2 * FT):
                act.wait_ge(s["gate_done"], n + 1)
                if n >= FT:
                    act.wait_ge(s["tile_free"], n - FT + 1)
                act.activation(gate[:, n % FT, :], ps[:, n % FT, :], ACT.Sigmoid).then_inc(s["gate_ready"], 1)

        @block.vector
        def _(dve):
            step = Steps(dve, s["vec_step"])
            for n in range(2 * FT):
                dve.wait_ge(s["gate_ready"], n + 1)
                dve.wait_ge(s["tile_done"], n + 1)
                if branch == 0:
                    dve.tensor_tensor(merged[:, n, :], gate[:, n % FT, :], ps[:, 4 + n % FT, :], ALU.mult).then_inc(s["tile_free"], 1)
                else:
                    step(dve.tensor_tensor(tmp[:, n % 2, :], gate[:, n % FT, :], ps[:, 4 + n % FT, :], ALU.mult))
                    dve.tensor_tensor(merged[:, n, :], merged[:, n, :], tmp[:, n % 2, :], ALU.add).then_inc(s["tile_free"], 1)


def pool_stage(k, pooled):
    ps, w_in = k.ps, k.ins["w_in"][0]
    with k.stage("pool", "zeroed", "counted", "recip", "copied", "pooled_done", "vec_step", *LINEAR, primed=LINEAR_PRIMED) as (block, s, sb):
        u = sb("u", [P, KD, PAD + T])
        a, b = sb("a", [P, PAD + T]), sb("b", [P, PAD + T])
        count = sb("count", [P, len(POOL_WINDOWS), PAD])
        pos = sb("pos", [P, PAD])
        free = (s["tile_free0"], s["tile_free1"])
        done = (s["tile_done0"], s["tile_done1"])
        linear(k, block, s, lambda i, slot: columns(w_in, U0 + (2 * i + slot) * STRIP), 1, lambda kk: k.h[:, kk, :], None)

        @block.gpsimd
        def _(pool):
            pool.memset(u[:, :, 0:PAD], 0.0).then_inc(s["zeroed"], 1)
            pool.memset(a[:], 0.0).then_inc(s["zeroed"], 1)
            pool.memset(b[:], 0.0).then_inc(s["zeroed"], 1)
            pool.iota(pos[:], pattern=[[1, PAD]], base=1, channel_multiplier=0,
                      allow_small_or_imprecise_dtypes=True).then_inc(s["zeroed"], 1)
            pool.wait_ge(s["zeroed"], 4)
            for g, w in enumerate(POOL_WINDOWS):
                pool.tensor_scalar(count[:, g, :], pos[:], float(w), None, ALU.min).then_inc(s["counted"], 1)

        @block.scalar
        def _(act):
            for c in range(KD):
                act.wait_ge(done[c // FT], 1 + c % FT + 1)
                act.activation(u[:, c, PAD:], ps[:, c, :], ACT.Copy).then_inc(free[c // FT], 1)

        @block.vector
        def _(dve):
            step = Steps(dve, s["vec_step"])
            dve.wait_ge(s["counted"], len(POOL_WINDOWS))
            step(dve.reciprocal(count[:], count[:]))
            for c in range(KD):
                g = c // (KD // len(POOL_WINDOWS))
                dve.wait_ge(free[c // FT], 1 + c % FT + 1)
                src, bufs = u[:, c, :], (a, b)
                for j in range(g + 1):
                    dst = bufs[j % 2]
                    step(dve.tensor_tensor(dst[:, PAD:], src[:, PAD:], src[:, PAD - 2 ** j:PAD + T - 2 ** j], ALU.add))
                    src = dst[:, :]
                w = POOL_WINDOWS[g]
                step(dve.scalar_tensor_tensor(out=pooled[:, c, PAD:], in0=src[:, 2 * PAD:], scalar=1.0 / w, in1=u[:, c, 2 * PAD:],
                                              op0=ALU.mult, op1=ALU.subtract))
                step(dve.tensor_tensor(src[:, PAD:2 * PAD], src[:, PAD:2 * PAD], count[:, g, :], ALU.mult))
                step(dve.tensor_tensor(pooled[:, c, 0:PAD], src[:, PAD:2 * PAD], u[:, c, PAD:2 * PAD], ALU.subtract))
    return


def pool_out_stage(k, pooled, merged):
    ps, w_in = k.ps, k.ins["w_in"][0]
    groups = len(POOL_WINDOWS)
    gk = KD // groups
    with k.stage("pool_out", "w_loaded", "g_loaded", "gate_done", "gate_ready", "tile_done", "tile_free", "vec_step") as (block, s, sb):
        gate = sb("gate", [P, 2, T])
        wp = k.w[:, 2, 0:groups * gk * gk * P].rearrange("p (g k n) -> p g k n", g=groups, k=gk)

        @block.sync
        def _(sp):
            k.clear(sp)
            sp.dma_start(wp.rearrange("p g k n -> p (g k) n"), k.ins["w_pool"][0].rearrange("g (k p) n -> p (g k) n", p=P)).then_inc(s["w_loaded"], 16)
            for half in range(2):
                sp.dma_start(strip(k, half), columns(w_in, GATE0 + D + half * STRIP)).then_inc(s["g_loaded"], 16)

        @block.tensor
        def _(pe):
            pe.wait_ge(s["w_loaded"], 16)
            pe.wait_ge(s["g_loaded"], 32)
            for c in range(KD):
                if c >= 4:
                    pe.wait_ge(s["tile_free"], c - 3)
                for kk in range(KD):
                    mm = pe.matmul(ps[:, c % 4, :], strip(k, c // FT)[:, kk, c % FT * P:(c % FT + 1) * P], k.h[:, kk, :],
                                   start=(kk == 0), stop=(kk == KD - 1))
                mm.then_inc(s["gate_done"], 1)
                g = c // gk
                for kk in range(gk):
                    mm = pe.matmul(ps[:, 4 + c % 4, :], wp[:, g, kk, c % gk * P:(c % gk + 1) * P], pooled[:, g * gk + kk, :],
                                   start=(kk == 0), stop=(kk == gk - 1))
                mm.then_inc(s["tile_done"], 1)

        @block.scalar
        def _(act):
            for c in range(KD):
                act.wait_ge(s["gate_done"], c + 1)
                if c >= 2:
                    act.wait_ge(s["tile_free"], c - 1)
                act.activation(gate[:, c % 2, :], ps[:, c % 4, :], ACT.Sigmoid).then_inc(s["gate_ready"], 1)

        @block.vector
        def _(dve):
            step = Steps(dve, s["vec_step"])
            for c in range(KD):
                dve.wait_ge(s["gate_ready"], c + 1)
                dve.wait_ge(s["tile_done"], c + 1)
                step(dve.scalar_tensor_tensor(out=gate[:, c % 2, :], in0=ps[:, 4 + c % 4, :], scalar=k.col("pool_scale", c),
                                              in1=gate[:, c % 2, :], op0=ALU.mult, op1=ALU.mult))
                dve.tensor_tensor(merged[:, c, :], merged[:, c, :], gate[:, c % 2, :], ALU.add).then_inc(s["tile_free"], 1)


def residual_stage(k, name, w, x, alpha, gate):
    ps = k.ps
    with k.stage(name, "vec_step", *SplitProducts.SEMS, primed=SplitProducts.PRIMED) as (block, s, sb):
        t = sb("t", [P, 2, T])
        lin = SplitLinear(k, block, s, sb, w, x)

        @block.scalar
        def _(act):
            lin.scalar(act)

        @block.vector
        def _(dve):
            step = Steps(dve, s["vec_step"])

            def add(n):
                dve.wait_ge(s["half_used"], 1 + n + 1)
                for c in range(n * HT, (n + 1) * HT):
                    step(dve.tensor_scalar(t[:, c % 2, :], ps[:, c, :], k.mod[:, gate + c:gate + c + 1], None, ALU.mult))
                    step(dve.scalar_tensor_tensor(out=k.x[:, c, :], in0=k.x[:, c, :], scalar=alpha, in1=t[:, c % 2, :], op0=ALU.mult,
                                                  op1=ALU.add))

            lin.vector(dve, add)


def router_stage(k, chosen, share):
    ps = k.ps
    GR = NE // EG
    with k.stage("router", "loaded", "logits_done", "vec_step", "exp_done") as (block, s, sb):
        wr = sb("wr", [P, KD, NE])
        br = sb("br", [P, NE])
        probs, sel = sb("probs", [P, TB, NE]), sb("sel", [P, TB, NE])
        rank, cmp = chosen, sb("cmp", [P, TB, NE])
        top = sb("top", [P, TB, NE])
        score, grank, gcmp = sb("score", [P, TB, GR]), sb("grank", [P, TB, GR]), sb("gcmp", [P, TB, GR])
        red = sb("red", [P, TB])

        @block.sync
        def _(sp):
            k.clear(sp)
            sp.dma_start(wr[:], k.ins["w_router"].rearrange("(k p) n -> p k n", p=P)).then_inc(s["loaded"], 16)
            sp.dma_start(br[:], k.ins["b_router"].rearrange("(o n) -> o n", o=1).to_broadcast([P, NE])).then_inc(s["loaded"], 16)

        @block.tensor
        def _(pe):
            pe.wait_ge(s["loaded"], 32)
            for b in range(TB):
                for kk in range(KD):
                    mm = pe.matmul(ps[:, 0, b * NE:(b + 1) * NE], k.h[:, kk, b * P:(b + 1) * P], wr[:, kk, :],
                                   start=(kk == 0), stop=(kk == KD - 1))
            mm.then_inc(s["logits_done"], 1)

        @block.scalar
        def _(act):
            act.wait_ge(s["vec_step"], 2)
            act.activation(probs[:], sel[:], ACT.Exp).then_inc(s["exp_done"], 1)

        @block.vector
        def _(dve):
            step = Steps(dve, s["vec_step"])

            def over(m, n):
                return m[:].rearrange("p (b o) -> p b o", o=1).to_broadcast([P, TB, n])

            dve.wait_ge(s["loaded"], 32)
            dve.wait_ge(s["logits_done"], 1)
            logits = ps[:, 0, 0:TB * NE].rearrange("p (b n) -> p b n", b=TB)
            step(dve.tensor_reduce(red[:], logits, AX.X, ALU.max))
            step(dve.tensor_tensor(sel[:], logits, over(red, NE), ALU.subtract))
            dve.wait_ge(s["exp_done"], 1)
            step(dve.tensor_reduce(red[:], probs[:], AX.X, ALU.add))
            step(dve.reciprocal(red[:], red[:]))
            step(dve.tensor_tensor(probs[:], probs[:], over(red, NE), ALU.mult))
            step(dve.tensor_tensor(sel[:], probs[:], br[:].rearrange("p (o n) -> p o n", o=1).to_broadcast([P, TB, NE]), ALU.add))

            def rank_in(rank, tmp, val, n, width):
                step(dve.memset(rank, 0.0))
                for a in range(n):
                    for b in range(n):
                        if a != b:
                            step(dve.tensor_tensor(tmp(a), val(b), val(a), ALU.is_ge if b < a else ALU.is_gt))
                            step(dve.tensor_tensor(rank_of(rank, a, n), rank_of(rank, a, n), tmp(a), ALU.add))

            def rank_of(m, a, n):
                return m.rearrange("p b (g n) -> p b g n", n=n)[:, :, :, a]

            rank_in(rank[:], lambda a: rank_of(cmp[:], a, EG), lambda a: rank_of(sel[:], a, EG), EG, GR)
            step(dve.tensor_scalar(rank[:], rank[:], float(2), None, ALU.is_lt))
            step(dve.tensor_tensor(top[:], sel[:], rank[:], ALU.mult))
            step(dve.tensor_reduce(score[:], top[:].rearrange("p b (g n) -> p b g n", n=EG), AX.X, ALU.add))
            rank_in(grank[:], lambda a: rank_of(gcmp[:], a, GR), lambda a: rank_of(score[:], a, GR), GR, 1)
            step(dve.tensor_scalar(grank[:], grank[:], 0.0, None, ALU.is_equal))
            for n in range(EG):
                step(dve.tensor_tensor(rank_of(rank[:], n, EG), rank_of(rank[:], n, EG), grank[:], ALU.mult))
            step(dve.tensor_tensor(share[:], probs[:], rank[:], ALU.mult))
            step(dve.tensor_reduce(red[:], share[:], AX.X, ALU.add))
            step(dve.reciprocal(red[:], red[:]))
            step(dve.tensor_tensor(share[:], share[:], over(red, NE), ALU.mult))
            assert step.n == ROUTER_STEPS, step.n


ROUTER_STEPS = 68


def dispatch_stage(k, m):
    ps = k.ps
    BIG = float(2 * NBLK * P)
    with k.stage("dispatch", "consts_ready", "pos_done", "vec_step", "h_turned", "h_copied", "h_stored", "zeros_stored",
                 "slots_ready", "total_stored") as (block, s, sb):
        earlier = sb("earlier", [P, P])
        ht = sb("ht", [P, TB, D])
        zeros = sb("zeros", [P, NBLK], I32)
        tokens = sb("tokens", [P, TB], I32)
        block_no = sb("block_no", [1, NBLK])
        ones = sb("ones", [P, NE])
        cnt, used, cmp1, end, start = (sb(n, [P, NE]) for n in ("cnt", "used", "cmp1", "end", "start"))
        slot, low, cmp = (sb(n, [P, TB, NE]) for n in ("slot", "low", "cmp"))
        g = [sb(f"g{j}", [P, TB]) for j in range(2)]
        passed = sb("passed", [1, NBLK, NE])
        plan_f = sb("plan_f", [1, NBLK + 1])

        @block.sync
        def _(sp):
            k.clear(sp)
            sp.wait_ge(s["consts_ready"], 6)
            sp.dma_start(m.slot_token.rearrange("(p n) o -> p (n o)", p=P), zeros[:]).then_inc(s["zeros_stored"], 16)
            for b in range(TB):
                sp.wait_ge(s["h_copied"], 2 * b + 2)
                sp.dma_start(m.h_rows[b * P:(b + 1) * P, :], ht[:, b, :]).then_inc(s["h_stored"], 16)
            sp.wait_ge(s["h_stored"], 16 * TB)

        @block.gpsimd
        def _(pool):
            pool.memset(earlier[:], 1.0).then_inc(s["consts_ready"], 1)
            pool.memset(zeros[:], 0).then_inc(s["consts_ready"], 1)
            pool.memset(ones[:], 1.0).then_inc(s["consts_ready"], 1)
            pool.iota(tokens[:], pattern=[[P, TB]], base=0, channel_multiplier=1).then_inc(s["consts_ready"], 1)
            pool.iota(block_no[:], pattern=[[1, NBLK]], base=0, channel_multiplier=0,
                      allow_small_or_imprecise_dtypes=True).then_inc(s["consts_ready"], 1)
            pool.wait_ge(s["consts_ready"], 5)
            pool.affine_select(out=earlier[:], in_=earlier[:], compare_op=ALU.is_ge, fill=0.0, base=-1,
                               pattern=[[1, P]], channel_multiplier=-1).then_inc(s["consts_ready"], 1)
            pool.wait_ge(s["slots_ready"], 1)
            pool.wait_ge(s["zeros_stored"], 16)
            for j in range(2):
                for b in range(TB):
                    pool.indirect_dma_start(m.slot_token, bass.IndirectOffsetOnAxis(ap=m.slots[j][:, b:b + 1], axis=0),
                                            tokens[:, b:b + 1], None).then_inc(m.tokens_stored, 16)
            pool.wait_ge(m.tokens_stored, 16 * 2 * TB)

        @block.tensor
        def _(pe):
            pe.wait_ge(s["consts_ready"], 6)
            for b in range(TB):
                at = ps[:, 0, b * NE:(b + 1) * NE]
                for bb in range(b):
                    pe.matmul(at, k.ones[:], m.chosen[:, bb, :], start=(bb == 0), stop=False)
                pe.matmul(at, earlier[:], m.chosen[:, b, :], start=(b == 0), stop=True)
            for b in range(TB):
                mm = pe.matmul(ps[:, 1, 0:NE], k.ones[:], m.chosen[:, b, :], start=(b == 0), stop=(b == TB - 1))
            mm.then_inc(s["pos_done"], 1)
            for n in range(2 * TB):
                if n >= 4:
                    pe.wait_ge(s["h_copied"], n - 3)
                for j in range(4):
                    mm = pe.transpose(ps[:, 2 + n % 4, j * P:(j + 1) * P], k.h[:, n % 2 * 4 + j, n // 2 * P:(n // 2 + 1) * P], k.ident[:])
                mm.then_inc(s["h_turned"], 1)

        @block.scalar
        def _(act):
            for n in range(2 * TB):
                act.wait_ge(s["h_turned"], n + 1)
                act.activation(ht[:, n // 2, n % 2 * 512:(n % 2 + 1) * 512], ps[:, 2 + n % 4, :], ACT.Copy).then_inc(s["h_copied"], 1)

        @block.vector
        def _(dve):
            step = Steps(dve, s["vec_step"])

            def over(m2):
                return m2.rearrange("p (b o) -> p b o", o=1).to_broadcast([P, TB, NE])

            dve.wait_ge(s["consts_ready"], 6)
            dve.wait_ge(s["pos_done"], 1)
            step(dve.tensor_copy(cnt[:], ps[:, 1, 0:NE]))
            step(dve.tensor_scalar(used[:], cnt[:], 0.0, None, ALU.is_gt))
            for j in range(1, TB):
                step(dve.tensor_scalar(cmp1[:], cnt[:], float(j * P), None, ALU.is_gt))
                step(dve.tensor_tensor(used[:], used[:], cmp1[:], ALU.add))
            step(dve.tensor_tensor_scan(end[:], ones[:], used[:], 0.0, ALU.mult, ALU.add))
            step(dve.tensor_tensor(start[:], end[:], used[:], ALU.subtract))
            step(dve.tensor_scalar(start[:], start[:], float(P), None, ALU.mult))
            step(dve.tensor_tensor(slot[:], ps[:, 0, 0:TB * NE].rearrange("p (b n) -> p b n", b=TB),
                                   start[:].rearrange("p (o n) -> p o n", o=1).to_broadcast([P, TB, NE]), ALU.add))
            step(dve.tensor_scalar(low[:], m.chosen[:], -BIG, BIG, ALU.mult, ALU.add))
            step(dve.tensor_tensor(low[:], low[:], slot[:], ALU.add))
            step(dve.tensor_reduce(g[0][:], low[:], AX.X, ALU.min))
            step(dve.scalar_tensor_tensor(out=slot[:], in0=slot[:], scalar=1.0, in1=m.chosen[:], op0=ALU.add, op1=ALU.mult))
            step(dve.tensor_reduce(g[1][:], slot[:], AX.X, ALU.max))
            for j, of in enumerate((low, slot)):
                step(dve.tensor_tensor(cmp[:], of[:], over(g[j][:]), ALU.is_equal))
                step(dve.tensor_tensor(cmp[:], cmp[:], m.share[:], ALU.mult))
                step(dve.tensor_reduce(m.weights[j][:], cmp[:], AX.X, ALU.add))
            step(dve.tensor_scalar(g[1][:], g[1][:], -1.0, None, ALU.add))
            step(dve.tensor_copy(m.slots[0][:], g[0][:]))
            step(dve.tensor_copy(m.slots[1][:], g[1][:]))
            step(dve.tensor_tensor(passed[:], end[0:1, :].rearrange("p (o n) -> p o n", o=1).to_broadcast([1, NBLK, NE]),
                                   block_no[:].rearrange("p (n o) -> p n o", o=1).to_broadcast([1, NBLK, NE]), ALU.is_le))
            step(dve.tensor_reduce(plan_f[:, 0:NBLK], passed[:], AX.X, ALU.add))
            step(dve.tensor_scalar(plan_f[:, 0:NBLK], plan_f[:, 0:NBLK], float(NE - 1), None, ALU.min))
            step(dve.tensor_copy(plan_f[:, NBLK:], end[0:1, NE - 1:NE]))
            dve.tensor_copy(m.plan[:], plan_f[:]).then_inc(s["slots_ready"], 1)


class Dispatch:

    def __init__(self, k, stack):
        self.chosen = k.sb("chosen", [P, TB, NE], stack=stack)
        self.share = k.sb("share", [P, TB, NE], stack=stack)
        self.slots = [k.sb(f"slots{j}", [P, TB], I32, stack) for j in range(2)]
        self.weights = [k.sb(f"weights{j}", [P, TB], F32, stack) for j in range(2)]
        self.plan = k.sb("plan", [1, NBLK + 1], I32, stack)
        self.h_rows = k.nc.dram_tensor("h_rows", (T, D), F32, kind="Internal").ap()
        self.slot_token = k.nc.dram_tensor("slot_token", (NBLK * P, 1), I32, kind="Internal").ap()
        self.y_rows = k.nc.dram_tensor("y_rows", (NBLK * P, D), F32, kind="Internal").ap()
        self.tokens_stored, self.gathered, self.y_gathered = (
            k.stack.enter_context(k.nc.semaphore(n)) for n in ("tokens_stored", "gathered", "y_gathered"))


def experts_stage(k, m):
    ps = k.ps
    w1, w3, w2 = k.ins["w_exp_gate"][0], k.ins["w_exp_up"][0], k.ins["w_exp_down"][0]
    with k.stage("experts", "index_loaded", "loaded0", "loaded1", "loaded2", "x_turned", "x_copied", "gate_done", "up_done",
                 "sig_done", "gated", "hidden_done", "hidden_turned", "hidden_copied", "down_done", "index_used", "y_copied0", "y_copied1", "y_stored", "zeroed", "x_free",
                 primed=("gate_done", "up_done", "down_done", "x_turned", "x_copied", "hidden_turned", "y_copied0",
                         "y_copied1", "y_stored", "hidden_done", "index_used")) as (block, s, sb):
        index = sb("index", [P, 1], I32)
        xg = sb("xg", [P, D])
        xt = sb("xt", [P, KD, P])
        sig, t, hidden = sb("sig", [P, DFF]), sb("t", [P, DFF]), sb("hidden", [P, DFF])
        ht = sb("ht", [P, KE, P])
        y = sb("y", [P, D])
        zeros = sb("zeros", [P, D])

        def in_use(eng):
            return eng.value_load(m.plan[0:1, NBLK:NBLK + 1], min_val=1, max_val=NBLK)

        @block.sync
        def _(sp):
            k.clear(sp)
            blocks = in_use(sp)
            with sp.Fori(0, NBLK) as n, sp.If(n < blocks):
                e = sp.value_load(m.plan[0:1, bass.ds(n, 1)], min_val=0, max_val=NE - 1)
                sp.wait_ge(s["index_used"], 1 + n)
                sp.dma_start(index[:], m.slot_token[bass.ds(n * P, P), :]).then_inc(s["index_loaded"], 16)
                sp.wait_ge(s["gate_done"], 1 + n)
                sp.dma_start(strip(k, 0), w1[bass.ds(e, 1)].rearrange("e (k p) n -> p (e k) n", p=P)).then_inc(s["loaded0"], 16)
                sp.wait_ge(s["up_done"], 1 + n)
                sp.dma_start(strip(k, 1), w3[bass.ds(e, 1)].rearrange("e (k p) n -> p (e k) n", p=P)).then_inc(s["loaded1"], 16)
                sp.wait_ge(s["down_done"], 1 + 2 * n)
                sp.dma_start(strip(k, 2, KE), w2[bass.ds(e, 1)].rearrange("e (k p) n -> p (e k) n", p=P)).then_inc(s["loaded2"], 16)

        @block.gpsimd
        def _(pool):
            pool.memset(zeros[:], 0.0).then_inc(s["zeroed"], 1)
            blocks = in_use(pool)
            with pool.Fori(0, NBLK) as n, pool.If(n < blocks):
                pool.wait_ge(s["index_loaded"], 16 * (n + 1))
                pool.wait_ge(s["x_turned"], 1 + n)
                pool.sem_inc(s["x_free"], 1)
                pool.indirect_dma_start(xg[:], None, m.h_rows, bass.IndirectOffsetOnAxis(ap=index[:], axis=0)).then_inc(m.gathered, 16)
                pool.wait_ge(m.gathered, 16 * (n + 1))
                pool.sem_inc(s["index_used"], 1)

        @block.tensor
        def _(pe):
            blocks = in_use(pe)
            with pe.Fori(0, NBLK) as n, pe.If(n < blocks):
                pe.wait_ge(m.gathered, 16 * (n + 1))
                pe.wait_ge(s["x_copied"], 1 + 2 * n)
                for c in range(KD):
                    mm = pe.transpose(ps[:, c // 4, c % 4 * P:(c % 4 + 1) * P], xg[:, c * P:(c + 1) * P], k.ident[:])
                mm.then_inc(s["x_turned"], 1)
                pe.wait_ge(s["x_copied"], 1 + 2 * (n + 1))
                pe.wait_ge(s["hidden_done"], 1 + n)
                for slot, done, loaded in ((0, "gate_done", "loaded0"), (1, "up_done", "loaded1")):
                    pe.wait_ge(s[loaded], 16 * (n + 1))
                    for kk in range(KD):
                        mm = pe.matmul(ps[:, 2 + slot, :], xt[:, kk, :], strip(k, slot)[:, kk, :], start=(kk == 0), stop=(kk == KD - 1))
                    mm.then_inc(s[done], 1)
                pe.wait_ge(s["hidden_done"], 1 + n + 1)
                for f in range(KE):
                    mm = pe.transpose(ps[:, 4, f * P:(f + 1) * P], hidden[:, f * P:(f + 1) * P], k.ident[:])
                mm.then_inc(s["hidden_turned"], 1)
                pe.wait_ge(s["hidden_copied"], n + 1)
                pe.wait_ge(s["loaded2"], 16 * (n + 1))
                pe.wait_ge(s["y_copied0"], 1 + n)
                pe.wait_ge(s["y_copied1"], 1 + n)
                for half in range(2):
                    for f in range(KE):
                        mm = pe.matmul(ps[:, 5 + half, :], ht[:, f, :], strip(k, 2, KE)[:, f, half * STRIP:(half + 1) * STRIP],
                                       start=(f == 0), stop=(f == KE - 1))
                    mm.then_inc(s["down_done"], 1)

        @block.scalar
        def _(act):
            blocks = in_use(act)
            with act.Fori(0, NBLK) as n, act.If(n < blocks):
                act.wait_ge(s["x_turned"], 1 + n + 1)
                act.wait_ge(s["up_done"], 1 + n)
                act.activation(xt[:, 0:4, :], ps[:, 0, :].rearrange("p (c n) -> p c n", c=4), ACT.Copy).then_inc(s["x_copied"], 1)
                act.wait_ge(s["gate_done"], 1 + n + 1)
                act.wait_ge(s["hidden_done"], 1 + n)
                act.activation(sig[:], ps[:, 2, :], ACT.Sigmoid).then_inc(s["sig_done"], 1)
                act.wait_ge(s["hidden_turned"], 1 + n + 1)
                act.wait_ge(s["down_done"], 1 + 2 * n)
                act.activation(ht[:], ps[:, 4, :].rearrange("p (c n) -> p c n", c=KE), ACT.Copy).then_inc(s["hidden_copied"], 1)
                act.wait_ge(s["down_done"], 1 + 2 * n + 1)
                act.wait_ge(s["y_stored"], 1 + 16 * n)
                act.activation(y[:, 0:STRIP], ps[:, 5, :], ACT.Copy).then_inc(s["y_copied0"], 1)
                act.wait_ge(s["y_copied0"], 1 + n + 1)
                act.wait_ge(s["y_copied1"], 1 + n + 1)
                act.dma_start(m.y_rows[bass.ds(n * P, P), :], y[:]).then_inc(s["y_stored"], 16)
            act.wait_ge(s["zeroed"], 1)
            with act.Fori(0, NBLK) as n, act.If(n >= blocks):
                act.dma_start(m.y_rows[bass.ds(n * P, P), :], zeros[:]).then_inc(s["y_stored"], 16)
            act.wait_ge(s["y_stored"], 1 + 16 * NBLK)

        @block.vector
        def _(dve):
            blocks = in_use(dve)
            with dve.Fori(0, NBLK) as n, dve.If(n < blocks):
                dve.wait_ge(s["x_turned"], 1 + n + 1)
                dve.wait_ge(s["up_done"], 1 + n)
                dve.tensor_copy(xt[:, 4:8, :], ps[:, 1, :].rearrange("p (c n) -> p c n", c=4)).then_inc(s["x_copied"], 1)
                dve.wait_ge(s["sig_done"], n + 1)
                dve.tensor_tensor(t[:], ps[:, 2, :], sig[:], ALU.mult).then_inc(s["gated"], 1)
                dve.wait_ge(s["gated"], n + 1)
                dve.wait_ge(s["up_done"], 1 + n + 1)
                dve.wait_ge(s["hidden_turned"], 1 + n)
                dve.tensor_tensor(hidden[:], t[:], ps[:, 3, :], ALU.mult).then_inc(s["hidden_done"], 1)
                dve.wait_ge(s["down_done"], 1 + 2 * n + 2)
                dve.wait_ge(s["y_stored"], 1 + 16 * n)
                dve.tensor_copy(y[:, STRIP:], ps[:, 6, :]).then_inc(s["y_copied1"], 1)


def combine_stage(k, m, gate):
    ps = k.ps
    with k.stage("combine", "weighed", "turned", "scaled", "vec_step", "added") as (block, s, sb):
        rows = [sb(f"rows{j}", [P, TB, D]) for j in range(2)]
        t = sb("t", [P, 2, T])

        @block.sync
        def _(sp):
            k.clear(sp)

        @block.gpsimd
        def _(pool):
            for b in range(TB):
                for j in range(2):
                    pool.indirect_dma_start(rows[j][:, b, :], None, m.y_rows,
                                            bass.IndirectOffsetOnAxis(ap=m.slots[j][:, b:b + 1], axis=0)).then_inc(m.y_gathered, 16)

        @block.vector
        def _(dve):
            step = Steps(dve, s["vec_step"])
            dve.wait_ge(m.y_gathered, 16 * 2 * TB)
            for b in range(TB):
                step(dve.tensor_scalar(rows[0][:, b, :], rows[0][:, b, :], m.weights[0][:, b:b + 1], None, ALU.mult))
                dve.scalar_tensor_tensor(out=rows[0][:, b, :], in0=rows[1][:, b, :], scalar=m.weights[1][:, b:b + 1], in1=rows[0][:, b, :],
                                         op0=ALU.mult, op1=ALU.add).then_inc(s["weighed"], 1)
            for c in range(KD):
                dve.wait_ge(s["scaled"], c + 1)
                dve.scalar_tensor_tensor(out=k.x[:, c, :], in0=k.x[:, c, :], scalar=ALPHA_1, in1=t[:, c % 2, :], op0=ALU.mult,
                                         op1=ALU.add).then_inc(s["added"], 1)

        @block.tensor
        def _(pe):
            pe.wait_ge(s["weighed"], TB)
            for c in range(KD):
                for b in range(TB):
                    mm = pe.transpose(ps[:, c, b * P:(b + 1) * P], rows[0][:, b, c * P:(c + 1) * P], k.ident[:])
                mm.then_inc(s["turned"], 1)

        @block.scalar
        def _(act):
            for c in range(KD):
                act.wait_ge(s["turned"], c + 1)
                if c >= 2:
                    act.wait_ge(s["added"], c - 1)
                act.activation(t[:, c % 2, :], ps[:, c, :], ACT.Copy, scale=k.mod[:, gate + c:gate + c + 1]).then_inc(s["scaled"], 1)


def output_stage(k, out):
    ps = k.ps
    with k.stage("output", "turned", "copied", "stored") as (block, s, sb):
        xt = sb("xt", [P, TB, D])

        @block.tensor
        def _(pe):
            for n in range(2 * TB):
                if n >= 4:
                    pe.wait_ge(s["copied"], n - 3)
                for j in range(4):
                    mm = pe.transpose(ps[:, n % 4, j * P:(j + 1) * P], k.x[:, n % 2 * 4 + j, n // 2 * P:(n // 2 + 1) * P], k.ident[:])
                mm.then_inc(s["turned"], 1)

        @block.scalar
        def _(act):
            for n in range(2 * TB):
                act.wait_ge(s["turned"], n + 1)
                act.activation(xt[:, n // 2, n % 2 * 512:(n % 2 + 1) * 512], ps[:, n % 4, :], ACT.Copy).then_inc(s["copied"], 1)

        @block.sync
        def _(sp):
            k.clear(sp)
            for b in range(TB):
                sp.wait_ge(s["copied"], 2 * b + 2)
                sp.dma_start(out[0, b * P:(b + 1) * P, :], xt[:, b, :]).then_inc(s["stored"], 16)
            sp.wait_ge(s["stored"], 16 * TB)


def modulate_stage(k, name, first):
    with k.stage(name, "done") as (block, s, sb):
        @block.sync
        def _(sp):
            k.clear(sp)

        @block.scalar
        def _(act):
            for c in range(0, KD, 2):
                act.activation(k.h[:, c, :], k.x[:, c, :], ACT.Identity, scale=k.mod[:, first + 8 + c:first + 9 + c],
                               bias=k.mod[:, first + c:first + c + 1]).then_inc(s["done"], 1)

        @block.vector
        def _(dve):
            for c in range(1, KD, 2):
                dve.tensor_scalar(k.h[:, c, :], k.x[:, c, :], k.mod[:, first + 8 + c:first + 9 + c],
                                  k.mod[:, first + c:first + c + 1], ALU.mult, ALU.add).then_inc(s["done"], 1)


def reduced_angle(step, dve, out, turns, angle, offset):
    step(dve.tensor_scalar(turns, angle, 1.0 / TWO_PI, offset / TWO_PI, ALU.mult, ALU.add))
    step(dve.tensor_scalar(turns, turns, ROUND, -ROUND, ALU.add, ALU.add))
    step(dve.scalar_tensor_tensor(out=out, in0=turns, scalar=-PI_A, in1=angle, op0=ALU.mult, op1=ALU.add))
    step(dve.scalar_tensor_tensor(out=out, in0=turns, scalar=-PI_B, in1=out, op0=ALU.mult, op1=ALU.add))
    step(dve.scalar_tensor_tensor(out=out, in0=turns, scalar=-PI_C, in1=out, op0=ALU.mult, op1=ALU.add))
    step(dve.tensor_scalar(out, out, offset, None, ALU.add))
    step(dve.tensor_scalar(out, out, PI_SAFE, -PI_SAFE, ALU.min, ALU.max))


def latent_stage(k, cq, ckv, k_pe, cos, sin):
    ps, w = k.ps, k.ins["mla_w_in_2"][0]
    width = QL + KVL + ROPE
    half = ROPE // 2
    with k.stage("latent", "loaded", "freq_ready", "pos_ready", "angle_done", "vec_step", "sin_done", "proj_done", "sq_done", "ms_done",
                 "std_done") as (block, s, sb):
        wl = k.w[:, 0, 0:KD * width].rearrange("p (k n) -> p k n", k=KD)
        pos_i, pos = sb("pos_i", [1, T], I32), sb("pos", [1, T])
        freq = sb("freq", [1, ROPE])
        angle, turns = sb("angle", [ROPE, T]), sb("turns", [ROPE, T])
        sq = sb("sq", [P, 3, T])
        std = sb("std", [P, 2, T])
        raw, swapped = sb("raw", [ROPE, T]), sb("swapped", [ROPE, T])
        NORMS = ((QL, 0, 2, "mla_q_norm_2"), (KVL, 2, 1, "mla_kv_norm_2"))

        @block.sync
        def _(sp):
            k.clear(sp)
            sp.dma_start(pos_i[:], k.ins["positions_2"]).then_inc(s["loaded"], 16)
            sp.dma_start(wl, w.rearrange("(k p) n -> p k n", p=P)).then_inc(s["loaded"], 16)

        @block.gpsimd
        def _(pool):
            for j in range(ROPE):
                pool.memset(freq[:, j:j + 1], ROPE_THETA ** (-2.0 * (j % half) / ROPE)).then_inc(s["freq_ready"], 1)

        @block.tensor
        def _(pe):
            pe.wait_ge(s["freq_ready"], ROPE)
            pe.wait_ge(s["pos_ready"], 1)
            pe.matmul(ps[0:ROPE, 0, :], freq[:], pos[:], start=True, stop=True).then_inc(s["angle_done"], 1)
            pe.wait_ge(s["loaded"], 32)
            for c in range(4):
                n = P if c < 3 else ROPE
                for kk in range(KD):
                    mm = pe.matmul(ps[0:n, 1 + c, :], wl[:, kk, c * P:c * P + n], k.h[:, kk, :], start=(kk == 0), stop=(kk == KD - 1))
                mm.then_inc(s["proj_done"], 1)
            for j, (_, first, n, _) in enumerate(NORMS):
                pe.wait_ge(s["sq_done"], first + n)
                for c in range(n):
                    mm = pe.matmul(ps[:, 5 + j, :], k.ones[:], sq[:, first + c, :], start=(c == 0), stop=(c == n - 1))
                mm.then_inc(s["ms_done"], 1)

        @block.scalar
        def _(act):
            act.wait_ge(s["vec_step"], 15)
            act.activation(sin[:], angle[:], ACT.Sin).then_inc(s["sin_done"], 1)
            act.activation(cos[:], cos[:], ACT.Sin).then_inc(s["sin_done"], 1)
            for c in range(3):
                act.wait_ge(s["proj_done"], c + 1)
                act.activation(sq[:, c, :], ps[:, 1 + c, :], ACT.Square).then_inc(s["sq_done"], 1)
            for j, (width_j, *_) in enumerate(NORMS):
                act.wait_ge(s["ms_done"], j + 1)
                act.activation(std[:, j, :], ps[:, 5 + j, :], ACT.Sqrt, scale=1.0 / width_j, bias=k.eps_rms[:]).then_inc(s["std_done"], 1)

        @block.vector
        def _(dve):
            step = Steps(dve, s["vec_step"])
            dve.wait_ge(s["loaded"], 32)
            dve.tensor_copy(pos[:], pos_i[:]).then_inc(s["pos_ready"], 1)
            dve.wait_ge(s["angle_done"], 1)
            step(dve.tensor_copy(raw[:], ps[0:ROPE, 0, :]))
            reduced_angle(step, dve, angle[:], turns[:], raw[:], 0.0)
            reduced_angle(step, dve, cos[:], turns[:], raw[:], math.pi / 2)
            dve.wait_ge(s["sin_done"], 2)
            step(dve.tensor_scalar(sin[0:half, :], sin[0:half, :], -1.0, None, ALU.mult))
            dve.wait_ge(s["proj_done"], 4)
            rotate(step, dve, k_pe, ps[0:ROPE, 4, :], raw, swapped, cos, sin, 1.0)
            for j, (_, first, n, norm) in enumerate(NORMS):
                dve.wait_ge(s["std_done"], j + 1)
                step(dve.reciprocal(std[:, j, :], std[:, j, :]))
                for c in range(n):
                    dst = cq[:, c, :] if j == 0 else ckv[:]
                    step(dve.scalar_tensor_tensor(out=dst, in0=ps[:, 1 + first + c, :], scalar=k.col(norm, c), in1=std[:, j, :],
                                                  op0=ALU.mult, op1=ALU.mult))


ROPE_THETA = 10000.0


def rotate(step, dve, out, src, raw, swapped, cos, sin, scale, last=None):
    half = ROPE // 2
    step(dve.tensor_scalar(swapped[0:half, :], src[half:ROPE], scale, None, ALU.mult))
    step(dve.tensor_scalar(swapped[half:ROPE, :], src[0:half], scale, None, ALU.mult))
    step(dve.tensor_tensor(swapped[:], swapped[:], sin[:], ALU.mult))
    step(dve.scalar_tensor_tensor(out=raw[:], in0=src, scalar=scale, in1=cos[:], op0=ALU.mult, op1=ALU.mult))
    ins = dve.tensor_tensor(out[:], raw[:], swapped[:], ALU.add)
    if last is None:
        step(ins)
    else:
        ins.then_inc(last, 1)


def latent_attention_stage(k, cq, ckv, k_pe, cos, sin, o):
    ps = k.ps
    scale = 1.0 / math.sqrt(NOPE + ROPE)
    nq = QL // P
    with k.stage("latent_attention", "w_loaded", "qn_done", "qp_done", "kn_done", "v_done", "copied", "q_turned", "rope_step", *SOFTMAX, primed=("copied", "exp_done", "o_copied", "scores_done", "v_done", "weighed")) as (block, s, sb):
        wq, wkv = sb("wq", [P, nq, NOPE + ROPE]), sb("wkv", [P, NOPE + VD])
        qn, kn, qp = sb("qn", [P, T]), sb("kn", [P, T]), sb("qp", [ROPE, T])
        raw, swapped = sb("raw", [ROPE, T]), sb("swapped", [ROPE, T])
        v = sb("v", [P, TB, VD])
        p_tiles, pt_tiles = sb("p_tiles", [P, 3, T]), sb("pt_tiles", [P, 2, T])
        nmax, rsum, rinv = sb("nmax", [P, TB]), sb("rsum", [P, TB]), sb("rinv", [P, TB])
        units = [(slice(0, VD), b) for b in range(TB)]

        def scores(pe, unit, bank):
            b = unit[1]
            n = (b + 1) * P
            pe.matmul(ps[:, bank, 0:n], qn[:, b * P:n], kn[:, 0:n], start=True, stop=False)
            return pe.matmul(ps[:, bank, 0:n], qp[:, b * P:n], k_pe[:, 0:n], start=False, stop=True)

        tensor, vector, scalar = scan_softmax(k, s, units, scores, p_tiles, pt_tiles, lambda unit, kb: v[:, kb, :], nmax, rsum, rinv)

        @block.sync
        def _(sp):
            k.clear(sp)
            with sp.Fori(0, MLA_HEADS) as i:
                sp.wait_ge(s["v_done"], 1 + i)
                sp.dma_start(wq[:], columns(k.ins["mla_w_qb_2"][0], i * (NOPE + ROPE), NOPE + ROPE)).then_inc(s["w_loaded"], 16)
                sp.dma_start(wkv[:], k.ins["mla_w_kvb_2"][0][:, bass.ds(i * (NOPE + VD), NOPE + VD)]).then_inc(s["w_loaded"], 16)

        @block.tensor
        def _(pe):
            with pe.Fori(0, MLA_HEADS) as i:
                pe.wait_ge(s["w_loaded"], 32 * (i + 1))
                pe.wait_ge(s["copied"], 1 + 3 * i)
                for c in range(nq):
                    mm = pe.matmul(ps[:, 6, :], wq[:, c, 0:NOPE], cq[:, c, :], start=(c == 0), stop=(c == nq - 1))
                mm.then_inc(s["qn_done"], 1)
                for c in range(nq):
                    mm = pe.matmul(ps[0:ROPE, 7, :], wq[:, c, NOPE:], cq[:, c, :], start=(c == 0), stop=(c == nq - 1))
                mm.then_inc(s["qp_done"], 1)
                pe.wait_ge(s["copied"], 1 + 3 * i + 1)
                pe.matmul(ps[:, 6, :], wkv[:, 0:NOPE], ckv[:], start=True, stop=True).then_inc(s["kn_done"], 1)
                pe.wait_ge(s["q_turned"], i + 1)
                for b in range(TB):
                    mm = pe.matmul(ps[:, 7, b * P:(b + 1) * P], ckv[:, b * P:(b + 1) * P], wkv[:, NOPE:], start=True, stop=True)
                mm.then_inc(s["v_done"], 1)
                pe.wait_ge(s["copied"], 1 + 3 * i + 3)
                tensor(pe, i)

        @block.scalar
        def _(act):
            with act.Fori(0, MLA_HEADS) as i:
                act.wait_ge(s["qn_done"], i + 1)
                act.wait_ge(s["weighed"], 1 + TB * i)
                act.activation(qn[:], ps[:, 6, :], ACT.Copy, scale=scale).then_inc(s["copied"], 1)
                act.wait_ge(s["kn_done"], i + 1)
                act.activation(kn[:], ps[:, 6, :], ACT.Copy).then_inc(s["copied"], 1)
                act.wait_ge(s["v_done"], 1 + i + 1)
                act.activation(v[:], ps[:, 7, :].rearrange("p (b n) -> p b n", b=TB), ACT.Copy).then_inc(s["copied"], 1)
                scalar(act, i)

        @block.vector
        def _(dve):
            with dve.Fori(0, MLA_HEADS) as i:
                step = Steps(dve, s["rope_step"], 4 * i)
                dve.wait_ge(s["qp_done"], i + 1)
                dve.wait_ge(s["scores_done"], 1 + TB * i)
                rotate(step, dve, qp, ps[0:ROPE, 7, :], raw, swapped, cos, sin, scale, s["q_turned"])
                assert step.n == 4
                n = vector(dve, i)
                assert n == 2 * TB
                dve.wait_ge(s["weighed"], 1 + TB * (i + 1))
                dve.tensor_copy(o[:, bass.ds(i, 1), :], ps[:, 5:6, :]).then_inc(s["o_copied"], 1)


def mlp_stage(k, name, layer, first):
    ps, w1, w2 = k.ps, k.ins["mlp_w1_2"][layer], k.ins["mlp_w2_2"][layer]
    STEPS = 2
    HK = K2 // STEPS
    UP = HK // HT
    N = 2 * UP
    b1 = k.places["mlp_b1_2"][0] + layer * K2
    gate = first + 2 * KD
    with k.stage(name, "h_done", "consts_done", "relu_done", "squared", "hidden_high", "hidden_low", "vec_step", *SplitProducts.SEMS,
                 primed=SplitProducts.PRIMED + ("relu_done", "squared", "hidden_high", "hidden_low", "vec_step")) as (block, s, sb):
        mul = SplitProducts(k, s, sb)
        h_parts = sb("h_parts", [P, 2, KD, T], F32R)
        hidden = sb("hidden", [P, 2, HK, T], F32R)
        h = sb("h", [P, 2, T])
        r, q = sb("r", [P, 2, T]), sb("q", [P, 2, T])
        bias2, keep = sb("bias2", [P, STEPS * KD]), sb("keep", [P, STEPS])
        bank_of = lambda n, f: (n % 2 * HT + f) if n < UP else 4 + ((n - UP) // 2 % 2) * HT + f

        @block.sync
        def _(sp):
            k.clear(sp)
            with sp.Fori(0, STEPS) as i:
                for n in range(N):
                    if n < UP:
                        src = columns(w1, i * (HK * P) + n * HALF, HALF)
                    else:
                        g, chunk = (n - UP) // 2, (n - UP) % 2
                        src = w2[bass.ds(i * (HK * P) + chunk * D, D), g * HALF:(g + 1) * HALF].rearrange("(k p) n -> p k n", p=P)
                    mul.load(sp, n, src, N * i)

        @block.tensor
        def _(pe):
            pe.wait_ge(s["x_low"], KD)
            with pe.Fori(0, STEPS) as i:
                for n in range(N):
                    outs = [ps[:, bank_of(n, f), :] for f in range(HT)]
                    if n < UP:
                        if n >= 2:
                            pe.wait_ge(s["relu_done"], 1 + HK * i + HT * (n - 1))
                        mul.products(pe, n, h_parts, outs, N * i)
                    else:
                        g, chunk = (n - UP) // 2, (n - UP) % 2
                        pe.wait_ge(s["hidden_low"], 1 + HK * i + KD * (chunk + 1))
                        if chunk == 0:
                            pe.wait_ge(s["vec_step"], 1 + 2 * KD * i + (2 * HT * (g - 1) if g >= 2 else 0))
                        mul.products(pe, n, hidden[:, :, chunk * KD:(chunk + 1) * KD, :], outs, N * i, chunk == 0, chunk == 1)

        @block.scalar
        def _(act):
            for c in range(KD):
                if c >= 2:
                    act.wait_ge(s["x_low"], c - 1)
                act.activation(h[:, c % 2, :], k.x[:, c, :], ACT.Identity, scale=k.mod[:, first + KD + c:first + KD + c + 1],
                               bias=k.mod[:, first + c:first + c + 1]).then_inc(s["h_done"], 1)
                act.wait_ge(s["h_done"], c + 1)
                act.activation(h_parts[:, 0, c], h[:, c % 2, :], ACT.Copy).then_inc(s["x_high"], 1)
            with act.Fori(0, STEPS) as i:
                def high(n):
                    mul.high(act, n, N * i, N // 4 * i)

                def relu(n):
                    act.wait_ge(s["half_used"], 1 + N * i + n + 1)
                    for c in range(n * HT, (n + 1) * HT):
                        act.wait_ge(s["squared"], 1 + HK * i + max(c - 1, 0))
                        act.activation(r[:, c % 2, :], ps[:, bank_of(n, c % HT), :], ACT.Relu,
                                       bias=k.cols[:, bass.ds(b1 + HK * i + c, 1)]).then_inc(s["relu_done"], 1)

                def hidden_high(n):
                    if n == 0:
                        act.wait_ge(s["half_used"], 1 + N * i)
                    for c in range(n * HT, (n + 1) * HT):
                        act.wait_ge(s["squared"], 1 + HK * i + c + 1)
                        act.activation(hidden[:, 0, c], q[:, c % 2, :], ACT.Copy).then_inc(s["hidden_high"], 1)

                high(0)
                high(1)
                for n in range(N):
                    if n < UP:
                        relu(n)
                    if n + 2 < N:
                        high(n + 2)
                    if n < UP:
                        hidden_high(n)

        @block.vector
        def _(dve):
            for c in range(KD):
                dve.wait_ge(s["x_high"], c + 1)
                dve.tensor_tensor(h_parts[:, 1, c], h[:, c % 2, :], h_parts[:, 0, c].bitcast(F32), ALU.subtract).then_inc(s["x_low"], 1)
            dve.wait_ge(s["consts_done"], 4)
            with dve.Fori(0, STEPS) as i:
                step = Steps(dve, s["vec_step"], 1 + 2 * KD * i)

                def square(n):
                    for c in range(n * HT, (n + 1) * HT):
                        dve.wait_ge(s["relu_done"], 1 + HK * i + c + 1)
                        dve.wait_ge(s["hidden_low"], 1 + HK * i + max(c - 1, 0))
                        dve.tensor_tensor(q[:, c % 2, :], r[:, c % 2, :], r[:, c % 2, :], ALU.mult).then_inc(s["squared"], 1)

                def hidden_low(n):
                    for c in range(n * HT, (n + 1) * HT):
                        dve.wait_ge(s["hidden_high"], 1 + HK * i + c + 1)
                        dve.tensor_tensor(hidden[:, 1, c], q[:, c % 2, :], hidden[:, 0, c].bitcast(F32), ALU.subtract).then_inc(s["hidden_low"], 1)

                def add(n):
                    g = (n - UP) // 2
                    dve.wait_ge(s["half_used"], 1 + N * i + n + 1)
                    for c in range(g * HT, (g + 1) * HT):
                        step(dve.tensor_scalar(h[:, c % 2, :], ps[:, bank_of(n, c % HT), :], bias2[:, bass.ds(KD * i + c, 1)],
                                               k.mod[:, gate + c:gate + c + 1], ALU.add, ALU.mult))
                        step(dve.scalar_tensor_tensor(out=k.x[:, c, :], in0=k.x[:, c, :], scalar=keep[:, bass.ds(i, 1)],
                                                      in1=h[:, c % 2, :], op0=ALU.mult, op1=ALU.add))

                mul.low(dve, 0, N * i)
                mul.low(dve, 1, N * i)
                for n in range(N):
                    if n < UP:
                        square(n)
                    if n + 2 < N:
                        mul.low(dve, n + 2, N * i)
                    if n < UP:
                        hidden_low(n)
                    elif (n - UP) % 2:
                        add(n)

        @block.gpsimd
        def _(pool):
            at = k.places["mlp_b2_2"][0] + layer * KD
            pool.memset(bias2[:, KD:], 0.0).then_inc(s["consts_done"], 1)
            pool.tensor_copy(bias2[:, 0:KD], k.cols[:, at:at + KD]).then_inc(s["consts_done"], 1)
            pool.memset(keep[:, 0:1], ALPHA_2).then_inc(s["consts_done"], 1)
            pool.memset(keep[:, 1:2], 1.0).then_inc(s["consts_done"], 1)


SB = 32


class S5Tables:

    def __init__(self, sb):
        self.mag = sb("mag", [P, S5_TILES])
        self.turn_b = sb("turn_b", [P, 2, S5_TILES, SB])
        self.turn_a = sb("turn_a", [P, 2, S5_TILES, T // SB + 1])
        self.b_t = sb("b_t", [P, 2, KD, P])
        self.c_t = sb("c_t", [P, 3, KD, P])


def s5_tables_stage(k, tab):
    ps = k.ps
    J = S5_TILES
    with k.stage("s5_tables", "loaded", "exp_done", "vec_step", "b_ready", "c_ready", "zeroed", "b_turned", "b_copied", "c_turned", "c_copied") as (block, s, sb):
        dt, angle, turns = sb("dt", [P, J]), sb("angle", [P, J]), sb("turns", [P, J])
        rs, rc = sb("rs", [P, J]), sb("rc", [P, J])
        t1, t2 = sb("t1", [P, J]), sb("t2", [P, J])
        c_re, c_im = sb("coef_re", [P, J]), sb("coef_im", [P, J])
        b_raw = sb("b_raw", [P, 2, J, GC])
        b_tmp = sb("b_tmp", [P, J, GC])
        b_out = sb("b_out", [P, J, GC])
        b_bd = sb("b_bd", [P, 2, J, 2 * GC])
        c_raw = sb("c_raw", [P, 2, KD, STATE])
        c_bd = sb("c_bd", [P, 2, KD, 2 * STATE])
        odd = sb("odd", [P, 2])
        tmp = sb("tmp", [P, J, SB])
        lr = k.cols[:, k.places["ssm_a_re_2"][0]:k.places["ssm_a_re_2"][0] + J]
        li = k.cols[:, k.places["ssm_a_im_2"][0]:k.places["ssm_a_im_2"][0] + J]

        @block.sync
        def _(sp):
            k.clear(sp)
            for half in range(2):
                sp.dma_start(dt[half * STATE:(half + 1) * STATE, :],
                             k.ins["ssm_log_dt_2"].rearrange("l (j two) -> two l j", two=2)[half].to_broadcast([STATE, J]),
                             allow_slow_non_contiguous=True).then_inc(s["loaded"], 16)
            for j, name in enumerate(("ssm_b_re_2", "ssm_b_im_2")):
                sp.dma_start(b_raw[:, j], k.ins[name][0].rearrange("(j two) s c -> (two s) j c", two=2)).then_inc(s["loaded"], 16)
            for j, name in enumerate(("ssm_c_re_2", "ssm_c_im_2")):
                sp.dma_start(c_raw[:, j], k.ins[name][0].rearrange("(k g) c s -> (g c) k s", k=KD)).then_inc(s["loaded"], 16)

        @block.gpsimd
        def _(pool):
            pool.memset(b_bd[:], 0.0).then_inc(s["zeroed"], 1)
            pool.memset(tab.turn_a[:, 0, :, 0:1], 1.0).then_inc(s["zeroed"], 1)
            pool.memset(tab.turn_a[:, 1, :, 0:1], 0.0).then_inc(s["zeroed"], 1)

        @block.scalar
        def _(act):
            act.wait_ge(s["loaded"], 96)
            act.activation(dt[:], dt[:], ACT.Exp).then_inc(s["exp_done"], 1)
            act.wait_ge(s["vec_step"], 2)
            act.activation(tab.mag[:], t1[:], ACT.Exp).then_inc(s["exp_done"], 1)
            act.wait_ge(s["vec_step"], 16)
            act.activation(rs[:], rs[:], ACT.Sin).then_inc(s["exp_done"], 1)
            act.activation(rc[:], rc[:], ACT.Sin).then_inc(s["exp_done"], 1)
            for n in range(2 * KD):
                if n % 4 == 0:
                    act.wait_ge(s["b_turned"], n // 4 + 1)
                    act.activation(tab.b_t[:, n // 8, n % 8:n % 8 + 4, :], ps[:, n // 4, :].rearrange("p (b n) -> p b n", b=4),
                                   ACT.Copy).then_inc(s["b_copied"], 1)
            for n in range(4):
                act.wait_ge(s["c_turned"], n + 1)
                src = ps[:, 4 + n, :].rearrange("p (b n) -> p b n", b=4)
                at = n % 2 * 4
                if n < 2:
                    act.activation(tab.c_t[:, 0, at:at + 4, :], src, ACT.Copy).then_inc(s["c_copied"], 1)
                act.activation(tab.c_t[:, 1 if n < 2 else 2, at:at + 4, :], src, ACT.Copy, scale=-1.0).then_inc(s["c_copied"], 1)

        @block.tensor
        def _(pe):
            pe.wait_ge(s["b_ready"], 4)
            for n in range(2 * KD):
                mm = pe.transpose(ps[:, n // 4, n % 4 * P:(n % 4 + 1) * P],
                                  b_bd[:, n // 8, n % 8 * 4:n % 8 * 4 + 4, :].rearrange("p j c -> p (j c)"), k.ident[:])
                if n % 4 == 3:
                    mm.then_inc(s["b_turned"], 1)
            pe.wait_ge(s["c_ready"], 4)
            for n in range(2 * KD):
                mm = pe.transpose(ps[:, 4 + n // 4, n % 4 * P:(n % 4 + 1) * P], c_bd[:, n // 8, n % 8, :], k.ident[:])
                if n % 4 == 3:
                    mm.then_inc(s["c_turned"], 1)

        @block.vector
        def _(dve):
            step = Steps(dve, s["vec_step"])
            dve.wait_ge(s["exp_done"], 1)
            step(dve.tensor_tensor(angle[:], li, dt[:], ALU.mult))
            step(dve.tensor_tensor(t1[:], lr, dt[:], ALU.mult))
            reduced_angle(step, dve, rs[:], turns[:], angle[:], 0.0)
            reduced_angle(step, dve, rc[:], turns[:], angle[:], math.pi / 2)
            dve.wait_ge(s["exp_done"], 4)
            step(dve.tensor_tensor(t1[:], tab.mag[:], rc[:], ALU.mult))
            step(dve.tensor_scalar(t1[:], t1[:], -1.0, None, ALU.add))
            step(dve.tensor_tensor(t2[:], tab.mag[:], rs[:], ALU.mult))
            step(dve.tensor_tensor(c_re[:], t1[:], lr, ALU.mult))
            step(dve.tensor_tensor(turns[:], t2[:], li, ALU.mult))
            step(dve.tensor_tensor(c_re[:], c_re[:], turns[:], ALU.add))
            step(dve.tensor_tensor(c_im[:], t2[:], lr, ALU.mult))
            step(dve.tensor_tensor(turns[:], t1[:], li, ALU.mult))
            step(dve.tensor_tensor(c_im[:], c_im[:], turns[:], ALU.subtract))
            step(dve.tensor_tensor(t1[:], lr, lr, ALU.mult))
            step(dve.tensor_tensor(t2[:], li, li, ALU.mult))
            step(dve.tensor_tensor(t1[:], t1[:], t2[:], ALU.add))
            step(dve.reciprocal(t1[:], t1[:]))
            step(dve.tensor_tensor(c_re[:], c_re[:], t1[:], ALU.mult))
            step(dve.tensor_tensor(c_im[:], c_im[:], t1[:], ALU.mult))

            def over(m, n):
                return m.rearrange("p (j o) -> p j o", o=1).to_broadcast([P, J, n])

            dve.wait_ge(s["zeroed"], 3)
            for out, (a, b), op in ((0, (c_re, c_im), ALU.subtract), (1, (c_im, c_re), ALU.add)):
                step(dve.tensor_tensor(b_out[:], b_raw[:, 0], over(a[:], GC), ALU.mult))
                step(dve.tensor_tensor(b_tmp[:], b_raw[:, 1], over(b[:], GC), ALU.mult))
                for half in range(2):
                    rows = slice(half * STATE, (half + 1) * STATE)
                    dve.tensor_tensor(b_bd[rows, out, :, half * GC:(half + 1) * GC], b_out[rows], b_tmp[rows], op).then_inc(s["b_ready"], 1)
                dve.wait_ge(s["b_ready"], 2 * out + 2)
            step(dve.tensor_reduce(odd[:, 1:2], k.ident[:].rearrange("p (j two c) -> p j two c", two=2, c=GC)[:, :, 1, :], AX.XY, ALU.add))
            step(dve.tensor_scalar(odd[:, 0:1], odd[:, 1:2], -1.0, 1.0, ALU.mult, ALU.add))
            for j in range(2):
                for half in range(2):
                    dve.tensor_scalar(c_bd[:, j, :, half * STATE:(half + 1) * STATE], c_raw[:, j], odd[:, half:half + 1], None,
                                      ALU.mult).then_inc(s["c_ready"], 1)

            def times(out, n, at, a, first):
                re, im = a[:, 0, :, first:first + n], a[:, 1, :, first:first + n]
                wr, wi = (a[:, j, :, at - 1:at].to_broadcast([P, J, n]) for j in range(2))
                ore, oim = out[:, 0, :, at:at + n], out[:, 1, :, at:at + n]
                step(dve.tensor_tensor(ore, re, wr, ALU.mult))
                step(dve.tensor_tensor(tmp[:, :, 0:n], im, wi, ALU.mult))
                step(dve.tensor_tensor(ore, ore, tmp[:, :, 0:n], ALU.subtract))
                step(dve.tensor_tensor(oim, re, wi, ALU.mult))
                step(dve.tensor_tensor(tmp[:, :, 0:n], im, wr, ALU.mult))
                step(dve.tensor_tensor(oim, oim, tmp[:, :, 0:n], ALU.add))

            for j, m in enumerate((rc, rs)):
                step(dve.tensor_copy(tab.turn_b[:, j, :, 0:1], m[:].rearrange("p (j o) -> p j o", o=1)))
            n = 1
            while n < SB:
                times(tab.turn_b, n, n, tab.turn_b, 0)
                n *= 2
            for j in range(2):
                step(dve.tensor_copy(tab.turn_a[:, j, :, 1:2], tab.turn_b[:, j, :, SB - 1:SB]))
            n = 1
            while n < T // SB:
                times(tab.turn_a, n, n + 1, tab.turn_a, 1)
                n *= 2


def s5_scan_stage(k, tab, u, g):
    ps = k.ps
    NT = S5_TILES // KD
    GELU = 2 * math.sqrt(2 / math.pi)
    VEC = 29
    A = T // 32
    with k.stage("s5_scan", "staged", "bu_done", "table_step", "table_done", "vec_step", "products_done", "table_used", "y_done", "y_out",
                 "sq_done", "inner_done", "sig_done", "g_done", primed=("g_done", "table_used", "y_out")) as (block, s, sb):
        uk, bk, ck = sb("uk", [P, T]), sb("bk", [P, 2, P]), sb("ck", [P, 3, P])
        ta, tb = sb("ta", [P, 2, A]), sb("tb", [P, 2, 32])
        turn, tt = sb("turn", [P, 2, 2, T]), sb("tt", [P, T])
        w, m = sb("w", [P, 2, T]), sb("m", [P, 2, T])
        z = sb("z", [P, 2, T])
        pr = sb("pr", [P, 2, 4, T])
        y, q = sb("y", [P, T]), sb("q", [P, T])

        @block.sync
        def _(sp):
            k.clear(sp)

        @block.gpsimd
        def _(pool):
            with pool.Fori(0, KD) as i:
                pool.wait_ge(s["y_out"], 1 + i)
                pool.tensor_copy(uk[:], u[:, bass.ds(i, 1), :].rearrange("p o t -> p (o t)")).then_inc(s["staged"], 1)
                pool.tensor_copy(bk[:], tab.b_t[:, :, bass.ds(i, 1), :].rearrange("p r o n -> p r (o n)")).then_inc(s["staged"], 1)
                pool.tensor_copy(ck[:], tab.c_t[:, :, bass.ds(i, 1), :].rearrange("p r o n -> p r (o n)")).then_inc(s["staged"], 1)
                step = Steps(pool, s["table_step"], 7 * NT * i)
                for j in range(NT):
                    tile = bass.ds(NT * i + j, 1)
                    step(pool.tensor_copy(ta[:], tab.turn_a[:, :, tile, 0:A].rearrange("p r o a -> p r (o a)")))
                    step(pool.tensor_copy(tb[:], tab.turn_b[:, :, tile, :].rearrange("p r o b -> p r (o b)")))
                    if j >= 2:
                        pool.wait_ge(s["products_done"], NT * i + j - 1)
                    ar, ai = (ta[:, r, :].rearrange("p (a b) -> p a b", b=1).to_broadcast([P, A, 32]) for r in range(2))
                    br, bi = (tb[:, r:r + 1, :].to_broadcast([P, A, 32]) for r in range(2))
                    c, sn = (turn[:, j % 2, r, :].rearrange("p (a b) -> p a b", a=A) for r in range(2))
                    t = tt[:].rearrange("p (a b) -> p a b", a=A)
                    step(pool.tensor_tensor(c, ar, br, ALU.mult))
                    step(pool.tensor_tensor(t, ai, bi, ALU.mult))
                    step(pool.tensor_tensor(c, c, t, ALU.subtract))
                    step(pool.tensor_tensor(sn, ar, bi, ALU.mult))
                    step(pool.tensor_tensor(t, ai, br, ALU.mult))
                    pool.tensor_tensor(sn, sn, t, ALU.add).then_inc(s["table_done"], 1)
                    pool.wait_ge(s["table_done"], NT * i + j + 1)
                assert step.n == 7 * NT

        @block.tensor
        def _(pe):
            with pe.Fori(0, KD) as i:
                pe.wait_ge(s["staged"], 3 * (i + 1))

                def inputs(j):
                    if j >= 2:
                        pe.wait_ge(s["table_used"], 1 + NT * i + j - 1)
                    else:
                        pe.wait_ge(s["table_used"], 1 + NT * i)
                    rows = slice(32 * j, 32 * j + 32)
                    for r in range(2):
                        mm = pe.matmul(ps[:, 2 * (j % 2) + r, :], bk[rows, r, :], uk[rows, :], start=True, stop=True)
                    mm.then_inc(s["bu_done"], 1)

                inputs(0)
                pe.wait_ge(s["y_out"], 1 + i)
                for j in range(NT):
                    if j + 1 < NT:
                        inputs(j + 1)
                    pe.wait_ge(s["products_done"], NT * i + j + 1)
                    rows = slice(32 * j, 32 * j + 32)
                    for n, r in enumerate((0, 1, 2, 2)):
                        mm = pe.matmul(ps[rows, 4, :], ck[:, r, 32 * j:32 * j + 32], pr[:, j % 2, n, :], start=(n == 0), stop=(n == 3))
                    mm.then_inc(s["y_done"], 1)

        @block.scalar
        def _(act):
            with act.Fori(0, KD) as i:
                act.wait_ge(s["y_out"], 1 + i + 1)
                act.activation(q[:], y[:], ACT.Square).then_inc(s["sq_done"], 1)
                act.wait_ge(s["inner_done"], i + 1)
                act.activation(q[:], q[:], ACT.Sigmoid, scale=GELU).then_inc(s["sig_done"], 1)

        @block.vector
        def _(dve):
            with dve.Fori(0, KD) as i:
                step = Steps(dve, s["vec_step"], VEC * i)
                for j in range(NT):
                    c, sn = turn[:, j % 2, 0, :], turn[:, j % 2, 1, :]
                    br, bi = ps[:, 2 * (j % 2), :], ps[:, 2 * (j % 2) + 1, :]
                    dve.wait_ge(s["table_done"], NT * i + j + 1)
                    dve.wait_ge(s["bu_done"], NT * i + j + 1)
                    step(dve.tensor_tensor(w[:, 0, :], c, br, ALU.mult))
                    step(dve.tensor_tensor(m[:, 0, :], sn, bi, ALU.mult))
                    step(dve.tensor_tensor(w[:, 0, :], w[:, 0, :], m[:, 0, :], ALU.add))
                    step(dve.tensor_tensor(w[:, 1, :], c, bi, ALU.mult))
                    dve.tensor_tensor(m[:, 1, :], sn, br, ALU.mult).then_inc(s["table_used"], 1)
                    dve.wait_ge(s["table_used"], 1 + NT * i + j + 1)
                    step(dve.tensor_tensor(w[:, 1, :], w[:, 1, :], m[:, 1, :], ALU.subtract))
                    mag = tab.mag[:, bass.ds(NT * i + j, 1)].to_broadcast([P, T])
                    for r in range(2):
                        step(dve.tensor_tensor_scan(z[:, r, :], mag, w[:, r, :], 0.0, ALU.mult, ALU.add))
                    if j >= 2:
                        dve.wait_ge(s["y_done"], NT * i + j - 1)
                    for n, (a, r) in enumerate(((c, 0), (sn, 1), (c, 1), (sn, 0))):
                        ins = dve.tensor_tensor(pr[:, j % 2, n, :], a, z[:, r, :], ALU.mult)
                    ins.then_inc(s["products_done"], 1)
                dve.wait_ge(s["y_done"], NT * (i + 1))
                dve.wait_ge(s["g_done"], 1 + i)
                dve.scalar_tensor_tensor(out=y[:], in0=uk[:], scalar=k.cols[:, bass.ds(k.places["ssm_d_2"][0] + i, 1)], in1=ps[:, 4, :],
                                         op0=ALU.mult, op1=ALU.add).then_inc(s["y_out"], 1)
                dve.wait_ge(s["y_out"], 1 + i + 1)
                dve.wait_ge(s["sq_done"], i + 1)
                step(dve.tensor_scalar(q[:], q[:], 0.044715, 1.0, ALU.mult, ALU.add))
                dve.tensor_tensor(q[:], q[:], y[:], ALU.mult).then_inc(s["inner_done"], 1)
                dve.wait_ge(s["sig_done"], i + 1)
                dve.tensor_tensor(g[:, bass.ds(i, 1), :], y[:].rearrange("p (o t) -> p o t", o=1), q[:].rearrange("p (o t) -> p o t", o=1),
                                  ALU.mult).then_inc(s["g_done"], 1)
                assert step.n == VEC, step.n


def project_stage(k, name, w, dst):
    ps = k.ps
    with k.stage(name, "copied", *SplitProducts.SEMS, primed=SplitProducts.PRIMED) as (block, s, sb):
        lin = SplitLinear(k, block, s, sb, w, k.h)

        @block.scalar
        def _(act):
            def copy(n):
                act.wait_ge(s["half_used"], 1 + n + 1)
                for c in range(n * HT, (n + 1) * HT):
                    act.activation(dst[:, c, :], ps[:, c, :], ACT.Copy).then_inc(s["copied"], 1)

            lin.scalar(act, copy)

        @block.vector
        def _(dve):
            lin.vector(dve)


def glu_stage(k, g, z):
    ps, w = k.ps, k.ins["ssm_w_glu_2"][0]
    with k.stage("glu", "sig_done", "gated", *SplitProducts.SEMS, primed=SplitProducts.PRIMED) as (block, s, sb):
        lin = SplitLinear(k, block, s, sb, w, g)
        sig = sb("sig", [P, 2, T])

        @block.scalar
        def _(act):
            def sigmoid(n):
                act.wait_ge(s["half_used"], 1 + n + 1)
                for c in range(n * HT, (n + 1) * HT):
                    if c >= 2:
                        act.wait_ge(s["gated"], c - 1)
                    act.activation(sig[:, c % 2, :], ps[:, c, :], ACT.Sigmoid, bias=k.col("ssm_b_glu_2", c)).then_inc(s["sig_done"], 1)

            lin.scalar(act, sigmoid)

        @block.vector
        def _(dve):
            def gated(n):
                for c in range(n * HT, (n + 1) * HT):
                    dve.wait_ge(s["sig_done"], c + 1)
                    dve.tensor_tensor(z[:, c, :], g[:, c, :], sig[:, c % 2, :], ALU.mult).then_inc(s["gated"], 1)

            lin.vector(dve, gated)


def second_block(k):
    col = lambda name, layer: (lambda c: k.col(name, layer * KD + c))
    for layer in range(2):
        mix, ffn = 48 + 48 * layer, 72 + 48 * layer
        with ExitStack() as branch:
            sb = lambda n, shape: k.sb(n, shape, stack=branch)
            k.h = sb(f"h{layer + 1}", [P, KD, T])
            modulate_stage(k, f"mod_mix{layer}", mix)
            if layer == 0:
                cq, ckv, k_pe = sb("cq", [P, QL // P, T]), sb("ckv", [P, T]), sb("k_pe", [ROPE, T])
                cos, sin = sb("cos", [ROPE, T]), sb("sin", [ROPE, T])
                o = sb("latent_out", [P, KD, T])
                latent_stage(k, cq, ckv, k_pe, cos, sin)
                latent_attention_stage(k, cq, ckv, k_pe, cos, sin, o)
                residual_stage(k, "latent_proj", k.ins["mla_w_o_2"][0], o, ALPHA_2, mix + 16)
            else:
                g = sb("g", [P, KD, T])
                with ExitStack() as scan:
                    u = k.sb("u", [P, KD, T], stack=scan)
                    project_stage(k, "s5_in", k.ins["ssm_w_in_2"][0], u)
                    tab = S5Tables(lambda n, shape: k.sb(n, shape, stack=scan))
                    s5_tables_stage(k, tab)
                    s5_scan_stage(k, tab, u, g)
                z = sb("z", [P, KD, T])
                glu_stage(k, g, z)
                residual_stage(k, "s5_proj", k.ins["ssm_w_out_2"][0], z, ALPHA_2, mix + 16)
        norm_stage(k, f"norm_mix{layer}", k.x, k.x, col("ln_mix_g_2", layer), col("ln_mix_b_2", layer))
        mlp_stage(k, f"mlp{layer}", layer, ffn)
        norm_stage(k, f"norm_ffn{layer}", k.x, k.x, col("ln_ffn_g_2", layer), col("ln_ffn_b_2", layer))


def build(nc, ins, out):
    with ExitStack() as stack:
        k = Kernel(nc, stack, ins)
        constants_stage(k)
        with ExitStack() as strips:
            k.w = k.sb("w", [P, 3, KD * STRIP], stack=strips)
            modulation_stage(k)
            ones = lambda c: 1.0
            mod = lambda first: (lambda c: k.mod[:, first + c:first + c + 1])
            with ExitStack() as block:
                k.h = k.sb("h", [P, KD, T], stack=block)
                norm_stage(k, "norm_in", k.x, k.h, mod(8), mod(0))
                with ExitStack() as mix:
                    merged = k.sb("merged", [P, KD, T], stack=mix)
                    forget_stage(k)
                    with ExitStack() as branch:
                        o = k.sb("attended", [P, KD, T], stack=branch)
                        attention_stage(k, o)
                        merge_stage(k, "merge_att", 0, lambda at, n: columns(k.ins["w_attn_o"][0], at, n), o, KD, merged)
                    with ExitStack() as branch:
                        pooled = k.sb("pooled", [P, KD, T], stack=branch)
                        pool_stage(k, pooled)
                        pool_out_stage(k, pooled, merged)
                    with ExitStack() as branch:
                        ys = k.sb("ys", [P, KI, T], stack=branch)
                        ssm_stage(k, ys)
                        merge_stage(k, "merge_ssm", 2, lambda at, n: columns(k.ins["w_ssm_o"][0], at, n), ys, KI, merged)
                    residual_stage(k, "mix_out", k.ins["w_out"][0], merged, ALPHA_1, 16)
                norm_stage(k, "norm_mix", k.x, k.x, lambda c: k.col("ln_mix_g", c), lambda c: k.col("ln_mix_b", c))
                norm_stage(k, "norm_ffn_in", k.x, k.h, mod(32), mod(24))
                with ExitStack() as ffn:
                    handed = Dispatch(k, ffn)
                    router_stage(k, handed.chosen, handed.share)
                    dispatch_stage(k, handed)
                    experts_stage(k, handed)
                    combine_stage(k, handed, 40)
                norm_stage(k, "norm_ffn", k.x, k.x, lambda c: k.col("ln_ffn_g", c), lambda c: k.col("ln_ffn_b", c))
        k.w = k.sb("w_second", [P, 2, KD * STRIP])
        second_block(k)
        output_stage(k, out)


_INS = ["x", "c", "w_in", "b_forget", "w_attn_o", "w_pool", "pool_scale", "conv_w", "conv_b", "dt_bias", "a_log", "d_skip",
        "ssm_norm_w", "w_ssm_o", "w_out", "w_ada", "b_ada", "ln_mix_g", "ln_mix_b", "ln_ffn_g", "ln_ffn_b", "w_router",
        "b_router", "w_exp_gate", "w_exp_up", "w_exp_down", "c_2", "positions_2", "mla_w_in_2", "mla_q_norm_2", "mla_w_qb_2",
        "mla_kv_norm_2", "mla_w_kvb_2", "mla_w_o_2", "ssm_w_in_2", "ssm_log_dt_2", "ssm_a_re_2", "ssm_a_im_2", "ssm_b_re_2",
        "ssm_b_im_2", "ssm_c_re_2", "ssm_c_im_2", "ssm_d_2", "ssm_w_glu_2", "ssm_b_glu_2", "ssm_w_out_2", "mlp_w1_2", "mlp_b1_2",
        "mlp_w2_2", "mlp_b2_2", "mod_mix_w_2", "mod_mix_b_2", "mod_ffn_w_2", "mod_ffn_b_2", "ln_mix_g_2", "ln_mix_b_2",
        "ln_ffn_g_2", "ln_ffn_b_2"]


def kernel(**inputs):
    import numpy as _np
    import concourse.bacc as _bacc
    from concourse import mybir as _mybir
    from concourse.bass_utils import run_bass_kernel_spmd as _run

    nc = _bacc.Bacc("TRN2", target_bir_lowering=False, num_devices=1)
    arrays, ins = {}, {}
    for name in _INS:
        a = _np.ascontiguousarray(inputs[name])
        arrays[f"in_{name}_dram"] = a
        ins[name] = nc.dram_tensor(f"in_{name}_dram", a.shape, _mybir.dt.from_np(a.dtype), kind="ExternalInput").ap()
    out = nc.dram_tensor("out_0_dram", (1, T, D), F32, kind="ExternalOutput").ap()
    build(nc, ins, out)
    r = _run(nc, [arrays], core_ids=[0])
    return r.results[0]["out_0_dram"]
```

```python
from contextlib import ExitStack, contextmanager
import math

import concourse.bass as bass
from concourse import mybir

F32 = mybir.dt.float32
I32 = mybir.dt.int32
F32R = mybir.dt.float32r
ALU = mybir.AluOpType
ACT = mybir.ActivationFunctionType
AX = mybir.AxisListType

P = 128
D = 1024
KD = D // P
T = 512
TB = T // P
STRIP = 512
FT = STRIP // P
HALF = STRIP // 2
HT = HALF // P

HEADS, HD = 16, 64
G_SSM, R_SSM, P_SSM, N_SSM = 4, 8, 64, 128
SSM_INNER = G_SSM * R_SSM * P_SSM
KG = SSM_INNER // G_SSM // P
KI = SSM_INNER // P
CONV = 4
XBC_TILES = (SSM_INNER + 2 * G_SSM * N_SSM) // P
Q0, K0, V0 = 0, D, 2 * D
F0 = 3 * D
U0 = F0 + HEADS
Z0 = U0 + D
XBC0 = Z0 + SSM_INNER
B0 = XBC0 + SSM_INNER
C0 = B0 + G_SSM * N_SSM
DT0 = XBC0 + XBC_TILES * P
GATE0 = DT0 + G_SSM * R_SSM
IN_WIDTH = GATE0 + 3 * D
POOL_WINDOWS = (2, 4, 8, 16)
PAD = max(POOL_WINDOWS)
NE, EG, DFF = 16, 4, 512
KE = DFF // P
TOP = 2
NBLK = NE + (TOP * T - NE) // P
ALPHA_1 = 2 ** 0.25
LN_EPS, RMS_EPS = 1e-5, 1e-6

MLA_HEADS, NOPE, ROPE, VD = 8, 128, 64, 128
QL, KVL = 256, 128
GC, STATE = 16, 64
S5_GROUPS = D // GC
S5_TILES = S5_GROUPS * STATE // P
DF2 = 4 * D
K2 = DF2 // P
ALPHA_2 = 4 ** 0.25

NEG = -1e30
TWO_PI = 2 * math.pi
PI_SAFE = 3.1415925
PI_A = 6.28125
PI_B = 0.0019350051879882812
PI_C = TWO_PI - PI_A - PI_B
ROUND = 12582912.0

VECTORS = [
    ("c", 8), ("b_ada", 48), ("pool_scale", 8), ("conv_b", 24), ("ssm_norm_w", 16), ("ln_mix_g", 8), ("ln_mix_b", 8),
    ("conv_w", 96), ("ln_ffn_g", 8), ("ln_ffn_b", 8), ("c_2", 8), ("mla_kv_norm_2", 1), ("mla_q_norm_2", 2),
    ("mod_mix_b_2", 48), ("mod_ffn_b_2", 48), ("ssm_a_re_2", 32),
    ("mlp_b1_2", 64), ("mlp_b2_2", 16), ("ssm_a_im_2", 32), ("ssm_d_2", 8), ("ssm_b_glu_2", 8),
    ("ln_mix_g_2", 16), ("ln_mix_b_2", 16), ("ln_ffn_g_2", 16), ("ln_ffn_b_2", 16),
]


def vector_places():
    at, places = 0, {}
    for name, rows in VECTORS:
        if at % P + rows > P:
            at += P - at % P
        places[name] = (at, rows)
        at += rows
    return places, (at + P - 1) // P


class Steps:

    def __init__(self, eng, sem, base=0):
        self.eng, self.sem, self.base, self.n = eng, sem, base, 0

    def __call__(self, ins):
        ins.then_inc(self.sem, 1)
        self.n += 1
        self.eng.wait_ge(self.sem, self.base + self.n)

    def start(self, ins):
        ins.then_inc(self.sem, 1)
        self.n += 1
        return self.n

    def after(self, n):
        self.eng.wait_ge(self.sem, self.base + n)


class Kernel:

    def __init__(self, nc, stack, ins):
        self.nc, self.stack, self.ins = nc, stack, ins
        self.finished = []
        self.ada_loaded = [stack.enter_context(nc.semaphore(f"ada_loaded{slot}")) for slot in range(3)]
        self.ps = stack.enter_context(nc.psum_tensor("banks", [P, 8, 512], F32))

    def sb(self, name, shape, dt=F32, stack=None):
        return (stack or self.stack).enter_context(self.nc.sbuf_tensor(name, shape, dt))

    @contextmanager
    def stage(self, name, *sems, primed=()):
        with ExitStack() as stack:
            s = {x: stack.enter_context(self.nc.semaphore(f"{name}_{x}")) for x in sems}
            self.primed = [(s[x], primed.count(x)) for x in dict.fromkeys(primed)]
            with self.nc.Block() as block:
                yield block, s, lambda n, shape, dt=F32: self.sb(f"{name}_{n}", shape, dt, stack)
            self.finished = list(s.values())

    def clear(self, sp):
        for x in self.finished:
            sp.sem_clear(x)
        for x, n in self.primed:
            sp.sem_inc(x, n)


def constant_tiles(k):
    places, groups = vector_places()
    k.places = places
    k.ident = k.sb("ident", [P, P])
    k.ones = k.sb("ones", [P, P])
    k.future_mask = k.sb("future_mask", [P, P])
    k.past_cap = k.sb("past_cap", [P, P])
    k.cols = k.sb("cols", [P, groups * P])
    k.eps_ln = k.sb("eps_ln", [P, 1])
    k.eps_rms = k.sb("eps_rms", [P, 1])
    k.silu_c = k.sb("silu_c", [P, 2, KD])
    k.mod = k.sb("mod", [P, 48 + 4 * 24])
    k.x = k.sb("x", [P, KD, T])
    k.neg_f = k.sb("neg_f", [HEADS, T])
    k.col = lambda name, j=0: k.cols[:, places[name][0] + j:places[name][0] + j + 1]


def constants_stage(k):
    ps, places = k.ps, k.places
    groups = vector_places()[1]
    rows_of = {"conv_w": "k (j p) -> (k j) p", "ssm_a_re_2": "(j two) s -> j (two s)", "ssm_a_im_2": "(j two) s -> j (two s)"}

    with k.stage("constants", "rows_zeroed", "rows_loaded", "x_loaded", "pool_step", "consts_ready", "params_turned",
                 "params_copied", "x_turned", "x_copied", "sig_done", "vec_step") as (block, s, sb):
        rows = sb("rows", [P, groups, P])
        xt = sb("xt", [P, TB, D])
        sig = sb("sig", [P, 2, KD])

        @block.sync
        def _(sp):
            k.clear(sp)
            sp.dma_start(xt[:], k.ins["x"][0].rearrange("(b p) d -> p b d", p=P)).then_inc(s["x_loaded"], 16)
            sp.wait_ge(s["rows_zeroed"], 1)
            for name, (at, n) in places.items():
                a = k.ins[name]
                if name in ("conv_w", "ssm_a_re_2", "ssm_a_im_2"):
                    a = a[0].rearrange(rows_of[name], p=P) if name == "conv_w" else a[0].rearrange(rows_of[name], two=2)
                else:
                    a = a.rearrange("l (j p) -> (l j) p", p=P)
                sp.dma_start(rows[at % P:at % P + n, at // P, :], a).then_inc(s["rows_loaded"], 16)
            for slot in range(3):
                sp.dma_start(strip(k, slot), columns(k.ins["w_ada"][0], slot * STRIP)).then_inc(k.ada_loaded[slot], 16)

        @block.gpsimd
        def _(pool):
            pool.memset(rows[:], 0.0).then_inc(s["rows_zeroed"], 1)
            pool.memset(k.ident[:], 0.0).then_inc(s["pool_step"], 1)
            pool.memset(k.ones[:], 1.0).then_inc(s["pool_step"], 1)
            pool.memset(k.future_mask[:], 0.0).then_inc(s["pool_step"], 1)
            pool.memset(k.past_cap[:], 0.0).then_inc(s["pool_step"], 1)
            pool.memset(k.eps_ln[:], LN_EPS).then_inc(s["pool_step"], 1)
            pool.memset(k.eps_rms[:], RMS_EPS).then_inc(s["pool_step"], 1)
            pool.wait_ge(s["pool_step"], 6)
            pool.affine_select(out=k.ident[:], in_=k.ident[:], compare_op=ALU.not_equal, fill=1.0, base=0,
                               pattern=[[-1, P]], channel_multiplier=1).then_inc(s["consts_ready"], 1)
            pool.affine_select(out=k.future_mask[:], in_=k.future_mask[:], compare_op=ALU.is_ge, fill=NEG, base=0,
                               pattern=[[-1, P]], channel_multiplier=1).then_inc(s["consts_ready"], 1)
            pool.affine_select(out=k.past_cap[:], in_=k.past_cap[:], compare_op=ALU.is_ge, fill=NEG, base=0,
                               pattern=[[1, P]], channel_multiplier=-1).then_inc(s["consts_ready"], 1)

        @block.tensor
        def _(pe):
            pe.wait_ge(s["consts_ready"], 3)
            pe.wait_ge(s["x_loaded"], 16)
            for c in range(KD):
                if c >= 4:
                    pe.wait_ge(s["x_copied"], c - 3)
                for b in range(TB):
                    mm = pe.transpose(ps[:, c % 4, b * P:(b + 1) * P], xt[:, b, c * P:(c + 1) * P], k.ident[:])
                mm.then_inc(s["x_turned"], 1)
            pe.wait_ge(s["rows_loaded"], 16 * len(places))
            for g in range(groups):
                mm = pe.transpose(ps[:, 4 + g // 4, (g % 4) * P:(g % 4 + 1) * P], rows[:, g, :], k.ident[:])
            mm.then_inc(s["params_turned"], 1)

        @block.scalar
        def _(act):
            for c in range(KD):
                act.wait_ge(s["x_turned"], c + 1)
                act.activation(k.x[:, c, :], ps[:, c % 4, :], ACT.Copy).then_inc(s["x_copied"], 1)
            act.wait_ge(s["params_turned"], 1)
            for g in range(0, groups, 4):
                n = min(4, groups - g) * P
                act.activation(k.cols[:, g * P:g * P + n], ps[:, 4 + g // 4, 0:n], ACT.Copy).then_inc(s["params_copied"], 1)
            act.wait_ge(s["params_copied"], (groups + 3) // 4)
            for j, name in enumerate(("c", "c_2")):
                at = places[name][0]
                act.activation(sig[:, j, :], k.cols[:, at:at + KD], ACT.Sigmoid).then_inc(s["sig_done"], 1)

        @block.vector
        def _(dve):
            dve.wait_ge(s["sig_done"], 2)
            for j, name in enumerate(("c", "c_2")):
                at = places[name][0]
                dve.tensor_tensor(k.silu_c[:, j, :], sig[:, j, :], k.cols[:, at:at + KD], ALU.mult).then_inc(s["vec_step"], 1)


def strip(k, slot, kt=KD):
    return k.w[:, slot, :].rearrange("p (k n) -> p k n", k=kt)


def modulation_stage(k):
    ps, SLOTS = k.ps, 3
    jobs = [(k.ins["w_ada"][0], 0, 12 // SLOTS, 0, "b_ada", 0)]
    names = [f"{x}{slot}" for x in ("used", "summed", "copied") for slot in range(SLOTS)]
    with k.stage("modulation", *names, "vec_step", "pool_step", primed=names) as (block, s, sb):
        used, summed, copied = (names[j * SLOTS:(j + 1) * SLOTS] for j in range(3))
        loaded = k.ada_loaded
        acc = sb("acc", [P, SLOTS, STRIP])

        @block.sync
        def _(sp):
            k.clear(sp)
            w, _, rounds, *_ = jobs[0]
            with sp.Fori(1, rounds) as i:
                for slot in range(SLOTS):
                    sp.wait_ge(s[used[slot]], 1 + i)
                    sp.dma_start(strip(k, slot), columns(w, (SLOTS * i + slot) * STRIP)).then_inc(loaded[slot], 16)

        @block.vector
        def _(dve):
            done = 0
            for _, c, rounds, *_ in jobs:
                with dve.Fori(0, rounds) as i:
                    step = Steps(dve, s["vec_step"], SLOTS * (KD - 1) * (done + i))
                    for slot in range(SLOTS):
                        dve.wait_ge(loaded[slot], 16 * (done + i + 1))
                        dve.wait_ge(s[summed[slot]], 1 + done + i)
                        for kk in range(KD):
                            w, by = strip(k, slot)[:, kk, :], k.silu_c[:, c, kk:kk + 1]
                            if kk == 0:
                                ins = dve.tensor_scalar(acc[:, slot, :], w, by, None, ALU.mult)
                            else:
                                ins = dve.scalar_tensor_tensor(out=acc[:, slot, :], in0=w, scalar=by, in1=acc[:, slot, :],
                                                               op0=ALU.mult, op1=ALU.add)
                            if kk < KD - 1:
                                step(ins)
                        ins.then_inc(s[used[slot]], 1)
                done += rounds

        @block.tensor
        def _(pe):
            sum_channels(k, pe)
            done = 0
            for _, _, rounds, *_ in jobs:
                with pe.Fori(0, rounds) as i:
                    for slot in range(SLOTS):
                        pe.wait_ge(s[used[slot]], 1 + done + i + 1)
                        pe.wait_ge(s[copied[slot]], 1 + done + i)
                        for f in range(FT):
                            mm = pe.matmul(ps[:, 1 + slot, f:f + 1], acc[:, slot, f * P:(f + 1) * P], k.ones[:, 0:1], start=True, stop=True)
                        mm.then_inc(s[summed[slot]], 1)
                done += rounds

        @block.scalar
        def _(act):
            done = 0
            for _, _, rounds, col, *_ in jobs:
                with act.Fori(0, rounds) as i:
                    for slot in range(SLOTS):
                        act.wait_ge(s[summed[slot]], 1 + done + i + 1)
                        act.activation(k.mod[:, bass.ds(col + (SLOTS * i + slot) * FT, FT)], ps[:, 1 + slot, 0:FT],
                                       ACT.Copy).then_inc(s[copied[slot]], 1)
                done += rounds

        @block.gpsimd
        def _(pool):
            total = sum(job[2] for job in jobs)
            for slot in range(SLOTS):
                pool.wait_ge(s[copied[slot]], 1 + total)
            for _, _, rounds, col, bias, at in jobs:
                n, b = rounds * SLOTS * FT, k.places[bias][0] + at
                pool.tensor_tensor(k.mod[:, col:col + n], k.mod[:, col:col + n], k.cols[:, b:b + n], ALU.add).then_inc(s["pool_step"], 1)
            pool.wait_ge(s["pool_step"], len(jobs))
            for first, n in ((8, 8), (32, 8)):
                pool.tensor_scalar(k.mod[:, first:first + n], k.mod[:, first:first + n], 1.0, None,
                                  ALU.add).then_inc(s["pool_step"], 1)


def sum_channels(k, pe, ready=None):
    for c in range(KD):
        if ready:
            ready(c)
        pe.matmul(k.ps[:, 0, :], k.ones[:], k.x[:, c, :], start=(c == 0), stop=(c == KD - 1))


def norm_stage(k, name, dst, scale, shift, sum_next=False, also=None):
    src = k.x
    ps = k.ps
    with k.stage(name, "sq_done", "var_done", "std_done", "vec_step", "centred", "scaled", "out_done", "h_done") as (block, s, sb):
        xc = sb("xc", [P, KD, T])
        sq = sb("sq", [P, KD, T])
        std = sb("std", [P, T])
        rstd = sb("rstd", [P, T])

        @block.sync
        def _(sp):
            k.clear(sp)

        @block.tensor
        def _(pe):
            for c in range(KD):
                pe.wait_ge(s["sq_done"], c + 1)
                mm = pe.matmul(ps[:, 1, :], k.ones[:], sq[:, c, :], start=(c == 0), stop=(c == KD - 1))
            mm.then_inc(s["var_done"], 1)
            if sum_next:
                sum_channels(k, pe, lambda c: pe.wait_ge(s["out_done"], c + 1))

        @block.vector
        def _(dve):
            for c in range(KD):
                dve.scalar_tensor_tensor(out=xc[:, c, :], in0=ps[:, 0, :], scalar=-1.0 / D, in1=src[:, c, :],
                                         op0=ALU.mult, op1=ALU.add).then_inc(s["centred"], 1)
            dve.wait_ge(s["std_done"], 1)
            dve.reciprocal(rstd[:], std[:]).then_inc(s["vec_step"], 1)
            dve.wait_ge(s["vec_step"], 1)
            for c in range(KD):
                dve.tensor_tensor(xc[:, c, :], xc[:, c, :], rstd[:], ALU.mult).then_inc(s["scaled"], 1)
            if also:
                h, h_scale, h_shift = also
                for c in range(KD):
                    dve.wait_ge(s["out_done"], c + 1)
                    dve.tensor_scalar(h[:, c, :], dst[:, c, :], h_scale(c), h_shift(c), ALU.mult, ALU.add).then_inc(s["h_done"], 1)

        @block.scalar
        def _(act):
            for c in range(KD):
                act.wait_ge(s["centred"], c + 1)
                act.activation(sq[:, c, :], xc[:, c, :], ACT.Square).then_inc(s["sq_done"], 1)
            act.wait_ge(s["var_done"], 1)
            act.activation(std[:], ps[:, 1, :], ACT.Sqrt, scale=1.0 / D, bias=k.eps_ln[:]).then_inc(s["std_done"], 1)
            for c in range(KD):
                act.wait_ge(s["scaled"], c + 1)
                act.activation(dst[:, c, :], xc[:, c, :], ACT.Identity, scale=scale(c), bias=shift(c)).then_inc(s["out_done"], 1)


def columns(w, first, n=STRIP):
    return w[:, bass.ds(first, n)].rearrange("(k p) n -> p k n", p=P)


class SplitProducts:

    SEMS = ("raw_loaded0", "raw_loaded1", "raw_loaded2", "raw_loaded3", "high_done", "low_done", "half_used", "x_high", "x_low")
    PRIMED = ("low_done", "half_used")

    def __init__(self, k, s, sb):
        self.k, self.s = k, s
        self.parts = sb("w_parts", [P, 2, 2, KD, HALF], F32R)

    def raw(self, n):
        slot = self.k.w[:, n % 4 // 2, :]
        return slot[:, n % 2 * KD * HALF:(n % 2 + 1) * KD * HALF].rearrange("p (k n) -> p k n", k=KD)

    def load(self, sp, n, src, base=0):
        if n >= 4:
            sp.wait_ge(self.s["low_done"], 1 + base + n - 3)
        elif not isinstance(base, int):
            sp.wait_ge(self.s["low_done"], 1 + base)
        sp.dma_start(self.raw(n), src).then_inc(self.s[f"raw_loaded{n % 4}"], 16)

    def high(self, act, n, base=0, rounds=0):
        s = self.s
        act.wait_ge(s[f"raw_loaded{n % 4}"], 16 * (rounds + n // 4 + 1))
        if n >= 2:
            act.wait_ge(s["half_used"], 1 + base + n - 1)
        elif not isinstance(base, int):
            act.wait_ge(s["half_used"], 1 + base)
        act.activation(self.parts[:, n % 2, 0], self.raw(n), ACT.Copy).then_inc(s["high_done"], 1)

    def low(self, dve, n, base=0):
        s = self.s
        dve.wait_ge(s["high_done"], base + n + 1)
        dve.tensor_tensor(self.parts[:, n % 2, 1], self.raw(n), self.parts[:, n % 2, 0].bitcast(F32),
                          ALU.subtract).then_inc(s["low_done"], 1)

    def products(self, pe, n, x, outs, base=0, start=True, stop=True, arriving=False, arrived=0):
        s = self.s
        pe.wait_ge(s["low_done"], 1 + base + n + 1)
        for f, out in enumerate(outs):
            for kk in range(KD):
                if arriving and f == 0:
                    pe.wait_ge(s["x_low"], arrived + kk + 1)
                for j, (w, v) in enumerate(((0, 0), (0, 1), (1, 0))):
                    mm = pe.matmul(out, self.parts[:, n % 2, w, kk, f * P:(f + 1) * P], x[:, v, kk, :],
                                   start=(start and kk == 0 and j == 0), stop=(stop and kk == KD - 1 and j == 2))
        mm.then_inc(s["half_used"], 1)


class SplitLinear(SplitProducts):

    HALVES = D // HALF

    def __init__(self, k, block, s, sb, w, x, then=None):
        super().__init__(k, s, sb)
        self.x = x
        self.x_parts = sb("x_parts", [P, 2, KD, T], F32R)

        @block.sync
        def _(sp):
            k.clear(sp)
            for n in range(self.HALVES):
                self.load(sp, n, columns(w, n * HALF, HALF))

        @block.tensor
        def _(pe):
            for n in range(self.HALVES):
                self.products(pe, n, self.x_parts, [k.ps[:, n * HT + f, :] for f in range(HT)], arriving=(n == 0))
            if then:
                then(pe)

    def scalar(self, act, epilogue=None):
        for kk in range(KD):
            act.activation(self.x_parts[:, 0, kk], self.x[:, kk, :], ACT.Copy).then_inc(self.s["x_high"], 1)
            if kk in (KD // 2, KD - 1):
                self.high(act, kk // (KD // 2 + 1))
        for n in range(self.HALVES):
            if n + 2 < self.HALVES:
                self.high(act, n + 2)
            if epilogue:
                epilogue(n)

    def vector(self, dve, epilogue=None):
        for kk in range(KD):
            dve.wait_ge(self.s["x_high"], kk + 1)
            dve.tensor_tensor(self.x_parts[:, 1, kk], self.x[:, kk, :], self.x_parts[:, 0, kk].bitcast(F32),
                              ALU.subtract).then_inc(self.s["x_low"], 1)
            if kk in (KD // 2, KD - 1):
                self.low(dve, kk // (KD // 2 + 1))
        for n in range(self.HALVES):
            if n + 2 < self.HALVES:
                self.low(dve, n + 2)
            if epilogue:
                epilogue(n)


def forget_stage(k):
    ps, w_in = k.ps, k.ins["w_in"][0]
    with k.stage("forget", "loaded", "f_done", "act_step", "vec_step") as (block, s, sb):
        wf = sb("wf", [P, KD, HEADS])
        bias = sb("bias", [HEADS, 1])
        v, e, ln = sb("v", [HEADS, T]), sb("e", [HEADS, T]), sb("ln", [HEADS, T])
        ones = sb("ones", [HEADS, T])

        @block.sync
        def _(sp):
            k.clear(sp)
            sp.dma_start(wf[:], columns(w_in, F0, HEADS)).then_inc(s["loaded"], 16)
            sp.dma_start(bias[:], k.ins["b_forget"].rearrange("l h -> h l")).then_inc(s["loaded"], 16)

        @block.tensor
        def _(pe):
            pe.wait_ge(s["loaded"], 32)
            for kk in range(KD):
                mm = pe.matmul(ps[0:HEADS, 0, :], wf[:, kk, :], k.h[:, kk, :], start=(kk == 0), stop=(kk == KD - 1))
            mm.then_inc(s["f_done"], 1)

        @block.scalar
        def _(act):
            act.wait_ge(s["vec_step"], 3)
            act.activation(e[:], e[:], ACT.Exp).then_inc(s["act_step"], 1)
            act.wait_ge(s["act_step"], 1)
            act.activation(ln[:], e[:], ACT.Ln, bias=1.0).then_inc(s["act_step"], 1)

        @block.vector
        def _(dve):
            step = Steps(dve, s["vec_step"])
            step(dve.memset(ones[:], 1.0))
            dve.wait_ge(s["loaded"], 32)
            dve.wait_ge(s["f_done"], 1)
            step(dve.tensor_scalar(v[:], ps[0:HEADS, 0, :], bias[:], None, ALU.add))
            step(dve.scalar_tensor_tensor(out=e[:], in0=v[:], scalar=-1.0, in1=v[:], op0=ALU.mult, op1=ALU.min))
            dve.wait_ge(s["act_step"], 2)
            step(dve.tensor_scalar(v[:], v[:], 0.0, None, ALU.min))
            step(dve.tensor_tensor(ln[:], ln[:], v[:], ALU.subtract))
            step(dve.tensor_tensor_scan(k.neg_f[:], ones[:], ln[:], 0.0, ALU.mult, ALU.add))


def scan_softmax(k, s, units, scores, p_tiles, pt_tiles, values, nmax, rsum, rinv):
    ps, n_units = k.ps, len(units)

    def tensor(pe, i):
        base = n_units * i

        def logits(n):
            if n >= 3:
                pe.wait_ge(s["exp_done"], 1 + base + n - 2)
            scores(pe, units[n], n % 3).then_inc(s["scores_done"], 1)

        def turn(n):
            pe.wait_ge(s["probs_done"], base + n + 1)
            if n >= 2:
                pe.wait_ge(s["turned_copied"], base + n - 1)
            for kb in range(units[n][1] + 1):
                mm = pe.transpose(ps[:, 3 + n % 2, kb * P:(kb + 1) * P], p_tiles[:, n % 3, kb * P:(kb + 1) * P], k.ident[:])
            mm.then_inc(s["turned"], 1)

        def weigh(n):
            rows, b = units[n]
            pe.wait_ge(s["turned_copied"], base + n + 1)
            if n == 0:
                pe.wait_ge(s["o_copied"], 1 + i)
            for kb in range(b + 1):
                mm = pe.matmul(ps[rows, 5, b * P:(b + 1) * P], values(units[n], kb), pt_tiles[:, n % 2, kb * P:(kb + 1) * P],
                               start=(kb == 0), stop=(kb == b))
            mm.then_inc(s["weighed"], 1)

        logits(0)
        logits(1)
        for n in range(n_units):
            if n + 2 < n_units:
                logits(n + 2)
            turn(n)
            if n >= 1:
                weigh(n - 1)
        weigh(n_units - 1)

    def vector(dve, i):
        base = n_units * i
        step = Steps(dve, s["soft_step"], 2 * base)

        def row_max(n):
            b = units[n][1]
            dve.wait_ge(s["scores_done"], 1 + base + n + 1)
            diagonal = ps[:, n % 3, b * P:(b + 1) * P]
            step(dve.tensor_tensor(diagonal, diagonal, k.future_mask[:], ALU.add))
            if n == 0:
                dve.wait_ge(s["exp_done"], 1 + base)
            dve.tensor_reduce(nmax[:, n:n + 1], ps[:, n % 3, 0:(b + 1) * P], AX.X, ALU.max, negate=True).then_inc(s["max_done"], 1)

        def normalise(n):
            b = units[n][1]
            dve.wait_ge(s["exp_done"], 1 + base + n + 1)
            step(dve.reciprocal(rinv[:, n:n + 1], rsum[:, n:n + 1]))
            row = p_tiles[:, n % 3, 0:(b + 1) * P]
            dve.tensor_scalar(row, row, rinv[:, n:n + 1], None, ALU.mult).then_inc(s["probs_done"], 1)

        row_max(0)
        for n in range(n_units):
            if n + 1 < n_units:
                row_max(n + 1)
            normalise(n)
        return step.n

    def scalar(act, i):
        base = n_units * i

        def exponent(n):
            b = units[n][1]
            act.wait_ge(s["max_done"], base + n + 1)
            if n >= 3:
                act.wait_ge(s["turned"], base + n - 2)
            act.activation(p_tiles[:, n % 3, 0:(b + 1) * P], ps[:, n % 3, 0:(b + 1) * P], ACT.Exp, bias=nmax[:, n:n + 1],
                           accum_out=rsum[:, n:n + 1]).then_inc(s["exp_done"], 1)

        def copy_turned(n):
            b = units[n][1]
            act.wait_ge(s["turned"], base + n + 1)
            if n >= 2:
                act.wait_ge(s["weighed"], 1 + base + n - 1)
            act.activation(pt_tiles[:, n % 2, 0:(b + 1) * P], ps[:, 3 + n % 2, 0:(b + 1) * P], ACT.Copy).then_inc(s["turned_copied"], 1)

        exponent(0)
        for n in range(n_units):
            if n + 1 < n_units:
                exponent(n + 1)
            copy_turned(n)

    return tensor, vector, scalar


SOFTMAX = ("scores_done", "exp_done", "probs_done", "turned", "turned_copied", "weighed", "max_done", "soft_step", "o_copied")


def attention_stage(k, o):
    ps, w_in = k.ps, k.ins["w_in"][0]
    pairs = HEADS // 2
    MOD_SLOTS, MOD_HALVES = 3, 6
    MOD_TILES = MOD_HALVES * HT
    mod_matrices = (k.ins["mod_mix_w_2"], k.ins["mod_ffn_w_2"])
    with k.stage("attention", "w_loaded", "q_done", "k_done", "v_done", "qkv_copied", "f_picked", *SOFTMAX,
                 "mod_loaded0", "mod_loaded1", "mod_loaded2", "mod_used", "mod_step", "mod_summed", "mod_copied", "mod_out",
                 primed=("mod_used",) * MOD_SLOTS + ("mod_summed", "mod_copied", "exp_done", "o_copied", "qkv_copied", "scores_done", "v_done", "weighed")) as (block, s, sb):
        qt, kt = sb("qt", [P, T]), sb("kt", [P, T])
        v = sb("v", [P, TB, P])
        picked = sb("picked", [HEADS, 2, T])
        p_tiles, pt_tiles = sb("p_tiles", [P, 3, T]), sb("pt_tiles", [P, 2, T])
        nmax, rsum, rinv = sb("nmax", [P, 8]), sb("rsum", [P, 8]), sb("rinv", [P, 8])
        mod_sum = sb("mod_sum", [P, MOD_HALVES, HALF])
        mod_w = [k.w[:, slot, KD * P:KD * (P + HALF)].rearrange("p (k n) -> p k n", k=KD) for slot in range(MOD_SLOTS)]
        wv = k.w[:, 0:3, 0:KD * P].rearrange("p s (k n) -> p s k n", k=KD)
        units = [(slice(hh * HD, (hh + 1) * HD), b) for hh in range(2) for b in range(TB)]

        def scores(pe, unit, bank):
            rows, b = unit
            hh, n = rows.start // HD, (b + 1) * P
            pe.matmul(ps[:, bank, 0:n], qt[rows, b * P:(b + 1) * P], kt[rows, 0:n], start=True, stop=False)
            return pe.matmul(ps[:, bank, 0:n], k.ones[0:HEADS, :], picked[:, hh, 0:n], start=False, stop=True)

        tensor, vector, scalar = scan_softmax(k, s, units, scores, p_tiles, pt_tiles,
                                              lambda unit, kb: v[:, kb, unit[0]], nmax, rsum, rinv)

        @block.sync
        def _(sp):
            k.clear(sp)
            for layer in range(2):
                start = pairs // 2 * layer
                with sp.Fori(start, start + pairs // 2) as i:
                    sp.wait_ge(s["v_done"], 1 + i)
                    for j, first in enumerate((Q0, K0, V0)):
                        sp.dma_start(wv[:, j], columns(w_in, first + i * P, P)).then_inc(s["w_loaded"], 16)
                    for j in range(MOD_HALVES):
                        w, col = mod_matrices[j // 3][layer], ((i - start) * 3 + j % 3) * HALF
                        sp.wait_ge(s["mod_used"], MOD_SLOTS + MOD_HALVES * i + j - (MOD_SLOTS - 1))
                        sp.dma_start(mod_w[j % MOD_SLOTS], columns(w, col, HALF)).then_inc(s[f"mod_loaded{j % MOD_SLOTS}"], 16)

        @block.tensor
        def _(pe):
            with pe.Fori(0, pairs) as i:
                pe.wait_ge(s["w_loaded"], 48 * (i + 1))
                pe.wait_ge(s["qkv_copied"], 1 + 3 * i)
                for j, done in enumerate((s["q_done"], s["k_done"])):
                    if j == 1:
                        pe.wait_ge(s["mod_copied"], 1 + 2 * i)
                    for kk in range(KD):
                        mm = pe.matmul(ps[:, 6 + j, :], wv[:, j, kk, :], k.h[:, kk, :], start=(kk == 0), stop=(kk == KD - 1))
                    mm.then_inc(done, 1)
                pe.wait_ge(s["qkv_copied"], 1 + 3 * i + 1)
                for b in range(TB):
                    for kk in range(KD):
                        mm = pe.matmul(ps[:, 6, b * P:(b + 1) * P], k.h[:, kk, b * P:(b + 1) * P], wv[:, 2, kk, :],
                                       start=(kk == 0), stop=(kk == KD - 1))
                mm.then_inc(s["v_done"], 1)
                pe.wait_ge(s["qkv_copied"], 1 + 3 * i + 3)
                pe.wait_ge(s["f_picked"], 2 * i + 2)
                tensor(pe, i)
                pe.wait_ge(s["mod_used"], MOD_SLOTS + MOD_HALVES * (i + 1))
                for c in range(MOD_TILES):
                    mm = pe.matmul(ps[:, 7, c:c + 1], mod_sum[:, c // HT, c % HT * P:(c % HT + 1) * P], k.ones[:, 0:1], start=True, stop=True)
                mm.then_inc(s["mod_summed"], 1)

        @block.scalar
        def _(act):
            with act.Fori(0, pairs) as i:
                act.wait_ge(s["q_done"], i + 1)
                act.wait_ge(s["weighed"], 1 + len(units) * i)
                act.activation(qt[:], ps[:, 6, :], ACT.Copy, scale=HD ** -0.5).then_inc(s["qkv_copied"], 1)
                act.wait_ge(s["k_done"], i + 1)
                act.activation(kt[:], ps[:, 7, :], ACT.Copy).then_inc(s["qkv_copied"], 1)
                act.wait_ge(s["v_done"], 1 + i + 1)
                act.activation(v[:], ps[:, 6, :].rearrange("p (b n) -> p b n", b=TB), ACT.Copy).then_inc(s["qkv_copied"], 1)
                scalar(act, i)
                act.wait_ge(s["mod_summed"], 1 + i + 1)
                for j in range(2):
                    act.activation(k.mod[:, bass.ds(48 + 48 * j + MOD_TILES // 2 * i, MOD_TILES // 2)],
                                   ps[:, 7, j * MOD_TILES // 2:(j + 1) * MOD_TILES // 2], ACT.Copy).then_inc(s["mod_copied"], 1)

        @block.vector
        def _(dve):
            with dve.Fori(0, pairs) as i:
                dve.wait_ge(s["scores_done"], 1 + len(units) * i)
                for hh in range(2):
                    dve.tensor_scalar(picked[:, hh, :], k.neg_f[:], k.ident[0:HEADS, bass.ds(2 * i + hh, 1)], None,
                                      ALU.mult).then_inc(s["f_picked"], 1)
                step = Steps(dve, s["mod_step"], MOD_HALVES * (KD - 1) * i)
                dve.wait_ge(s["mod_summed"], 1 + i)
                for j in range(MOD_HALVES):
                    dve.wait_ge(s[f"mod_loaded{j % MOD_SLOTS}"], 16 * (MOD_HALVES // MOD_SLOTS * i + j // MOD_SLOTS + 1))
                    for kk in range(KD):
                        w, by = mod_w[j % MOD_SLOTS][:, kk, :], k.silu_c[:, 1, kk:kk + 1]
                        if kk == 0:
                            ins = dve.tensor_scalar(mod_sum[:, j], w, by, None, ALU.mult)
                        else:
                            ins = dve.scalar_tensor_tensor(out=mod_sum[:, j], in0=w, scalar=by, in1=mod_sum[:, j], op0=ALU.mult, op1=ALU.add)
                        if kk < KD - 1:
                            step(ins)
                    ins.then_inc(s["mod_used"], 1)
                n = vector(dve, i)
                assert n == 2 * len(units)
                dve.wait_ge(s["weighed"], 1 + len(units) * (i + 1))
                dve.tensor_copy(o[:, bass.ds(i, 1), :], ps[:, 5:6, :]).then_inc(s["o_copied"], 1)

        @block.gpsimd
        def _(pool):
            pool.wait_ge(s["mod_copied"], 1 + 2 * pairs)
            for j, bias in enumerate(("mod_mix_b_2", "mod_ffn_b_2")):
                at, b = 48 + 48 * j, k.places[bias][0]
                pool.tensor_tensor(k.mod[:, at:at + 48], k.mod[:, at:at + 48], k.cols[:, b:b + 48], ALU.add).then_inc(s["mod_out"], 1)
            pool.wait_ge(s["mod_out"], 2)
            for first in range(48 + KD, 48 + 96, 3 * KD):
                pool.tensor_scalar(k.mod[:, first:first + 2 * KD], k.mod[:, first:first + 2 * KD], 1.0, None, ALU.add).then_inc(s["mod_out"], 1)


def ssm_stage(k, ys):
    ps, w_in = k.ps, k.ins["w_in"][0]
    H = R_SSM
    conv0, convb0 = k.places["conv_w"][0], k.places["conv_b"][0]
    NC = 2 + KG
    VEC_STEPS = 47
    with k.stage("ssm", "w_loaded", "z_loaded", "small_loaded", "dt_done", "tile_done", "tile_copied", "conv_done", "sig_done",
                 "act_done", "z_done", "z_sig", "z_gated", "zeroed", "d_loaded", "wend_in", "a_ready", "vec_step", "act_step", "acs_ready", "small_turned", "small_copied",
                 "turned", "turned_copied", "ends_done", "ends_copied", "decay_done", "xw_ready", "cb_done", "cb_copied", "state_done", "state_ready",
                 "row_done", "row_seen", "seg_exp", "row_exp", "scores_ready", "y_done", "y_read", "sq_done",
                 "ms_done", "std_done", "group_done", primed=("y_read", "std_done", "ms_done", "tile_done", "z_done")) as (block, s, sb):
        wxs = strip(k, 0)
        wz = strip(k, 1)
        wbc = k.w[:, 2, 0:KD * 2 * P].rearrange("p (k n) -> p k n", k=KD)
        wdt = sb("wdt", [P, KD, H])
        dt_bias, a_log = sb("dt_bias", [H, G_SSM]), sb("a_log", [H, G_SSM])
        d_col = sb("d_col", [P, KI])
        u = sb("u", [P, 2, T + CONV - 1])
        acc = sb("acc", [P, 2, T])
        sig = sb("sig", [P, 2, T])
        xbc = sb("xbc", [P, NC, T])
        z = sb("z", [P, KG, T])
        xt = k.w[:, 2, KD * 2 * P:].rearrange("p (b n) -> p b n", b=TB)
        bt = sb("bt", [P, TB, P])
        xw = sb("xw", [P, TB - 1, KG * P])
        hp = sb("hp", [P, TB - 1, KG * P])
        cb = sb("cb", [P, TB, P])
        dt, acs = sb("dt", [H, T]), sb("acs", [H, T])
        e, t1, t2 = xw[0:H, 0, :], xw[0:H, 1, :], xw[0:H, 2, :]
        ones = sb("ones", [H, T])
        small = sb("small", [P, 2, TB, H])
        ends_in = sb("ends_in", [H, TB, H])
        ends = sb("ends", [P, TB, H])
        decay, wend = sb("decay", [P, TB, H]), sb("wend", [P, TB, H])
        seg, rowx = sb("seg", [P, 2, T]), sb("rowx", [P, 2, T])
        sc, ce = sb("sc", [P, 2, TB, P]), sb("ce", [P, 2, T])
        sq = acc
        std, rstd = seg[:, 0, :], seg[:, 1, :]

        def wcols(i, tile, j):
            at = (16 + i) if tile == 0 else (20 + i) if tile == 1 else KG * i + tile - 2
            first = convb0 if j is None else conv0 + j * XBC_TILES
            return k.cols[:, bass.ds(first + at, 1)]

        @block.sync
        def _(sp):
            k.clear(sp)
            for half in range(2):
                sp.dma_start(d_col[half * P_SSM:(half + 1) * P_SSM, :],
                               k.ins["d_skip"].rearrange("l (j two) -> two l j", two=2)[half].to_broadcast([P_SSM, KI]),
                               allow_slow_non_contiguous=True).then_inc(s["d_loaded"], 16)
            for dst, name in ((dt_bias, "dt_bias"), (a_log, "a_log")):
                sp.dma_start(dst[:], k.ins[name].rearrange("l (g h) -> h (l g)", h=H), allow_slow_non_contiguous=True).then_inc(s["small_loaded"], 16)
            with sp.Fori(0, G_SSM) as i:
                sp.wait_ge(s["tile_done"], 1 + NC * i)
                sp.dma_start(wdt[:], columns(w_in, DT0 + i * H, H)).then_inc(s["w_loaded"], 16)
                sp.dma_start(wbc[:, :, 0:P], columns(w_in, B0 + i * P, P)).then_inc(s["w_loaded"], 16)
                sp.dma_start(wbc[:, :, P:2 * P], columns(w_in, C0 + i * P, P)).then_inc(s["w_loaded"], 16)
                sp.dma_start(wxs, columns(w_in, XBC0 + i * STRIP)).then_inc(s["w_loaded"], 16)
                sp.wait_ge(s["z_done"], 1 + KG * i)
                sp.dma_start(wz, columns(w_in, Z0 + i * STRIP)).then_inc(s["z_loaded"], 16)

        @block.gpsimd
        def _(pool):
            for b in range(2):
                pool.memset(u[:, b, 0:CONV - 1], 0.0).then_inc(s["zeroed"], 1)

        @block.tensor
        def _(pe):
            with pe.Fori(0, G_SSM) as i:
                pe.wait_ge(s["w_loaded"], 64 * (i + 1))
                pe.wait_ge(s["y_read"], 1 + KG * i)
                for kk in range(KD):
                    mm = pe.matmul(ps[0:H, 7, :], wdt[:, kk, :], k.h[:, kk, :], start=(kk == 0), stop=(kk == KD - 1))
                mm.then_inc(s["dt_done"], 1)
                for c in range(NC):
                    for kk in range(KD):
                        w = wbc[:, kk, c * P:(c + 1) * P] if c < 2 else wxs[:, kk, (c - 2) * P:(c - 1) * P]
                        mm = pe.matmul(ps[:, c, :], w, k.h[:, kk, :], start=(kk == 0), stop=(kk == KD - 1))
                    mm.then_inc(s["tile_done"], 1)
                pe.wait_ge(s["std_done"], 1 + i)
                pe.wait_ge(s["acs_ready"], i + 1)
                pe.matmul(ps[:, 7, 0:TB * H], k.ones[0:H, :], ends_in[:].rearrange("p c h -> p (c h)"), start=True,
                          stop=True).then_inc(s["ends_done"], 1)
                for j, m in enumerate((dt, acs)):
                    for c in range(TB):
                        mm = pe.transpose(ps[:, 6, (j * TB + c) * H:(j * TB + c + 1) * H], m[:, c * P:(c + 1) * P], k.ident[0:H, 0:H])
                mm.then_inc(s["small_turned"], 1)
                pe.wait_ge(s["z_loaded"], 16 * (i + 1))
                for f in range(KG):
                    pe.wait_ge(s["tile_copied"], NC * i + f + 1)
                    for kk in range(KD):
                        mm = pe.matmul(ps[:, f, :], wz[:, kk, f * P:(f + 1) * P], k.h[:, kk, :], start=(kk == 0), stop=(kk == KD - 1))
                    mm.then_inc(s["z_done"], 1)
                pe.wait_ge(s["tile_copied"], NC * (i + 1))
                pe.wait_ge(s["act_done"], NC * (i + 1))
                for n in range(1 + TB):
                    if n >= 2:
                        pe.wait_ge(s["turned_copied"], (1 + TB) * i + n - 1)
                    for m in range(TB if n == 0 else KG):
                        src = xbc[:, 0, m * P:(m + 1) * P] if n == 0 else xbc[:, 2 + m, (n - 1) * P:n * P]
                        mm = pe.transpose(ps[:, 4 + n % 2, m * P:(m + 1) * P], src, k.ident[:])
                    mm.then_inc(s["turned"], 1)
                pe.wait_ge(s["small_copied"], i + 1)
                for c in range(TB):
                    mm = pe.matmul(ps[:, 6, c * P:(c + 1) * P], xbc[:, 0, c * P:(c + 1) * P], xbc[:, 1, c * P:(c + 1) * P],
                                   start=True, stop=True)
                mm.then_inc(s["cb_done"], 1)
                pe.wait_ge(s["turned_copied"], (1 + TB) * (i + 1))
                pe.wait_ge(s["z_gated"], KG * (i + 1))
                for c in range(TB - 1):
                    pe.wait_ge(s["xw_ready"], (TB - 1) * i + c + 1)
                    pe.matmul(ps[:, c, :], bt[:, c, :], xw[:, c, :], start=True, stop=True).then_inc(s["state_done"], 1)

                def row(h):
                    if h >= 2:
                        pe.wait_ge(s["row_exp"], H * i + h - 1)
                        pe.wait_ge(s["row_seen"], H * i + h - 1)
                    pe.matmul(ps[:, 4 + h % 2, :], k.ident[0:H, h:h + 1].to_broadcast([H, P]), acs[:], start=True,
                              stop=True).then_inc(s["row_done"], 1)

                pe.wait_ge(s["ends_copied"], i + 1)
                row(0)
                row(1)
                for h in range(H):
                    rows = slice(h % 2 * P_SSM, (h % 2 + 1) * P_SSM)
                    bank = (3, 7)[h // 2 % 2]
                    if h + 2 < H:
                        row(h + 2)
                    if h >= 4:
                        pe.wait_ge(s["y_read"], 1 + KG * i + h // 2 - 1)
                    pe.wait_ge(s["scores_ready"], H * i + h + 1)
                    if h == 0:
                        pe.wait_ge(s["state_ready"], i + 1)
                    for c in range(TB):
                        mine = slice(c * P, (c + 1) * P)
                        mm = pe.matmul(ps[rows, bank, mine], xt[:, c, h * P_SSM:(h + 1) * P_SSM], sc[:, h % 2, c, :],
                                       start=True, stop=(c == 0))
                        if c:
                            mm = pe.matmul(ps[rows, bank, mine], hp[:, c - 1, h * P_SSM:(h + 1) * P_SSM], ce[:, h % 2, mine],
                                           start=False, stop=True)
                    mm.then_inc(s["y_done"], 1)
                for f in range(KG):
                    pe.wait_ge(s["sq_done"], KG * i + f + 1)
                    mm = pe.matmul(ps[:, 6, :], k.ones[:], sq[:, f % 2, :], start=(f == 0), stop=(f == KG - 1))
                    mm.then_inc(s["ms_done"], 1)

        @block.scalar
        def _(act):
            act.wait_ge(s["small_loaded"], 32)
            act.activation(a_log[:], a_log[:], ACT.Exp).then_inc(s["a_ready"], 1)
            with act.Fori(0, G_SSM) as i:
                act.wait_ge(s["vec_step"], VEC_STEPS * i + 2)
                act.activation(e[:], e[:], ACT.Exp).then_inc(s["act_step"], 1)
                act.wait_ge(s["vec_step"], VEC_STEPS * i + 3)
                act.activation(t2[:], t1[:], ACT.Ln).then_inc(s["act_step"], 1)
                for c in range(NC):
                    act.wait_ge(s["tile_done"], 1 + NC * i + c + 1)
                    if c >= 2:
                        act.wait_ge(s["conv_done"], NC * i + c - 1)
                    act.activation(u[:, c % 2, CONV - 1:], ps[:, c, :], ACT.Copy).then_inc(s["tile_copied"], 1)
                    if c >= 1:
                        act.wait_ge(s["conv_done"], NC * i + c)
                        act.activation(sig[:, (c - 1) % 2, :], acc[:, (c - 1) % 2, :], ACT.Sigmoid).then_inc(s["sig_done"], 1)
                act.wait_ge(s["conv_done"], NC * (i + 1))
                act.activation(sig[:, (NC - 1) % 2, :], acc[:, (NC - 1) % 2, :], ACT.Sigmoid).then_inc(s["sig_done"], 1)
                act.wait_ge(s["small_turned"], i + 1)
                act.activation(small[:], ps[:, 6, 0:2 * TB * H].rearrange("p (j c h) -> p j c h", j=2, c=TB), ACT.Copy).then_inc(s["small_copied"], 1)
                act.wait_ge(s["ends_done"], i + 1)
                act.activation(ends[:], ps[:, 7, 0:TB * H].rearrange("p (c h) -> p c h", c=TB), ACT.Copy).then_inc(s["ends_copied"], 1)
                for f in range(KG):
                    act.wait_ge(s["z_done"], 1 + KG * i + f + 1)
                    act.wait_ge(s["act_done"], NC * (i + 1))
                    if f >= 2:
                        act.wait_ge(s["z_gated"], KG * i + f - 1)
                    act.activation(sig[:, f % 2, :], ps[:, f, :], ACT.Sigmoid).then_inc(s["z_sig"], 1)
                for n in range(1 + TB):
                    act.wait_ge(s["turned"], (1 + TB) * i + n + 1)
                    dst = bt[:] if n == 0 else xt[:, n - 1, :].rearrange("p (b n) -> p b n", b=KG)
                    act.activation(dst, ps[:, 4 + n % 2, :].rearrange("p (b n) -> p b n", b=TB), ACT.Copy).then_inc(s["turned_copied"], 1)
                act.wait_ge(s["cb_done"], i + 1)
                act.activation(cb[:], ps[:, 6, :].rearrange("p (b n) -> p b n", b=TB), ACT.Copy).then_inc(s["cb_copied"], 1)
                act.wait_ge(s["ends_copied"], i + 1)
                act.activation(decay[:], ends[:], ACT.Exp).then_inc(s["decay_done"], 1)
                act.wait_ge(s["wend_in"], i + 1)
                act.activation(wend[:], wend[:], ACT.Exp).then_inc(s["decay_done"], 1)
                def row_exp(h):
                    act.wait_ge(s["row_done"], H * i + h + 1)
                    if h >= 2:
                        act.wait_ge(s["scores_ready"], H * i + h - 1)
                    act.activation(rowx[:, h % 2, :], ps[:, 4 + h % 2, :], ACT.Exp).then_inc(s["row_exp"], 1)

                row_exp(0)
                for h in range(H):
                    if h + 1 < H:
                        row_exp(h + 1)
                    act.wait_ge(s["row_seen"], H * i + h + 1)
                    act.activation(seg[:, h % 2, :], seg[:, h % 2, :], ACT.Exp).then_inc(s["seg_exp"], 1)
                for f in range(KG):
                    act.wait_ge(s["y_read"], 1 + KG * i + f + 1)
                    if f >= 2:
                        act.wait_ge(s["ms_done"], 1 + KG * i + f - 1)
                    act.activation(sq[:, f % 2, :], z[:, f, :], ACT.Square).then_inc(s["sq_done"], 1)
                act.wait_ge(s["ms_done"], 1 + KG * (i + 1))
                act.activation(std[:], ps[:, 6, :], ACT.Sqrt, scale=1.0 / (KG * P), bias=k.eps_rms[:]).then_inc(s["std_done"], 1)

        @block.vector
        def _(dve):
            dve.memset(ones[:], 1.0).then_inc(s["zeroed"], 1)
            dve.wait_ge(s["zeroed"], 3)
            dve.wait_ge(s["d_loaded"], 32)
            dve.wait_ge(s["small_loaded"], 32)
            dve.wait_ge(s["a_ready"], 1)
            with dve.Fori(0, G_SSM) as i:
                step = Steps(dve, s["vec_step"], VEC_STEPS * i)
                dve.wait_ge(s["dt_done"], i + 1)
                step(dve.tensor_scalar(dt[:], ps[0:H, 7, :], dt_bias[:, bass.ds(i, 1)], None, ALU.add))
                step(dve.scalar_tensor_tensor(out=e[:], in0=dt[:], scalar=-1.0, in1=dt[:], op0=ALU.mult, op1=ALU.min))
                dve.wait_ge(s["act_step"], 2 * i + 1)
                step(dve.tensor_scalar(t1[:], e[:], 1.0, None, ALU.add))
                dve.wait_ge(s["act_step"], 2 * i + 2)
                step(dve.tensor_scalar(t1[:], t1[:], -1.0, None, ALU.add))
                step(dve.tensor_scalar(acs[:], t1[:], 0.0, None, ALU.is_equal))
                step(dve.tensor_tensor(t1[:], t1[:], acs[:], ALU.add))
                step(dve.tensor_tensor(t2[:], t2[:], acs[:], ALU.add))
                step(dve.reciprocal(t1[:], t1[:]))
                step(dve.tensor_tensor(t2[:], t2[:], e[:], ALU.mult))
                step(dve.tensor_tensor(t2[:], t2[:], t1[:], ALU.mult))
                step(dve.scalar_tensor_tensor(out=dt[:], in0=dt[:], scalar=0.0, in1=t2[:], op0=ALU.max, op1=ALU.add))
                step(dve.tensor_scalar(t1[:], dt[:], a_log[:, bass.ds(i, 1)], -1.0, ALU.mult, ALU.mult))
                for c in range(TB):
                    mine = slice(c * P, (c + 1) * P)
                    step(dve.tensor_tensor_scan(acs[:, mine], ones[:, mine], t1[:, mine], 0.0, ALU.mult, ALU.add))
                for c in range(TB):
                    ins = dve.tensor_scalar(ends_in[:, c, :], k.ident[0:H, 0:H], acs[:, (c + 1) * P - 1:(c + 1) * P], None, ALU.mult)
                    if c < TB - 1:
                        step(ins)
                ins.then_inc(s["acs_ready"], 1)
                def silu(c):
                    dve.wait_ge(s["sig_done"], NC * i + c + 1)
                    dve.tensor_tensor(xbc[:, c, :], acc[:, c % 2, :], sig[:, c % 2, :], ALU.mult).then_inc(s["act_done"], 1)

                dve.wait_ge(s["ms_done"], 1 + KG * i)
                for c in range(NC):
                    if c >= 2:
                        silu(c - 2)
                        dve.wait_ge(s["act_done"], NC * i + c - 1)
                    dve.wait_ge(s["tile_copied"], NC * i + c + 1)
                    a = acc[:, c % 2, :]
                    step(dve.tensor_scalar(a, u[:, c % 2, 0:T], wcols(i, c, 0), wcols(i, c, None), ALU.mult, ALU.add))
                    for j in range(1, CONV):
                        ins = dve.scalar_tensor_tensor(out=a, in0=u[:, c % 2, j:j + T], scalar=wcols(i, c, j), in1=a,
                                                       op0=ALU.mult, op1=ALU.add)
                        if j < CONV - 1:
                            step(ins)
                    ins.then_inc(s["conv_done"], 1)
                silu(NC - 2)
                silu(NC - 1)
                dve.wait_ge(s["small_copied"], i + 1)
                dve.wait_ge(s["ends_copied"], i + 1)
                dve.tensor_tensor(wend[:], ends[:], small[:, 1], ALU.subtract).then_inc(s["wend_in"], 1)
                for f in range(KG):
                    dve.wait_ge(s["z_sig"], KG * i + f + 1)
                    dve.tensor_tensor(z[:, f, :], ps[:, f, :], sig[:, f % 2, :], ALU.mult).then_inc(s["z_gated"], 1)
                dve.wait_ge(s["decay_done"], 2 * i + 2)
                step(dve.tensor_tensor(wend[:], wend[:], small[:, 0], ALU.mult))
                dve.wait_ge(s["turned_copied"], (1 + TB) * (i + 1))
                for c in range(TB - 1):
                    dve.tensor_tensor(xw[:, c, :].rearrange("p (h n) -> p h n", h=H), xt[:, c, :].rearrange("p (h n) -> p h n", h=H),
                                      wend[:, c, :].rearrange("p (h o) -> p h o", o=1).to_broadcast([P, H, P_SSM]), ALU.mult).then_inc(s["xw_ready"], 1)
                for c in range(TB - 1):
                    dve.wait_ge(s["state_done"], (TB - 1) * i + c + 1)
                    if c == 0:
                        step(dve.tensor_copy(hp[:, 0, :], ps[:, 0, :]))
                    else:
                        step(dve.tensor_tensor(hp[:, c, :].rearrange("p (h n) -> p h n", h=H), hp[:, c - 1, :].rearrange("p (h n) -> p h n", h=H),
                                               decay[:, c, :].rearrange("p (h o) -> p h o", o=1).to_broadcast([P, H, P_SSM]), ALU.mult))
                        ins = dve.tensor_tensor(hp[:, c, :], hp[:, c, :], ps[:, c, :], ALU.add)
                        if c < TB - 2:
                            step(ins)
                ins.then_inc(s["state_ready"], 1)

                def segment(h):
                    dve.wait_ge(s["row_exp"], H * i + h + 1)
                    for c in range(TB):
                        mine = slice(c * P, (c + 1) * P)
                        ins = dve.scalar_tensor_tensor(out=seg[:, h % 2, mine], in0=ps[:, 4 + h % 2, mine], scalar=small[:, 1, c, h:h + 1],
                                                       in1=k.past_cap[:], op0=ALU.subtract, op1=ALU.min)
                    ins.then_inc(s["row_seen"], 1)

                def outputs(f):
                    bank = (3, 7)[f % 2]
                    dve.wait_ge(s["y_done"], H * i + 2 * f + 2)
                    step(dve.scalar_tensor_tensor(out=xbc[:, 2 + f, :], in0=xbc[:, 2 + f, :], scalar=d_col[:, bass.ds(KG * i + f, 1)],
                                                  in1=ps[:, bank, :], op0=ALU.mult, op1=ALU.add))
                    dve.tensor_tensor(z[:, f, :], z[:, f, :], xbc[:, 2 + f, :], ALU.mult).then_inc(s["y_read"], 1)

                dve.wait_ge(s["cb_copied"], i + 1)
                segment(0)
                for h in range(H):
                    if h + 1 < H:
                        if h >= 1:
                            dve.wait_ge(s["seg_exp"], H * i + h)
                        segment(h + 1)
                    dve.wait_ge(s["seg_exp"], H * i + h + 1)
                    if h >= 2:
                        dve.wait_ge(s["y_done"], H * i + h - 1)
                    for c in range(TB):
                        mine = slice(c * P, (c + 1) * P)
                        dve.scalar_tensor_tensor(out=sc[:, h % 2, c, :], in0=seg[:, h % 2, mine], scalar=small[:, 0, c, h:h + 1],
                                                 in1=cb[:, c, :], op0=ALU.mult, op1=ALU.mult)
                    dve.tensor_tensor(ce[:, h % 2, P:], rowx[:, h % 2, P:], xbc[:, 1, P:], ALU.mult).then_inc(s["scores_ready"], 1)
                    if h >= 2 and h % 2 == 0:
                        outputs(h // 2 - 1)
                outputs(KG - 1)
                dve.wait_ge(s["std_done"], 1 + i + 1)
                step(dve.reciprocal(rstd[:], std[:]))
                for f in range(KG):
                    at = k.places["ssm_norm_w"][0] + KG * i + f
                    dve.scalar_tensor_tensor(out=ys[:, bass.ds(KG * i + f, 1), :], in0=z[:, f:f + 1, :], scalar=k.cols[:, bass.ds(at, 1)],
                                             in1=rstd[:].rearrange("p (o t) -> p o t", o=1), op0=ALU.mult, op1=ALU.mult).then_inc(s["group_done"], 1)
                assert step.n == VEC_STEPS, step.n


def merge_stage(k, name, branch, w_out, x, kt, merged):
    ps, w_in = k.ps, k.ins["w_in"][0]
    PER = D // HALF
    phases = 1 + kt // KD
    N = PER * phases
    with k.stage(name, "gate_ready", "vec_step", *SplitProducts.SEMS, primed=SplitProducts.PRIMED) as (block, s, sb):
        mul = SplitProducts(k, s, sb)
        parts = sb("x_parts", [P, 2, KD, T], F32R)
        gate = k.w[:, 2, :].rearrange("p (c n) -> p c n", c=KD)
        operand = lambda phase, kk: k.h[:, kk, :] if phase == 0 else x[:, (phase - 1) * KD + kk, :]
        tiles = lambda n: range(n % PER * HT, (n % PER + 1) * HT)

        @block.sync
        def _(sp):
            k.clear(sp)
            for n in range(N):
                phase, col = n // PER, n % PER * HALF
                src = columns(w_in, GATE0 + branch * D + col, HALF) if phase == 0 else columns(w_out[(phase - 1) * D:phase * D, :], col, HALF)
                mul.load(sp, n, src)

        @block.tensor
        def _(pe):
            for n in range(N):
                phase = n // PER
                if phase == 1:
                    pe.wait_ge(s["gate_ready"], HT * (n % PER + 1))
                mul.products(pe, n, parts, [ps[:, c, :] for c in tiles(n)], start=(phase <= 1), stop=(phase in (0, phases - 1)),
                             arriving=(n % PER == 0), arrived=KD * phase)

        @block.scalar
        def _(act):
            def high(phase, kk):
                act.activation(parts[:, 0, kk], operand(phase, kk), ACT.Copy).then_inc(s["x_high"], 1)

            for kk in range(KD):
                high(0, kk)
            mul.high(act, 0)
            mul.high(act, 1)
            for n in range(N):
                if n + 2 < N:
                    mul.high(act, n + 2)
                if n < PER:
                    act.wait_ge(s["half_used"], 1 + n + 1)
                    for c in tiles(n):
                        act.activation(gate[:, c, :], ps[:, c, :], ACT.Sigmoid).then_inc(s["gate_ready"], 1)
                if n % PER == PER - 1 and n + 1 < N:
                    act.wait_ge(s["half_used"], 1 + n + 1)
                    for kk in range(KD):
                        high(n // PER + 1, kk)

        @block.vector
        def _(dve):
            step = Steps(dve, s["vec_step"])

            def low(phase):
                for kk in range(KD):
                    dve.wait_ge(s["x_high"], KD * phase + kk + 1)
                    dve.tensor_tensor(parts[:, 1, kk], operand(phase, kk), parts[:, 0, kk].bitcast(F32), ALU.subtract).then_inc(s["x_low"], 1)

            low(0)
            mul.low(dve, 0)
            mul.low(dve, 1)
            for n in range(N):
                if n + 2 < N:
                    mul.low(dve, n + 2)
                if n >= N - PER:
                    dve.wait_ge(s["half_used"], 1 + n + 1)
                    for c in tiles(n):
                        if branch == 0:
                            step(dve.tensor_tensor(merged[:, c, :], gate[:, c, :], ps[:, c, :], ALU.mult))
                        else:
                            step(dve.tensor_tensor(gate[:, c, :], gate[:, c, :], ps[:, c, :], ALU.mult))
                            step(dve.tensor_tensor(merged[:, c, :], merged[:, c, :], gate[:, c, :], ALU.add))
                if n % PER == PER - 1 and n + 1 < N:
                    low(n // PER + 1)


def pool_stage(k, pooled):
    ps, w_in = k.ps, k.ins["w_in"][0]
    with k.stage("pool", "zeroed", "counted", "copied", "vec_step", *SplitProducts.SEMS, primed=SplitProducts.PRIMED) as (block, s, sb):
        u = sb("u", [P, KD, PAD + T])
        a, b = sb("a", [P, PAD + T]), sb("b", [P, PAD + T])
        count = sb("count", [P, len(POOL_WINDOWS), PAD])
        pos = sb("pos", [P, PAD])
        lin = SplitLinear(k, block, s, sb, w_in[:, U0:U0 + D], k.h)

        @block.gpsimd
        def _(pool):
            pool.memset(u[:, :, 0:PAD], 0.0).then_inc(s["zeroed"], 1)
            pool.memset(a[:], 0.0).then_inc(s["zeroed"], 1)
            pool.memset(b[:], 0.0).then_inc(s["zeroed"], 1)
            pool.iota(pos[:], pattern=[[1, PAD]], base=1, channel_multiplier=0,
                      allow_small_or_imprecise_dtypes=True).then_inc(s["zeroed"], 1)
            pool.wait_ge(s["zeroed"], 4)
            for g, w in enumerate(POOL_WINDOWS):
                pool.tensor_scalar(count[:, g, :], pos[:], float(w), None, ALU.min).then_inc(s["counted"], 1)

        @block.scalar
        def _(act):
            def copy(n):
                act.wait_ge(s["half_used"], 1 + n + 1)
                for c in range(n * HT, (n + 1) * HT):
                    act.activation(u[:, c, PAD:], ps[:, c, :], ACT.Copy).then_inc(s["copied"], 1)

            lin.scalar(act, copy)

        @block.vector
        def _(dve):
            step = Steps(dve, s["vec_step"])
            dve.wait_ge(s["counted"], len(POOL_WINDOWS))
            step(dve.reciprocal(count[:], count[:]))
            def window_means(n):
                for c in range(n * HT, (n + 1) * HT):
                    g = c // (KD // len(POOL_WINDOWS))
                    dve.wait_ge(s["copied"], c + 1)
                    src, bufs = u[:, c, :], (a, b)
                    for j in range(g + 1):
                        dst = bufs[j % 2]
                        step(dve.tensor_tensor(dst[:, PAD:], src[:, PAD:], src[:, PAD - 2 ** j:PAD + T - 2 ** j], ALU.add))
                        src = dst[:, :]
                    w = POOL_WINDOWS[g]
                    step(dve.scalar_tensor_tensor(out=pooled[:, c, PAD:], in0=src[:, 2 * PAD:], scalar=1.0 / w, in1=u[:, c, 2 * PAD:],
                                                  op0=ALU.mult, op1=ALU.subtract))
                    step(dve.tensor_tensor(src[:, PAD:2 * PAD], src[:, PAD:2 * PAD], count[:, g, :], ALU.mult))
                    step(dve.tensor_tensor(pooled[:, c, 0:PAD], src[:, PAD:2 * PAD], u[:, c, PAD:2 * PAD], ALU.subtract))

            lin.vector(dve, window_means)


def pool_out_stage(k, pooled, merged):
    ps, w_in = k.ps, k.ins["w_in"][0]
    groups = len(POOL_WINDOWS)
    gk = KD // groups
    N = D // HALF
    with k.stage("pool_out", "w_loaded", "gate_ready", "tile_done", "tile_free", "vec_step", *SplitProducts.SEMS,
                 primed=SplitProducts.PRIMED) as (block, s, sb):
        mul = SplitProducts(k, s, sb)
        parts = sb("x_parts", [P, 2, KD, T], F32R)
        gate = sb("gate", [P, 2, T])
        wp = k.w[:, 2, 0:groups * gk * gk * P].rearrange("p (g k n) -> p g k n", g=groups, k=gk)
        tiles = lambda n: range(n * HT, (n + 1) * HT)

        @block.sync
        def _(sp):
            k.clear(sp)
            for n in range(N):
                mul.load(sp, n, columns(w_in, GATE0 + D + n * HALF, HALF))
            sp.dma_start(wp.rearrange("p g k n -> p (g k) n"), k.ins["w_pool"][0].rearrange("g (k p) n -> p (g k) n", p=P)).then_inc(s["w_loaded"], 16)

        @block.tensor
        def _(pe):
            for n in range(N):
                if n >= 2:
                    pe.wait_ge(s["tile_free"], HT * (n - 1))
                mul.products(pe, n, parts, [ps[:, c % 4, :] for c in tiles(n)], arriving=(n == 0))
                if n == 0:
                    pe.wait_ge(s["w_loaded"], 16)
                for c in tiles(n):
                    g = c // gk
                    for kk in range(gk):
                        mm = pe.matmul(ps[:, 4 + c % 4, :], wp[:, g, kk, c % gk * P:(c % gk + 1) * P], pooled[:, g * gk + kk, :],
                                       start=(kk == 0), stop=(kk == gk - 1))
                    mm.then_inc(s["tile_done"], 1)

        @block.scalar
        def _(act):
            for kk in range(KD):
                act.activation(parts[:, 0, kk], k.h[:, kk, :], ACT.Copy).then_inc(s["x_high"], 1)
            mul.high(act, 0)
            mul.high(act, 1)
            for n in range(N):
                if n + 2 < N:
                    mul.high(act, n + 2)
                act.wait_ge(s["half_used"], 1 + n + 1)
                for c in tiles(n):
                    if c >= 2:
                        act.wait_ge(s["tile_free"], c - 1)
                    act.activation(gate[:, c % 2, :], ps[:, c % 4, :], ACT.Sigmoid).then_inc(s["gate_ready"], 1)

        @block.vector
        def _(dve):
            step = Steps(dve, s["vec_step"])
            for kk in range(KD):
                dve.wait_ge(s["x_high"], kk + 1)
                dve.tensor_tensor(parts[:, 1, kk], k.h[:, kk, :], parts[:, 0, kk].bitcast(F32), ALU.subtract).then_inc(s["x_low"], 1)
            mul.low(dve, 0)
            mul.low(dve, 1)
            for n in range(N):
                if n + 2 < N:
                    mul.low(dve, n + 2)
                for c in tiles(n):
                    dve.wait_ge(s["gate_ready"], c + 1)
                    dve.wait_ge(s["tile_done"], c + 1)
                    step(dve.scalar_tensor_tensor(out=gate[:, c % 2, :], in0=ps[:, 4 + c % 4, :], scalar=k.col("pool_scale", c),
                                                  in1=gate[:, c % 2, :], op0=ALU.mult, op1=ALU.mult))
                    dve.tensor_tensor(merged[:, c, :], merged[:, c, :], gate[:, c % 2, :], ALU.add).then_inc(s["tile_free"], 1)


def residual_stage(k, name, w, x, alpha, gate):
    ps = k.ps
    with k.stage(name, "vec_step", *SplitProducts.SEMS, primed=SplitProducts.PRIMED) as (block, s, sb):
        t = sb("t", [P, 2, T])
        lin = SplitLinear(k, block, s, sb, w, x,
                          lambda pe: sum_channels(k, pe, lambda c: pe.wait_ge(s["vec_step"], 2 * (c + 1))))

        @block.scalar
        def _(act):
            lin.scalar(act)

        @block.vector
        def _(dve):
            step = Steps(dve, s["vec_step"])

            def add(n):
                dve.wait_ge(s["half_used"], 1 + n + 1)
                for c in range(n * HT, (n + 1) * HT):
                    step(dve.tensor_scalar(t[:, c % 2, :], ps[:, c, :], k.mod[:, gate + c:gate + c + 1], None, ALU.mult))
                    step(dve.scalar_tensor_tensor(out=k.x[:, c, :], in0=k.x[:, c, :], scalar=alpha, in1=t[:, c % 2, :], op0=ALU.mult,
                                                  op1=ALU.add))

            lin.vector(dve, add)


def router_stage(k, chosen, share):
    ps = k.ps
    GR = NE // EG
    with k.stage("router", "loaded", "logits_done", "vec_step", "exp_done") as (block, s, sb):
        wr = sb("wr", [P, KD, NE])
        br = sb("br", [P, NE])
        probs, sel = sb("probs", [P, TB, NE]), sb("sel", [P, TB, NE])
        rank, cmp = chosen, sb("cmp", [P, TB, NE])
        top = sb("top", [P, TB, NE])
        score, grank, gcmp = sb("score", [P, TB, GR]), sb("grank", [P, TB, GR]), sb("gcmp", [P, TB, GR])
        red = sb("red", [P, TB])

        @block.sync
        def _(sp):
            k.clear(sp)
            sp.dma_start(wr[:], k.ins["w_router"].rearrange("(k p) n -> p k n", p=P)).then_inc(s["loaded"], 16)
            sp.dma_start(br[:], k.ins["b_router"].rearrange("(o n) -> o n", o=1).to_broadcast([P, NE])).then_inc(s["loaded"], 16)

        @block.tensor
        def _(pe):
            pe.wait_ge(s["loaded"], 32)
            for b in range(TB):
                for kk in range(KD):
                    mm = pe.matmul(ps[:, 0, b * NE:(b + 1) * NE], k.h[:, kk, b * P:(b + 1) * P], wr[:, kk, :],
                                   start=(kk == 0), stop=(kk == KD - 1))
            mm.then_inc(s["logits_done"], 1)

        @block.scalar
        def _(act):
            act.wait_ge(s["vec_step"], 2)
            act.activation(probs[:], sel[:], ACT.Exp).then_inc(s["exp_done"], 1)

        @block.vector
        def _(dve):
            step = Steps(dve, s["vec_step"])

            def over(m, n):
                return m[:].rearrange("p (b o) -> p b o", o=1).to_broadcast([P, TB, n])

            dve.wait_ge(s["loaded"], 32)
            dve.wait_ge(s["logits_done"], 1)
            logits = ps[:, 0, 0:TB * NE].rearrange("p (b n) -> p b n", b=TB)
            step(dve.tensor_reduce(red[:], logits, AX.X, ALU.max))
            step(dve.tensor_tensor(sel[:], logits, over(red, NE), ALU.subtract))
            dve.wait_ge(s["exp_done"], 1)
            step(dve.tensor_reduce(red[:], probs[:], AX.X, ALU.add))
            step(dve.reciprocal(red[:], red[:]))
            step(dve.tensor_tensor(probs[:], probs[:], over(red, NE), ALU.mult))
            step(dve.tensor_tensor(sel[:], probs[:], br[:].rearrange("p (o n) -> p o n", o=1).to_broadcast([P, TB, NE]), ALU.add))

            def rank_in(rank, tmp, val, n, width):
                step(dve.memset(rank, 0.0))
                for a in range(n):
                    for b in range(n):
                        if a != b:
                            step(dve.tensor_tensor(tmp(a), val(b), val(a), ALU.is_ge if b < a else ALU.is_gt))
                            step(dve.tensor_tensor(rank_of(rank, a, n), rank_of(rank, a, n), tmp(a), ALU.add))

            def rank_of(m, a, n):
                return m.rearrange("p b (g n) -> p b g n", n=n)[:, :, :, a]

            rank_in(rank[:], lambda a: rank_of(cmp[:], a, EG), lambda a: rank_of(sel[:], a, EG), EG, GR)
            step(dve.tensor_scalar(rank[:], rank[:], float(2), None, ALU.is_lt))
            step(dve.tensor_tensor(top[:], sel[:], rank[:], ALU.mult))
            step(dve.tensor_reduce(score[:], top[:].rearrange("p b (g n) -> p b g n", n=EG), AX.X, ALU.add))
            rank_in(grank[:], lambda a: rank_of(gcmp[:], a, GR), lambda a: rank_of(score[:], a, GR), GR, 1)
            step(dve.tensor_scalar(grank[:], grank[:], 0.0, None, ALU.is_equal))
            for n in range(EG):
                step(dve.tensor_tensor(rank_of(rank[:], n, EG), rank_of(rank[:], n, EG), grank[:], ALU.mult))
            step(dve.tensor_tensor(share[:], probs[:], rank[:], ALU.mult))
            step(dve.tensor_reduce(red[:], share[:], AX.X, ALU.add))
            step(dve.reciprocal(red[:], red[:]))
            step(dve.tensor_tensor(share[:], share[:], over(red, NE), ALU.mult))
            assert step.n == ROUTER_STEPS, step.n


ROUTER_STEPS = 68


def dispatch_stage(k, m):
    ps = k.ps
    BIG = float(2 * NBLK * P)
    with k.stage("dispatch", "consts_ready", "pos_done", "vec_step", "h_turned", "h_copied", "h_stored", "zeros_stored",
                 "slots_ready") as (block, s, sb):
        earlier = sb("earlier", [P, P])
        ht = sb("ht", [P, TB, D])
        zeros = sb("zeros", [P, NBLK + 1], I32)
        tokens = sb("tokens", [P, TB], I32)
        block_no = sb("block_no", [1, NBLK])
        ones = sb("ones", [P, NE])
        cnt, used, cmp1, end, start = (sb(n, [P, NE]) for n in ("cnt", "used", "cmp1", "end", "start"))
        slot, low, cmp = (sb(n, [P, TB, NE]) for n in ("slot", "low", "cmp"))
        g = [sb(f"g{j}", [P, TB]) for j in range(2)]
        passed = sb("passed", [1, NBLK, NE])
        plan_f = sb("plan_f", [1, NBLK + 1])

        @block.sync
        def _(sp):
            k.clear(sp)
            sp.wait_ge(s["consts_ready"], 6)
            sp.dma_start(m.slot_token.rearrange("(p n) o -> p (n o)", p=P), zeros[:]).then_inc(s["zeros_stored"], 16)
            for b in range(TB):
                sp.wait_ge(s["h_copied"], 2 * b + 2)
                sp.dma_start(m.h_rows[b * P:(b + 1) * P, :], ht[:, b, :]).then_inc(s["h_stored"], 16)
            sp.wait_ge(s["h_stored"], 16 * TB)

        @block.gpsimd
        def _(pool):
            pool.memset(earlier[:], 1.0).then_inc(s["consts_ready"], 1)
            pool.memset(zeros[:], 0).then_inc(s["consts_ready"], 1)
            pool.memset(ones[:], 1.0).then_inc(s["consts_ready"], 1)
            pool.iota(tokens[:], pattern=[[P, TB]], base=0, channel_multiplier=1).then_inc(s["consts_ready"], 1)
            pool.iota(block_no[:], pattern=[[1, NBLK]], base=0, channel_multiplier=0,
                      allow_small_or_imprecise_dtypes=True).then_inc(s["consts_ready"], 1)
            pool.wait_ge(s["consts_ready"], 5)
            pool.affine_select(out=earlier[:], in_=earlier[:], compare_op=ALU.is_ge, fill=0.0, base=-1,
                               pattern=[[1, P]], channel_multiplier=-1).then_inc(s["consts_ready"], 1)
            pool.wait_ge(s["slots_ready"], 1)
            pool.wait_ge(s["zeros_stored"], 16)
            for j in range(2):
                for b in range(TB):
                    pool.indirect_dma_start(m.slot_token, bass.IndirectOffsetOnAxis(ap=m.slots[j][:, b:b + 1], axis=0),
                                            tokens[:, b:b + 1], None).then_inc(m.tokens_stored, 16)
            pool.wait_ge(m.tokens_stored, 16 * 2 * TB)

        @block.tensor
        def _(pe):
            pe.wait_ge(s["consts_ready"], 6)
            for b in range(TB):
                at = ps[:, 0, b * NE:(b + 1) * NE]
                for bb in range(b):
                    pe.matmul(at, k.ones[:], m.chosen[:, bb, :], start=(bb == 0), stop=False)
                pe.matmul(at, earlier[:], m.chosen[:, b, :], start=(b == 0), stop=True)
            for b in range(TB):
                mm = pe.matmul(ps[:, 1, 0:NE], k.ones[:], m.chosen[:, b, :], start=(b == 0), stop=(b == TB - 1))
            mm.then_inc(s["pos_done"], 1)
            for n in range(2 * TB):
                if n >= 4:
                    pe.wait_ge(s["h_copied"], n - 3)
                for j in range(4):
                    mm = pe.transpose(ps[:, 2 + n % 4, j * P:(j + 1) * P], k.h[:, n % 2 * 4 + j, n // 2 * P:(n // 2 + 1) * P], k.ident[:])
                mm.then_inc(s["h_turned"], 1)

        @block.scalar
        def _(act):
            for n in range(2 * TB):
                act.wait_ge(s["h_turned"], n + 1)
                act.activation(ht[:, n // 2, n % 2 * 512:(n % 2 + 1) * 512], ps[:, 2 + n % 4, :], ACT.Copy).then_inc(s["h_copied"], 1)

        @block.vector
        def _(dve):
            step = Steps(dve, s["vec_step"])

            def over(m2):
                return m2.rearrange("p (b o) -> p b o", o=1).to_broadcast([P, TB, NE])

            dve.wait_ge(s["consts_ready"], 6)
            dve.wait_ge(s["pos_done"], 1)
            step(dve.tensor_copy(cnt[:], ps[:, 1, 0:NE]))
            step(dve.tensor_scalar(used[:], cnt[:], 0.0, None, ALU.is_gt))
            for j in range(1, TB):
                step(dve.tensor_scalar(cmp1[:], cnt[:], float(j * P), None, ALU.is_gt))
                step(dve.tensor_tensor(used[:], used[:], cmp1[:], ALU.add))
            step(dve.tensor_tensor_scan(end[:], ones[:], used[:], 0.0, ALU.mult, ALU.add))
            step(dve.tensor_tensor(start[:], end[:], used[:], ALU.subtract))
            step(dve.tensor_scalar(start[:], start[:], float(P), None, ALU.mult))
            step(dve.tensor_tensor(slot[:], ps[:, 0, 0:TB * NE].rearrange("p (b n) -> p b n", b=TB),
                                   start[:].rearrange("p (o n) -> p o n", o=1).to_broadcast([P, TB, NE]), ALU.add))
            step(dve.tensor_scalar(low[:], m.chosen[:], -BIG, BIG, ALU.mult, ALU.add))
            step(dve.tensor_tensor(low[:], low[:], slot[:], ALU.add))
            step(dve.tensor_reduce(g[0][:], low[:], AX.X, ALU.min))
            step(dve.scalar_tensor_tensor(out=slot[:], in0=slot[:], scalar=1.0, in1=m.chosen[:], op0=ALU.add, op1=ALU.mult))
            step(dve.tensor_reduce(g[1][:], slot[:], AX.X, ALU.max))
            for j, of in enumerate((low, slot)):
                step(dve.tensor_tensor(cmp[:], of[:], over(g[j][:]), ALU.is_equal))
                step(dve.tensor_tensor(cmp[:], cmp[:], m.share[:], ALU.mult))
                step(dve.tensor_reduce(m.weights[j][:], cmp[:], AX.X, ALU.add))
            step(dve.tensor_scalar(g[1][:], g[1][:], -1.0, None, ALU.add))
            step(dve.tensor_copy(m.slots[0][:], g[0][:]))
            step(dve.tensor_copy(m.slots[1][:], g[1][:]))
            step(dve.tensor_tensor(passed[:], end[0:1, :].rearrange("p (o n) -> p o n", o=1).to_broadcast([1, NBLK, NE]),
                                   block_no[:].rearrange("p (n o) -> p n o", o=1).to_broadcast([1, NBLK, NE]), ALU.is_le))
            step(dve.tensor_reduce(plan_f[:, 0:NBLK], passed[:], AX.X, ALU.add))
            step(dve.tensor_scalar(plan_f[:, 0:NBLK], plan_f[:, 0:NBLK], float(NE - 1), None, ALU.min))
            step(dve.tensor_copy(plan_f[:, NBLK:], end[0:1, NE - 1:NE]))
            dve.tensor_copy(m.plan[:], plan_f[:]).then_inc(s["slots_ready"], 1)


class Dispatch:

    def __init__(self, k, stack):
        self.chosen = k.sb("chosen", [P, TB, NE], stack=stack)
        self.share = k.sb("share", [P, TB, NE], stack=stack)
        self.slots = [k.sb(f"slots{j}", [P, TB], I32, stack) for j in range(2)]
        self.weights = [k.sb(f"weights{j}", [P, TB], F32, stack) for j in range(2)]
        self.plan = k.sb("plan", [1, NBLK + 1], I32, stack)
        self.h_rows = k.nc.dram_tensor("h_rows", (T, D), F32, kind="Internal").ap()
        self.slot_token = k.nc.dram_tensor("slot_token", ((NBLK + 1) * P, 1), I32, kind="Internal").ap()
        self.y_rows = k.nc.dram_tensor("y_rows", (NBLK * P, D), F32, kind="Internal").ap()
        self.tokens_stored, self.gathered, *self.y_gathered = (
            k.stack.enter_context(k.nc.semaphore(n)) for n in ("tokens_stored", "gathered", *(f"y_gathered{b}" for b in range(TB))))


def experts_stage(k, m):
    ps = k.ps
    w1, w3, w2 = k.ins["w_exp_gate"][0], k.ins["w_exp_up"][0], k.ins["w_exp_down"][0]
    with k.stage("experts", "index_loaded", "loaded0", "loaded1", "loaded2", "x_turned", "x_copied", "gate_done", "up_done",
                 "sig_done", "gated", "hidden_done", "hidden_turned", "hidden_copied", "down_done", "index_used", "y_copied0", "y_copied1", "y_stored", "zeroed", "x_free",
                 primed=("gate_done", "up_done", "down_done", "x_turned", "x_copied", "hidden_turned", "y_copied0",
                         "y_copied1", "y_stored", "hidden_done")) as (block, s, sb):
        index = sb("index", [P, 1], I32)
        xg = sb("xg", [P, D])
        xt = sb("xt", [P, KD, P])
        sig, t, hidden = sb("sig", [P, DFF]), sb("t", [P, DFF]), sb("hidden", [P, DFF])
        ht = sb("ht", [P, KE, P])
        y = sb("y", [P, D])
        zeros = sb("zeros", [P, D])

        def in_use(eng):
            return eng.value_load(m.plan[0:1, NBLK:NBLK + 1], min_val=1, max_val=NBLK)

        @block.sync
        def _(sp):
            k.clear(sp)
            def load_index(n):
                sp.dma_start(index[:], m.slot_token[bass.ds(n * P, P), :]).then_inc(s["index_loaded"], 16)

            blocks = in_use(sp)
            load_index(0)
            with sp.Fori(0, NBLK) as n, sp.If(n < blocks):
                e = sp.value_load(m.plan[0:1, bass.ds(n, 1)], min_val=0, max_val=NE - 1)
                sp.wait_ge(s["gate_done"], 1 + n)
                sp.dma_start(strip(k, 0), w1[bass.ds(e, 1)].rearrange("e (k p) n -> p (e k) n", p=P)).then_inc(s["loaded0"], 16)
                sp.wait_ge(s["up_done"], 1 + n)
                sp.dma_start(strip(k, 1), w3[bass.ds(e, 1)].rearrange("e (k p) n -> p (e k) n", p=P)).then_inc(s["loaded1"], 16)
                sp.wait_ge(s["index_used"], n + 1)
                load_index(n + 1)
                sp.wait_ge(s["down_done"], 1 + 2 * n)
                sp.dma_start(strip(k, 2, KE), w2[bass.ds(e, 1)].rearrange("e (k p) n -> p (e k) n", p=P)).then_inc(s["loaded2"], 16)

        @block.gpsimd
        def _(pool):
            pool.memset(zeros[:], 0.0).then_inc(s["zeroed"], 1)
            blocks = in_use(pool)
            with pool.Fori(0, NBLK + 1) as n, pool.If(n <= blocks):
                pool.wait_ge(s["index_loaded"], 16 * (n + 1))
                pool.wait_ge(s["x_turned"], 1 + n)
                pool.sem_inc(s["x_free"], 1)
                pool.indirect_dma_start(xg[:], None, m.h_rows, bass.IndirectOffsetOnAxis(ap=index[:], axis=0)).then_inc(m.gathered, 16)
                pool.wait_ge(m.gathered, 16 * (n + 1))
                pool.sem_inc(s["index_used"], 1)

        @block.tensor
        def _(pe):
            def turn_rows(n):
                pe.wait_ge(m.gathered, 16 * (n + 1))
                pe.wait_ge(s["x_copied"], 1 + 2 * n)
                for c in range(KD):
                    mm = pe.transpose(ps[:, c // 4, c % 4 * P:(c % 4 + 1) * P], xg[:, c * P:(c + 1) * P], k.ident[:])
                mm.then_inc(s["x_turned"], 1)

            blocks = in_use(pe)
            turn_rows(0)
            with pe.Fori(0, NBLK) as n, pe.If(n < blocks):
                pe.wait_ge(s["x_copied"], 1 + 2 * (n + 1))
                pe.wait_ge(s["hidden_done"], 1 + n)
                for slot, done, loaded in ((0, "gate_done", "loaded0"), (1, "up_done", "loaded1")):
                    pe.wait_ge(s[loaded], 16 * (n + 1))
                    for kk in range(KD):
                        mm = pe.matmul(ps[:, 2 + slot, :], xt[:, kk, :], strip(k, slot)[:, kk, :], start=(kk == 0), stop=(kk == KD - 1))
                    mm.then_inc(s[done], 1)
                turn_rows(n + 1)
                pe.wait_ge(s["hidden_done"], 1 + n + 1)
                for f in range(KE):
                    mm = pe.transpose(ps[:, 4, f * P:(f + 1) * P], hidden[:, f * P:(f + 1) * P], k.ident[:])
                mm.then_inc(s["hidden_turned"], 1)
                pe.wait_ge(s["hidden_copied"], n + 1)
                pe.wait_ge(s["loaded2"], 16 * (n + 1))
                pe.wait_ge(s["y_copied0"], 1 + n)
                pe.wait_ge(s["y_copied1"], 1 + n)
                for half in range(2):
                    for f in range(KE):
                        mm = pe.matmul(ps[:, 5 + half, :], ht[:, f, :], strip(k, 2, KE)[:, f, half * STRIP:(half + 1) * STRIP],
                                       start=(f == 0), stop=(f == KE - 1))
                    mm.then_inc(s["down_done"], 1)

        @block.scalar
        def _(act):
            def copy_rows(n):
                act.wait_ge(s["x_turned"], 1 + n + 1)
                act.wait_ge(s["up_done"], 1 + n)
                act.activation(xt[:, 0:4, :], ps[:, 0, :].rearrange("p (c n) -> p c n", c=4), ACT.Copy).then_inc(s["x_copied"], 1)

            blocks = in_use(act)
            copy_rows(0)
            with act.Fori(0, NBLK) as n, act.If(n < blocks):
                act.wait_ge(s["gate_done"], 1 + n + 1)
                act.wait_ge(s["hidden_done"], 1 + n)
                act.activation(sig[:], ps[:, 2, :], ACT.Sigmoid).then_inc(s["sig_done"], 1)
                copy_rows(n + 1)
                act.wait_ge(s["hidden_turned"], 1 + n + 1)
                act.wait_ge(s["down_done"], 1 + 2 * n)
                act.activation(ht[:], ps[:, 4, :].rearrange("p (c n) -> p c n", c=KE), ACT.Copy).then_inc(s["hidden_copied"], 1)
                act.wait_ge(s["down_done"], 1 + 2 * n + 1)
                act.wait_ge(s["y_stored"], 1 + 16 * n)
                act.activation(y[:, 0:STRIP], ps[:, 5, :], ACT.Copy).then_inc(s["y_copied0"], 1)
                act.wait_ge(s["y_copied0"], 1 + n + 1)
                act.wait_ge(s["y_copied1"], 1 + n + 1)
                act.dma_start(m.y_rows[bass.ds(n * P, P), :], y[:]).then_inc(s["y_stored"], 16)
            act.wait_ge(s["zeroed"], 1)
            with act.Fori(0, NBLK) as n, act.If(n >= blocks):
                act.dma_start(m.y_rows[bass.ds(n * P, P), :], zeros[:]).then_inc(s["y_stored"], 16)
            act.wait_ge(s["y_stored"], 1 + 16 * NBLK)

        @block.vector
        def _(dve):
            def copy_rows(n):
                dve.wait_ge(s["x_turned"], 1 + n + 1)
                dve.wait_ge(s["up_done"], 1 + n)
                dve.tensor_copy(xt[:, 4:8, :], ps[:, 1, :].rearrange("p (c n) -> p c n", c=4)).then_inc(s["x_copied"], 1)

            blocks = in_use(dve)
            copy_rows(0)
            with dve.Fori(0, NBLK) as n, dve.If(n < blocks):
                dve.wait_ge(s["sig_done"], n + 1)
                dve.tensor_tensor(t[:], ps[:, 2, :], sig[:], ALU.mult).then_inc(s["gated"], 1)
                dve.wait_ge(s["gated"], n + 1)
                dve.wait_ge(s["up_done"], 1 + n + 1)
                dve.wait_ge(s["hidden_turned"], 1 + n)
                dve.tensor_tensor(hidden[:], t[:], ps[:, 3, :], ALU.mult).then_inc(s["hidden_done"], 1)
                copy_rows(n + 1)
                dve.wait_ge(s["down_done"], 1 + 2 * n + 2)
                dve.wait_ge(s["y_stored"], 1 + 16 * n)
                dve.tensor_copy(y[:, STRIP:], ps[:, 6, :]).then_inc(s["y_copied1"], 1)


def combine_stage(k, m, gate):
    ps = k.ps
    with k.stage("combine", "weighed", "turned", "scaled", "vec_step", "added") as (block, s, sb):
        rows = [sb(f"rows{j}", [P, TB, D]) for j in range(2)]
        t = sb("t", [P, 2, T])

        @block.sync
        def _(sp):
            k.clear(sp)

        @block.gpsimd
        def _(pool):
            for b in range(TB):
                for j in range(2):
                    pool.indirect_dma_start(rows[j][:, b, :], None, m.y_rows,
                                            bass.IndirectOffsetOnAxis(ap=m.slots[j][:, b:b + 1], axis=0)).then_inc(m.y_gathered[b], 16)

        @block.vector
        def _(dve):
            step = Steps(dve, s["vec_step"])
            for b in range(TB):
                dve.wait_ge(m.y_gathered[b], 32)
                step(dve.tensor_scalar(rows[0][:, b, :], rows[0][:, b, :], m.weights[0][:, b:b + 1], None, ALU.mult))
                dve.scalar_tensor_tensor(out=rows[0][:, b, :], in0=rows[1][:, b, :], scalar=m.weights[1][:, b:b + 1], in1=rows[0][:, b, :],
                                         op0=ALU.mult, op1=ALU.add).then_inc(s["weighed"], 1)
            for c in range(KD):
                dve.wait_ge(s["scaled"], c + 1)
                dve.scalar_tensor_tensor(out=k.x[:, c, :], in0=k.x[:, c, :], scalar=ALPHA_1, in1=t[:, c % 2, :], op0=ALU.mult,
                                         op1=ALU.add).then_inc(s["added"], 1)

        @block.tensor
        def _(pe):
            for b in range(TB):
                pe.wait_ge(s["weighed"], b + 1)
                for c in range(KD):
                    mm = pe.transpose(ps[:, c, b * P:(b + 1) * P], rows[0][:, b, c * P:(c + 1) * P], k.ident[:])
                    if b == TB - 1:
                        mm.then_inc(s["turned"], 1)
            sum_channels(k, pe, lambda c: pe.wait_ge(s["added"], c + 1))

        @block.scalar
        def _(act):
            for c in range(KD):
                act.wait_ge(s["turned"], c + 1)
                if c >= 2:
                    act.wait_ge(s["added"], c - 1)
                act.activation(t[:, c % 2, :], ps[:, c, :], ACT.Copy, scale=k.mod[:, gate + c:gate + c + 1]).then_inc(s["scaled"], 1)


def output_stage(k, out):
    ps = k.ps
    with k.stage("output", "turned", "copied", "stored") as (block, s, sb):
        xt = sb("xt", [P, TB, D])

        @block.tensor
        def _(pe):
            for n in range(2 * TB):
                if n >= 4:
                    pe.wait_ge(s["copied"], n - 3)
                for j in range(4):
                    mm = pe.transpose(ps[:, n % 4, j * P:(j + 1) * P], k.x[:, n % 2 * 4 + j, n // 2 * P:(n // 2 + 1) * P], k.ident[:])
                mm.then_inc(s["turned"], 1)

        @block.scalar
        def _(act):
            for n in range(2 * TB):
                act.wait_ge(s["turned"], n + 1)
                act.activation(xt[:, n // 2, n % 2 * 512:(n % 2 + 1) * 512], ps[:, n % 4, :], ACT.Copy).then_inc(s["copied"], 1)

        @block.sync
        def _(sp):
            k.clear(sp)
            for b in range(TB):
                sp.wait_ge(s["copied"], 2 * b + 2)
                sp.dma_start(out[0, b * P:(b + 1) * P, :], xt[:, b, :]).then_inc(s["stored"], 16)
            sp.wait_ge(s["stored"], 16 * TB)


def reduced_angle(step, dve, out, turns, angle, offset):
    step(dve.tensor_scalar(turns, angle, 1.0 / TWO_PI, offset / TWO_PI, ALU.mult, ALU.add))
    step(dve.tensor_scalar(turns, turns, ROUND, -ROUND, ALU.add, ALU.add))
    step(dve.scalar_tensor_tensor(out=out, in0=turns, scalar=-PI_A, in1=angle, op0=ALU.mult, op1=ALU.add))
    step(dve.scalar_tensor_tensor(out=out, in0=turns, scalar=-PI_B, in1=out, op0=ALU.mult, op1=ALU.add))
    step(dve.scalar_tensor_tensor(out=out, in0=turns, scalar=-PI_C, in1=out, op0=ALU.mult, op1=ALU.add))
    step(dve.tensor_scalar(out, out, offset, None, ALU.add))
    step(dve.tensor_scalar(out, out, PI_SAFE, -PI_SAFE, ALU.min, ALU.max))


def latent_stage(k, cq, ckv, k_pe, cos, sin):
    ps, w = k.ps, k.ins["mla_w_in_2"][0]
    width = QL + KVL + ROPE
    half = ROPE // 2
    with k.stage("latent", "loaded", "freq_ready", "pos_ready", "angle_done", "vec_step", "sin_done", "proj_done", "sq_done", "ms_done",
                 "std_done") as (block, s, sb):
        wl = k.w[:, 0, 0:KD * width].rearrange("p (k n) -> p k n", k=KD)
        pos_i, pos = sb("pos_i", [1, T], I32), sb("pos", [1, T])
        freq = sb("freq", [1, ROPE])
        angle, turns = sb("angle", [ROPE, T]), sb("turns", [ROPE, T])
        sq = sb("sq", [P, 3, T])
        std = sb("std", [P, 2, T])
        raw, swapped = sb("raw", [ROPE, T]), sb("swapped", [ROPE, T])
        NORMS = ((QL, 0, 2, "mla_q_norm_2"), (KVL, 2, 1, "mla_kv_norm_2"))

        @block.sync
        def _(sp):
            k.clear(sp)
            sp.dma_start(pos_i[:], k.ins["positions_2"]).then_inc(s["loaded"], 16)
            sp.dma_start(wl, w.rearrange("(k p) n -> p k n", p=P)).then_inc(s["loaded"], 16)

        @block.gpsimd
        def _(pool):
            for j in range(ROPE):
                pool.memset(freq[:, j:j + 1], ROPE_THETA ** (-2.0 * (j % half) / ROPE)).then_inc(s["freq_ready"], 1)

        @block.tensor
        def _(pe):
            pe.wait_ge(s["freq_ready"], ROPE)
            pe.wait_ge(s["pos_ready"], 1)
            pe.matmul(ps[0:ROPE, 0, :], freq[:], pos[:], start=True, stop=True).then_inc(s["angle_done"], 1)
            pe.wait_ge(s["loaded"], 32)
            for c in range(4):
                n = P if c < 3 else ROPE
                for kk in range(KD):
                    mm = pe.matmul(ps[0:n, 1 + c, :], wl[:, kk, c * P:c * P + n], k.h[:, kk, :], start=(kk == 0), stop=(kk == KD - 1))
                mm.then_inc(s["proj_done"], 1)
            for j, (_, first, n, _) in enumerate(NORMS):
                pe.wait_ge(s["sq_done"], first + n)
                for c in range(n):
                    mm = pe.matmul(ps[:, 5 + j, :], k.ones[:], sq[:, first + c, :], start=(c == 0), stop=(c == n - 1))
                mm.then_inc(s["ms_done"], 1)

        @block.scalar
        def _(act):
            act.wait_ge(s["vec_step"], 15)
            act.activation(sin[:], angle[:], ACT.Sin).then_inc(s["sin_done"], 1)
            act.activation(cos[:], cos[:], ACT.Sin).then_inc(s["sin_done"], 1)
            for c in range(3):
                act.wait_ge(s["proj_done"], c + 1)
                act.activation(sq[:, c, :], ps[:, 1 + c, :], ACT.Square).then_inc(s["sq_done"], 1)
            for j, (width_j, *_) in enumerate(NORMS):
                act.wait_ge(s["ms_done"], j + 1)
                act.activation(std[:, j, :], ps[:, 5 + j, :], ACT.Sqrt, scale=1.0 / width_j, bias=k.eps_rms[:]).then_inc(s["std_done"], 1)

        @block.vector
        def _(dve):
            step = Steps(dve, s["vec_step"])
            dve.wait_ge(s["loaded"], 32)
            dve.tensor_copy(pos[:], pos_i[:]).then_inc(s["pos_ready"], 1)
            dve.wait_ge(s["angle_done"], 1)
            step(dve.tensor_copy(raw[:], ps[0:ROPE, 0, :]))
            reduced_angle(step, dve, angle[:], turns[:], raw[:], 0.0)
            reduced_angle(step, dve, cos[:], turns[:], raw[:], math.pi / 2)
            dve.wait_ge(s["sin_done"], 2)
            step(dve.tensor_scalar(sin[0:half, :], sin[0:half, :], -1.0, None, ALU.mult))
            dve.wait_ge(s["proj_done"], 4)
            rotate(step, dve, k_pe, ps[0:ROPE, 4, :], raw, swapped, cos, sin, 1.0)
            for j, (_, first, n, norm) in enumerate(NORMS):
                dve.wait_ge(s["std_done"], j + 1)
                step(dve.reciprocal(std[:, j, :], std[:, j, :]))
                for c in range(n):
                    dst = cq[:, c, :] if j == 0 else ckv[:]
                    step(dve.scalar_tensor_tensor(out=dst, in0=ps[:, 1 + first + c, :], scalar=k.col(norm, c), in1=std[:, j, :],
                                                  op0=ALU.mult, op1=ALU.mult))


ROPE_THETA = 10000.0


def rotate(step, dve, out, src, raw, swapped, cos, sin, scale, last=None):
    half = ROPE // 2
    step(dve.tensor_scalar(swapped[0:half, :], src[half:ROPE], scale, None, ALU.mult))
    step(dve.tensor_scalar(swapped[half:ROPE, :], src[0:half], scale, None, ALU.mult))
    step(dve.tensor_tensor(swapped[:], swapped[:], sin[:], ALU.mult))
    step(dve.scalar_tensor_tensor(out=raw[:], in0=src, scalar=scale, in1=cos[:], op0=ALU.mult, op1=ALU.mult))
    ins = dve.tensor_tensor(out[:], raw[:], swapped[:], ALU.add)
    if last is None:
        step(ins)
    else:
        ins.then_inc(last, 1)


def latent_attention_stage(k, cq, ckv, k_pe, cos, sin, o):
    ps = k.ps
    scale = 1.0 / math.sqrt(NOPE + ROPE)
    nq = QL // P
    with k.stage("latent_attention", "w_loaded", "qn_done", "qp_done", "kn_done", "v_done", "copied", "q_turned", "rope_step", *SOFTMAX, primed=("copied", "exp_done", "o_copied", "scores_done", "v_done", "weighed")) as (block, s, sb):
        wq, wkv = sb("wq", [P, nq, NOPE + ROPE]), sb("wkv", [P, NOPE + VD])
        qn, kn, qp = sb("qn", [P, T]), sb("kn", [P, T]), sb("qp", [ROPE, T])
        raw, swapped = sb("raw", [ROPE, T]), sb("swapped", [ROPE, T])
        v = sb("v", [P, TB, VD])
        p_tiles, pt_tiles = sb("p_tiles", [P, 3, T]), sb("pt_tiles", [P, 2, T])
        nmax, rsum, rinv = sb("nmax", [P, TB]), sb("rsum", [P, TB]), sb("rinv", [P, TB])
        units = [(slice(0, VD), b) for b in range(TB)]

        def scores(pe, unit, bank):
            b = unit[1]
            n = (b + 1) * P
            pe.matmul(ps[:, bank, 0:n], qn[:, b * P:n], kn[:, 0:n], start=True, stop=False)
            return pe.matmul(ps[:, bank, 0:n], qp[:, b * P:n], k_pe[:, 0:n], start=False, stop=True)

        tensor, vector, scalar = scan_softmax(k, s, units, scores, p_tiles, pt_tiles, lambda unit, kb: v[:, kb, :], nmax, rsum, rinv)

        @block.sync
        def _(sp):
            k.clear(sp)
            with sp.Fori(0, MLA_HEADS) as i:
                sp.wait_ge(s["v_done"], 1 + i)
                sp.dma_start(wq[:], columns(k.ins["mla_w_qb_2"][0], i * (NOPE + ROPE), NOPE + ROPE)).then_inc(s["w_loaded"], 16)
                sp.dma_start(wkv[:], k.ins["mla_w_kvb_2"][0][:, bass.ds(i * (NOPE + VD), NOPE + VD)]).then_inc(s["w_loaded"], 16)

        @block.tensor
        def _(pe):
            with pe.Fori(0, MLA_HEADS) as i:
                pe.wait_ge(s["w_loaded"], 32 * (i + 1))
                pe.wait_ge(s["copied"], 1 + 3 * i)
                for c in range(nq):
                    mm = pe.matmul(ps[0:ROPE, 7, :], wq[:, c, NOPE:], cq[:, c, :], start=(c == 0), stop=(c == nq - 1))
                mm.then_inc(s["qp_done"], 1)
                for c in range(nq):
                    mm = pe.matmul(ps[:, 6, :], wq[:, c, 0:NOPE], cq[:, c, :], start=(c == 0), stop=(c == nq - 1))
                mm.then_inc(s["qn_done"], 1)
                pe.matmul(ps[:, 4, :], wkv[:, 0:NOPE], ckv[:], start=True, stop=True).then_inc(s["kn_done"], 1)
                for b in range(TB):
                    mm = pe.matmul(ps[:, 3, b * P:(b + 1) * P], ckv[:, b * P:(b + 1) * P], wkv[:, NOPE:], start=True, stop=True)
                mm.then_inc(s["v_done"], 1)
                pe.wait_ge(s["q_turned"], i + 1)
                pe.wait_ge(s["copied"], 1 + 3 * i + 3)
                tensor(pe, i)

        @block.scalar
        def _(act):
            with act.Fori(0, MLA_HEADS) as i:
                act.wait_ge(s["qn_done"], i + 1)
                act.wait_ge(s["weighed"], 1 + TB * i)
                act.activation(qn[:], ps[:, 6, :], ACT.Copy, scale=scale).then_inc(s["copied"], 1)
                act.wait_ge(s["kn_done"], i + 1)
                act.activation(kn[:], ps[:, 4, :], ACT.Copy).then_inc(s["copied"], 1)
                act.wait_ge(s["v_done"], 1 + i + 1)
                act.activation(v[:], ps[:, 3, :].rearrange("p (b n) -> p b n", b=TB), ACT.Copy).then_inc(s["copied"], 1)
                scalar(act, i)

        @block.vector
        def _(dve):
            with dve.Fori(0, MLA_HEADS) as i:
                step = Steps(dve, s["rope_step"], 4 * i)
                dve.wait_ge(s["qp_done"], i + 1)
                dve.wait_ge(s["scores_done"], 1 + TB * i)
                rotate(step, dve, qp, ps[0:ROPE, 7, :], raw, swapped, cos, sin, scale, s["q_turned"])
                assert step.n == 4
                n = vector(dve, i)
                assert n == 2 * TB
                dve.wait_ge(s["weighed"], 1 + TB * (i + 1))
                dve.tensor_copy(o[:, bass.ds(i, 1), :], ps[:, 5:6, :]).then_inc(s["o_copied"], 1)


def mlp_stage(k, name, layer, first):
    ps, w1, w2 = k.ps, k.ins["mlp_w1_2"][layer], k.ins["mlp_w2_2"][layer]
    STEPS = 2
    HK = K2 // STEPS
    UP = HK // HT
    N = 2 * UP
    b1 = k.places["mlp_b1_2"][0] + layer * K2
    gate = first + 2 * KD
    with k.stage(name, "h_done", "consts_done", "relu_done", "squared", "hidden_high", "hidden_low", "vec_step", *SplitProducts.SEMS,
                 primed=SplitProducts.PRIMED + ("relu_done", "squared", "hidden_high", "hidden_low", "vec_step")) as (block, s, sb):
        mul = SplitProducts(k, s, sb)
        h_parts = sb("h_parts", [P, 2, KD, T], F32R)
        hidden = sb("hidden", [P, 2, HK, T], F32R)
        h = sb("h", [P, 4, T])
        r, q = sb("r", [P, 2, T]), sb("q", [P, 2, T])
        bias2, keep = sb("bias2", [P, STEPS * KD]), sb("keep", [P, STEPS])
        bank_of = lambda n, f: (n % 2 * HT + f) if n < UP else 4 + ((n - UP) // 2 % 2) * HT + f

        @block.sync
        def _(sp):
            k.clear(sp)
            with sp.Fori(0, STEPS) as i:
                for n in range(N):
                    if n < UP:
                        src = columns(w1, i * (HK * P) + n * HALF, HALF)
                    else:
                        g, chunk = (n - UP) // 2, (n - UP) % 2
                        src = w2[bass.ds(i * (HK * P) + chunk * D, D), g * HALF:(g + 1) * HALF].rearrange("(k p) n -> p k n", p=P)
                    mul.load(sp, n, src, N * i)

        @block.tensor
        def _(pe):
            with pe.Fori(0, STEPS) as i:
                for n in range(N):
                    outs = [ps[:, bank_of(n, f), :] for f in range(HT)]
                    if n < UP:
                        if n >= 2:
                            pe.wait_ge(s["relu_done"], 1 + HK * i + HT * (n - 1))
                        mul.products(pe, n, h_parts, outs, N * i, arriving=(n == 0))
                    else:
                        g, chunk = (n - UP) // 2, (n - UP) % 2
                        pe.wait_ge(s["hidden_low"], 1 + HK * i + KD * (chunk + 1))
                        if chunk == 0:
                            pe.wait_ge(s["vec_step"], 1 + 2 * KD * i + (2 * HT * (g - 1) if g >= 2 else 0))
                        mul.products(pe, n, hidden[:, :, chunk * KD:(chunk + 1) * KD, :], outs, N * i, chunk == 0, chunk == 1)
            sum_channels(k, pe, lambda c: pe.wait_ge(s["vec_step"], 1 + 2 * KD * (STEPS - 1) + 2 * (c + 1)))

        @block.scalar
        def _(act):
            for c in range(KD):
                if c >= 4:
                    act.wait_ge(s["x_low"], c - 3)
                act.activation(h[:, c % 4, :], k.x[:, c, :], ACT.Identity, scale=k.mod[:, first + KD + c:first + KD + c + 1],
                               bias=k.mod[:, first + c:first + c + 1]).then_inc(s["h_done"], 1)
            with act.Fori(0, STEPS) as i:
                def high(n):
                    mul.high(act, n, N * i, N // 4 * i)

                def relu(n):
                    act.wait_ge(s["half_used"], 1 + N * i + n + 1)
                    for c in range(n * HT, (n + 1) * HT):
                        act.wait_ge(s["squared"], 1 + HK * i + max(c - 1, 0))
                        act.activation(r[:, c % 2, :], ps[:, bank_of(n, c % HT), :], ACT.Relu,
                                       bias=k.cols[:, bass.ds(b1 + HK * i + c, 1)]).then_inc(s["relu_done"], 1)

                def hidden_high(n):
                    if n == 0:
                        act.wait_ge(s["half_used"], 1 + N * i)
                    for c in range(n * HT, (n + 1) * HT):
                        act.wait_ge(s["squared"], 1 + HK * i + c + 1)
                        act.activation(hidden[:, 0, c], q[:, c % 2, :], ACT.Copy).then_inc(s["hidden_high"], 1)

                high(0)
                high(1)
                for n in range(N):
                    if n < UP:
                        relu(n)
                    if n + 2 < N:
                        high(n + 2)
                    if n < UP:
                        hidden_high(n)

        @block.vector
        def _(dve):
            def h_high(c):
                dve.wait_ge(s["h_done"], c + 1)
                dve.tensor_copy(h_parts[:, 0, c], h[:, c % 4, :]).then_inc(s["x_high"], 1)

            h_high(0)
            for c in range(KD):
                if c + 1 < KD:
                    h_high(c + 1)
                dve.wait_ge(s["x_high"], c + 1)
                dve.tensor_tensor(h_parts[:, 1, c], h[:, c % 4, :], h_parts[:, 0, c].bitcast(F32), ALU.subtract).then_inc(s["x_low"], 1)
            dve.wait_ge(s["consts_done"], 4)
            with dve.Fori(0, STEPS) as i:
                step = Steps(dve, s["vec_step"], 1 + 2 * KD * i)

                def square(n):
                    for c in range(n * HT, (n + 1) * HT):
                        dve.wait_ge(s["relu_done"], 1 + HK * i + c + 1)
                        dve.wait_ge(s["hidden_low"], 1 + HK * i + max(c - 1, 0))
                        dve.tensor_tensor(q[:, c % 2, :], r[:, c % 2, :], r[:, c % 2, :], ALU.mult).then_inc(s["squared"], 1)

                def hidden_low(n):
                    for c in range(n * HT, (n + 1) * HT):
                        dve.wait_ge(s["hidden_high"], 1 + HK * i + c + 1)
                        dve.tensor_tensor(hidden[:, 1, c], q[:, c % 2, :], hidden[:, 0, c].bitcast(F32), ALU.subtract).then_inc(s["hidden_low"], 1)

                def add(n):
                    g = (n - UP) // 2
                    dve.wait_ge(s["half_used"], 1 + N * i + n + 1)
                    for c in range(g * HT, (g + 1) * HT):
                        step(dve.tensor_scalar(h[:, c % 2, :], ps[:, bank_of(n, c % HT), :], bias2[:, bass.ds(KD * i + c, 1)],
                                               k.mod[:, gate + c:gate + c + 1], ALU.add, ALU.mult))
                        step(dve.scalar_tensor_tensor(out=k.x[:, c, :], in0=k.x[:, c, :], scalar=keep[:, bass.ds(i, 1)],
                                                      in1=h[:, c % 2, :], op0=ALU.mult, op1=ALU.add))

                mul.low(dve, 0, N * i)
                mul.low(dve, 1, N * i)
                for n in range(N):
                    if n < UP:
                        square(n)
                    if n + 2 < N:
                        mul.low(dve, n + 2, N * i)
                    if n < UP:
                        hidden_low(n)
                    elif (n - UP) % 2:
                        add(n)

        @block.gpsimd
        def _(pool):
            at = k.places["mlp_b2_2"][0] + layer * KD
            pool.memset(bias2[:, KD:], 0.0).then_inc(s["consts_done"], 1)
            pool.tensor_copy(bias2[:, 0:KD], k.cols[:, at:at + KD]).then_inc(s["consts_done"], 1)
            pool.memset(keep[:, 0:1], ALPHA_2).then_inc(s["consts_done"], 1)
            pool.memset(keep[:, 1:2], 1.0).then_inc(s["consts_done"], 1)


SB = 32


class S5Tables:

    def __init__(self, sb):
        self.mag = sb("mag", [P, S5_TILES])
        self.turn_b = sb("turn_b", [P, 2, S5_TILES, SB])
        self.turn_a = sb("turn_a", [P, 2, S5_TILES, T // SB + 1])
        self.b_t = sb("b_t", [P, 2, KD, P])
        self.c_t = sb("c_t", [P, 3, KD, P])


def s5_tables_stage(k, tab):
    ps = k.ps
    J = S5_TILES
    with k.stage("s5_tables", "loaded", "exp_done", "vec_step", "b_ready", "c_ready", "zeroed", "b_turned", "b_copied", "c_turned", "c_copied") as (block, s, sb):
        dt, angle, turns = sb("dt", [P, J]), sb("angle", [P, J]), sb("turns", [P, J])
        rs, rc = sb("rs", [P, J]), sb("rc", [P, J])
        t1, t2 = sb("t1", [P, J]), sb("t2", [P, J])
        c_re, c_im = sb("coef_re", [P, J]), sb("coef_im", [P, J])
        b_raw = sb("b_raw", [P, 2, J, GC])
        b_tmp = sb("b_tmp", [P, J, GC])
        b_out = sb("b_out", [P, J, GC])
        b_bd = sb("b_bd", [P, 2, J, 2 * GC])
        c_raw = sb("c_raw", [P, 2, KD, STATE])
        c_bd = sb("c_bd", [P, 2, KD, 2 * STATE])
        odd = sb("odd", [P, 2])
        tmp = sb("tmp", [P, J, SB])
        lr = k.cols[:, k.places["ssm_a_re_2"][0]:k.places["ssm_a_re_2"][0] + J]
        li = k.cols[:, k.places["ssm_a_im_2"][0]:k.places["ssm_a_im_2"][0] + J]

        @block.sync
        def _(sp):
            k.clear(sp)
            for half in range(2):
                sp.dma_start(dt[half * STATE:(half + 1) * STATE, :],
                             k.ins["ssm_log_dt_2"].rearrange("l (j two) -> two l j", two=2)[half].to_broadcast([STATE, J]),
                             allow_slow_non_contiguous=True).then_inc(s["loaded"], 16)
            for j, name in enumerate(("ssm_b_re_2", "ssm_b_im_2")):
                sp.dma_start(b_raw[:, j], k.ins[name][0].rearrange("(j two) s c -> (two s) j c", two=2)).then_inc(s["loaded"], 16)
            for j, name in enumerate(("ssm_c_re_2", "ssm_c_im_2")):
                sp.dma_start(c_raw[:, j], k.ins[name][0].rearrange("(k g) c s -> (g c) k s", k=KD)).then_inc(s["loaded"], 16)

        @block.gpsimd
        def _(pool):
            pool.memset(b_bd[:], 0.0).then_inc(s["zeroed"], 1)
            pool.memset(tab.turn_a[:, 0, :, 0:1], 1.0).then_inc(s["zeroed"], 1)
            pool.memset(tab.turn_a[:, 1, :, 0:1], 0.0).then_inc(s["zeroed"], 1)

        @block.scalar
        def _(act):
            act.wait_ge(s["loaded"], 96)
            act.activation(dt[:], dt[:], ACT.Exp).then_inc(s["exp_done"], 1)
            act.wait_ge(s["vec_step"], 2)
            act.activation(tab.mag[:], t1[:], ACT.Exp).then_inc(s["exp_done"], 1)
            act.wait_ge(s["vec_step"], 16)
            act.activation(rs[:], rs[:], ACT.Sin).then_inc(s["exp_done"], 1)
            act.activation(rc[:], rc[:], ACT.Sin).then_inc(s["exp_done"], 1)
            for n in range(2 * KD):
                if n % 4 == 0:
                    act.wait_ge(s["b_turned"], n // 4 + 1)
                    act.activation(tab.b_t[:, n // 8, n % 8:n % 8 + 4, :], ps[:, n // 4, :].rearrange("p (b n) -> p b n", b=4),
                                   ACT.Copy).then_inc(s["b_copied"], 1)
            for n in range(4):
                act.wait_ge(s["c_turned"], n + 1)
                src = ps[:, 4 + n, :].rearrange("p (b n) -> p b n", b=4)
                at = n % 2 * 4
                if n < 2:
                    act.activation(tab.c_t[:, 0, at:at + 4, :], src, ACT.Copy).then_inc(s["c_copied"], 1)
                act.activation(tab.c_t[:, 1 if n < 2 else 2, at:at + 4, :], src, ACT.Copy, scale=-1.0).then_inc(s["c_copied"], 1)

        @block.tensor
        def _(pe):
            pe.wait_ge(s["b_ready"], 4)
            for n in range(2 * KD):
                mm = pe.transpose(ps[:, n // 4, n % 4 * P:(n % 4 + 1) * P],
                                  b_bd[:, n // 8, n % 8 * 4:n % 8 * 4 + 4, :].rearrange("p j c -> p (j c)"), k.ident[:])
                if n % 4 == 3:
                    mm.then_inc(s["b_turned"], 1)
            pe.wait_ge(s["c_ready"], 4)
            for n in range(2 * KD):
                mm = pe.transpose(ps[:, 4 + n // 4, n % 4 * P:(n % 4 + 1) * P], c_bd[:, n // 8, n % 8, :], k.ident[:])
                if n % 4 == 3:
                    mm.then_inc(s["c_turned"], 1)

        @block.vector
        def _(dve):
            step = Steps(dve, s["vec_step"])
            dve.wait_ge(s["exp_done"], 1)
            step(dve.tensor_tensor(angle[:], li, dt[:], ALU.mult))
            step(dve.tensor_tensor(t1[:], lr, dt[:], ALU.mult))
            reduced_angle(step, dve, rs[:], turns[:], angle[:], 0.0)
            reduced_angle(step, dve, rc[:], turns[:], angle[:], math.pi / 2)
            dve.wait_ge(s["exp_done"], 4)
            step(dve.tensor_tensor(t1[:], tab.mag[:], rc[:], ALU.mult))
            step(dve.tensor_scalar(t1[:], t1[:], -1.0, None, ALU.add))
            step(dve.tensor_tensor(t2[:], tab.mag[:], rs[:], ALU.mult))
            step(dve.tensor_tensor(c_re[:], t1[:], lr, ALU.mult))
            step(dve.tensor_tensor(turns[:], t2[:], li, ALU.mult))
            step(dve.tensor_tensor(c_re[:], c_re[:], turns[:], ALU.add))
            step(dve.tensor_tensor(c_im[:], t2[:], lr, ALU.mult))
            step(dve.tensor_tensor(turns[:], t1[:], li, ALU.mult))
            step(dve.tensor_tensor(c_im[:], c_im[:], turns[:], ALU.subtract))
            step(dve.tensor_tensor(t1[:], lr, lr, ALU.mult))
            step(dve.tensor_tensor(t2[:], li, li, ALU.mult))
            step(dve.tensor_tensor(t1[:], t1[:], t2[:], ALU.add))
            step(dve.reciprocal(t1[:], t1[:]))
            step(dve.tensor_tensor(c_re[:], c_re[:], t1[:], ALU.mult))
            step(dve.tensor_tensor(c_im[:], c_im[:], t1[:], ALU.mult))

            def over(m, n):
                return m.rearrange("p (j o) -> p j o", o=1).to_broadcast([P, J, n])

            dve.wait_ge(s["zeroed"], 3)
            for out, (a, b), op in ((0, (c_re, c_im), ALU.subtract), (1, (c_im, c_re), ALU.add)):
                step(dve.tensor_tensor(b_out[:], b_raw[:, 0], over(a[:], GC), ALU.mult))
                step(dve.tensor_tensor(b_tmp[:], b_raw[:, 1], over(b[:], GC), ALU.mult))
                for half in range(2):
                    rows = slice(half * STATE, (half + 1) * STATE)
                    dve.tensor_tensor(b_bd[rows, out, :, half * GC:(half + 1) * GC], b_out[rows], b_tmp[rows], op).then_inc(s["b_ready"], 1)
                dve.wait_ge(s["b_ready"], 2 * out + 2)
            step(dve.tensor_reduce(odd[:, 1:2], k.ident[:].rearrange("p (j two c) -> p j two c", two=2, c=GC)[:, :, 1, :], AX.XY, ALU.add))
            step(dve.tensor_scalar(odd[:, 0:1], odd[:, 1:2], -1.0, 1.0, ALU.mult, ALU.add))
            for j in range(2):
                for half in range(2):
                    dve.tensor_scalar(c_bd[:, j, :, half * STATE:(half + 1) * STATE], c_raw[:, j], odd[:, half:half + 1], None,
                                      ALU.mult).then_inc(s["c_ready"], 1)

            def times(out, n, at, a, first):
                re, im = a[:, 0, :, first:first + n], a[:, 1, :, first:first + n]
                wr, wi = (a[:, j, :, at - 1:at].to_broadcast([P, J, n]) for j in range(2))
                ore, oim = out[:, 0, :, at:at + n], out[:, 1, :, at:at + n]
                step(dve.tensor_tensor(ore, re, wr, ALU.mult))
                step(dve.tensor_tensor(tmp[:, :, 0:n], im, wi, ALU.mult))
                step(dve.tensor_tensor(ore, ore, tmp[:, :, 0:n], ALU.subtract))
                step(dve.tensor_tensor(oim, re, wi, ALU.mult))
                step(dve.tensor_tensor(tmp[:, :, 0:n], im, wr, ALU.mult))
                step(dve.tensor_tensor(oim, oim, tmp[:, :, 0:n], ALU.add))

            for j, m in enumerate((rc, rs)):
                step(dve.tensor_copy(tab.turn_b[:, j, :, 0:1], m[:].rearrange("p (j o) -> p j o", o=1)))
            n = 1
            while n < SB:
                times(tab.turn_b, n, n, tab.turn_b, 0)
                n *= 2
            for j in range(2):
                step(dve.tensor_copy(tab.turn_a[:, j, :, 1:2], tab.turn_b[:, j, :, SB - 1:SB]))
            n = 1
            while n < T // SB:
                times(tab.turn_a, n, n + 1, tab.turn_a, 1)
                n *= 2


def s5_scan_stage(k, tab, u, g):
    ps = k.ps
    NT = S5_TILES // KD
    GELU = 2 * math.sqrt(2 / math.pi)
    VEC, TABLE_STEPS = NT * 9, 6
    A = T // 32
    with k.stage("s5_scan", "staged", "c_staged", "bu_done", "table_step", "table_done", "vec_step", "products_done", "table_used", "y_done", "y_out",
                 "sq_done", "inner_done", "sig_done", "g_done", primed=("table_used", "y_out", "bu_done", "y_done") + ("products_done",) * NT) as (block, s, sb):
        uk, bk, ck = sb("uk", [P, T]), sb("bk", [P, 2, P]), sb("ck", [P, 3, P])
        ta, tb = sb("ta", [P, 2, A]), sb("tb", [P, 2, 32])
        turn, tt = sb("turn", [P, NT, 2, T]), sb("tt", [P, 2, T])
        w, m = sb("w", [P, 2, T]), sb("m", [P, 2, T])
        z = sb("z", [P, 2, T])
        pr = k.h[:].rearrange("p (b n) t -> p b n t", b=2)
        q = sb("q", [P, 3, T])

        @block.sync
        def _(sp):
            k.clear(sp)

        @block.gpsimd
        def _(pool):
            with pool.Fori(0, KD) as i:
                step = Steps(pool, s["table_step"], TABLE_STEPS * NT * i)
                for j in range(NT):
                    tile = bass.ds(NT * i + j, 1)
                    step(pool.tensor_copy(ta[:], tab.turn_a[:, :, tile, 0:A].rearrange("p r o a -> p r (o a)")))
                    step(pool.tensor_copy(tb[:], tab.turn_b[:, :, tile, :].rearrange("p r o b -> p r (o b)")))
                    pool.wait_ge(s["products_done"], NT + NT * i + j - (NT - 1))
                    ar, ai = (ta[:, r, :].rearrange("p (a b) -> p a b", b=1).to_broadcast([P, A, 32]) for r in range(2))
                    br, bi = (tb[:, r:r + 1, :].to_broadcast([P, A, 32]) for r in range(2))
                    c, sn = (turn[:, j, r, :].rearrange("p (a b) -> p a b", a=A) for r in range(2))
                    t = [tt[:, r, :].rearrange("p (a b) -> p a b", a=A) for r in range(2)]
                    step.start(pool.tensor_tensor(c, ar, br, ALU.mult))
                    first = step.start(pool.tensor_tensor(t[0], ai, bi, ALU.mult))
                    step.start(pool.tensor_tensor(sn, ar, bi, ALU.mult))
                    second = step.start(pool.tensor_tensor(t[1], ai, br, ALU.mult))
                    step.after(first)
                    pool.tensor_tensor(c, c, t[0], ALU.subtract).then_inc(s["table_done"], 1)
                    step.after(second)
                    pool.tensor_tensor(sn, sn, t[1], ALU.add).then_inc(s["table_done"], 1)
                    pool.wait_ge(s["table_done"], 2 * (NT * i + j + 1))
                assert step.n == TABLE_STEPS * NT

        @block.tensor
        def _(pe):
            with pe.Fori(0, KD) as i:
                pe.wait_ge(s["staged"], 2 * (i + 1))

                def inputs(j):
                    if j >= 2:
                        pe.wait_ge(s["table_used"], 1 + NT * i + j - 1)
                    else:
                        pe.wait_ge(s["table_used"], 1 + NT * i)
                    rows = slice(32 * j, 32 * j + 32)
                    for r in range(2):
                        mm = pe.matmul(ps[:, 2 * (j % 2) + r, :], bk[rows, r, :], uk[rows, :], start=True, stop=True)
                    mm.then_inc(s["bu_done"], 1)

                inputs(0)
                pe.wait_ge(s["c_staged"], i + 1)
                pe.wait_ge(s["y_out"], 1 + i)
                for j in range(NT):
                    if j + 1 < NT:
                        inputs(j + 1)
                    pe.wait_ge(s["products_done"], NT + NT * i + j + 1)
                    rows = slice(32 * j, 32 * j + 32)
                    for n, r in enumerate((0, 1, 2, 2)):
                        mm = pe.matmul(ps[rows, 4, :], ck[:, r, 32 * j:32 * j + 32], pr[:, j % 2, n, :], start=(n == 0), stop=(n == 3))
                    mm.then_inc(s["y_done"], 1)

        @block.scalar
        def _(act):
            def sigmoid(act, c):
                act.wait_ge(s["inner_done"], c + 1)
                act.activation(q[:, c % 3], q[:, c % 3], ACT.Sigmoid, scale=GELU).then_inc(s["sig_done"], 1)

            with act.Fori(0, KD) as i:
                act.wait_ge(s["bu_done"], 1 + NT * i)
                act.activation(uk[:], u[:, bass.ds(i, 1), :].rearrange("p o t -> p (o t)"), ACT.Copy).then_inc(s["staged"], 1)
                act.activation(bk[:], tab.b_t[:, :, bass.ds(i, 1), :].rearrange("p r o n -> p r (o n)"), ACT.Copy).then_inc(s["staged"], 1)
                act.wait_ge(s["y_done"], 1 + NT * i)
                act.activation(ck[:], tab.c_t[:, :, bass.ds(i, 1), :].rearrange("p r o n -> p r (o n)"), ACT.Copy).then_inc(s["c_staged"], 1)
            for c in range(KD):
                act.wait_ge(s["y_out"], 1 + c + 1)
                if c >= 3:
                    act.wait_ge(s["g_done"], c - 2)
                act.activation(q[:, c % 3], g[:, c, :], ACT.Square).then_inc(s["sq_done"], 1)
                if c >= 1:
                    sigmoid(act, c - 1)
            sigmoid(act, KD - 1)

        @block.vector
        def _(dve):
            with dve.Fori(0, KD) as i:
                step = Steps(dve, s["vec_step"], VEC * i)
                for j in range(NT):
                    c, sn = turn[:, j, 0, :], turn[:, j, 1, :]
                    br, bi = ps[:, 2 * (j % 2), :], ps[:, 2 * (j % 2) + 1, :]
                    dve.wait_ge(s["table_done"], 2 * (NT * i + j + 1))
                    dve.wait_ge(s["bu_done"], 1 + NT * i + j + 1)
                    step.start(dve.tensor_tensor(w[:, 0, :], c, br, ALU.mult))
                    re = step.start(dve.tensor_tensor(m[:, 0, :], sn, bi, ALU.mult))
                    step.start(dve.tensor_tensor(w[:, 1, :], c, bi, ALU.mult))
                    dve.tensor_tensor(m[:, 1, :], sn, br, ALU.mult).then_inc(s["table_used"], 1)
                    step.after(re)
                    re = step.start(dve.tensor_tensor(w[:, 0, :], w[:, 0, :], m[:, 0, :], ALU.add))
                    dve.wait_ge(s["table_used"], 1 + NT * i + j + 1)
                    im = step.start(dve.tensor_tensor(w[:, 1, :], w[:, 1, :], m[:, 1, :], ALU.subtract))
                    mag = tab.mag[:, bass.ds(NT * i + j, 1)].to_broadcast([P, T])
                    step.after(re)
                    re = step.start(dve.tensor_tensor_scan(z[:, 0, :], mag, w[:, 0, :], 0.0, ALU.mult, ALU.add))
                    step.after(im)
                    im = step.start(dve.tensor_tensor_scan(z[:, 1, :], mag, w[:, 1, :], 0.0, ALU.mult, ALU.add))
                    if j >= 2:
                        dve.wait_ge(s["y_done"], 1 + NT * i + j - 1)
                    step.after(re)
                    step.start(dve.tensor_tensor(pr[:, j % 2, 0, :], c, z[:, 0, :], ALU.mult))
                    step.start(dve.tensor_tensor(pr[:, j % 2, 3, :], sn, z[:, 0, :], ALU.mult))
                    step.after(im)
                    dve.tensor_tensor(pr[:, j % 2, 1, :], sn, z[:, 1, :], ALU.mult)
                    dve.tensor_tensor(pr[:, j % 2, 2, :], c, z[:, 1, :], ALU.mult).then_inc(s["products_done"], 1)
                dve.wait_ge(s["y_done"], 1 + NT * (i + 1))
                dve.scalar_tensor_tensor(out=g[:, bass.ds(i, 1), :], in0=u[:, bass.ds(i, 1), :],
                                         scalar=k.cols[:, bass.ds(k.places["ssm_d_2"][0] + i, 1)], in1=ps[:, 4:5, :],
                                         op0=ALU.mult, op1=ALU.add).then_inc(s["y_out"], 1)
                assert step.n == VEC, step.n
            step = Steps(dve, s["vec_step"], VEC * KD)

            def gated(c):
                dve.wait_ge(s["sig_done"], c + 1)
                dve.tensor_tensor(g[:, c, :], g[:, c, :], q[:, c % 3], ALU.mult).then_inc(s["g_done"], 1)

            dve.wait_ge(s["y_out"], 1 + KD)
            for c in range(KD):
                dve.wait_ge(s["sq_done"], c + 1)
                step(dve.tensor_scalar(q[:, c % 3], q[:, c % 3], 0.044715, 1.0, ALU.mult, ALU.add))
                dve.tensor_tensor(q[:, c % 3], q[:, c % 3], g[:, c, :], ALU.mult).then_inc(s["inner_done"], 1)
                if c >= 1:
                    gated(c - 1)
            gated(KD - 1)


def project_stage(k, name, w, dst):
    ps = k.ps
    with k.stage(name, "copied", *SplitProducts.SEMS, primed=SplitProducts.PRIMED) as (block, s, sb):
        lin = SplitLinear(k, block, s, sb, w, k.h)

        @block.scalar
        def _(act):
            def copy(n):
                act.wait_ge(s["half_used"], 1 + n + 1)
                for c in range(n * HT, (n + 1) * HT):
                    act.activation(dst[:, c, :], ps[:, c, :], ACT.Copy).then_inc(s["copied"], 1)

            lin.scalar(act, copy)

        @block.vector
        def _(dve):
            lin.vector(dve)


def glu_stage(k, g, z):
    ps, w = k.ps, k.ins["ssm_w_glu_2"][0]
    with k.stage("glu", "sig_done", "gated", *SplitProducts.SEMS, primed=SplitProducts.PRIMED) as (block, s, sb):
        lin = SplitLinear(k, block, s, sb, w, g)
        sig = sb("sig", [P, 2, T])

        @block.scalar
        def _(act):
            def sigmoid(n):
                act.wait_ge(s["half_used"], 1 + n + 1)
                for c in range(n * HT, (n + 1) * HT):
                    if c >= 2:
                        act.wait_ge(s["gated"], c - 1)
                    act.activation(sig[:, c % 2, :], ps[:, c, :], ACT.Sigmoid, bias=k.col("ssm_b_glu_2", c)).then_inc(s["sig_done"], 1)

            lin.scalar(act, sigmoid)

        @block.vector
        def _(dve):
            def gated(n):
                for c in range(n * HT, (n + 1) * HT):
                    dve.wait_ge(s["sig_done"], c + 1)
                    dve.tensor_tensor(z[:, c, :], g[:, c, :], sig[:, c % 2, :], ALU.mult).then_inc(s["gated"], 1)

            lin.vector(dve, gated)


def second_block(k):
    col = lambda name, layer: (lambda c: k.col(name, layer * KD + c))
    norm = ("norm_ffn", k.x, col("ln_ffn_g", 0), col("ln_ffn_b", 0))
    for layer in range(2):
        mix, ffn = 48 + 24 * layer, 96 + 24 * layer
        with ExitStack() as branch:
            sb = lambda n, shape: k.sb(n, shape, stack=branch)
            k.h = sb(f"h{layer + 1}", [P, KD, T])
            norm_stage(k, *norm, also=(k.h, lambda c: k.mod[:, mix + KD + c:mix + KD + c + 1], lambda c: k.mod[:, mix + c:mix + c + 1]))
            if layer == 0:
                cq, ckv, k_pe = sb("cq", [P, QL // P, T]), sb("ckv", [P, T]), sb("k_pe", [ROPE, T])
                cos, sin = sb("cos", [ROPE, T]), sb("sin", [ROPE, T])
                o = sb("latent_out", [P, KD, T])
                latent_stage(k, cq, ckv, k_pe, cos, sin)
                latent_attention_stage(k, cq, ckv, k_pe, cos, sin, o)
                residual_stage(k, "latent_proj", k.ins["mla_w_o_2"][0], o, ALPHA_2, mix + 16)
            else:
                g = sb("g", [P, KD, T])
                with ExitStack() as scan:
                    u = k.sb("u", [P, KD, T], stack=scan)
                    project_stage(k, "s5_in", k.ins["ssm_w_in_2"][0], u)
                    tab = S5Tables(lambda n, shape: k.sb(n, shape, stack=scan))
                    s5_tables_stage(k, tab)
                    s5_scan_stage(k, tab, u, g)
                z = sb("z", [P, KD, T])
                glu_stage(k, g, z)
                residual_stage(k, "s5_proj", k.ins["ssm_w_out_2"][0], z, ALPHA_2, mix + 16)
        norm_stage(k, f"norm_mix{layer}", k.x, col("ln_mix_g_2", layer), col("ln_mix_b_2", layer))
        mlp_stage(k, f"mlp{layer}", layer, ffn)
        norm = (f"norm_ffn{layer}", k.x, col("ln_ffn_g_2", layer), col("ln_ffn_b_2", layer))
    norm_stage(k, *norm)


def build(nc, ins, out):
    with ExitStack() as stack:
        k = Kernel(nc, stack, ins)
        constant_tiles(k)
        with ExitStack() as strips:
            k.w = k.sb("w", [P, 3, KD * STRIP], stack=strips)
            constants_stage(k)
            modulation_stage(k)
            mod = lambda first: (lambda c: k.mod[:, first + c:first + c + 1])
            with ExitStack() as block:
                k.h = k.sb("h", [P, KD, T], stack=block)
                norm_stage(k, "norm_in", k.h, mod(8), mod(0))
                with ExitStack() as mix:
                    merged = k.sb("merged", [P, KD, T], stack=mix)
                    forget_stage(k)
                    with ExitStack() as branch:
                        o = k.sb("attended", [P, KD, T], stack=branch)
                        attention_stage(k, o)
                        merge_stage(k, "merge_att", 0, k.ins["w_attn_o"][0], o, KD, merged)
                    with ExitStack() as branch:
                        pooled = k.sb("pooled", [P, KD, T], stack=branch)
                        pool_stage(k, pooled)
                        pool_out_stage(k, pooled, merged)
                    with ExitStack() as branch:
                        ys = k.sb("ys", [P, KI, T], stack=branch)
                        ssm_stage(k, ys)
                        merge_stage(k, "merge_ssm", 2, k.ins["w_ssm_o"][0], ys, KI, merged)
                    residual_stage(k, "mix_out", k.ins["w_out"][0], merged, ALPHA_1, 16)
                norm_stage(k, "norm_mix", k.x, lambda c: k.col("ln_mix_g", c), lambda c: k.col("ln_mix_b", c), sum_next=True)
                norm_stage(k, "norm_ffn_in", k.h, mod(32), mod(24))
                with ExitStack() as ffn:
                    handed = Dispatch(k, ffn)
                    router_stage(k, handed.chosen, handed.share)
                    dispatch_stage(k, handed)
                    experts_stage(k, handed)
                    combine_stage(k, handed, 40)
        k.w = k.sb("w_second", [P, 2, KD * STRIP])
        second_block(k)
        output_stage(k, out)


_INS = ["x", "c", "w_in", "b_forget", "w_attn_o", "w_pool", "pool_scale", "conv_w", "conv_b", "dt_bias", "a_log", "d_skip",
        "ssm_norm_w", "w_ssm_o", "w_out", "w_ada", "b_ada", "ln_mix_g", "ln_mix_b", "ln_ffn_g", "ln_ffn_b", "w_router",
        "b_router", "w_exp_gate", "w_exp_up", "w_exp_down", "c_2", "positions_2", "mla_w_in_2", "mla_q_norm_2", "mla_w_qb_2",
        "mla_kv_norm_2", "mla_w_kvb_2", "mla_w_o_2", "ssm_w_in_2", "ssm_log_dt_2", "ssm_a_re_2", "ssm_a_im_2", "ssm_b_re_2",
        "ssm_b_im_2", "ssm_c_re_2", "ssm_c_im_2", "ssm_d_2", "ssm_w_glu_2", "ssm_b_glu_2", "ssm_w_out_2", "mlp_w1_2", "mlp_b1_2",
        "mlp_w2_2", "mlp_b2_2", "mod_mix_w_2", "mod_mix_b_2", "mod_ffn_w_2", "mod_ffn_b_2", "ln_mix_g_2", "ln_mix_b_2",
        "ln_ffn_g_2", "ln_ffn_b_2"]


def kernel(**inputs):
    import numpy as _np
    import concourse.bacc as _bacc
    from concourse import mybir as _mybir
    from concourse.bass_utils import run_bass_kernel_spmd as _run

    nc = _bacc.Bacc("TRN2", target_bir_lowering=False, num_devices=1)
    arrays, ins = {}, {}
    for name in _INS:
        a = _np.ascontiguousarray(inputs[name])
        arrays[f"in_{name}_dram"] = a
        ins[name] = nc.dram_tensor(f"in_{name}_dram", a.shape, _mybir.dt.from_np(a.dtype), kind="ExternalInput").ap()
    out = nc.dram_tensor("out_0_dram", (1, T, D), F32, kind="ExternalOutput").ap()
    build(nc, ins, out)
    r = _run(nc, [arrays], core_ids=[0])
    return r.results[0]["out_0_dram"]
```
